# Optimizing a Trainium2 kernel written in Bass

```python
import math
import jax, jax.numpy as jnp
from jax import lax
import numpy as np

D_MODEL = 1024
BATCH = 1
SEQ = 1024
DEPTH = 1
DEC_BATCH = 8
DEC_SEQ = 8
PAST_LEN = 4096
PAGE_SIZE = 128

HG_HEADS = 4
HG_DIM = 128
HG_WIDTH = HG_HEADS * HG_DIM
HG_CHUNK = 64
LB_FLOOR = 1e-30
S5_GROUP = 16
S5_GROUPS = 32
S5_WIDTH = S5_GROUP * S5_GROUPS
S5_STATE = 64
NSA_HEADS = 8
NSA_KV = 2
NSA_REP = NSA_HEADS // NSA_KV
HEAD_DIM = 64
NSA_WIDTH = NSA_HEADS * HEAD_DIM
CMP_LEN = 32
CMP_STRIDE = 16
CMP_HIDDEN = 128
SEL_BLOCK = 64
SEL_TOPN = 16
SEL_QBLK = 64
WINDOW = 512
WIN_QBLK = 128
N_BUCKETS = 32
MAX_DIST = 128
N_BRANCH = 3
BR_WIDTH = 512
D_FF = -(-8 * D_MODEL // (3 * 256)) * 256
KV_W = NSA_KV * HEAD_DIM
IN_SPLITS = (HG_WIDTH, HG_WIDTH, HG_WIDTH, HG_WIDTH, S5_WIDTH, NSA_WIDTH, KV_W, KV_W, KV_W, KV_W, KV_W, KV_W, 3 * NSA_HEADS, D_MODEL, D_MODEL, D_MODEL)
N_IN = sum(IN_SPLITS)
IN_OFFSETS = tuple(sum(IN_SPLITS[:i + 1]) for i in range(len(IN_SPLITS) - 1))
NEG = -1e30
FORCE = 1e9
F32 = jnp.float32

kernel_name = "hgrn2_s5_nsa_gated_hybrid_step"

def rms_norm(x, g, eps=1e-6):
    xf = x.astype(F32)
    y = xf * lax.rsqrt(jnp.mean(xf * xf, axis=-1, keepdims=True) + eps)
    return (y * g.astype(F32)).astype(x.dtype)

def rel_bucket(dist):
    n = jnp.maximum(dist, 0)
    exact = N_BUCKETS // 2
    nf = jnp.maximum(n, 1).astype(F32)
    large = exact + (jnp.log(nf / exact) / math.log(MAX_DIST / exact) * (N_BUCKETS - exact)).astype(jnp.int32)
    return jnp.where(n < exact, n, jnp.minimum(large, N_BUCKETS - 1))

def hgrn2_scan(q, log_f, k, v, s0):
    B, T, H, _ = q.shape
    C = math.gcd(T, HG_CHUNK)
    n = T // C

    def chunks(a):
        return a.reshape(B, n, C, H, a.shape[-1]).transpose(1, 0, 3, 2, 4)

    causal = jnp.tril(jnp.ones((C, C), dtype=bool))[:, :, None]

    def step(S, inp):
        qc, gc, kc, vc = inp
        G = jnp.cumsum(gc, axis=2)
        decay = jnp.exp(jnp.where(causal, G[:, :, :, None, :] - G[:, :, None, :, :], NEG))
        attn = jnp.einsum("bhtd,bhtsd,bhsd->bhts", qc, decay, kc)
        o = attn @ vc + jnp.einsum("bhtd,bhdv->bhtv", qc * jnp.exp(G), S)
        g_end = G[:, :, -1]
        S = jnp.exp(g_end)[..., None] * S + jnp.einsum("bhsd,bhsv->bhdv", kc * jnp.exp(g_end[:, :, None] - G), vc)
        return S, o

    S, o = lax.scan(step, s0, (chunks(q), chunks(log_f), chunks(k), chunks(v)))
    return o.transpose(1, 0, 3, 2, 4).reshape(B, T, H, -1), S

def _complex_affine_combine(e1, e2):
    ar1, ai1, br1, bi1 = e1
    ar2, ai2, br2, bi2 = e2
    return (ar1 * ar2 - ai1 * ai2, ar1 * ai2 + ai1 * ar2,
            ar2 * br1 - ai2 * bi1 + br2, ar2 * bi1 + ai2 * br1 + bi2)

def s5_layer(u, a_re, a_im, log_dt, b_re, b_im, c_re, c_im, d, w_glu, h0_re, h0_im):
    B, T, _ = u.shape
    uf = u.astype(F32)
    ug = uf.reshape(B, T, S5_GROUPS, S5_GROUP)
    a_re, a_im = a_re.astype(F32), a_im.astype(F32)
    step = jnp.exp(log_dt.astype(F32))[:, None]
    mag = jnp.exp(a_re * step)
    ab_re, ab_im = mag * jnp.cos(a_im * step), mag * jnp.sin(a_im * step)
    den = a_re * a_re + a_im * a_im
    z_re = ((ab_re - 1.0) * a_re + ab_im * a_im) / den
    z_im = (ab_im * a_re - (ab_re - 1.0) * a_im) / den
    b_re, b_im = b_re.astype(F32), b_im.astype(F32)
    bb_re = z_re[..., None] * b_re - z_im[..., None] * b_im
    bb_im = z_re[..., None] * b_im + z_im[..., None] * b_re
    x_re = jnp.einsum("gpn,btgn->btgp", bb_re, ug)
    x_im = jnp.einsum("gpn,btgn->btgp", bb_im, ug)
    a_re_t = jnp.broadcast_to(ab_re, (1, T) + ab_re.shape)
    a_im_t = jnp.broadcast_to(ab_im, (1, T) + ab_im.shape)
    cum_re, cum_im, h_re, h_im = lax.associative_scan(_complex_affine_combine, (a_re_t, a_im_t, x_re, x_im), axis=1)
    h0r, h0i = h0_re[:, None], h0_im[:, None]
    h_re, h_im = h_re + cum_re * h0r - cum_im * h0i, h_im + cum_re * h0i + cum_im * h0r
    y = jnp.einsum("gnp,btgp->btgn", c_re.astype(F32), h_re) - jnp.einsum("gnp,btgp->btgn", c_im.astype(F32), h_im)
    y = jax.nn.gelu(y.reshape(B, T, S5_WIDTH) + d.astype(F32) * uf)
    y = y * jax.nn.sigmoid(y @ w_glu.astype(F32))
    return y.astype(u.dtype), h_re[:, -1], h_im[:, -1]

def compress(rows, pe, w1, w2):
    B, L = rows.shape[:2]
    r = CMP_LEN // CMP_STRIDE
    nc = L // CMP_STRIDE
    nb = nc - r + 1
    ch = rows[:, :nc * CMP_STRIDE].reshape(B, nc, CMP_STRIDE, NSA_KV, HEAD_DIM)
    blk = jnp.concatenate([ch[:, j:j + nb] for j in range(r)], axis=2) + pe[:, None, :]
    flat = blk.transpose(0, 1, 3, 2, 4).reshape(B, nb, NSA_KV, CMP_LEN * HEAD_DIM)
    return jax.nn.gelu(flat @ w1) @ w2

def attend_dense(qg, k, v, dist, valid, rel_bias):
    T, N = dist.shape
    bias = rel_bias.astype(F32)[rel_bucket(dist)].reshape(T, N, NSA_KV, NSA_REP).transpose(2, 3, 0, 1)
    s = jnp.einsum("btgrd,bngd->bgrtn", qg, k, preferred_element_type=F32) + bias
    s = jnp.where(valid, s, NEG)
    p = jax.nn.softmax(s, axis=-1) * jnp.any(valid, axis=-1)[:, None].astype(F32)
    o = jnp.einsum("bgrtn,bngd->btgrd", p.astype(v.dtype), v)
    return o, p

def select_blocks(imp, qpos, n_sel):
    nb = imp.shape[-1]
    cs = jnp.arange(nb) * CMP_STRIDE
    ss = jnp.arange(n_sel) * SEL_BLOCK
    overlap = ((cs[:, None] < ss[None, :] + SEL_BLOCK) & (cs[:, None] + CMP_LEN > ss[None, :])).astype(F32)
    score = jnp.einsum("bgtn,nj->bgtj", imp, overlap)
    cur = (qpos // SEL_BLOCK)[:, None]
    j = jnp.arange(n_sel)[None, :]
    forced = (j == 0) | (j == cur) | (j == cur - 1)
    future = ss[None, :] > qpos[:, None]
    score = jnp.where(forced, FORCE, jnp.where(future, -FORCE, score))
    _, idx = lax.top_k(score, min(SEL_TOPN, n_sel))
    return idx

def sel_attend_chunk(qg, qpos, idx, kb, vb, rel_bias):
    B = qg.shape[0]
    bi = jnp.arange(B)[:, None, None, None]
    gi = jnp.arange(NSA_KV)[None, :, None, None]
    ks = kb[bi, gi, idx]
    vs = vb[bi, gi, idx]
    kpos = idx[..., None] * SEL_BLOCK + jnp.arange(SEL_BLOCK)
    dist = qpos[None, None, :, None, None] - kpos
    tbl = rel_bias.astype(F32).reshape(N_BUCKETS * NSA_KV, NSA_REP)
    bias = tbl[rel_bucket(dist) * NSA_KV + gi[..., None]]
    s = jnp.einsum("bqgrd,bgqknd->bgqknr", qg, ks, preferred_element_type=F32) + bias
    s = jnp.where((dist >= 0)[..., None], s, NEG)
    p = jax.nn.softmax(s, axis=(3, 4))
    return jnp.einsum("bgqknr,bgqknd->bqgrd", p.astype(vs.dtype), vs)

def sel_attend(qg, qpos, idx, kb, vb, rel_bias):
    B, T = qg.shape[:2]
    qc = math.gcd(T, SEL_QBLK)
    n = T // qc
    K = idx.shape[-1]
    q_ch = qg.reshape(B, n, qc, NSA_KV, NSA_REP, HEAD_DIM).swapaxes(0, 1)
    p_ch = qpos.reshape(n, qc)
    i_ch = idx.reshape(B, NSA_KV, n, qc, K).transpose(2, 0, 1, 3, 4)
    o = lax.map(lambda c: sel_attend_chunk(c[0], c[1], c[2], kb, vb, rel_bias), (q_ch, p_ch, i_ch))
    return o.swapaxes(0, 1).reshape(B, T, NSA_KV, NSA_REP, HEAD_DIM)

def win_attend_prompt(qg, k, v, rel_bias):
    B, T = qg.shape[:2]
    wq = math.gcd(T, WIN_QBLK)
    nq = T // wq
    nprev = -(-WINDOW // wq)
    pad = nprev * wq
    padw = ((0, 0), (pad, 0), (0, 0), (0, 0))
    kp = jnp.pad(k, padw).reshape(B, nq + nprev, wq, NSA_KV, HEAD_DIM)
    vp = jnp.pad(v, padw).reshape(B, nq + nprev, wq, NSA_KV, HEAD_DIM)
    kw = jnp.concatenate([kp[:, j:j + nq] for j in range(nprev + 1)], axis=2)
    vw = jnp.concatenate([vp[:, j:j + nq] for j in range(nprev + 1)], axis=2)
    kw_len = (nprev + 1) * wq
    i = jnp.arange(wq)[:, None]
    jj = jnp.arange(kw_len)[None, :]
    dist = i + pad - jj
    kpos = jnp.arange(nq)[:, None] * wq - pad + jj
    valid = ((dist >= 0) & (dist < WINDOW))[None] & (kpos >= 0)[:, None, :]
    bias = rel_bias.astype(F32)[rel_bucket(dist)].reshape(wq, kw_len, NSA_KV, NSA_REP).transpose(2, 3, 0, 1)
    qb = qg.reshape(B, nq, wq, NSA_KV, NSA_REP, HEAD_DIM)
    s = jnp.einsum("bqigrd,bqjgd->bqgrij", qb, kw, preferred_element_type=F32) + bias
    s = jnp.where(valid[:, None, None], s, NEG)
    p = jax.nn.softmax(s, axis=-1)
    o = jnp.einsum("bqgrij,bqjgd->bqigrd", p.astype(vw.dtype), vw)
    return o.reshape(B, T, NSA_KV, NSA_REP, HEAD_DIM)

def layer_forward(x, past, lb, rel_bias, w):
    B, T, _ = x.shape
    dt = x.dtype
    p0 = 0 if past is None else past["kv"].shape[1]
    qpos = p0 + jnp.arange(T, dtype=jnp.int32)
    xn = rms_norm(x, w["norm_mix"])
    (hq, hf, hi, hg, su, nq, kc, vc, ksl, vsl, kwn, vwn, ngate, ga, gb, gc) = jnp.split(xn @ w["w_in"], IN_OFFSETS, axis=-1)

    fp = hf.astype(F32)
    log_f = jnp.logaddexp(jnp.log(jnp.maximum(lb, LB_FLOOR)), jnp.log1p(-lb) + jax.nn.log_sigmoid(fp))
    k_in = (1.0 - lb) * jax.nn.sigmoid(-fp)
    hs = (B, T, HG_HEADS, HG_DIM)
    s0 = jnp.zeros((B, HG_HEADS, HG_DIM, HG_DIM), F32) if past is None else past["hgrn"].astype(F32)
    o_hg, s_hg = hgrn2_scan(jax.nn.silu(hq.astype(F32)).reshape(hs), log_f.reshape(hs), k_in.reshape(hs), hi.astype(F32).reshape(hs), s0)
    o_a = (rms_norm(o_hg, w["hg_out_norm"]) * jax.nn.silu(hg.astype(F32)).reshape(hs)).reshape(B, T, HG_WIDTH).astype(dt)

    if past is None:
        h0_re = jnp.zeros((B, S5_GROUPS, S5_STATE), F32)
        h0_im = jnp.zeros((B, S5_GROUPS, S5_STATE), F32)
    else:
        h0_re, h0_im = past["s5_re"].astype(F32), past["s5_im"].astype(F32)
    o_b, s5_re, s5_im = s5_layer(su, w["s5_a_re"], w["s5_a_im"], w["s5_log_dt"], w["s5_b_re"], w["s5_b_im"],
                                 w["s5_c_re"], w["s5_c_im"], w["s5_d"], w["s5_w_glu"], h0_re, h0_im)

    qkn = w["nsa_qk_norm"]
    kvs = (B, T, NSA_KV, HEAD_DIM)
    q = (rms_norm(nq.reshape(B, T, NSA_HEADS, HEAD_DIM), qkn[0]) * HEAD_DIM ** -0.5).reshape(B, T, NSA_KV, NSA_REP, HEAD_DIM)
    k_sel = rms_norm(ksl.reshape(kvs), qkn[2])
    k_win = rms_norm(kwn.reshape(kvs), qkn[3])
    v_win = vwn.reshape(kvs)
    new_kv = jnp.stack([kc.reshape(kvs), vc.reshape(kvs), k_sel, vsl.reshape(kvs)], axis=2)
    full = new_kv if past is None else jnp.concatenate([past["kv"].astype(dt), new_kv], axis=1)
    L = full.shape[1]
    k_cmp = rms_norm(compress(full[:, :, 0], w["cmp_pe"][0], w["cmp_w1"][0], w["cmp_w2"][0]), qkn[1])
    v_cmp = compress(full[:, :, 1], w["cmp_pe"][1], w["cmp_w1"][1], w["cmp_w2"][1])
    kend = jnp.arange(k_cmp.shape[1]) * CMP_STRIDE + CMP_LEN - 1
    dist_c = qpos[:, None] - kend[None, :]
    o_cmp, p_cmp = attend_dense(q, k_cmp, v_cmp, dist_c, dist_c >= 0, rel_bias)
    n_sel = -(-L // SEL_BLOCK)
    idx = select_blocks(p_cmp.sum(axis=2), qpos, n_sel)
    sel = jnp.pad(full[:, :, 2:4], ((0, 0), (0, n_sel * SEL_BLOCK - L), (0, 0), (0, 0), (0, 0)))
    kb = sel[:, :, 0].reshape(B, n_sel, SEL_BLOCK, NSA_KV, HEAD_DIM).transpose(0, 3, 1, 2, 4)
    vb = sel[:, :, 1].reshape(B, n_sel, SEL_BLOCK, NSA_KV, HEAD_DIM).transpose(0, 3, 1, 2, 4)
    o_sel = sel_attend(q, qpos, idx, kb, vb, rel_bias)
    kv_win = jnp.stack([k_win, v_win], axis=2)
    if past is None:
        o_win = win_attend_prompt(q, k_win, v_win, rel_bias)
        new_win = kv_win[:, T - min(WINDOW, T):]
    else:
        lw = past["win"].shape[1]
        buf = jnp.concatenate([past["win"].astype(dt), kv_win], axis=1)
        kpos = p0 - lw + jnp.arange(lw + T, dtype=jnp.int32)
        dist_w = qpos[:, None] - kpos[None, :]
        o_win, _ = attend_dense(q, buf[:, :, 0], buf[:, :, 1], dist_w, (dist_w >= 0) & (dist_w < WINDOW), rel_bias)
        new_win = buf[:, T:]
    g = jax.nn.sigmoid(ngate.astype(F32)).reshape(B, T, 3, NSA_KV, NSA_REP)[..., None]
    o_c = (g[:, :, 0] * o_cmp + g[:, :, 1] * o_sel + g[:, :, 2] * o_win).reshape(B, T, NSA_WIDTH).astype(dt)

    wb = w["w_branch"]
    m = jax.nn.sigmoid(ga) * (o_a @ wb[0]) + jax.nn.sigmoid(gb) * (o_b @ wb[1]) + jax.nn.sigmoid(gc) * (o_c @ wb[2])
    x = x + m @ w["w_out"]

    gate, up = jnp.split(rms_norm(x, w["norm_ffn"]) @ w["w_gate_up"], [D_FF], axis=-1)
    x = x + (jax.nn.silu(gate) * up) @ w["w_down"]
    return x, (new_kv, new_win.astype(dt), s_hg.astype(dt), s5_re.astype(dt), s5_im.astype(dt))

def setup_inputs(seed: int = 0) -> dict:
    key = jax.random.key(seed)
    ks = iter(jax.random.split(key, 40))

    def nrm(shape, scale=1.0):
        return scale * jax.random.normal(next(ks), shape, F32)

    n_pages = PAST_LEN // PAGE_SIZE
    n_used = DEC_BATCH * n_pages
    n_phys = n_used + -(-n_used // 4)
    win_len = min(WINDOW, PAST_LEN)
    x_prompt = nrm((BATCH, SEQ, D_MODEL))
    x_sample = nrm((DEC_BATCH, DEC_SEQ, D_MODEL))
    cache_nsa_kv = nrm((DEPTH, n_phys, PAGE_SIZE, 4, NSA_KV, HEAD_DIM))
    cache_win_kv = nrm((DEPTH, DEC_BATCH, win_len, 2, NSA_KV, HEAD_DIM))
    state_hgrn = nrm((DEPTH, DEC_BATCH, HG_HEADS, HG_DIM, HG_DIM), 0.5)
    state_s5_re = nrm((DEPTH, DEC_BATCH, S5_GROUPS, S5_STATE), 0.1)
    state_s5_im = nrm((DEPTH, DEC_BATCH, S5_GROUPS, S5_STATE), 0.1)
    page_table = jax.random.permutation(next(ks), n_phys)[:n_used].reshape(DEC_BATCH, n_pages).astype(jnp.int32)
    norm_mix = 1.0 + nrm((DEPTH, D_MODEL), 0.02)
    w_in = nrm((DEPTH, D_MODEL, N_IN), D_MODEL ** -0.5)
    hg_lb_logits = nrm((DEPTH, HG_WIDTH), 0.1)
    hg_out_norm = 1.0 + nrm((DEPTH, HG_DIM), 0.02)
    s5_a_re = -0.5 + nrm((DEPTH, S5_GROUPS, S5_STATE), 0.01)
    s5_a_im = jnp.pi * jnp.arange(S5_STATE, dtype=F32) + nrm((DEPTH, S5_GROUPS, S5_STATE), 0.01)
    s5_log_dt = jax.random.uniform(next(ks), (DEPTH, S5_GROUPS), F32, math.log(1e-3), math.log(1e-1))
    s5_b_re = nrm((DEPTH, S5_GROUPS, S5_STATE, S5_GROUP), (2 * S5_GROUP) ** -0.5)
    s5_b_im = nrm((DEPTH, S5_GROUPS, S5_STATE, S5_GROUP), (2 * S5_GROUP) ** -0.5)
    s5_c_re = nrm((DEPTH, S5_GROUPS, S5_GROUP, S5_STATE), S5_STATE ** -0.5)
    s5_c_im = nrm((DEPTH, S5_GROUPS, S5_GROUP, S5_STATE), S5_STATE ** -0.5)
    s5_d = nrm((DEPTH, S5_WIDTH))
    s5_w_glu = nrm((DEPTH, S5_WIDTH, S5_WIDTH), S5_WIDTH ** -0.5)
    nsa_qk_norm = 1.0 + nrm((DEPTH, 4, HEAD_DIM), 0.02)
    cmp_pe = nrm((DEPTH, 2, CMP_LEN, HEAD_DIM), 0.02)
    cmp_w1 = nrm((DEPTH, 2, CMP_LEN * HEAD_DIM, CMP_HIDDEN), (CMP_LEN * HEAD_DIM) ** -0.5)
    cmp_w2 = nrm((DEPTH, 2, CMP_HIDDEN, HEAD_DIM), CMP_HIDDEN ** -0.5)
    rel_bias = nrm((N_BUCKETS, NSA_HEADS), 0.5)
    w_branch = nrm((DEPTH, N_BRANCH, BR_WIDTH, D_MODEL), BR_WIDTH ** -0.5)
    w_out = nrm((DEPTH, D_MODEL, D_MODEL), D_MODEL ** -0.5)
    norm_ffn = 1.0 + nrm((DEPTH, D_MODEL), 0.02)
    w_gate_up = nrm((DEPTH, D_MODEL, 2 * D_FF), D_MODEL ** -0.5)
    w_down = nrm((DEPTH, D_FF, D_MODEL), D_FF ** -0.5)
    return {"x_prompt": x_prompt, "x_sample": x_sample, "cache_nsa_kv": cache_nsa_kv, "cache_win_kv": cache_win_kv,
            "state_hgrn": state_hgrn, "state_s5_re": state_s5_re, "state_s5_im": state_s5_im, "page_table": page_table,
            "norm_mix": norm_mix, "w_in": w_in, "hg_lb_logits": hg_lb_logits, "hg_out_norm": hg_out_norm,
            "s5_a_re": s5_a_re, "s5_a_im": s5_a_im, "s5_log_dt": s5_log_dt, "s5_b_re": s5_b_re, "s5_b_im": s5_b_im,
            "s5_c_re": s5_c_re, "s5_c_im": s5_c_im, "s5_d": s5_d, "s5_w_glu": s5_w_glu,
            "nsa_qk_norm": nsa_qk_norm, "cmp_pe": cmp_pe, "cmp_w1": cmp_w1, "cmp_w2": cmp_w2, "rel_bias": rel_bias,
            "w_branch": w_branch, "w_out": w_out, "norm_ffn": norm_ffn, "w_gate_up": w_gate_up, "w_down": w_down}

def reference(x_prompt, x_sample, cache_nsa_kv, cache_win_kv, state_hgrn, state_s5_re, state_s5_im, page_table,
              norm_mix, w_in, hg_lb_logits, hg_out_norm, s5_a_re, s5_a_im, s5_log_dt, s5_b_re, s5_b_im,
              s5_c_re, s5_c_im, s5_d, s5_w_glu, nsa_qk_norm, cmp_pe, cmp_w1, cmp_w2, rel_bias,
              w_branch, w_out, norm_ffn, w_gate_up, w_down):
    lb_sm = jax.nn.softmax(hg_lb_logits.astype(F32), axis=0)
    lower_bounds = jnp.cumsum(lb_sm, axis=0) - lb_sm[0]
    dec_b = x_sample.shape[0]
    n_past = page_table.shape[1] * PAGE_SIZE
    hp, hs = x_prompt, x_sample
    st_p, st_s = [], []
    for l in range(DEPTH):
        w = {"norm_mix": norm_mix[l], "w_in": w_in[l], "hg_out_norm": hg_out_norm[l],
             "s5_a_re": s5_a_re[l], "s5_a_im": s5_a_im[l], "s5_log_dt": s5_log_dt[l], "s5_b_re": s5_b_re[l],
             "s5_b_im": s5_b_im[l], "s5_c_re": s5_c_re[l], "s5_c_im": s5_c_im[l], "s5_d": s5_d[l], "s5_w_glu": s5_w_glu[l],
             "nsa_qk_norm": nsa_qk_norm[l], "cmp_pe": cmp_pe[l], "cmp_w1": cmp_w1[l], "cmp_w2": cmp_w2[l],
             "w_branch": w_branch[l], "w_out": w_out[l], "norm_ffn": norm_ffn[l], "w_gate_up": w_gate_up[l], "w_down": w_down[l]}
        past = {"kv": cache_nsa_kv[l, page_table].reshape(dec_b, n_past, 4, NSA_KV, HEAD_DIM),
                "win": cache_win_kv[l], "hgrn": state_hgrn[l], "s5_re": state_s5_re[l], "s5_im": state_s5_im[l]}
        hp, sp = layer_forward(hp, None, lower_bounds[l], rel_bias, w)
        hs, ss = layer_forward(hs, past, lower_bounds[l], rel_bias, w)
        st_p.append(sp)
        st_s.append(ss)
    kv_p = jnp.stack([s[0] for s in st_p])
    kv_s = jnp.stack([s[0] for s in st_s])
    win_p = jnp.stack([s[1] for s in st_p])
    win_s = jnp.stack([s[1] for s in st_s])
    hg_p = jnp.stack([s[2] for s in st_p])
    hg_s = jnp.stack([s[2] for s in st_s])
    s5r_p = jnp.stack([s[3] for s in st_p])
    s5i_p = jnp.stack([s[4] for s in st_p])
    s5r_s = jnp.stack([s[3] for s in st_s])
    s5i_s = jnp.stack([s[4] for s in st_s])
    return (hp, hs, kv_p, kv_s, win_p, win_s, hg_p, hg_s, s5r_p, s5i_p, s5r_s, s5i_s)


_drawn_inputs = setup_inputs


def setup_inputs(seed=0):
    import zlib

    import numpy as np

    out = dict(_drawn_inputs(seed))
    spreads = {}
    factors = {'hg_out_norm': 7.826,
     's5_a_re': 69.134,
     's5_c_re': 8.335,
     's5_c_im': 8.207,
     'nsa_qk_norm': 10.694,
     'cmp_pe': 8.0,
     'norm_ffn': 3.913,
     'rel_bias': 2.909}
    for name, (base, spread) in spreads.items():
        noise = np.random.default_rng([zlib.crc32(name.encode()), seed]).standard_normal(out[name].shape)
        drawn = base * np.exp(spread * noise) if base else spread * noise
        out[name] = __import__('jax').numpy.asarray(drawn.astype(out[name].dtype))
    for name, factor in factors.items():
        out[name] = (out[name] * factor).astype(out[name].dtype)
    return out
```

```python
import concourse.bass as bass
from concourse import mybir
from contextlib import ExitStack, contextmanager
import numpy as np

F32 = mybir.dt.float32
I32 = mybir.dt.int32
ACT = mybir.ActivationFunctionType
ALU = mybir.AluOpType
AX = mybir.AxisListType

P = 128
BANK = 512
D = 1024
KD = D // P
TP = 1024
SB, ST = 8, 8
T = TP + SB * ST
PAST = 4096
EPS = 1e-6
NEG = -1e30
FORCE = 1e9
HD = 64
NH, NG, NR = 8, 2, 4
COLS = [(0, 512), (512, 1024), (1024, T)]
TILES = [(i * P, P) for i in range(TP // P)] + [(TP, T - TP)]
NTOK = 2328
TOK_CHUNK = NTOK // 6
C_SU, C_HI, C_NQ, C_KV, C_NGATE = 0, 512, 1024, 1536, 2304
R_HQ, R_HF, R_HG, R_GATES = 0, 512, 1024, 1536
NQKV = 512 + 768

STRIP = 2048
STRIP_AT = 1023
N_BUCKETS, MAX_DIST, WINDOW = 32, 128, 512
CMP_HID, CMP_STRIDE, CMP_LEN = 128, 16, 32
TINY = 1.17549435e-38


@contextmanager
def stage_semaphores(nc):
    held = []

    def new(name):
        held.append(nc.alloc_semaphore(name))
        return held[-1]

    yield new
    nc.clear_and_free_semaphores(held)
    nc.all_engine_barrier()


def norm_project_stage(nc, x_t, g_mix, w_feat, w_tok, feat_out, tok_out):
    with ExitStack() as ctx:
        new_sem = ctx.enter_context(stage_semaphores(nc))
        sb = lambda name, shape: ctx.enter_context(nc.sbuf_tensor("np_" + name, shape, F32))
        sem = lambda name: new_sem("np_" + name)
        x = sb("x", [P, KD, T])
        rstd = sb("rstd", [P, T])
        sq = sb("sq", [P, 2, T])
        gain = sb("gain", [P, KD])
        ones = sb("ones", [P, P])
        wf = sb("wf", [P, 2, KD, P])
        wt = sb("wt", [P, 2, KD, TOK_CHUNK])
        stage = sb("stage", [P, 2, T])
        stage_t = sb("stage_t", [P, 4, TOK_CHUNK])
        ps = ctx.enter_context(nc.psum_tensor("np_ps", [P, 8, BANK], F32))
        x_in, ones_set, squared, sq_used = sem("x_in"), sem("ones_set"), sem("squared"), sem("sq_used")
        var_eps, root, rstd_set, normed = sem("var_eps"), sem("root"), sem("rstd_set"), sem("normed")
        wf_in = [sem("wf_in0"), sem("wf_in1")]
        wt_in = [sem("wt_in0"), sem("wt_in1")]
        f_mm, f_copied_a, f_copied_v, f_out = sem("f_mm"), sem("f_copied_a"), sem("f_copied_v"), [sem("f_out0"), sem("f_out1")]
        t_mm, t_copied = sem("t_mm"), sem("t_copied")
        t_out = [sem(f"t_out{i}") for i in range(4)]
        NF = w_feat.shape[0]
        NT = w_tok.shape[0]
        tiles = TILES

        block = ctx.enter_context(nc.Block())

        @block.sync
        def _(sp):
            for k in range(KD):
                sp.dma_start(x[:, k], x_t[:, k]).then_inc(x_in, 16)
            sp.dma_start(gain[:], g_mix).then_inc(x_in, 16)
            for s in range(2):
                sp.dma_start(wf[:, s], w_feat[s]).then_inc(wf_in[s], 16)
            for s in range(2):
                sp.dma_start(wt[:, s], w_tok[s]).then_inc(wt_in[s], 16)
            with sp.Fori(0, NF // 2 - 1) as i:
                for s in range(2):
                    sp.wait_ge(f_mm, i * 6 + 3 * s + 3)
                    sp.dma_start(wf[:, s], w_feat[i * 2 + (s + 2)]).then_inc(wf_in[s], 16)
            for c in range(2, NT):
                sp.wait_ge(t_mm, len(tiles) * (c - 1))
                sp.dma_start(wt[:, c % 2], w_tok[c]).then_inc(wt_in[c % 2], 16)

        @block.gpsimd
        def _(pool):
            pool.memset(ones[:], 1.0).then_inc(ones_set, 1)
            with pool.Fori(0, NF // 2) as i:
                for s in range(2):
                    pool.wait_ge(f_copied_a, i * 2 + s + 1)
                    pool.wait_ge(f_copied_v, i * 2 + s + 1)
                    pool.dma_start(feat_out[bass.ds(i * 256 + s * 128, P), :], stage[:, s]).then_inc(f_out[s], 16)
            for n in range(NT * len(tiles)):
                c, t = divmod(n, len(tiles))
                t0, tn = tiles[t]
                pool.wait_ge(t_copied, n + 1)
                pool.dma_start(tok_out[t0:t0 + tn, c * TOK_CHUNK:(c + 1) * TOK_CHUNK], stage_t[0:tn, n % 4]).then_inc(t_out[n % 4], 16)
            for s in range(2):
                pool.wait_ge(f_out[s], 16 * (NF // 2))
            for s in range(4):
                pool.wait_ge(t_out[s], 16 * len(range(s, NT * len(tiles), 4)))

        @block.tensor
        def _(pe):
            pe.wait_ge(ones_set, 1)
            for k in range(KD):
                pe.wait_ge(squared, k + 1)
                for n, (a, b) in enumerate(COLS):
                    last = pe.matmul(ps[:, n, 0:b - a], ones[:], sq[:, k % 2, a:b], start=(k == 0), stop=(k == KD - 1))
                last.then_inc(sq_used, 1)
            pe.wait_ge(normed, KD)
            pe.wait_ge(var_eps, 3)
            with pe.Fori(0, NF // 2) as i:
                for s in range(2):
                    pe.wait_ge(wf_in[s], i * 16 + 16)
                    pe.wait_ge(f_copied_a, i * 2 + (s - 1 if s else 0) if s == 0 else i * 2)
                    pe.wait_ge(f_copied_v, i * 2)
                    for n, (a, b) in enumerate(COLS):
                        for k in range(KD):
                            last = pe.matmul(ps[:, 4 * s + n, 0:b - a], wf[:, s, k], x[:, k, a:b], start=(k == 0), stop=(k == KD - 1))
                        last.then_inc(f_mm, 1)
            pe.wait_ge(f_copied_a, NF)
            pe.wait_ge(f_copied_v, NF)
            for c in range(NT):
                pe.wait_ge(wt_in[c % 2], 16 * (c // 2 + 1))
                for t, (t0, tn) in enumerate(tiles):
                    n = c * len(tiles) + t
                    if n >= 8:
                        pe.wait_ge(t_copied, n - 7)
                    for k in range(KD):
                        last = pe.matmul(ps[0:tn, n % 8, 0:TOK_CHUNK], x[:, k, t0:t0 + tn], wt[:, c % 2, k], start=(k == 0), stop=(k == KD - 1))
                    last.then_inc(t_mm, 1)

        @block.scalar
        def _(act):
            for k in range(KD):
                act.wait_ge(x_in, 16 * (KD + 1))
                if k >= 2:
                    act.wait_ge(sq_used, k - 1)
                act.activation(sq[:, k % 2], x[:, k], ACT.Square).then_inc(squared, 1)
            act.wait_ge(var_eps, 3)
            act.activation(rstd[:], rstd[:], ACT.Sqrt).then_inc(root, 1)
            with act.Fori(0, NF // 2) as i:
                for s in range(2):
                    act.wait_ge(f_out[s], i * 16)
                    act.wait_ge(f_mm, i * 6 + 3 * s + 1)
                    act.activation(stage[:, s, 0:512], ps[:, 4 * s, 0:512], ACT.Copy).then_inc(f_copied_a, 1)

        @block.vector
        def _(dve):
            dve.wait_ge(sq_used, KD)
            for n, (a, b) in enumerate(COLS):
                dve.tensor_scalar(rstd[:, a:b], ps[:, n, 0:b - a], 1.0 / D, EPS, ALU.mult, ALU.add).then_inc(var_eps, 1)
            dve.wait_ge(root, 1)
            dve.reciprocal(rstd[:], rstd[:]).then_inc(rstd_set, 1)
            dve.wait_ge(rstd_set, 1)
            for k in range(KD):
                dve.scalar_tensor_tensor(out=x[:, k], in0=x[:, k], scalar=gain[:, k:k + 1], in1=rstd[:], op0=ALU.mult, op1=ALU.mult).then_inc(normed, 1)
            with dve.Fori(0, NF // 2) as i:
                for s in range(2):
                    dve.wait_ge(f_out[s], i * 16)
                    dve.wait_ge(f_mm, i * 6 + 3 * s + 3)
                    dve.tensor_copy(stage[:, s, 512:1024], ps[:, 4 * s + 1, 0:512])
                    dve.tensor_copy(stage[:, s, 1024:T], ps[:, 4 * s + 2, 0:T - 1024]).then_inc(f_copied_v, 1)
            for n in range(NT * len(tiles)):
                tn = tiles[n % len(tiles)][1]
                dve.wait_ge(t_mm, n + 1)
                if n >= 4:
                    dve.wait_ge(t_out[n % 4], 16 * (n // 4))
                dve.tensor_copy(stage_t[0:tn, n % 4], ps[0:tn, n % 8, 0:TOK_CHUNK]).then_inc(t_copied, 1)


def attention_rows_stage(nc, tok, qk_norm, ident_in, rows_out, qkv, heads_t):
    NHD = NQKV // HD
    K_SEL, K_WIN = (512 + 256) // HD, 1024 // HD
    with ExitStack() as ctx:
        new_sem = ctx.enter_context(stage_semaphores(nc))
        sb = lambda name, shape: ctx.enter_context(nc.sbuf_tensor("ar_" + name, shape, F32))
        sem = lambda name: new_sem("ar_" + name)
        rows = sb("rows", [P, 2, NHD, HD])
        sq = sb("sq", [P, 12, HD])
        ssq = sb("ssq", [P, 12])
        rstd = sb("rstd", [P, 12])
        gain = sb("gain", [P, 4, HD])
        ident = sb("ident", [P, P])
        turned = sb("turned", [P, 2, 6, P])
        ps = ctx.enter_context(nc.psum_tensor("ar_ps", [P, 4, BANK], F32))
        rows_in = [sem("rows_in0"), sem("rows_in1")]
        rows_stored = [sem("rows_stored0"), sem("rows_stored1")]
        turned_stored = [sem("turned_stored0"), sem("turned_stored1")]
        const_in, q_gain, var_set, root, normed, tr_done, copied = (
            sem("const_in"), sem("q_gain"), sem("var_set"), sem("root"), sem("normed"), sem("tr_done"), sem("copied"))
        NTL = len(TILES)
        parts = [(0, 8, 0, 0), (K_SEL, 2, 8, 2), (K_WIN, 2, 10, 3)]
        block = ctx.enter_context(nc.Block())

        @block.sync
        def _(sp):
            sp.dma_start(gain[:], qk_norm.unsqueeze(0).to_broadcast([P, 4, HD])).then_inc(const_in, 16)
            sp.dma_start(ident[:], ident_in).then_inc(const_in, 16)
            for t, (t0, tn) in enumerate(TILES):
                if t >= 2:
                    sp.wait_ge(rows_stored[t % 2], 32 * (t // 2))
                    sp.wait_ge(tr_done, 6 * (t - 1))
                sp.dma_start(rows[0:tn, t % 2].rearrange("p h d -> p (h d)"), tok[t0:t0 + tn, C_NQ:C_NQ + NQKV]).then_inc(rows_in[t % 2], 16)

        @block.gpsimd
        def _(pool):
            for t, (t0, tn) in enumerate(TILES):
                r = rows[0:tn, t % 2].rearrange("p h d -> p (h d)")
                pool.wait_ge(normed, 3 * (t + 1))
                pool.dma_start(rows_out[t0:t0 + tn, :], r[:, 512:1024]).then_inc(rows_stored[t % 2], 16)
                pool.dma_start(qkv[t0:t0 + tn, :], r).then_inc(rows_stored[t % 2], 16)
                pool.wait_ge(copied, 2 * (t + 1))
                pool.dma_start(heads_t[:, t0:t0 + tn].rearrange("(a p) t -> p a t", p=P), turned[:, t % 2, :, 0:tn]).then_inc(turned_stored[t % 2], 16)
            for s in range(2):
                n = len(range(s, NTL, 2))
                pool.wait_ge(rows_stored[s], 32 * n)
                pool.wait_ge(turned_stored[s], 16 * n)

        @block.scalar
        def _(act):
            for t, (t0, tn) in enumerate(TILES):
                act.wait_ge(var_set, t + 1)
                act.activation(rstd[0:tn], ssq[0:tn], ACT.Sqrt).then_inc(root, 1)

        @block.tensor
        def _(pe):
            pe.wait_ge(const_in, 32)
            for t, (t0, tn) in enumerate(TILES):
                pe.wait_ge(normed, 3 * (t + 1))
                if t >= 2:
                    pe.wait_ge(copied, 2 * (t - 1))
                for n, slot in enumerate((0, 2, 4, 6, K_SEL, K_WIN)):
                    pe.transpose(ps[:, 2 * (t % 2) + n // 4, (n % 4) * P:(n % 4) * P + tn],
                                 rows[0:tn, t % 2, slot:slot + 2].rearrange("p h d -> p (h d)"), ident[0:tn, 0:tn]).then_inc(tr_done, 1)

        @block.vector
        def _(dve):
            dve.wait_ge(const_in, 32)
            dve.tensor_scalar(gain[:, 0], gain[:, 0], HD ** -0.5, None, ALU.mult).then_inc(q_gain, 1)
            dve.wait_ge(q_gain, 1)
            for t, (t0, tn) in enumerate(TILES):
                dve.wait_ge(rows_in[t % 2], 16 * (t // 2 + 1))
                for slot, n, at, _g in parts:
                    r = rows[0:tn, t % 2, slot:slot + n]
                    dve.tensor_tensor(sq[0:tn, at:at + n], r, r, ALU.mult)
                dve.drain()
                dve.tensor_reduce(ssq[0:tn], sq[0:tn], AX.X, ALU.add)
                dve.drain()
                dve.tensor_scalar(ssq[0:tn], ssq[0:tn], 1.0 / HD, EPS, ALU.mult, ALU.add).then_inc(var_set, 1)
                dve.wait_ge(root, t + 1)
                dve.reciprocal(rstd[0:tn], rstd[0:tn])
                dve.drain()
                for slot, n, at, _g in parts:
                    r = rows[0:tn, t % 2, slot:slot + n]
                    dve.tensor_tensor(r, r, rstd[0:tn, at:at + n].unsqueeze(2).to_broadcast([tn, n, HD]), ALU.mult)
                dve.drain()
                for slot, n, at, g in parts:
                    r = rows[0:tn, t % 2, slot:slot + n]
                    dve.tensor_tensor(r, r, gain[0:tn, g:g + 1].to_broadcast([tn, n, HD]), ALU.mult).then_inc(normed, 1)
                if t >= 2:
                    dve.wait_ge(turned_stored[t % 2], 16 * (t // 2))
                for b, (h0, hn) in enumerate(((0, 4), (4, 2))):
                    dve.wait_ge(tr_done, 6 * t + h0 + hn)
                    dve.tensor_copy(turned[:, t % 2, h0:h0 + hn, 0:tn],
                                    ps[:, 2 * (t % 2) + b, 0:hn * P].rearrange("p (h t) -> p h t", t=P)[:, :, 0:tn]).then_inc(copied, 1)


def bias_strip_stage(nc, rel_ext, onehot, qkv, win_cache, strips, win_p, win_s):
    with ExitStack() as ctx:
        new_sem = ctx.enter_context(stage_semaphores(nc))
        lhs = ctx.enter_context(nc.sbuf_tensor("bs_lhs", [N_BUCKETS + 1, NH], F32))
        rhs = ctx.enter_context(nc.sbuf_tensor("bs_rhs", [N_BUCKETS + 1, 2 * STRIP], F32))
        out = ctx.enter_context(nc.sbuf_tensor("bs_out", [NH, 2 * STRIP], F32))
        ps = ctx.enter_context(nc.psum_tensor("bs_ps", [P, 8, BANK], F32))
        loaded, summed, copied, stored = (new_sem("bs_" + n) for n in ("loaded", "summed", "copied", "stored"))
        windows_stored = new_sem("bs_windows_stored")
        block = ctx.enter_context(nc.Block())

        @block.scalar
        def _(act):
            act.dma_start(win_p, qkv[TP - WINDOW:TP, 1024:NQKV]).then_inc(windows_stored, 16)
            act.dma_start(win_s[:, 0:WINDOW - ST], win_cache[:, ST:WINDOW]).then_inc(windows_stored, 16)
            act.dma_start(win_s[:, WINDOW - ST:WINDOW], qkv[TP:T, 1024:NQKV].rearrange("(b t) c -> b t c", b=SB)).then_inc(windows_stored, 16)
            act.wait_ge(windows_stored, 48)

        @block.sync
        def _(sp):
            sp.dma_start(lhs[:], rel_ext).then_inc(loaded, 16)
            sp.dma_start(rhs[:], onehot.rearrange("b w m -> b (w m)")).then_inc(loaded, 16)
            sp.wait_ge(copied, 8)
            sp.dma_start(strips.rearrange("w h m -> h w m"), out[:].rearrange("h (w m) -> h w m", w=2)).then_inc(stored, 16)
            sp.wait_ge(stored, 16)

        @block.tensor
        def _(pe):
            pe.wait_ge(loaded, 32)
            for n in range(8):
                pe.matmul(ps[0:NH, n, :], lhs[:], rhs[:, n * BANK:(n + 1) * BANK], start=True, stop=True).then_inc(summed, 1)

        @block.vector
        def _(dve):
            for n in range(8):
                dve.wait_ge(summed, n + 1)
                dve.tensor_copy(out[:, n * BANK:(n + 1) * BANK], ps[0:NH, n, :]).then_inc(copied, 1)


def sample_attention_stage(nc, cache, page_table, win_cache, heads_t, qkv, tok, strips, w1_in, w2_in, pe_in,
                           qk_norm, overlap_in, rep_in, ident_in, out_t):
    NB = (PAST // CMP_STRIDE) - 1
    NU = PAST // 256
    NPG = PAST // 128
    NS = PAST // 64 + 1
    R = NH * ST
    KEYS = PAST + ST
    with ExitStack() as ctx:
        new_sem = ctx.enter_context(stage_semaphores(nc))
        sb = lambda name, shape, dt=F32: ctx.enter_context(nc.sbuf_tensor("sa_" + name, shape, dt))
        sem = lambda name: new_sem("sa_" + name)
        pages = sb("pages", [P, NU, 2, 512])
        paired = sb("paired", [P, 2, 4, 2, HD])
        vals = sb("vals", [P, NU, 2, P])
        raw_t = sb("raw_t", [P, 4, NU * P])
        keys_t = sb("keys_t", [P, KEYS])
        scores = sb("scores", [R, KEYS])
        near_bias = sb("near_bias", [R, 256 + ST])
        probs_t = sb("probs_t", [P, 2 * NU + 1, R])
        w1 = sb("w1", [P, 2, 16, CMP_HID])
        w2 = sb("w2", [P, 2, HD])
        pe_cols = sb("pe_cols", [P, 2, 16])
        hid_bias = sb("hid_bias", [P, 2])
        hid = sb("hid", [P, 2, 2, NB])
        k_norm = sb("k_norm", [P, HD])
        cmp_kv = sb("cmp_kv", [P, 2, 2, P])
        cmp_sq = sb("cmp_sq", [P, 2, P])
        cmp_ssq = sb("cmp_ssq", [P, 4])
        cmp_kt = sb("cmp_kt", [P, NB])
        cmp_s = sb("cmp_s", [R, NB])
        cmp_bias = sb("cmp_bias", [R, NB])
        cmp_pt = sb("cmp_pt", [P, 2, R])
        overlap = sb("overlap", [P, 2, NS])
        rep = sb("rep", [R, R])
        ident = sb("ident", [P, P])
        blk = sb("blk", [R, NS])
        blk_rep = sb("blk_rep", [R, NS])
        top = sb("top", [R, 16])
        mask = sb("mask", [R, NS])
        win = sb("win", [P, 4, 256])
        win_kt = sb("win_kt", [P, WINDOW + ST])
        win_s = sb("win_s", [R, WINDOW + ST])
        win_bias = sb("win_bias", [R, WINDOW + ST])
        win_pt = sb("win_pt", [P, 5, R])
        new_v = sb("new_v", [ST, 2, P])
        q_diag = sb("q_diag", [P, R])
        near = sb("near", [R, 264])
        gates = sb("gates", [R, 3])
        cols = sb("cols", [R, 16])
        out_rows = sb("out_rows", [R, HD])
        out_cols = sb("out_cols", [HD, R])
        table = sb("table", [1, SB * NPG], I32)
        ps = ctx.enter_context(nc.psum_tensor("sa_ps", [P, 8, BANK], F32))
        names = ("const_in table_in bias_in zeroed bias_set pe_done hid_bias_set small_in win_in unit_in tr cmp_copied key_copied val_copied "
                 "hid_mm gelu_done sel_mm sel_biased out2_mm var_set root kv_set kt_tr kt_copied cs_mm cs_neg cs_exp cs_norm cpt_tr cpt_copied "
                 "oc_mm blk_copied rep_mm sel_neg sel_exp spt_tr spt_copied os_mm wk_tr wk_copied ws_mm ws_neg ws_exp wpt_tr wpt_copied ow_mm "
                 "gate_exp out_set ot_tr ot_copied out_stored passed oc_copied new_pt_copied pairs_set").split()
        S = {n: sem(n) for n in names}
        unit_in = [sem(f"unit_in{u}") for u in range(NU)]
        block = ctx.enter_context(nc.Block())
        NPT = 5
        strip_q = lambda w, q, lo, n: strips[w, :, lo - q:lo - q + n]
        cmp_far = 192
        mn = ctx.enter_context(nc.allow_non_contiguous_dma(reason="small strided tables, once"))

        @block.sync
        def _(sp):
            sp.dma_start(table[:], page_table).then_inc(S["table_in"], 16)
            sp.wait_ge(S["table_in"], 16)
            with sp.Fori(0, SB) as b:
                for u in range(NU):
                    for j in range(2):
                        page = sp.value_load(table[0:1, bass.ds(b * NPG + (2 * u + j), 1)], min_val=0, max_val=cache.shape[0] - 1)
                        if j == 0:
                            sp.wait_ge(S["tr"], b * (2 * NU))
                            sp.sem_inc(S["passed"], 1)
                            sp.wait_ge(S["pairs_set"], b * NU)
                            sp.sem_inc(S["passed"], 1)
                            sp.wait_ge(S["val_copied"], b * NU)
                            sp.sem_inc(S["passed"], 1)
                        sp.dma_start(pages[64 * j:64 * j + 64, u].rearrange("p t c -> p (t c)"),
                                     cache[page].rearrange("(p t) c -> p (t c)", t=2)).then_inc(unit_in[u], 16)

        @block.gpsimd
        def _(pool):
            pool.memset(q_diag[:], 0.0).then_inc(S["zeroed"], 1)
            pool.wait_ge(S["zeroed"], 1)
            with pool.Fori(0, SB) as b:
                pool.wait_ge(S["cs_mm"], b)
                pool.wait_ge(S["ws_mm"], b)
                pool.wait_ge(S["ow_mm"], b)
                pool.wait_ge(S["os_mm"], b)
                pool.wait_ge(S["out_set"], b)
                pool.sem_inc(S["passed"], 1)
                at = b * ST + TP
                for g in range(NG):
                    for r in range(NR):
                        h = g * NR + r
                        pool.dma_start(q_diag[HD * g:HD * (g + 1), h * ST:(h + 1) * ST], heads_t[h * HD:(h + 1) * HD, bass.ds(at, ST)]).then_inc(S["small_in"], 16)
                pool.dma_start(keys_t[:, PAST:KEYS], heads_t[4 * P:5 * P, bass.ds(at, ST)]).then_inc(S["small_in"], 16)
                pool.dma_start(win_kt[:, WINDOW:], heads_t[5 * P:6 * P, bass.ds(at, ST)]).then_inc(S["small_in"], 16)
                pool.dma_start(new_v[:, 0], qkv[bass.ds(at, ST), 512 + 384:512 + 512]).then_inc(S["small_in"], 16)
                pool.dma_start(new_v[:, 1], qkv[bass.ds(at, ST), 1024 + 128:1024 + 256]).then_inc(S["small_in"], 16)
                for h in range(NH):
                    pool.dma_start(gates[h * ST:(h + 1) * ST, :], tok[bass.ds(at, ST), C_NGATE:C_NGATE + 24].rearrange("q (n h) -> q n h", n=3)[:, :, h]).then_inc(S["small_in"], 16)
                pool.dma_start(win[:], win_cache[b].rearrange("(a p) c -> p a c", p=P)).then_inc(S["win_in"], 16)
                for u in range(NU):
                    pool.wait_ge(unit_in[u], b * 32 + 32)
                    if u == 0:
                        pool.wait_ge(S["os_mm"], b)
                    pool.sem_inc(S["passed"], 1)
                    pool.tensor_copy(vals[:, u], pages[:, u, :, 384:512]).then_inc(S["val_copied"], 1)
                pool.wait_ge(S["ot_copied"], b + 1)
                pool.sem_inc(S["passed"], 1)
                pool.dma_start(out_t[:, bass.ds(at, ST)].rearrange("(h d) q -> d h q", d=HD), out_cols[:].rearrange("d (h q) -> d h q", q=ST)).then_inc(S["out_stored"], 16)
            pool.wait_ge(S["out_stored"], 16 * SB)

        @block.scalar
        def _(act):
            n_const = 0
            for dst, src in ((w1[:], w1_in), (w2[:], w2_in), (pe_cols[:], pe_in), (k_norm[:], qk_norm[1:2, :].to_broadcast([P, HD])),
                             (overlap[:], overlap_in), (rep[:], rep_in), (ident[:], ident_in)):
                act.dma_start(dst, src).then_inc(S["const_in"], 16)
            for q in range(ST):
                act.dma_start(near[q:R:ST], strip_q(0, q, STRIP_AT - 256, 264)).then_inc(S["bias_in"], 16)
                act.dma_start(win_bias[q:R:ST], strip_q(1, q, STRIP_AT - WINDOW, WINDOW + ST)).then_inc(S["bias_in"], 16)
                lo = STRIP_AT - (PAST - (CMP_LEN - 1)) + CMP_STRIDE * cmp_far - q
                act.dma_start(cmp_bias[q:R:ST, cmp_far:].unsqueeze(2), strips[0, :, lo:lo + CMP_STRIDE * (NB - cmp_far)].rearrange("h (i s) -> h i s", s=CMP_STRIDE)[:, :, 0:1]).then_inc(S["bias_in"], 16)
            act.wait_ge(S["pe_done"], 1)
            act.activation(hid_bias[:], ps[:, 6, 0:2], ACT.Copy).then_inc(S["hid_bias_set"], 1)
            with act.Fori(0, SB) as b:
                act.wait_ge(S["wk_tr"], b + 1)
                act.activation(win_kt[:, 0:WINDOW], ps[:, 7, :], ACT.Copy).then_inc(S["wk_copied"], 1)
                for u in range(NU):
                    act.wait_ge(S["tr"], b * (2 * NU) + (2 * u + 1))
                    act.activation(raw_t[:, :, u * P:(u + 1) * P], ps[:, 2 * (u % 2), :].rearrange("p (s t) -> p s t", t=P), ACT.Copy).then_inc(S["cmp_copied"], 1)
                for s in range(2):
                    act.wait_ge(S["hid_mm"], b * 2 + (s + 1))
                    act.activation(hid[:, s].rearrange("p g i -> p (g i)"), ps[:, 4 + s, 0:2 * NB], ACT.Gelu_apprx_tanh, bias=hid_bias[:, s:s + 1]).then_inc(S["gelu_done"], 1)
                act.wait_ge(S["var_set"], b + 1)
                act.activation(cmp_ssq[:], cmp_ssq[:], ACT.Sqrt).then_inc(S["root"], 1)
                act.wait_ge(S["ws_neg"], b + 1)
                act.activation(win_s[:], win_s[:], ACT.Exp, bias=cols[:, 0:1], accum_out=cols[:, 1:2]).then_inc(S["ws_exp"], 1)
                act.wait_ge(S["small_in"], (b + 1) * 320)
                act.activation(gates[:], gates[:], ACT.Exp, scale=-1.0).then_inc(S["gate_exp"], 1)
                act.wait_ge(S["cs_neg"], b + 1)
                act.activation(cmp_s[:], cmp_s[:], ACT.Exp, bias=cols[:, 2:3], accum_out=cols[:, 3:4]).then_inc(S["cs_exp"], 1)
                act.wait_ge(S["sel_neg"], b + 1)
                act.activation(scores[:], scores[:], ACT.Exp, bias=cols[:, 4:5], accum_out=cols[:, 5:6]).then_inc(S["sel_exp"], 1)
                for n in range(4):
                    act.wait_ge(S["spt_tr"], b * NPT + (n + 1))
                    act.activation(probs_t[:, 8 * n:8 * n + 8].rearrange("p a r -> p (a r)"), ps[:, n, :], ACT.Copy).then_inc(S["spt_copied"], 1)

        @block.tensor
        def _(pe):
            pe.wait_ge(S["const_in"], 16 * 7)
            for s in range(2):
                for j in range(16):
                    last = pe.matmul(ps[:, 6, s:s + 1], w1[:, s, j], pe_cols[:, s, j:j + 1], start=(j == 0), stop=(j == 15))
            last.then_inc(S["pe_done"], 1)
            pe.wait_ge(S["hid_bias_set"], 1)
            with pe.Fori(0, SB) as b:
                pe.wait_ge(S["win_in"], b * 16 + 16)
                pe.wait_ge(S["wpt_copied"], b)
                for a in range(4):
                    last = pe.transpose(ps[:, 7, a * P:(a + 1) * P], win[:, a, 0:P], ident[:])
                last.then_inc(S["wk_tr"], 1)
                for u in range(NU):
                    pe.wait_ge(unit_in[u], b * 32 + 32)
                    pe.wait_ge(S["pairs_set"], b * NU + (u + 1))
                    A = 2 * (u % 2)
                    if u < 2:
                        pe.wait_ge(S["spt_copied"], b * 4)
                    else:
                        pe.wait_ge(S["cmp_copied"], b * NU + (u - 1))
                        pe.wait_ge(S["key_copied"], b * NU + (u - 1))
                    for sg in range(4):
                        last = pe.transpose(ps[:, A, sg * P:(sg + 1) * P], paired[:, u % 2, sg].rearrange("p t d -> p (t d)"), ident[:])
                    last.then_inc(S["tr"], 1)
                    for t in range(2):
                        last = pe.transpose(ps[:, A + 1, t * P:(t + 1) * P], pages[:, u, t, 256:384], ident[:])
                    last.then_inc(S["tr"], 1)
                pe.wait_ge(S["cmp_copied"], b * NU + NU)
                pe.wait_ge(S["out_set"], b)
                for s in range(2):
                    for j in range(16):
                        last = pe.matmul(ps[:, 4 + s, 0:2 * NB], w1[:, s, j], raw_t[:, 2 * s:2 * s + 2, j:j + 8 * (NB - 1) + 1:8], start=(j == 0), stop=(j == 15))
                    last.then_inc(S["hid_mm"], 1)
                pe.wait_ge(S["small_in"], (b + 1) * 320)
                pe.wait_ge(S["wk_copied"], b + 1)
                pe.matmul(ps[0:R, 7, :], q_diag[:], win_kt[:, 0:WINDOW], start=True, stop=True)
                pe.matmul(ps[0:R, 6, 8:16], q_diag[:], win_kt[:, WINDOW:], start=True, stop=True).then_inc(S["ws_mm"], 1)
                pe.wait_ge(S["key_copied"], b * NU + NU)
                for n in range(8):
                    if n >= 4:
                        pe.wait_ge(S["sel_biased"], b * 9 + (n - 3))
                    pe.matmul(ps[0:R, n % 4, :], q_diag[:], keys_t[:, n * 512:(n + 1) * 512], start=True, stop=True).then_inc(S["sel_mm"], 1)
                pe.matmul(ps[0:R, 6, 0:8], q_diag[:], keys_t[:, PAST:KEYS], start=True, stop=True).then_inc(S["sel_mm"], 1)
                pe.wait_ge(S["gelu_done"], b * 2 + 2)
                for s in range(2):
                    for g in range(2):
                        for c in range(2):
                            m = P if c == 0 else NB - P
                            last = pe.matmul(ps[0:m, 4, ((s * 2 + c) * 2 + g) * HD:((s * 2 + c) * 2 + g + 1) * HD], hid[:, s, g, c * P:c * P + m], w2[:, s], start=True, stop=True)
                last.then_inc(S["out2_mm"], 1)
                pe.wait_ge(S["kv_set"], b + 1)
                pe.transpose(ps[:, 5, 0:P], cmp_kv[:, 0, 0], ident[:])
                pe.transpose(ps[:, 5, P:NB], cmp_kv[0:NB - P, 0, 1], ident[0:NB - P, 0:NB - P]).then_inc(S["kt_tr"], 1)
                pe.wait_ge(S["kt_copied"], b + 1)
                pe.matmul(ps[0:R, 5, 256:256 + NB], q_diag[:], cmp_kt[:], start=True, stop=True).then_inc(S["cs_mm"], 1)
                pe.wait_ge(S["ws_exp"], b + 1)
                pe.sem_inc(S["passed"], 1)
                for a in range(4):
                    pe.transpose(ps[:, 7, a * R:(a + 1) * R], win_s[:, a * P:(a + 1) * P], ident[0:R, 0:R])
                pe.transpose(ps[0:ST, 7, 4 * R:5 * R], win_s[:, WINDOW:], ident[0:R, 0:R]).then_inc(S["wpt_tr"], 1)
                pe.wait_ge(S["wpt_copied"], b + 1)
                for a in range(4):
                    pe.matmul(ps[0:R, 6, 128:256], win_pt[:, a], win[:, a, P:2 * P], start=(a == 0), stop=False)
                pe.matmul(ps[0:R, 6, 128:256], win_pt[0:ST, 4], new_v[:, 1], start=False, stop=True).then_inc(S["ow_mm"], 1)
                pe.wait_ge(S["cs_norm"], b + 1)
                pe.sem_inc(S["passed"], 1)
                pe.transpose(ps[:, 4, 0:R], cmp_s[:, 0:P], ident[0:R, 0:R])
                pe.transpose(ps[0:NB - P, 4, R:2 * R], cmp_s[:, P:NB], ident[0:R, 0:R]).then_inc(S["cpt_tr"], 1)
                pe.wait_ge(S["cpt_copied"], b + 1)
                for c, m in ((0, P), (1, NB - P)):
                    pe.matmul(ps[0:R, 4, 256:256 + NS], cmp_pt[0:m, c], overlap[0:m, c], start=(c == 0), stop=(c == 1))
                for c, m in ((0, P), (1, NB - P)):
                    last = pe.matmul(ps[0:R, 4, 128:256], cmp_pt[0:m, c], cmp_kv[0:m, 1, c], start=(c == 0), stop=(c == 1))
                last.then_inc(S["oc_mm"], 1)
                pe.wait_ge(S["blk_copied"], b + 1)
                pe.sem_inc(S["passed"], 1)
                pe.matmul(ps[0:R, 4, 384:384 + NS], rep[:], blk[:], start=True, stop=True).then_inc(S["rep_mm"], 1)
                pe.wait_ge(S["sel_exp"], b + 1)
                pe.sem_inc(S["passed"], 1)
                for n in range(32):
                    last = pe.transpose(ps[:, n // 8, (n % 8) * R:(n % 8 + 1) * R], scores[:, n * P:(n + 1) * P], ident[0:R, 0:R])
                    if n % 8 == 7:
                        last.then_inc(S["spt_tr"], 1)
                pe.transpose(ps[0:ST, 6, 64:128], scores[:, PAST:KEYS], ident[0:R, 0:R]).then_inc(S["spt_tr"], 1)
                pe.wait_ge(S["val_copied"], b * NU + NU)
                for n in range(32):
                    if n % 8 == 0:
                        pe.wait_ge(S["spt_copied"], b * 4 + (n // 8 + 1))
                    pe.matmul(ps[0:R, 5, 0:P], probs_t[:, n], vals[:, n // 2, n % 2], start=(n == 0), stop=False)
                pe.wait_ge(S["new_pt_copied"], b + 1)
                pe.sem_inc(S["passed"], 1)
                pe.matmul(ps[0:R, 5, 0:P], probs_t[0:ST, 32], new_v[:, 0], start=False, stop=True).then_inc(S["os_mm"], 1)
                pe.wait_ge(S["out_set"], b + 1)
                pe.sem_inc(S["passed"], 1)
                pe.transpose(ps[0:HD, 6, 256:256 + R], out_rows[:], ident[0:R, 0:R]).then_inc(S["ot_tr"], 1)

        @block.vector
        def _(dve):
            dve.wait_ge(S["bias_in"], 16 * 3 * ST)
            dve.memset(cmp_bias[:, 0:cmp_far], 0.0)
            dve.drain()
            dve.tensor_scalar(cmp_bias[:, 0:cmp_far], cmp_bias[:, 0:cmp_far], near[:, 0:1], None, ALU.add)
            for t in range(2):
                dve.tensor_copy(near_bias[:, t * P:(t + 1) * P], near[:, 0:256].rearrange("r (p t) -> r t p", t=2)[:, t])
            dve.tensor_copy(near_bias[:, 256:], near[:, 256:264])
            dve.drain()
            dve.wait_ge(S["const_in"], 16 * 7)
            with dve.Fori(0, SB) as b:
                def pair(u):
                    dve.wait_ge(unit_in[u], b * 32 + 32)
                    dve.wait_ge(S["tr"], b * (2 * NU) + (2 * (u - 2) + 1) if u >= 2 else b * (2 * NU))
                    dve.tensor_copy(paired[:, u % 2], pages[:, u, :, 0:256].rearrange("p t (s d) -> p s t d", d=HD)).then_inc(S["pairs_set"], 1)

                pair(0)
                for u in range(NU):
                    if u + 1 < NU:
                        pair(u + 1)
                    dve.wait_ge(S["tr"], b * (2 * NU) + (2 * u + 2))
                    dve.tensor_copy(keys_t[:, u * 256:(u + 1) * 256], ps[:, 2 * (u % 2) + 1, 0:256]).then_inc(S["key_copied"], 1)
                dve.wait_ge(S["ws_mm"], b + 1)
                dve.tensor_tensor(win_s[:, 0:WINDOW], ps[0:R, 7, :], win_bias[:, 0:WINDOW], ALU.add)
                dve.tensor_tensor(win_s[:, WINDOW:], ps[0:R, 6, 8:16], win_bias[:, WINDOW:], ALU.add)
                dve.drain()
                dve.tensor_reduce(cols[:, 6:7], win_s[:], AX.X, ALU.max)
                dve.drain()
                dve.tensor_scalar(cols[:, 0:1], cols[:, 6:7], -1.0, None, ALU.mult).then_inc(S["ws_neg"], 1)
                for n in range(9):
                    dve.wait_ge(S["sel_mm"], b * 9 + (n + 1))
                    if n < 7:
                        last = dve.tensor_scalar(scores[:, n * 512:(n + 1) * 512], ps[0:R, n % 4, :], near[:, 0:1], None, ALU.add)
                    elif n == 7:
                        dve.tensor_scalar(scores[:, PAST - 512:PAST - 256], ps[0:R, 3, 0:256], near[:, 0:1], None, ALU.add)
                        last = dve.tensor_tensor(scores[:, PAST - 256:PAST], ps[0:R, 3, 256:512], near_bias[:, 0:256], ALU.add)
                    else:
                        last = dve.tensor_tensor(scores[:, PAST:KEYS], ps[0:R, 6, 0:ST], near_bias[:, 256:], ALU.add)
                    last.then_inc(S["sel_biased"], 1)
                dve.wait_ge(S["out2_mm"], b + 1)
                for c, m in ((0, P), (1, NB - P)):
                    for s in range(2):
                        dve.tensor_copy(cmp_kv[0:m, s, c], ps[0:m, 4, (s * 2 + c) * P:(s * 2 + c + 1) * P])
                dve.drain()
                for c, m in ((0, P), (1, NB - P)):
                    dve.tensor_tensor(cmp_sq[0:m, c], cmp_kv[0:m, 0, c], cmp_kv[0:m, 0, c], ALU.mult)
                dve.drain()
                dve.memset(cmp_ssq[:], 1.0)
                dve.drain()
                for c, m in ((0, P), (1, NB - P)):
                    dve.tensor_reduce(cmp_ssq[0:m, 2 * c:2 * c + 2], cmp_sq[0:m, c].rearrange("p (g d) -> p g d", g=2), AX.X, ALU.add)
                dve.drain()
                dve.tensor_scalar(cmp_ssq[:], cmp_ssq[:], 1.0 / HD, EPS, ALU.mult, ALU.add).then_inc(S["var_set"], 1)
                dve.wait_ge(S["root"], b + 1)
                dve.reciprocal(cmp_ssq[:], cmp_ssq[:])
                dve.drain()
                for c, m in ((0, P), (1, NB - P)):
                    for g in range(2):
                        k = cmp_kv[0:m, 0, c, g * HD:(g + 1) * HD]
                        last = dve.scalar_tensor_tensor(out=k, in0=k, scalar=cmp_ssq[0:m, 2 * c + g:2 * c + g + 1], in1=k_norm[0:m], op0=ALU.mult, op1=ALU.mult)
                last.then_inc(S["kv_set"], 1)
                dve.wait_ge(S["kt_tr"], b + 1)
                dve.tensor_copy(cmp_kt[:], ps[:, 5, 0:NB]).then_inc(S["kt_copied"], 1)
                dve.wait_ge(S["cs_mm"], b + 1)
                dve.tensor_tensor(cmp_s[:], ps[0:R, 5, 256:256 + NB], cmp_bias[:], ALU.add)
                dve.drain()
                dve.tensor_reduce(cols[:, 6:7], cmp_s[:], AX.X, ALU.max)
                dve.drain()
                dve.tensor_scalar(cols[:, 2:3], cols[:, 6:7], -1.0, None, ALU.mult).then_inc(S["cs_neg"], 1)
                dve.wait_ge(S["wpt_tr"], b + 1)
                dve.tensor_copy(win_pt[:, 0:4].rearrange("p a r -> p (a r)"), ps[:, 7, 0:4 * R])
                dve.tensor_copy(win_pt[0:ST, 4], ps[0:ST, 7, 4 * R:5 * R]).then_inc(S["wpt_copied"], 1)
                dve.wait_ge(S["cs_exp"], b + 1)
                dve.reciprocal(cols[:, 7:8], cols[:, 3:4])
                dve.drain()
                dve.tensor_scalar(cmp_s[:], cmp_s[:], cols[:, 7:8], None, ALU.mult)
                dve.drain()
                dve.scalar_tensor_tensor(out=cmp_s[:], in0=cmp_s[:], scalar=TINY, in1=cmp_s[:], op0=ALU.is_ge, op1=ALU.mult).then_inc(S["cs_norm"], 1)
                dve.wait_ge(S["cpt_tr"], b + 1)
                dve.tensor_copy(cmp_pt[:, 0], ps[:, 4, 0:R])
                dve.tensor_copy(cmp_pt[0:NB - P, 1], ps[0:NB - P, 4, R:2 * R]).then_inc(S["cpt_copied"], 1)
                dve.wait_ge(S["oc_mm"], b + 1)
                dve.tensor_copy(blk[:], ps[0:R, 4, 256:256 + NS]).then_inc(S["blk_copied"], 1)
                dve.wait_ge(S["gate_exp"], b + 1)
                dve.tensor_scalar(gates[:], gates[:], 1.0, None, ALU.add)
                dve.drain()
                dve.reciprocal(gates[:], gates[:])
                dve.wait_ge(S["rep_mm"], b + 1)
                dve.tensor_copy(blk_rep[:], ps[0:R, 4, 384:384 + NS])
                dve.drain()
                dve.memset(blk_rep[:, 0:1], FORCE)
                dve.memset(blk_rep[:, NS - 2:NS], FORCE)
                dve.drain()
                for k in range(2):
                    dve.max(top[:, 8 * k:8 * k + 8], blk_rep[:])
                    dve.drain()
                    dve.match_replace(blk_rep[:], top[:, 8 * k:8 * k + 8], blk_rep[:], -FORCE)
                    dve.drain()
                dve.tensor_scalar(mask[:], blk_rep[:], -1.0, NEG, ALU.is_gt, ALU.mult)
                dve.drain()
                for t in range(2):
                    v = scores[:, 0:PAST].rearrange("r (u t k p) -> r t u k p", u=NU, t=2, k=4)[:, t]
                    dve.tensor_tensor(v, v, mask[:, 0:NS - 1].rearrange("r (u k) -> r u k", k=4).unsqueeze(3).to_broadcast([R, NU, 4, 32]), ALU.add)
                dve.drain()
                dve.tensor_reduce(cols[:, 6:7], scores[:], AX.X, ALU.max)
                dve.drain()
                dve.tensor_scalar(cols[:, 4:5], cols[:, 6:7], -1.0, None, ALU.mult).then_inc(S["sel_neg"], 1)
                for g in range(2):
                    last = dve.tensor_scalar(out_rows[32 * g:32 * g + 32], ps[32 * g:32 * g + 32, 4, 128 + HD * g:128 + HD * (g + 1)], gates[32 * g:32 * g + 32, 0:1], None, ALU.mult)
                last.then_inc(S["oc_copied"], 1)
                dve.wait_ge(S["ws_exp"], b + 1)
                dve.reciprocal(cols[:, 8:9], cols[:, 1:2])
                dve.wait_ge(S["spt_tr"], b * NPT + NPT)
                dve.tensor_copy(probs_t[0:ST, 32], ps[0:ST, 6, 64:128]).then_inc(S["new_pt_copied"], 1)
                dve.reciprocal(cols[:, 9:10], cols[:, 5:6])
                dve.drain()
                dve.tensor_tensor(cols[:, 8:9], cols[:, 8:9], gates[:, 2:3], ALU.mult)
                dve.tensor_tensor(cols[:, 9:10], cols[:, 9:10], gates[:, 1:2], ALU.mult)
                dve.drain()
                dve.wait_ge(S["ow_mm"], b + 1)
                for g in range(2):
                    o = out_rows[32 * g:32 * g + 32]
                    dve.scalar_tensor_tensor(out=o, in0=ps[32 * g:32 * g + 32, 6, 128 + HD * g:128 + HD * (g + 1)], scalar=cols[32 * g:32 * g + 32, 8:9], in1=o, op0=ALU.mult, op1=ALU.add)
                dve.drain()
                dve.wait_ge(S["os_mm"], b + 1)
                for g in range(2):
                    o = out_rows[32 * g:32 * g + 32]
                    last = dve.scalar_tensor_tensor(out=o, in0=ps[32 * g:32 * g + 32, 5, HD * g:HD * (g + 1)], scalar=cols[32 * g:32 * g + 32, 9:10], in1=o, op0=ALU.mult, op1=ALU.add)
                last.then_inc(S["out_set"], 1)
                dve.wait_ge(S["ot_tr"], b + 1)
                dve.wait_ge(S["out_stored"], b * 16)
                dve.tensor_copy(out_cols[:], ps[0:HD, 6, 256:256 + R]).then_inc(S["ot_copied"], 1)


def prompt_compress_stage(nc, tok, w1_in, w2_in, pe_in, qk_norm, ident_in, kt_out, v_out):
    NB = TP // CMP_STRIDE - 1
    NU = TP // 256
    with ExitStack() as ctx:
        new_sem = ctx.enter_context(stage_semaphores(nc))
        sb = lambda name, shape: ctx.enter_context(nc.sbuf_tensor("pc_" + name, shape, F32))
        raw = sb("raw", [P, NU, 2, 256])
        paired = sb("paired", [P, NU, 4, 2, HD])
        raw_t = sb("raw_t", [P, 4, NU * P])
        w1 = sb("w1", [P, 2, 16, CMP_HID])
        w2 = sb("w2", [P, 2, HD])
        pe_cols = sb("pe_cols", [P, 2, 16])
        k_norm = sb("k_norm", [P, HD])
        ident = sb("ident", [P, P])
        hid_bias = sb("hid_bias", [P, 2])
        hid = sb("hid", [P, 2, 2, NB])
        kv = sb("kv", [NB, 2, P])
        sq = sb("sq", [NB, P])
        ssq = sb("ssq", [NB, 2])
        kt = sb("kt", [P, NB])
        ps = ctx.enter_context(nc.psum_tensor("pc_ps", [P, 8, BANK], F32))
        S = {n: new_sem("pc_" + n) for n in
             "loaded paired_set tr copied hid_mm bias_set gelu_done out_mm var_set root kv_set kt_tr kt_copied stored".split()}
        block = ctx.enter_context(nc.Block())

        @block.sync
        def _(sp):
            for u in range(NU):
                sp.dma_start(raw[:, u], tok[u * 256:(u + 1) * 256, C_KV:C_KV + 256].rearrange("(p t) c -> p t c", t=2)).then_inc(S["loaded"], 16)
            for dst, src in ((w1[:], w1_in), (w2[:], w2_in), (pe_cols[:], pe_in), (k_norm[:], qk_norm[1:2, :].to_broadcast([P, HD])), (ident[:], ident_in)):
                sp.dma_start(dst, src).then_inc(S["loaded"], 16)
            sp.wait_ge(S["kv_set"], 2)
            sp.dma_start(v_out, kv[:, 1]).then_inc(S["stored"], 16)
            sp.wait_ge(S["kt_copied"], 1)
            sp.dma_start(kt_out, kt[:]).then_inc(S["stored"], 16)
            sp.wait_ge(S["stored"], 32)

        @block.tensor
        def _(pe):
            pe.wait_ge(S["loaded"], 16 * (NU + 5))
            for s in range(2):
                for j in range(16):
                    last = pe.matmul(ps[:, 7, s:s + 1], w1[:, s, j], pe_cols[:, s, j:j + 1], start=(j == 0), stop=(j == 15))
            last.then_inc(S["hid_mm"], 1)
            for u in range(NU):
                pe.wait_ge(S["paired_set"], u + 1)
                for sg in range(4):
                    last = pe.transpose(ps[:, u, sg * P:(sg + 1) * P], paired[:, u, sg].rearrange("p t d -> p (t d)"), ident[:])
                last.then_inc(S["tr"], 1)
            pe.wait_ge(S["copied"], NU)
            for s in range(2):
                for j in range(16):
                    last = pe.matmul(ps[:, 4 + s, 0:2 * NB], w1[:, s, j], raw_t[:, 2 * s:2 * s + 2, j:j + 8 * (NB - 1) + 1:8], start=(j == 0), stop=(j == 15))
                last.then_inc(S["hid_mm"], 1)
            pe.wait_ge(S["gelu_done"], 2)
            for s in range(2):
                for g in range(2):
                    last = pe.matmul(ps[0:NB, 6, (2 * s + g) * HD:(2 * s + g + 1) * HD], hid[:, s, g], w2[:, s], start=True, stop=True)
            last.then_inc(S["out_mm"], 1)
            pe.wait_ge(S["kv_set"], 2)
            pe.transpose(ps[:, 0, 0:NB], kv[:, 0], ident[0:NB, 0:NB]).then_inc(S["kt_tr"], 1)

        @block.scalar
        def _(act):
            act.wait_ge(S["hid_mm"], 1)
            act.activation(hid_bias[:], ps[:, 7, 0:2], ACT.Copy).then_inc(S["bias_set"], 1)
            act.wait_ge(S["bias_set"], 1)
            for s in range(2):
                act.wait_ge(S["hid_mm"], s + 2)
                act.activation(hid[:, s].rearrange("p g i -> p (g i)"), ps[:, 4 + s, 0:2 * NB], ACT.Gelu_apprx_tanh, bias=hid_bias[:, s:s + 1]).then_inc(S["gelu_done"], 1)
            act.wait_ge(S["var_set"], 1)
            act.activation(ssq[:], ssq[:], ACT.Sqrt).then_inc(S["root"], 1)

        @block.vector
        def _(dve):
            dve.wait_ge(S["loaded"], 16 * (NU + 5))
            for u in range(NU):
                dve.tensor_copy(paired[:, u], raw[:, u].rearrange("p t (s d) -> p s t d", d=HD)).then_inc(S["paired_set"], 1)
            for u in range(NU):
                dve.wait_ge(S["tr"], u + 1)
                dve.tensor_copy(raw_t[:, :, u * P:(u + 1) * P], ps[:, u, :].rearrange("p (s t) -> p s t", t=P)).then_inc(S["copied"], 1)
            dve.wait_ge(S["out_mm"], 1)
            dve.tensor_copy(kv[:].rearrange("p s c -> p (s c)"), ps[0:NB, 6, 0:256]).then_inc(S["kv_set"], 1)
            dve.drain()
            dve.tensor_tensor(sq[:], kv[:, 0], kv[:, 0], ALU.mult)
            dve.drain()
            dve.tensor_reduce(ssq[:], sq[:].rearrange("p (g d) -> p g d", g=2), AX.X, ALU.add)
            dve.drain()
            dve.tensor_scalar(ssq[:], ssq[:], 1.0 / HD, EPS, ALU.mult, ALU.add).then_inc(S["var_set"], 1)
            dve.wait_ge(S["root"], 1)
            dve.reciprocal(ssq[:], ssq[:])
            dve.drain()
            for g in range(2):
                k = kv[:, 0, g * HD:(g + 1) * HD]
                last = dve.scalar_tensor_tensor(out=k, in0=k, scalar=ssq[:, g:g + 1], in1=k_norm[0:NB], op0=ALU.mult, op1=ALU.mult)
            last.then_inc(S["kv_set"], 1)
            dve.wait_ge(S["kt_tr"], 1)
            dve.tensor_copy(kt[:], ps[:, 0, 0:NB]).then_inc(S["kt_copied"], 1)


def prompt_attention_stage(nc, heads_t, qkv, tok, strips, kt_cmp, v_cmp, flip_in, ident_in, out_rows):
    NT = TP // P
    NB = TP // CMP_STRIDE - 1
    TW = 1920
    with ExitStack() as ctx:
        new_sem = ctx.enter_context(stage_semaphores(nc))
        sb = lambda name, shape: ctx.enter_context(nc.sbuf_tensor("pa_" + name, shape, F32))
        q_t = sb("q_t", [HD, 2, TP])
        ks_t = sb("ks_t", [HD, 2, TP])
        kw_t = sb("kw_t", [HD, 2, TP])
        kc_t = sb("kc_t", [HD, 2, NB])
        v_all = sb("v_all", [P, 3, NT, P])
        vc = sb("vc", [NB, P])
        flip = sb("flip", [P, P])
        ident = sb("ident", [P, P])
        strip = sb("strip", [P, 2, TW])
        strip_w = sb("strip_w", [P, 2, P])
        table = sb("table", [P, TW])
        far_w = sb("far_w", [P, P])
        s_sel = sb("s_sel", [P, 2, TP])
        s_win = sb("s_win", [P, 2, 5 * P + NB])
        p_sel = sb("p_sel", [P, NT, P])
        p_win = sb("p_win", [P, 6, P])
        gates = sb("gates", [P, NT, 3, NH])
        any_cmp = sb("any_cmp", [P, 1])
        cols = sb("cols", [P, 2, 16])
        out = sb("out", [P, 2, NT, HD])
        ps = ctx.enter_context(nc.psum_tensor("pa_ps", [P, 8, BANK], F32))
        S = {n: new_sem("pa_" + n) for n in
             ("const_in gate_exp gates_set strip_used flip_mm table_set sel_mm win_mm sel_neg win_neg exp_done pt_tr pt_copied_a pt_copied_v o_mm o_read tile_set passed anyc").split()}
        out_stored = [new_sem(f"pa_out_stored{n}") for n in range(2)]
        head_in = [new_sem(f"pa_head_in{n}") for n in range(2)]
        block = ctx.enter_context(nc.Block())
        NTB = 4

        def win_first(i):
            return max(0, i - 4)

        def p_all(n, k, rows):
            return p_sel[0:rows, k] if k < NT else p_win[0:rows, k - NT]

        base_chunk = [0]
        n_tiles = []
        for h in range(NH):
            for i in range(NT):
                n_tiles.append(i + 1 + (i - win_first(i) + 1) + 1)
                base_chunk.append(base_chunk[-1] + (n_tiles[-1] + 3) // 4)

        @block.sync
        def _(sp):
            consts = [(flip[:], flip_in), (ident[:], ident_in), (vc[:], v_cmp)]
            for g in range(NG):
                consts += [(ks_t[:, g], heads_t[4 * P + g * HD:4 * P + (g + 1) * HD, 0:TP]), (kw_t[:, g], heads_t[5 * P + g * HD:5 * P + (g + 1) * HD, 0:TP]),
                           (kc_t[:, g], kt_cmp[g * HD:(g + 1) * HD, :])]
            consts += [(v_all[:, 0], qkv[0:TP, 512 + 384:512 + 512].rearrange("(n p) c -> p n c", p=P)),
                       (v_all[:, 1], qkv[0:TP, 1024 + 128:1024 + 256].rearrange("(n p) c -> p n c", p=P)),
                       (gates[:].rearrange("p n a h -> p n (a h)"), tok[0:TP, C_NGATE:C_NGATE + 24].rearrange("(n p) c -> p n c", p=P))]
            for dst, src in consts:
                sp.dma_start(dst, src).then_inc(S["const_in"], 16)
            for h in range(NH):
                if h >= 2:
                    sp.wait_ge(S["tile_set"], NT * (h - 1))
                sp.dma_start(q_t[:, h % 2], heads_t[h * HD:(h + 1) * HD, 0:TP]).then_inc(head_in[h % 2], 16)
                sp.dma_start(strip[:, h % 2], bass.AP(tensor=strips.tensor, offset=strips[0, h, 0:1].offset, ap=[[1, P], [1, TW]])).then_inc(head_in[h % 2], 16)
                sp.dma_start(strip_w[:, h % 2], bass.AP(tensor=strips.tensor, offset=strips[1, h, 384:385].offset, ap=[[1, P], [1, P]])).then_inc(head_in[h % 2], 16)

        @block.gpsimd
        def _(pool):
            pool.memset(any_cmp[:], 1.0).then_inc(S["anyc"], 1)
            pool.wait_ge(S["anyc"], 1)
            pool.affine_select(out=any_cmp[:], in_=any_cmp[:], compare_op=ALU.is_ge, fill=0.0, base=-(CMP_LEN - 1), pattern=[[0, 1]], channel_multiplier=1).then_inc(S["anyc"], 1)
            for h in range(NH):
                pool.wait_ge(S["tile_set"], NT * (h + 1))
                pool.dma_start(out_rows[:, h * HD:(h + 1) * HD].rearrange("(n p) d -> p n d", p=P), out[:, h % 2]).then_inc(out_stored[h % 2], 16)
            for x in range(2):
                pool.wait_ge(out_stored[x], 16 * (NH // 2))

        @block.tensor
        def _(pe):
            pe.wait_ge(S["const_in"], 16 * 12)

            def scores(h, i):
                g, q = h // NR, q_t[:, h % 2, i * P:(i + 1) * P]
                n = h * NT + i
                if n >= 1:
                    pe.wait_ge(S["sel_neg"], n)
                    pe.wait_ge(S["win_neg"], n)
                hi = (i + 1) * P
                for a in range(0, hi, BANK):
                    z = min(a + BANK, hi)
                    last = pe.matmul(ps[:, a // BANK, 0:z - a], q, ks_t[:, g, a:z], start=True, stop=True)
                last.then_inc(S["sel_mm"], 1)
                w0 = win_first(i) * P
                nw = hi - w0
                m = min(nw, BANK)
                pe.matmul(ps[:, 2, 0:m], q, kw_t[:, g, w0:w0 + m], start=True, stop=True)
                if nw > BANK:
                    pe.matmul(ps[:, 3, 0:nw - BANK], q, kw_t[:, g, w0 + BANK:hi], start=True, stop=True)
                pe.matmul(ps[:, 3, P:P + NB], q, kc_t[:, g], start=True, stop=True).then_inc(S["win_mm"], 1)

            def values(h, i):
                g = h // NR
                n = h * NT + i
                pe.wait_ge(S["exp_done"], 3 * (n + 1))
                tiles = [("s", k) for k in range(i + 1)] + [("w", k) for k in range(i - win_first(i) + 1)] + [("c", 0)]
                for c in range(0, len(tiles), 4):
                    m = base_chunk[n] + c // 4
                    if m >= 3:
                        pe.wait_ge(S["pt_copied_v"], m - 2)
                    for x, (kind, k) in enumerate(tiles[c:c + 4]):
                        if kind == "s":
                            src, w = s_sel[:, n % 2, k * P:(k + 1) * P], P
                        elif kind == "w":
                            src, w = s_win[:, n % 2, k * P:(k + 1) * P], P
                        else:
                            src, w = s_win[:, n % 2, 5 * P:5 * P + NB], NB
                        last = pe.transpose(ps[0:w, 4 + m % 3, x * P:(x + 1) * P], src, ident[:])
                    last.then_inc(S["pt_tr"], 1)
                if n >= 1:
                    pe.wait_ge(S["tile_set"], n)
                pe.wait_ge(S["pt_copied_v"], base_chunk[n] + (len(tiles) + 3) // 4)
                for k in range(i + 1):
                    pe.matmul(ps[:, 7, 0:HD], p_all(n, k, P), v_all[:, 0, k, g * HD:(g + 1) * HD], start=(k == 0), stop=(k == i))
                w0 = win_first(i)
                for k in range(w0, i + 1):
                    pe.matmul(ps[:, 7, HD:2 * HD], p_all(n, i + 1 + k - w0, P), v_all[:, 1, k, g * HD:(g + 1) * HD], start=(k == w0), stop=(k == i))
                pe.matmul(ps[:, 7, 2 * HD:3 * HD], p_all(n, len(tiles) - 1, NB), vc[:, g * HD:(g + 1) * HD], start=True, stop=True).then_inc(S["o_mm"], 1)

            for h in range(NH):
                pe.wait_ge(head_in[h % 2], 48 * (h // 2 + 1))
                for n in range(NTB):
                    a, z = n * BANK, min((n + 1) * BANK, TW)
                    if h >= 1:
                        pe.wait_ge(S["sel_neg"], NT * h)
                        pe.wait_ge(S["win_neg"], NT * h)
                    pe.matmul(ps[:, n, 0:z - a], flip[:], strip[:, h % 2, a:z], start=True, stop=True)
                if h >= 1:
                    values(h - 1, NT - 1)
                    pe.wait_ge(S["pt_copied_v"], base_chunk[NT * h])
                pe.matmul(ps[:, 4, 0:P], flip[:], strip_w[:, h % 2], start=True, stop=True).then_inc(S["flip_mm"], 1)
                pe.wait_ge(S["table_set"], h + 1)
                for i in range(NT):
                    scores(h, i)
                    if i >= 1:
                        values(h, i - 1)
            values(NH - 1, NT - 1)

        @block.scalar
        def _(act):
            act.wait_ge(S["const_in"], 16 * 12)
            act.activation(gates[:], gates[:], ACT.Exp, scale=-1.0).then_inc(S["gate_exp"], 1)
            for h in range(NH):
                for i in range(NT):
                    n = h * NT + i
                    hi = (i + 1) * P
                    nw = hi - win_first(i) * P
                    c = cols[:, n % 2]
                    act.wait_ge(S["sel_neg"], n + 1)
                    act.activation(s_sel[:, n % 2, 0:hi], s_sel[:, n % 2, 0:hi], ACT.Exp, bias=c[:, 0:1], accum_out=c[:, 4:5]).then_inc(S["exp_done"], 1)
                    act.wait_ge(S["win_neg"], n + 1)
                    act.activation(s_win[:, n % 2, 0:nw], s_win[:, n % 2, 0:nw], ACT.Exp, bias=c[:, 1:2], accum_out=c[:, 5:6]).then_inc(S["exp_done"], 1)
                    act.activation(s_win[:, n % 2, 5 * P:5 * P + NB], s_win[:, n % 2, 5 * P:5 * P + NB], ACT.Exp, bias=c[:, 2:3], accum_out=c[:, 6:7]).then_inc(S["exp_done"], 1)

        @block.vector
        def _(dve):
            dve.wait_ge(S["gate_exp"], 1)
            dve.tensor_scalar(gates[:], gates[:], 1.0, None, ALU.add)
            dve.drain()
            dve.reciprocal(gates[:], gates[:])
            dve.wait_ge(S["anyc"], 2)
            dve.drain()
            dve.tensor_scalar(gates[:, 0, 0], gates[:, 0, 0], any_cmp[:], None, ALU.mult)

            def bias_and_max(h, i):
                n = h * NT + i
                hi = (i + 1) * P
                c = cols[:, n % 2]
                s, w = s_sel[:, n % 2], s_win[:, n % 2]
                off = (NT - 1) * P - i * P
                dve.wait_ge(S["sel_mm"], n + 1)
                if n >= 2:
                    dve.wait_ge(S["pt_tr"], base_chunk[n - 1])
                for a in range(0, hi, BANK):
                    z = min(a + BANK, hi)
                    dve.tensor_tensor(s[:, a:z], ps[:, a // BANK, 0:z - a], table[:, off + a:off + z], ALU.add)
                dve.drain()
                dve.tensor_reduce(c[:, 8:9], s[:, 0:hi], AX.X, ALU.max)
                dve.drain()
                dve.tensor_scalar(c[:, 0:1], c[:, 8:9], -1.0, None, ALU.mult).then_inc(S["sel_neg"], 1)
                dve.wait_ge(S["win_mm"], n + 1)
                w0 = win_first(i) * P
                nw = hi - w0
                m = min(nw, BANK)
                if nw > BANK:
                    dve.tensor_tensor(w[:, 0:P], ps[:, 2, 0:P], far_w[:], ALU.add)
                    dve.tensor_tensor(w[:, P:m], ps[:, 2, P:m], table[:, off + w0 + P:off + w0 + m], ALU.add)
                    dve.tensor_tensor(w[:, m:nw], ps[:, 3, 0:nw - BANK], table[:, off + w0 + m:off + hi], ALU.add)
                else:
                    dve.tensor_tensor(w[:, 0:m], ps[:, 2, 0:m], table[:, off + w0:off + hi], ALU.add)
                c0 = off + CMP_LEN - 1
                dve.tensor_tensor(w[:, 5 * P:5 * P + NB], ps[:, 3, P:P + NB], table[:, c0:c0 + CMP_STRIDE * (NB - 1) + 1:CMP_STRIDE], ALU.add)
                dve.drain()
                dve.tensor_reduce(c[:, 9:10], w[:, 0:nw], AX.X, ALU.max)
                dve.tensor_reduce(c[:, 10:11], w[:, 5 * P:5 * P + NB], AX.X, ALU.max)
                dve.drain()
                dve.tensor_scalar(c[:, 1:3], c[:, 9:11], -1.0, None, ALU.mult).then_inc(S["win_neg"], 1)

            def finish(h, i):
                n = h * NT + i
                c = cols[:, n % 2]
                nt = n_tiles[n]
                for k0 in range(0, nt, 4):
                    m = base_chunk[n] + k0 // 4
                    dve.wait_ge(S["pt_tr"], m + 1)
                    if k0 == 0 and n >= 1:
                        dve.wait_ge(S["o_mm"], n)
                    k1 = min(k0 + 4, nt)
                    for a, z, dst in ((k0, min(k1, NT), p_sel), (max(k0, NT), k1, p_win)):
                        for a_, z_, rows in ((a, min(z, nt - 1), P), (max(a, nt - 1), z, NB)):
                            if z_ > a_:
                                base = 0 if dst is p_sel else NT
                                dve.tensor_copy(dst[0:rows, a_ - base:z_ - base], ps[0:rows, 4 + m % 3, (a_ - k0) * P:(z_ - k0) * P].rearrange("p (a b) -> p a b", b=P))
                    dve.drain().then_inc(S["pt_copied_v"], 1)
                dve.wait_ge(S["exp_done"], 3 * (n + 1))
                dve.reciprocal(c[:, 12:15], c[:, 4:7])
                dve.drain()
                for k, br in ((0, 1), (1, 2), (2, 0)):
                    dve.tensor_tensor(c[:, 12 + k:13 + k], c[:, 12 + k:13 + k], gates[:, i, br, h:h + 1], ALU.mult)
                dve.drain()
                dve.wait_ge(S["o_mm"], n + 1)
                if i == 0 and h >= 2:
                    dve.wait_ge(out_stored[h % 2], 16 * (h // 2))
                o = out[:, h % 2, i]
                dve.tensor_scalar(o, ps[:, 7, 0:HD], c[:, 12:13], None, ALU.mult)
                dve.drain()
                dve.scalar_tensor_tensor(out=o, in0=ps[:, 7, HD:2 * HD], scalar=c[:, 13:14], in1=o, op0=ALU.mult, op1=ALU.add)
                dve.drain()
                dve.scalar_tensor_tensor(out=o, in0=ps[:, 7, 2 * HD:3 * HD], scalar=c[:, 14:15], in1=o, op0=ALU.mult, op1=ALU.add).then_inc(S["tile_set"], 1)

            for h in range(NH):
                if h >= 1:
                    finish(h - 1, NT - 1)
                dve.wait_ge(S["flip_mm"], h + 1)
                for n in range(NTB):
                    a, z = n * BANK, min((n + 1) * BANK, TW)
                    dve.tensor_copy(table[:, a:z], ps[:, n, 0:z - a])
                dve.tensor_copy(far_w[:], ps[:, 4, 0:P])
                dve.drain().then_inc(S["table_set"], 1)
                for i in range(NT):
                    bias_and_max(h, i)
                    if i >= 1:
                        finish(h, i - 1)
            finish(NH - 1, NT - 1)


HC = 8
LB_FLOOR = 1e-30


def hgrn_stage(nc, feat, tok, lb_logits, out_gain, state_in, diag_in, ident_in, own_in, out_t, state_p, state_s):
    NHG = 4
    NTL = TP // P
    NBK = P // HC
    NBT = T // HC
    with ExitStack() as ctx:
        new_sem = ctx.enter_context(stage_semaphores(nc))
        sb = lambda name, shape: ctx.enter_context(nc.sbuf_tensor("hg_" + name, shape, F32))
        raw = sb("raw", [P, 3, T])
        v = sb("v", [P, NTL + 1, P])
        state0 = sb("state0", [P, SB, P])
        f = sb("f", [P, T])
        k = sb("k", [P, T])
        q = sb("q", [P, T])
        gate = sb("gate", [P, T])
        sig = sb("sig", [P, 2, T])
        decay = sb("decay", [P, T])
        q_dec = sb("q_dec", [P, T])
        q_tile = sb("q_tile", [P, TP])
        before = sb("before", [P, NTL, NBK + 1])
        kb = sb("kb", [P, 2, T])
        kt = sb("kt", [P, 2, TP])
        attn = sb("attn", [P, NTL + 1, P])
        k_rows = sb("k_rows", [P, NTL + 1, P])
        v_own = sb("v_own", [SB * ST, SB, P])
        states = sb("states", [P, NTL + 1, P])
        s_new = sb("s_new", [P, SB, P])
        o = sb("o", [P, T])
        rstd = sb("rstd", [P, T])
        lb = sb("lb", [P, 6, NHG])
        gain = sb("gain", [P, 1])
        diag = sb("diag", [P, P])
        ident = sb("ident", [P, P])
        own = sb("own", [SB * ST, SB])
        ones = sb("ones", [P, P])
        ps = ctx.enter_context(nc.psum_tensor("hg_ps", [P, 8, BANK], F32))
        S = {n: new_sem("hg_" + n) for n in
             ("const_in ones_set lb_sub lb_exp lb_set raw_in v_in state_in sig_done1 sig_done2 sig_used raw_used kb_set diag_mm kt_set off_mm attn_set "
              "tr rows_copied u_mm states_set o_mm o_copied sq_done ssq_mm var_set root out_set stored state_stored passed k_end v_own_set s_new_set").split()}
        block = ctx.enter_context(nc.Block())
        blocks = lambda t: t.rearrange("p (b j) -> p b j", j=HC)
        STEPS = NBK + 1

        @block.sync
        def _(sp):
            for dst, src in ((lb[:, 0], lb_logits), (gain[:], out_gain), (diag[:], diag_in), (ident[:], ident_in), (own[:], own_in)):
                sp.dma_start(dst, src).then_inc(S["const_in"], 16)
            with sp.Fori(0, NHG) as h:
                sp.wait_ge(S["raw_used"], h * 3)
                sp.sem_inc(S["passed"], 1)
                for n, row in enumerate((R_HQ, R_HF, R_HG)):
                    sp.dma_start(raw[:, n], feat[bass.ds(h * P + row, P), :]).then_inc(S["raw_in"], 16)
                sp.wait_ge(S["o_mm"], h)
                sp.sem_inc(S["passed"], 1)
                sp.wait_ge(S["v_own_set"], h)
                sp.sem_inc(S["passed"], 1)
                sp.dma_start(v[:, 0:NTL], tok[0:TP, bass.ds(h * P + C_HI, P)].rearrange("(n p) c -> p n c", p=P)).then_inc(S["v_in"], 16)
                sp.dma_start(v[0:SB * ST, NTL], tok[TP:T, bass.ds(h * P + C_HI, P)]).then_inc(S["v_in"], 16)
                sp.wait_ge(S["s_new_set"], h)
                sp.sem_inc(S["passed"], 1)
                sp.dma_start(state0[:], state_in[:, bass.ds(h, 1)].rearrange("b o d v -> (o d) b v")).then_inc(S["state_in"], 16)

        @block.gpsimd
        def _(pool):
            pool.memset(ones[:], 1.0).then_inc(S["ones_set"], 1)
            with pool.Fori(0, NHG) as h:
                pool.wait_ge(S["s_new_set"], h + 1)
                pool.sem_inc(S["passed"], 1)
                pool.dma_start(state_p[bass.ds(h, 1)].rearrange("o d v -> (o d) v"), states[:, NTL]).then_inc(S["state_stored"], 16)
                pool.dma_start(state_s[:, bass.ds(h, 1)].rearrange("b o d v -> (o d) b v"), s_new[:]).then_inc(S["state_stored"], 16)
                pool.wait_ge(S["out_set"], h + 1)
                pool.sem_inc(S["passed"], 1)
                pool.dma_start(out_t[bass.ds(h * P, P), :], o[:]).then_inc(S["stored"], 16)
            pool.wait_ge(S["stored"], 16 * NHG)
            pool.wait_ge(S["state_stored"], 32 * NHG)

        @block.scalar
        def _(act):
            act.wait_ge(S["lb_sub"], 1)
            act.activation(lb[:, 1], lb[:, 1], ACT.Exp).then_inc(S["lb_exp"], 1)
            with act.Fori(0, NHG) as h:
                act.wait_ge(S["raw_in"], (h + 1) * 48)
                act.wait_ge(S["sig_used"], h * 4)
                act.activation(sig[:, 0], raw[:, 1], ACT.Sigmoid).then_inc(S["sig_done1"], 1)
                act.activation(sig[:, 1], raw[:, 1], ACT.Sigmoid, scale=-1.0).then_inc(S["sig_done1"], 1)
                act.wait_ge(S["sig_used"], h * 4 + 1)
                act.activation(sig[:, 0], raw[:, 0], ACT.Sigmoid).then_inc(S["sig_done2"], 1)
                act.wait_ge(S["sig_used"], h * 4 + 2)
                act.activation(sig[:, 1], raw[:, 2], ACT.Sigmoid).then_inc(S["sig_done2"], 1)
                for n in range(3):
                    act.wait_ge(S["tr"], h * 3 + (n + 1))
                    if n < 2:
                        act.activation(k_rows[:, 4 * n:4 * n + 4].rearrange("p a d -> p (a d)"), ps[:, 5 + n, :], ACT.Copy).then_inc(S["rows_copied"], 1)
                    else:
                        act.activation(k_rows[0:SB * ST, NTL], ps[0:SB * ST, 7, 0:P], ACT.Copy).then_inc(S["rows_copied"], 1)
                act.wait_ge(S["o_mm"], h + 1)
                for n, (a, z) in enumerate(COLS):
                    act.activation(rstd[:, a:z], ps[:, n, 0:z - a], ACT.Square).then_inc(S["sq_done"], 1)
                act.wait_ge(S["var_set"], h + 1)
                act.activation(rstd[:], rstd[:], ACT.Sqrt).then_inc(S["root"], 1)

        @block.tensor
        def _(pe):
            pe.wait_ge(S["const_in"], 80)
            pe.wait_ge(S["ones_set"], 1)
            with pe.Fori(0, NHG) as h:
                pe.wait_ge(S["o_copied"], h)
                for j in range(HC):
                    pe.wait_ge(S["kb_set"], h * HC + (j + 1))
                    for t, (t0, tn) in enumerate(TILES):
                        last = pe.matmul(ps[0:tn, t // 4, (t % 4) * P + j:(t % 4) * P + tn - HC + j + 1:HC], kb[:, j % 2, t0:t0 + tn],
                                         q[:, t0 + j:t0 + tn - HC + j + 1:HC], start=True, stop=True)
                    last.then_inc(S["diag_mm"], 1)
                for i in range(1, NBK):
                    pe.wait_ge(S["kt_set"], h * NBK + i)
                    for t in range(NTL):
                        last = pe.matmul(ps[:, 3 + t // 4, (t % 4) * P + i * HC:(t % 4) * P + (i + 1) * HC], kt[:, i % 2, t * P:(t + 1) * P],
                                         q_dec[:, t * P + i * HC:t * P + (i + 1) * HC], start=True, stop=True)
                    last.then_inc(S["off_mm"], 1)
                pe.wait_ge(S["kt_set"], h * NBK + NBK)
                for t in range(NTL):
                    last = pe.transpose(ps[:, 5 + t // 4, (t % 4) * P:(t % 4 + 1) * P], kt[:, NBK % 2, t * P:(t + 1) * P], ident[:])
                    if t % 4 == 3:
                        last.then_inc(S["tr"], 1)
                pe.transpose(ps[0:SB * ST, 7, 0:P], kb[:, (HC - 1) % 2, TP:T], ident[:]).then_inc(S["tr"], 1)
                pe.wait_ge(S["attn_set"], h + 1)
                pe.wait_ge(S["rows_copied"], h * 3 + 3)
                pe.wait_ge(S["v_in"], h * 32 + 32)
                for t in range(NTL):
                    pe.matmul(ps[:, 3 + t // 4, (t % 4) * P:(t % 4 + 1) * P], k_rows[:, t], v[:, t], start=True, stop=True)
                pe.wait_ge(S["v_own_set"], h + 1)
                for n in range(2):
                    last = pe.matmul(ps[:, 5 + n, :], k_rows[0:SB * ST, NTL], v_own[:, 4 * n:4 * n + 4].rearrange("p b v -> p (b v)"), start=True, stop=True)
                last.then_inc(S["u_mm"], 1)
                pe.wait_ge(S["states_set"], h + 1)
                pe.wait_ge(S["state_in"], h * 16 + 16)
                for t in range(NTL):
                    dst = ps[:, t // 4, (t % 4) * P:(t % 4 + 1) * P]
                    pe.matmul(dst, v[:, t], attn[:, t], start=True, stop=(t == 0))
                    if t:
                        pe.matmul(dst, states[:, t], q_tile[:, t * P:(t + 1) * P], start=False, stop=True)
                for b in range(SB):
                    dst = ps[:, 2, b * ST:(b + 1) * ST]
                    pe.matmul(dst, v[0:SB * ST, NTL], attn[0:SB * ST, NTL, b * ST:(b + 1) * ST], start=True, stop=False)
                    last = pe.matmul(dst, state0[:, b], q_dec[:, TP + b * ST:TP + (b + 1) * ST], start=False, stop=True)
                last.then_inc(S["o_mm"], 1)
                pe.wait_ge(S["sq_done"], h * 3 + 3)
                for n, (a, z) in enumerate(COLS):
                    last = pe.matmul(ps[:, (3, 4, 7)[n], 0:z - a], ones[:], rstd[:, a:z], start=True, stop=True)
                last.then_inc(S["ssq_mm"], 1)

        @block.vector
        def _(dve):
            dve.wait_ge(S["const_in"], 80)
            dve.tensor_tensor(lb[:, 1], lb[:, 0], lb[:, 0], ALU.subtract).then_inc(S["lb_sub"], 1)
            dve.wait_ge(S["lb_exp"], 1)
            dve.reciprocal(lb[:, 2], lb[:, 1])
            dve.drain()
            dve.tensor_tensor(lb[:, 2], lb[:, 1], lb[:, 2], ALU.mult)
            dve.drain()
            dve.tensor_tensor(lb[:, 3], lb[:, 2], lb[:, 2], ALU.subtract)
            dve.drain()
            dve.tensor_scalar(lb[:, 4], lb[:, 3], LB_FLOOR, None, ALU.max)
            dve.tensor_scalar(lb[:, 5], lb[:, 3], -1.0, 1.0, ALU.mult, ALU.add)
            dve.drain()
            f8, k8, q8, d8, qd8 = blocks(f[:]), blocks(k[:]), blocks(q[:]), blocks(decay[:]), blocks(q_dec[:])
            with dve.Fori(0, NHG) as h:
                floor, rest = lb[:, 4, bass.ds(h, 1)], lb[:, 5, bass.ds(h, 1)]
                dve.wait_ge(S["sig_done1"], h * 2 + 2)
                dve.tensor_scalar(f[:], sig[:, 0], rest, floor, ALU.mult, ALU.add).then_inc(S["sig_used"], 1)
                dve.tensor_scalar(k[:], sig[:, 1], rest, None, ALU.mult).then_inc(S["sig_used"], 1)
                dve.wait_ge(S["sig_done2"], h * 2 + 2)
                dve.tensor_tensor(q[:], sig[:, 0], raw[:, 0], ALU.mult).then_inc(S["sig_used"], 1)
                dve.tensor_tensor(gate[:], sig[:, 1], raw[:, 2], ALU.mult).then_inc(S["sig_used"], 1)
                dve.drain().then_inc(S["raw_used"], 3)
                dve.memset(kb[:], 0.0)
                dve.memset(kt[:], 0.0)
                dve.tensor_copy(d8[:, :, 0], f8[:, :, 0])
                dve.drain()
                for j in range(HC):
                    new, old = blocks(kb[:, j % 2]), blocks(kb[:, 1 - j % 2])
                    if j >= 2:
                        dve.wait_ge(S["diag_mm"], h * HC + (j - 1))
                    if j:
                        dve.tensor_tensor(new[:, :, 0:j], old[:, :, 0:j], f8[:, :, j:j + 1].to_broadcast([P, NBT, j]), ALU.mult)
                        dve.tensor_tensor(d8[:, :, j], d8[:, :, j - 1], f8[:, :, j], ALU.mult)
                    dve.tensor_copy(new[:, :, j], k8[:, :, j])
                    dve.drain().then_inc(S["kb_set"], 1)
                dve.tensor_tensor(q_dec[:], q[:], decay[:], ALU.mult)
                dve.memset(before[:, :, 0:1], 1.0)
                dve.drain()
                ends = d8[:, 0:TP // HC, HC - 1].rearrange("p (t b) -> p t b", b=NBK)
                kb_end = kb[:, (HC - 1) % 2, 0:TP].rearrange("p (t s) -> p t s", s=P)
                for i in range(1, NBK + 1):
                    new, old = (kt[:, x].rearrange("p (t s) -> p t s", s=P) for x in (i % 2, 1 - i % 2))
                    if i >= 3:
                        dve.wait_ge(S["off_mm"], h * (NBK - 1) + (i - 2))
                    n = (i - 1) * HC
                    if n:
                        dve.tensor_tensor(new[:, :, 0:n], old[:, :, 0:n], ends[:, :, i - 1:i].to_broadcast([P, NTL, n]), ALU.mult)
                    dve.tensor_tensor(before[:, :, i], before[:, :, i - 1], ends[:, :, i - 1], ALU.mult)
                    dve.tensor_copy(new[:, :, n:n + HC], kb_end[:, :, n:n + HC])
                    dve.drain().then_inc(S["kt_set"], 1)
                dve.tensor_tensor(q_tile[:].rearrange("p (t b j) -> p t b j", b=NBK, j=HC), q_dec[:, 0:TP].rearrange("p (t b j) -> p t b j", b=NBK, j=HC),
                                  before[:, :, 0:NBK].unsqueeze(3).to_broadcast([P, NTL, NBK, HC]), ALU.mult)
                dve.wait_ge(S["v_in"], h * 32 + 32)
                dve.tensor_tensor(v_own[:], v[0:SB * ST, NTL:NTL + 1].to_broadcast([SB * ST, SB, P]), own[:].unsqueeze(2).to_broadcast([SB * ST, SB, P]), ALU.mult).then_inc(S["v_own_set"], 1)
                dve.wait_ge(S["diag_mm"], h * HC + HC)
                dve.wait_ge(S["off_mm"], h * (NBK - 1) + (NBK - 1))
                for n in range(2):
                    dve.tensor_tensor(attn[:, 4 * n:4 * n + 4], ps[:, n, :].rearrange("p (t s) -> p t s", s=P), diag[:].unsqueeze(1).to_broadcast([P, 4, P]), ALU.mult)
                dve.tensor_tensor(attn[0:SB * ST, NTL, 0:SB * ST], ps[0:SB * ST, 2, 0:SB * ST], diag[0:SB * ST, 0:SB * ST], ALU.mult)
                dve.drain()
                for n in range(2):
                    a = attn[:, 4 * n:4 * n + 4, HC:P]
                    dve.tensor_tensor(a, a, ps[:, 3 + n, :].rearrange("p (t s) -> p t s", s=P)[:, :, HC:P], ALU.add)
                dve.memset(states[:, 0], 0.0)
                dve.drain().then_inc(S["attn_set"], 1)
                dve.wait_ge(S["u_mm"], h + 1)
                dve.wait_ge(S["state_in"], h * 16 + 16)
                dve.wait_ge(S["state_stored"], h * 32)
                for t in range(NTL):
                    dve.scalar_tensor_tensor(out=states[:, t + 1], in0=states[:, t], scalar=before[:, t, NBK:NBK + 1], in1=ps[:, 3 + t // 4, (t % 4) * P:(t % 4 + 1) * P],
                                             op0=ALU.mult, op1=ALU.add)
                    dve.drain()
                dve.sem_inc(S["states_set"], 1)
                dve.tensor_tensor(s_new[:], state0[:], d8[:, TP // HC:NBT, HC - 1:HC].to_broadcast([P, SB, P]), ALU.mult)
                dve.drain()
                for n in range(2):
                    last = dve.tensor_tensor(s_new[:, 4 * n:4 * n + 4], s_new[:, 4 * n:4 * n + 4], ps[:, 5 + n, :].rearrange("p (b v) -> p b v", v=P), ALU.add)
                last.then_inc(S["s_new_set"], 1)
                dve.wait_ge(S["o_mm"], h + 1)
                dve.wait_ge(S["sq_done"], h * 3 + 3)
                dve.wait_ge(S["stored"], h * 16)
                for n, (a, z) in enumerate(COLS):
                    dve.scalar_tensor_tensor(out=o[:, a:z], in0=ps[:, n, 0:z - a], scalar=gain[:], in1=gate[:, a:z], op0=ALU.mult, op1=ALU.mult)
                dve.drain().then_inc(S["o_copied"], 1)
                dve.wait_ge(S["ssq_mm"], h + 1)
                for n, (a, z) in enumerate(COLS):
                    last = dve.tensor_scalar(rstd[:, a:z], ps[:, (3, 4, 7)[n], 0:z - a], 1.0 / P, EPS, ALU.mult, ALU.add)
                last.then_inc(S["var_set"], 1)
                dve.wait_ge(S["root"], h + 1)
                dve.reciprocal(rstd[:], rstd[:])
                dve.drain()
                dve.tensor_tensor(o[:], o[:], rstd[:], ALU.mult).then_inc(S["out_set"], 1)


SC = 8
NCH = TP // SC
NCA = T // SC
NGR, GW, NST = 32, 16, 64
NPR = NGR // 2
TWO_PI = 6.283185307179586
TWO_PI_HI = 6.28125
ROUND = 12582912.0


def s5_state_stage(nc, tok, a_re, a_im, log_dt, b_in, c_in, d_in, h0_in, ident_in, rows_out, h_prompt, h_sample):
    with ExitStack() as ctx:
        new_sem = ctx.enter_context(stage_semaphores(nc))
        sb = lambda name, shape: ctx.enter_context(nc.sbuf_tensor("ss_" + name, shape, F32))
        u = sb("u", [P, NGR, NCA])
        rows = sb("rows", [P, SC, 512])
        by_group = sb("by_group", [P, NGR, P])
        small = sb("small", [P, NGR * P])
        toep = sb("toep", [P, NGR, P])
        w_t = sb("w_t", [P, NPR, 2, P])
        w_h = sb("w_h", [P, 2, NPR, NCA])
        ca = sb("ca", [P, 2, NPR, (SC + 1) * GW])
        x = sb("x", [P, 2, NPR, NCA])
        turn = sb("turn", [P, 2, NPR, NCH])
        m0 = sb("m0", [P, NPR, NCH])
        tmp = sb("tmp", [P, 2, NPR, NCH])
        par = sb("par", [P, 24, NPR])
        pw = sb("pw", [P, 2, SC + 1, NPR])
        bb = sb("bb", [P, 2, NPR, GW])
        b_raw = sb("b_raw", [P, 2, NPR, GW])
        c_raw = sb("c_raw", [P, 2, NPR, GW])
        dcol = sb("dcol", [P, NGR])
        ident = sb("ident", [P, P])
        h_end_p = sb("h_end_p", [P, 2, NPR, 1])
        h_end_s = sb("h_end_s", [P, 2, NPR, SB])
        ps = ctx.enter_context(nc.psum_tensor("ss_ps", [P, 8, BANK], F32))
        S = {n: new_sem("ss_" + n) for n in
             ("par_in rows_in grouped grouped_s u_tr u_copied step_set exp_in exp_done sin_in sin_done w_set wt_tr wt_copied ca_set k_mm k_copied k_read toep_zero toep_in "
              "x_mm x_copied h_set y_mm y_sum gelu y_tr y_copied rows_used stored h_stored").split()}
        block = ctx.enter_context(nc.Block())
        ARE, AIM, LDT, STEP, MAG, COS, SIN, MAG8, TH, R_, N_, A_, B_, C_, D_, E_, ZR, ZI, DEN, CS8, SN8 = range(21)
        p = lambda i: par[:, i]
        batches = [(a, min(a + 3, NGR)) for a in range(0, NGR, 3)]
        pair_batches = [(a, min(a + 3, NPR)) for a in range(0, NPR, 3)]
        small_rows = small[32:32 + SB].rearrange("p (s c) -> p s c", s=SC)
        small_group = small[64:64 + SB].rearrange("p (g c) -> p g c", g=NGR)
        taps = small[0:GW].rearrange("p (g c) -> p g c", g=NGR)

        y_batches = [list(range(6 * n + q, min(6 * n + 6, NGR), 2)) for n in range(6) for q in range(2)]
        y_batch_of = {g: n for n, gs in enumerate(y_batches) for g in gs}

        @block.sync
        def _(sp):
            sp.dma_start(rows[:], tok[0:TP, 0:512].rearrange("(c s) n -> c s n", s=SC)).then_inc(S["rows_in"], 16)
            sp.dma_start(small_rows, tok[TP:T, 0:512].rearrange("(c s) n -> c s n", s=SC)).then_inc(S["rows_in"], 16)
            for dst, src in ((par[:, ARE], a_re), (par[:, AIM], a_im), (par[:, LDT], log_dt), (b_raw[:], b_in), (c_raw[:], c_in), (dcol[:], d_in), (ident[:], ident_in),
                             (w_h[:, :, :, NCH:NCA], h0_in)):
                sp.dma_start(dst, src).then_inc(S["par_in"], 16)
            sp.wait_ge(S["k_copied"], 8)
            sp.wait_ge(S["toep_zero"], 1)
            for s in range(SC):
                sp.dma_start(toep[s * GW:(s + 1) * GW, :, s * GW:P], taps[:, :, 0:P - s * GW]).then_inc(S["toep_in"], 16)
            sp.wait_ge(S["h_set"], 1)
            sp.dma_start(h_prompt, h_end_p[:]).then_inc(S["h_stored"], 16)
            sp.dma_start(h_sample, h_end_s[:]).then_inc(S["h_stored"], 16)
            sp.wait_ge(S["y_copied"], 16)
            sp.dma_start(rows_out[0:TP].rearrange("(c s) n -> c s n", s=SC), rows[:]).then_inc(S["stored"], 16)
            sp.dma_start(rows_out[TP:T].rearrange("(c s) n -> c s n", s=SC), small_rows).then_inc(S["stored"], 16)
            sp.wait_ge(S["stored"], 32)
            sp.wait_ge(S["h_stored"], 32)

        @block.gpsimd
        def _(pool):
            pool.memset(toep[:], 0.0).then_inc(S["toep_zero"], 1)
            pool.wait_ge(S["toep_zero"], 1)
            pool.wait_ge(S["rows_in"], 32)
            pool.tensor_copy(small_group.rearrange("p g (s n) -> p g s n", n=GW), small_rows.rearrange("p s (g n) -> p g s n", n=GW)).then_inc(S["grouped_s"], 1)

        @block.scalar
        def _(act):
            act.wait_ge(S["par_in"], 128)
            act.activation(p(STEP), p(LDT), ACT.Exp).then_inc(S["step_set"], 1)
            act.wait_ge(S["exp_in"], 1)
            act.activation(p(MAG), p(A_), ACT.Exp).then_inc(S["exp_done"], 1)
            act.activation(p(MAG8), p(A_), ACT.Exp, scale=float(SC)).then_inc(S["exp_done"], 1)
            act.wait_ge(S["sin_in"], 1)
            act.activation(p(SIN), p(R_), ACT.Sin)
            act.activation(p(COS), p(N_), ACT.Sin).then_inc(S["sin_done"], 1)
            for n, (a, z) in enumerate(batches):
                act.wait_ge(S["u_tr"], n + 1)
                act.activation(u[:, a:z].rearrange("p g c -> p (g c)"), ps[:, n % 2, 0:(z - a) * NCA], ACT.Copy).then_inc(S["u_copied"], 1)
            for n in range(8):
                act.wait_ge(S["wt_tr"], n + 1)
                act.activation(w_t[:, 2 * n:2 * n + 2].rearrange("p a r s -> p (a r s)"), ps[:, 2 + n % 2, :], ACT.Copy).then_inc(S["wt_copied"], 1)
            for n in range(8):
                act.wait_ge(S["k_mm"], n + 1)
                if n == 0:
                    act.wait_ge(S["u_copied"], len(batches))
                g0 = 8 * (n // 2) + n % 2
                act.activation(taps[:, g0:g0 + 7:2], ps[0:GW, 4 + n % 2, :].rearrange("p (g c) -> p g c", c=P), ACT.Copy).then_inc(S["k_copied"], 1)
            for n, gs in enumerate(y_batches):
                act.wait_ge(S["y_sum"], n + 1)
                y = u[:, gs[0]:gs[-1] + 1:2]
                act.activation(y, y, ACT.Gelu_apprx_tanh).then_inc(S["gelu"], 1)

        @block.tensor
        def _(pe):
            pe.wait_ge(S["par_in"], 128)
            pe.wait_ge(S["grouped_s"], 1)
            for n, (a, z) in enumerate(batches):
                pe.wait_ge(S["grouped"], min((z - 1) // 8 + 1, 4))
                if n >= 2:
                    pe.wait_ge(S["u_copied"], n - 1)
                for g in range(a, z):
                    o = (g - a) * NCA
                    pe.transpose(ps[:, n % 2, o:o + NCH], by_group[:, g], ident[:])
                    last = pe.transpose(ps[:, n % 2, o + NCH:o + NCA], small_group[:, g], ident[64:64 + SB, 64:64 + SB])
                last.then_inc(S["u_tr"], 1)
            pe.wait_ge(S["w_set"], 1)
            for n in range(8):
                if n >= 2:
                    pe.wait_ge(S["wt_copied"], n - 1)
                for k in range(4):
                    last = pe.transpose(ps[:, 2 + n % 2, k * P:(k + 1) * P], w_h[:, k % 2, 2 * n + k // 2, 0:P], ident[:])
                last.then_inc(S["wt_tr"], 1)
            pe.wait_ge(S["ca_set"], 1)
            for n in range(8):
                if n >= 2:
                    pe.wait_ge(S["k_copied"], n - 1)
                for k in range(4):
                    g = 8 * (n // 2) + 2 * k + n % 2
                    r = slice(NST * (g % 2), NST * (g % 2) + NST)
                    for c in range(2):
                        last = pe.matmul(ps[0:GW, 4 + n % 2, k * P:(k + 1) * P], bb[r, c, g // 2], ca[r, c, g // 2, 0:P], start=(c == 0), stop=(c == 1))
                last.then_inc(S["k_mm"], 1)
            pe.wait_ge(S["wt_copied"], 8)
            pe.wait_ge(S["u_copied"], len(batches))
            for n, (a, z) in enumerate(pair_batches):
                for c in range(2):
                    m = 2 * n + c
                    if m >= 2:
                        pe.wait_ge(S["x_copied"], m - 1)
                    for pr in range(a, z):
                        for g2 in range(2):
                            last = pe.matmul(ps[NST * g2:NST * (g2 + 1), 6 + c, (pr - a) * NCA:(pr - a + 1) * NCA], w_t[:, pr, c, NST * g2:NST * (g2 + 1)], u[:, 2 * pr + g2], start=True, stop=True)
                    last.then_inc(S["x_mm"], 1)
            pe.wait_ge(S["toep_in"], 16 * SC)
            pe.wait_ge(S["h_set"], 1)
            for n, gs in enumerate(y_batches):
                if n >= 2:
                    pe.wait_ge(S["y_sum"], n - 1)
                for k, g in enumerate(gs):
                    r = slice(NST * (g % 2), NST * (g % 2) + NST)
                    dst = ps[:, n % 2, k * NCA:(k + 1) * NCA]
                    pe.matmul(dst, toep[:, g], u[:, g], start=True, stop=False)
                    pe.matmul(dst, ca[r, 0, g // 2, GW:], w_h[r, 0, g // 2], start=False, stop=False)
                    last = pe.matmul(dst, ca[r, 1, g // 2, GW:], w_h[r, 1, g // 2], start=False, stop=True)
                last.then_inc(S["y_mm"], 1)
            for n in range(8):
                pe.wait_ge(S["gelu"], max(y_batch_of[g] for g in range(4 * n, 4 * n + 4)) + 1)
                if n >= 2:
                    pe.wait_ge(S["y_copied"], 2 * (n - 1))
                for k in range(4):
                    pe.transpose(ps[:, 2 + n % 2, k * P:(k + 1) * P], u[:, 4 * n + k, 0:NCH], ident[:])
                    last = pe.transpose(ps[0:SB, 4 + n % 2, k * P:(k + 1) * P], u[:, 4 * n + k, NCH:NCA], ident[:])
                last.then_inc(S["y_tr"], 1)

        @block.vector
        def _(dve):
            tt, ts = dve.tensor_tensor, dve.tensor_scalar
            MUL, ADD, SUB = ALU.mult, ALU.add, ALU.subtract

            def cmul(out_r, out_i, xr, xi, yr, yi, t1, t2, conj=False):
                tt(t1, xi, yi, MUL)
                tt(t2, xr, yi, MUL)
                dve.drain()
                tt(out_r, xr, yr, MUL)
                tt(out_i, xi, yr, MUL)
                dve.drain()
                tt(out_r, out_r, t1, ADD if conj else SUB)
                tt(out_i, out_i, t2, SUB if conj else ADD)
                dve.drain()

            dve.wait_ge(S["rows_in"], 32)
            for n in range(4):
                dve.tensor_copy(by_group[:, 8 * n:8 * n + 8].rearrange("p g (s n) -> p g s n", n=GW),
                                rows[:, :, n * P:(n + 1) * P].rearrange("p s (g n) -> p g s n", n=GW)).then_inc(S["grouped"], 1)
            dve.wait_ge(S["par_in"], 128)
            dve.wait_ge(S["step_set"], 1)
            tt(p(A_), p(ARE), p(STEP), MUL)
            tt(p(TH), p(AIM), p(STEP), MUL)
            dve.drain().then_inc(S["exp_in"], 1)
            ts(p(B_), p(TH), 1.0 / TWO_PI, None, MUL)
            ts(p(C_), p(TH), 1.0 / TWO_PI, 0.25, MUL, ADD)
            dve.drain()
            for src, dst, quarter in ((B_, R_, 0.0), (C_, N_, TWO_PI / 4)):
                ts(p(D_), p(src), ROUND, None, ADD)
                dve.drain()
                ts(p(D_), p(D_), ROUND, None, SUB)
                dve.drain()
                dve.scalar_tensor_tensor(out=p(E_), in0=p(D_), scalar=-TWO_PI_HI, in1=p(TH), op0=MUL, op1=ADD)
                dve.drain()
                dve.scalar_tensor_tensor(out=p(E_), in0=p(D_), scalar=-(TWO_PI - TWO_PI_HI), in1=p(E_), op0=MUL, op1=ADD)
                dve.drain()
                ts(p(E_), p(E_), quarter, 3.1415925, ADD, ALU.min)
                dve.drain()
                ts(p(dst), p(E_), -3.1415925, None, ALU.max)
                dve.drain()
            dve.sem_inc(S["sin_in"], 1)
            dve.wait_ge(S["exp_done"], 2)
            dve.wait_ge(S["sin_done"], 1)
            dve.memset(pw[:, 0, 0], 1.0)
            dve.memset(pw[:, 1, 0], 0.0)
            tt(pw[:, 0, 1], p(MAG), p(COS), MUL)
            tt(pw[:, 1, 1], p(MAG), p(SIN), MUL)
            dve.drain()
            for k in range(2, SC + 1):
                cmul(pw[:, 0, k], pw[:, 1, k], pw[:, 0, k - 1], pw[:, 1, k - 1], pw[:, 0, 1], pw[:, 1, 1], p(A_), p(B_))
            ts(p(A_), pw[:, 0, 1], -1.0, None, ADD)
            tt(p(DEN), p(ARE), p(ARE), MUL)
            tt(p(B_), p(AIM), p(AIM), MUL)
            dve.drain()
            tt(p(DEN), p(DEN), p(B_), ADD)
            dve.drain()
            dve.reciprocal(p(DEN), p(DEN))
            cmul(p(ZR), p(ZI), p(A_), pw[:, 1, 1], p(ARE), p(AIM), p(C_), p(D_), conj=True)
            tt(p(ZR), p(ZR), p(DEN), MUL)
            tt(p(ZI), p(ZI), p(DEN), MUL)
            dve.drain()
            wide = lambda t, n=GW: t.unsqueeze(2).to_broadcast([P, NPR, n])
            t1, t2 = tmp[:, 0, :, 0:GW], tmp[:, 1, :, 0:GW]
            cmul(bb[:, 0], bb[:, 1], b_raw[:, 0], b_raw[:, 1], wide(p(ZR)), wide(p(ZI)), t1, t2)
            for s in range(SC):
                k = SC - 1 - s
                cmul(w_h[:, 0, :, s * GW:(s + 1) * GW], w_h[:, 1, :, s * GW:(s + 1) * GW], bb[:, 0], bb[:, 1], wide(pw[:, 0, k]), wide(pw[:, 1, k]), t1, t2)
            dve.sem_inc(S["w_set"], 1)
            for k in range(SC + 1):
                cmul(ca[:, 0, :, k * GW:(k + 1) * GW], ca[:, 1, :, k * GW:(k + 1) * GW], c_raw[:, 0], c_raw[:, 1], wide(pw[:, 0, k]), wide(pw[:, 1, k]), t1, t2)
            ts(ca[:, 1], ca[:, 1], -1.0, None, MUL)
            dve.drain()
            dve.sem_inc(S["ca_set"], 1)
            tt(p(CS8), p(COS), p(COS), MUL)
            for n in range(3):
                c, s = (p(COS), p(SIN)) if n == 0 else (p(CS8), p(SN8))
                tt(p(A_), c, c, MUL)
                tt(p(B_), s, s, MUL)
                tt(p(C_), c, s, MUL)
                dve.drain()
                tt(p(CS8), p(A_), p(B_), SUB)
                ts(p(SN8), p(C_), 2.0, None, MUL)
                dve.drain()
            dve.tensor_copy(turn[:, 0, :, 0], p(CS8))
            dve.tensor_copy(turn[:, 1, :, 0], p(SN8))
            dve.memset(m0[:], 0.0)
            dve.drain()
            n = 1
            while n < NCH:
                cmul(turn[:, 0, :, n:2 * n], turn[:, 1, :, n:2 * n], turn[:, 0, :, 0:n], turn[:, 1, :, 0:n],
                     turn[:, 0, :, n - 1:n].to_broadcast([P, NPR, n]), turn[:, 1, :, n - 1:n].to_broadcast([P, NPR, n]), tmp[:, 0, :, 0:n], tmp[:, 1, :, 0:n])
                n *= 2
            tt(tmp[:, 0], turn[:, 0], turn[:, 0], MUL)
            tt(tmp[:, 1], turn[:, 1], turn[:, 1], MUL)
            dve.drain()
            tt(tmp[:, 0], tmp[:, 0], tmp[:, 1], ADD)
            dve.drain()
            ts(tmp[:, 0], tmp[:, 0], -0.5, 1.5, MUL, ADD)
            dve.drain()
            tt(turn[:, 0], turn[:, 0], tmp[:, 0], MUL)
            tt(turn[:, 1], turn[:, 1], tmp[:, 0], MUL)
            tt(m0[:, :, 1:], m0[:, :, 1:], p(MAG8).unsqueeze(2).to_broadcast([P, NPR, NCH - 1]), ADD)
            dve.drain()
            for n, (a, z) in enumerate(pair_batches):
                for c in range(2):
                    dve.wait_ge(S["x_mm"], 2 * n + c + 1)
                    dve.tensor_copy(x[:, c, a:z].rearrange("p g c -> p (g c)"), ps[:, 6 + c, 0:(z - a) * NCA]).then_inc(S["x_copied"], 1)
            dve.drain()
            xr, xi = x[:, 0, :, 0:NCH], x[:, 1, :, 0:NCH]
            dve.wait_ge(S["wt_tr"], 8)
            hr, hi = w_h[:, 0, :, 0:NCH], w_h[:, 1, :, 0:NCH]
            cmul(tmp[:, 0], tmp[:, 1], xr, xi, turn[:, 0], turn[:, 1], hr, hi, conj=True)
            for c in range(2):
                flat = tmp[:, c].rearrange("p g c -> p (g c)")
                dve.tensor_tensor_scan(flat, m0[:].rearrange("p g c -> p (g c)"), flat, 0.0, MUL, ADD)
            dve.drain()
            cmul(xr, xi, tmp[:, 0], tmp[:, 1], turn[:, 0], turn[:, 1], hr, hi)
            for c in range(2):
                dve.tensor_copy(w_h[:, c, :, 1:NCH], x[:, c, :, 0:NCH - 1])
                dve.memset(w_h[:, c, :, 0:1], 0.0)
                dve.tensor_copy(h_end_p[:, c], x[:, c, :, NCH - 1:NCH])
            s0r, s0i = w_h[:, 0, :, NCH:NCA], w_h[:, 1, :, NCH:NCA]
            cmul(h_end_s[:, 0], h_end_s[:, 1], s0r, s0i, wide(pw[:, 0, SC], SB), wide(pw[:, 1, SC], SB), tmp[:, 0, :, 0:SB], tmp[:, 1, :, 0:SB])
            for c in range(2):
                tt(h_end_s[:, c], h_end_s[:, c], x[:, c, :, NCH:NCA], ADD)
            dve.drain().then_inc(S["h_set"], 1)
            for n, gs in enumerate(y_batches):
                dve.wait_ge(S["y_mm"], n + 1)
                for k, g in enumerate(gs):
                    last = dve.scalar_tensor_tensor(out=u[:, g], in0=u[:, g], scalar=dcol[:, g:g + 1], in1=ps[:, n % 2, k * NCA:(k + 1) * NCA], op0=MUL, op1=ADD)
                last.then_inc(S["y_sum"], 1)
            for n in range(8):
                dve.wait_ge(S["y_tr"], n + 1)
                dve.tensor_copy(rows[:, :, n * HD:(n + 1) * HD].rearrange("p s (g n) -> p g s n", n=GW), ps[:, 2 + n % 2, :].rearrange("p (g s n) -> p g s n", s=SC, n=GW)).then_inc(S["y_copied"], 1)
                dve.tensor_copy(small_rows[:, :, n * HD:(n + 1) * HD].rearrange("p s (g n) -> p g s n", n=GW), ps[0:SB, 4 + n % 2, :].rearrange("p (g s n) -> p g s n", s=SC, n=GW)).then_inc(S["y_copied"], 1)


def s5_glu_stage(nc, rows_in, w_in, ident_in, out_t):
    NK = 4
    with ExitStack() as ctx:
        new_sem = ctx.enter_context(stage_semaphores(nc))
        sb = lambda name, shape: ctx.enter_context(nc.sbuf_tensor("gl_" + name, shape, F32))
        rows = sb("rows", [P, len(TILES), 512])
        y = sb("y", [P, NK, T])
        w = sb("w", [P, NK, 512])
        ident = sb("ident", [P, P])
        gate = sb("gate", [P, NK, T])
        ps = ctx.enter_context(nc.psum_tensor("gl_ps", [P, 8, BANK], F32))
        S = {n: new_sem("gl_" + n) for n in "w_in rows_in tr copied mm sig out_set stored".split()}
        block = ctx.enter_context(nc.Block())
        NTL = len(TILES)

        @block.sync
        def _(sp):
            sp.dma_start(rows[:, 0:TP // P], rows_in[0:TP].rearrange("(n p) c -> p n c", p=P)).then_inc(S["rows_in"], 16)
            sp.dma_start(rows[0:T - TP, TP // P], rows_in[TP:T]).then_inc(S["rows_in"], 16)
            sp.dma_start(ident[:], ident_in).then_inc(S["rows_in"], 16)
            sp.dma_start(w[:], w_in.rearrange("(k p) n -> p k n", p=P)).then_inc(S["w_in"], 16)
            for n in range(NK):
                sp.wait_ge(S["out_set"], n + 1)
                sp.dma_start(out_t[n * P:(n + 1) * P], gate[:, n]).then_inc(S["stored"], 16)
            sp.wait_ge(S["stored"], 16 * NK)

        @block.tensor
        def _(pe):
            pe.wait_ge(S["rows_in"], 48)
            for t, (t0, tn) in enumerate(TILES):
                if t >= 2:
                    pe.wait_ge(S["copied"], t - 1)
                for k in range(NK):
                    last = pe.transpose(ps[:, t % 2, k * P:k * P + tn], rows[0:tn, t, k * P:(k + 1) * P], ident[0:tn, 0:tn])
                last.then_inc(S["tr"], 1)
            pe.wait_ge(S["copied"], NTL)
            pe.wait_ge(S["w_in"], 16)
            for n in range(NK):
                if n >= 2:
                    pe.wait_ge(S["sig"], 3 * (n - 1))
                for c, (a, z) in enumerate(COLS):
                    for k in range(NK):
                        last = pe.matmul(ps[:, 2 + 3 * (n % 2) + c, 0:z - a], w[:, k, n * P:(n + 1) * P], y[:, k, a:z], start=(k == 0), stop=(k == NK - 1))
                    last.then_inc(S["mm"], 1)

        @block.scalar
        def _(act):
            for n in range(NK):
                for c, (a, z) in enumerate(COLS):
                    act.wait_ge(S["mm"], 3 * n + c + 1)
                    act.activation(gate[:, n, a:z], ps[:, 2 + 3 * (n % 2) + c, 0:z - a], ACT.Sigmoid).then_inc(S["sig"], 1)

        @block.vector
        def _(dve):
            for t, (t0, tn) in enumerate(TILES):
                dve.wait_ge(S["tr"], t + 1)
                dve.tensor_copy(y[:, :, t0:t0 + tn], ps[:, t % 2, :].rearrange("p (k t) -> p k t", t=P)[:, :, 0:tn]).then_inc(S["copied"], 1)
            for n in range(NK):
                dve.wait_ge(S["sig"], 3 * n + 3)
                if n == 0:
                    dve.wait_ge(S["copied"], NTL)
                dve.tensor_tensor(gate[:, n], gate[:, n], y[:, n], ALU.mult).then_inc(S["out_set"], 1)


D_FF = 2816
KF = D_FF // P


def trunk_stage(nc, x_t, feat, a_t, b_t, c_rows, c_t, w_branch, w_out, w_gu, w_down, g_ffn, ident_in, x1_t, y_t):
    with ExitStack() as ctx:
        new_sem = ctx.enter_context(stage_semaphores(nc))
        sb = lambda name, shape: ctx.enter_context(nc.sbuf_tensor("tr_" + name, shape, F32))
        sem = lambda name: new_sem("tr_" + name)
        big = sb("big", [P, KF, T])
        x = sb("x", [P, KD, T])
        w = sb("w", [P, 2, KF, P])
        side = sb("side", [P, 2, 3, T])
        gain = sb("gain", [P, KD])
        ident = sb("ident", [P, P])
        ones = sb("ones", [P, P])
        ps = ctx.enter_context(nc.psum_tensor("tr_ps", [P, 8, BANK], F32))
        NTL = TP // P
        ROWS_AT, BR_AT = 0, KD
        def bank(s, c):
            a, z = COLS[c]
            return ps[:, 3 * s + c, 0:z - a]

        S = {n: sem("ld_" + n) for n in "rows_in in_ tr copied ones_set".split()}
        rows = x[:, 0:4].rearrange("p k t -> p (k t)")[:, 0:NTL * 512].rearrange("p (n c) -> p n c", c=512)
        with nc.Block() as block:
            @block.sync
            def _(sp):
                sp.dma_start(rows, c_rows.rearrange("(n p) c -> p n c", p=P)).then_inc(S["rows_in"], 16)
                sp.dma_start(ident[:], ident_in).then_inc(S["rows_in"], 16)
                sp.dma_start(gain[:], g_ffn).then_inc(S["in_"], 16)
                sp.dma_start(big[:, BR_AT:BR_AT + 4], a_t.rearrange("(k p) t -> p k t", p=P)).then_inc(S["in_"], 16)
                sp.dma_start(big[:, BR_AT + 4:BR_AT + 8], b_t.rearrange("(k p) t -> p k t", p=P)).then_inc(S["in_"], 16)
                sp.dma_start(big[:, BR_AT + 8:BR_AT + 12, TP:T], c_t.rearrange("(k p) t -> p k t", p=P)[:, :, TP:T]).then_inc(S["in_"], 16)
                sp.wait_ge(S["in_"], 64)

            @block.gpsimd
            def _(pool):
                pool.memset(ones[:], 1.0).then_inc(S["ones_set"], 1)
                pool.wait_ge(S["ones_set"], 1)

            @block.tensor
            def _(pe):
                pe.wait_ge(S["rows_in"], 32)
                for t in range(NTL):
                    if t >= 2:
                        pe.wait_ge(S["copied"], t - 1)
                    for k in range(4):
                        last = pe.transpose(ps[:, t % 2, k * P:(k + 1) * P], rows[:, t, k * P:(k + 1) * P], ident[:])
                    last.then_inc(S["tr"], 1)

            @block.vector
            def _(dve):
                for t in range(NTL):
                    dve.wait_ge(S["tr"], t + 1)
                    dve.tensor_copy(big[:, BR_AT + 8:BR_AT + 12, t * P:(t + 1) * P], ps[:, t % 2, :].rearrange("p (k t) -> p k t", t=P)).then_inc(S["copied"], 1)

        M = {n: sem("mg_" + n) for n in "mm mul sig gate_free merged passed".split()}
        w_in = [sem("mg_w_in0"), sem("mg_w_in1")]
        g_in = [sem("mg_g_in0"), sem("mg_g_in1")]
        with nc.Block() as block:
            @block.sync
            def _(sp):
                with sp.Fori(0, KD // 2) as i:
                    for s in range(2):
                        sp.wait_ge(M["merged"], i * 2 + s)
                        sp.sem_inc(M["passed"], 1)
                        sp.dma_start(w[:, s, 0:12], w_branch[i * 2 + s]).then_inc(w_in[s], 16)
                        for b in range(3):
                            sp.dma_start(side[:, s, b], feat[bass.ds(i * 256 + (R_GATES + b * D + s * P), P), :]).then_inc(g_in[s], 16)

            @block.tensor
            def _(pe):
                with pe.Fori(0, KD // 2) as i:
                    for s in range(2):
                        pe.wait_ge(w_in[s], i * 16 + 16)
                        for b in range(3):
                            pe.wait_ge(M["mul"], i * 6 + (3 * s + b))
                            for c, (a, z) in enumerate(COLS):
                                if c == 2:
                                    pe.wait_ge(M["mul"], i * 6 + (3 * s + b + 1))
                                dst = ps[:, 2 * b + c if c < 2 else 6 + (3 * s + b) % 2, 0:z - a]
                                for k in range(4):
                                    last = pe.matmul(dst, w[:, s, 4 * b + k], big[:, BR_AT + 4 * b + k, a:z], start=(k == 0), stop=(k == 3))
                            last.then_inc(M["mm"], 1)

            @block.scalar
            def _(act):
                with act.Fori(0, KD // 2) as i:
                    for s in range(2):
                        act.wait_ge(g_in[s], i * 48 + 48)
                        act.activation(side[:, s], side[:, s], ACT.Sigmoid).then_inc(M["sig"], 1)

            @block.vector
            def _(dve):
                dve.sem_inc(M["mul"], 2)
                dve.sem_inc(M["merged"], 1)
                with dve.Fori(0, KD // 2) as i:
                    for s in range(2):
                        dve.wait_ge(M["sig"], i * 2 + (s + 1))
                        for b in range(3):
                            dve.wait_ge(M["mm"], i * 6 + (3 * s + b + 1))
                            g = side[:, s, b]
                            dve.tensor_tensor(g[:, 0:1024], g[:, 0:1024], ps[:, 2 * b:2 * b + 2, :].rearrange("p a c -> p (a c)"), ALU.mult)
                            dve.tensor_tensor(g[:, 1024:T], g[:, 1024:T], ps[:, 6 + (3 * s + b) % 2, 0:T - 1024], ALU.mult)
                            dve.drain().then_inc(M["mul"], 1)
                        dve.tensor_tensor(side[:, s, 0], side[:, s, 0], side[:, s, 1], ALU.add)
                        dve.drain()
                        dve.tensor_tensor(big[:, bass.ds(i * 2 + s, 1), :].rearrange("p o t -> p (o t)"), side[:, s, 0], side[:, s, 2], ALU.add).then_inc(M["merged"], 1)

        O = {n: sem("op_" + n) for n in "mm added passed".split()}
        ow_in, xr_in, o_out = ([sem(f"op_{n}{s}") for s in range(2)] for n in ("w_in", "x_in", "out"))
        with nc.Block() as block:
            @block.sync
            def _(sp):
                with sp.Fori(0, KD // 2) as i:
                    for s in range(2):
                        sp.wait_ge(O["mm"], i * 2 + s)
                        sp.sem_inc(O["passed"], 1)
                        sp.dma_start(w[:, s, 0:KD], w_out[i * 2 + s]).then_inc(ow_in[s], 16)
                        sp.wait_ge(o_out[s], i * 16)
                        sp.sem_inc(O["passed"], 1)
                        sp.dma_start(side[:, s, 0], x_t[:, bass.ds(i * 2 + s, 1)].rearrange("p o t -> p (o t)")).then_inc(xr_in[s], 16)

            @block.tensor
            def _(pe):
                pe.sem_inc(O["mm"], 1)
                with pe.Fori(0, KD // 2) as i:
                    for s in range(2):
                        pe.wait_ge(ow_in[s], i * 16 + 16)
                        pe.wait_ge(O["added"], i * 2 + s)
                        for c, (a, z) in enumerate(COLS):
                            for k in range(KD):
                                last = pe.matmul(bank(s, c), w[:, s, k], big[:, k, a:z], start=(k == 0), stop=(k == KD - 1))
                        last.then_inc(O["mm"], 1)

            @block.vector
            def _(dve):
                dve.sem_inc(O["added"], 1)
                with dve.Fori(0, KD // 2) as i:
                    for s in range(2):
                        dve.wait_ge(xr_in[s], i * 16 + 16)
                        dve.wait_ge(O["mm"], i * 2 + (s + 2))
                        for c, (a, z) in enumerate(COLS):
                            dve.tensor_tensor(side[:, s, 0, a:z], side[:, s, 0, a:z], bank(s, c), ALU.add)
                        dve.drain()
                        dve.tensor_copy(x[:, bass.ds(i * 2 + s, 1), :].rearrange("p o t -> p (o t)"), side[:, s, 0])
                        dve.drain().then_inc(O["added"], 1)

            @block.gpsimd
            def _(pool):
                with pool.Fori(0, KD // 2) as i:
                    for s in range(2):
                        pool.wait_ge(O["added"], i * 2 + (s + 2))
                        pool.dma_start(x1_t[bass.ds(i * 256 + s * P, P), :], side[:, s, 0]).then_inc(o_out[s], 16)
                for s in range(2):
                    pool.wait_ge(o_out[s], 16 * (KD // 2))

        N = {n: sem("nm_" + n) for n in "squared sq_used var_set root normed".split()}
        sq, rstd = side[:, 0, 0:2], side[:, 1, 0]
        with nc.Block() as block:
            @block.scalar
            def _(act):
                for k in range(KD):
                    if k >= 2:
                        act.wait_ge(N["sq_used"], k - 1)
                    act.activation(sq[:, k % 2], x[:, k], ACT.Square).then_inc(N["squared"], 1)
                act.wait_ge(N["var_set"], 3)
                act.activation(rstd, rstd, ACT.Sqrt).then_inc(N["root"], 1)

            @block.tensor
            def _(pe):
                for k in range(KD):
                    pe.wait_ge(N["squared"], k + 1)
                    for c, (a, z) in enumerate(COLS):
                        last = pe.matmul(bank(0, c), ones[:], sq[:, k % 2, a:z], start=(k == 0), stop=(k == KD - 1))
                    last.then_inc(N["sq_used"], 1)

            @block.vector
            def _(dve):
                dve.wait_ge(N["sq_used"], KD)
                for c, (a, z) in enumerate(COLS):
                    dve.tensor_scalar(rstd[:, a:z], bank(0, c), 1.0 / D, EPS, ALU.mult, ALU.add).then_inc(N["var_set"], 1)
                dve.wait_ge(N["root"], 1)
                dve.reciprocal(rstd, rstd)
                dve.drain()
                for k in range(KD):
                    dve.scalar_tensor_tensor(out=x[:, k], in0=x[:, k], scalar=gain[:, k:k + 1], in1=rstd, op0=ALU.mult, op1=ALU.mult).then_inc(N["normed"], 1)

        H = {n: sem("gu_" + n) for n in "mm silu hid passed".split()}
        def hid_bank(s, c, h):
            a, z = COLS[c]
            if c < 2:
                return ps[:, (0, 2, 5, 2)[2 * s + c] + h, 0:z - a]
            return ps[:, (4, 7)[s], h * 64:h * 64 + z - a]

        gw_in = [sem("gu_w_in0"), sem("gu_w_in1")]
        with nc.Block() as block:
            @block.sync
            def _(sp):
                with sp.Fori(0, KF // 2) as i:
                    for s in range(2):
                        sp.wait_ge(H["mm"], i * 6 + 3 * s)
                        sp.sem_inc(H["passed"], 1)
                        sp.dma_start(w[:, s, 0:2 * KD], w_gu[i * 2 + s]).then_inc(gw_in[s], 16)

            @block.tensor
            def _(pe):
                pe.sem_inc(H["mm"], 3)
                with pe.Fori(0, KF // 2) as i:
                    for s in range(2):
                        pe.wait_ge(gw_in[s], i * 16 + 16)
                        for c, (a, z) in enumerate(COLS):
                            pe.wait_ge(H["hid"], i * 6 + (0, 4, 2, 3, 7, 5)[3 * s + c])
                            for h in range(2):
                                dst = hid_bank(s, c, h)
                                for k in range(KD):
                                    last = pe.matmul(dst, w[:, s, h * KD + k], x[:, k, a:z], start=(k == 0), stop=(k == KD - 1))
                            last.then_inc(H["mm"], 1)

            @block.scalar
            def _(act):
                with act.Fori(0, KF // 2) as i:
                    for s in range(2):
                        for c, (a, z) in enumerate(COLS):
                            act.wait_ge(H["mm"], i * 6 + (3 * s + c + 4))
                            act.sem_inc(H["passed"], 1)
                            act.activation(big[:, bass.ds(i * 2 + s, 1), a:z].rearrange("p o t -> p (o t)"), hid_bank(s, c, 0), ACT.Silu).then_inc(H["silu"], 1)

            @block.vector
            def _(dve):
                dve.sem_inc(H["hid"], 5)
                with dve.Fori(0, KF // 2) as i:
                    for s in range(2):
                        for c, (a, z) in enumerate(COLS):
                            dve.wait_ge(H["silu"], i * 6 + (3 * s + c + 1))
                            h = big[:, bass.ds(i * 2 + s, 1), a:z].rearrange("p o t -> p (o t)")
                            dve.tensor_tensor(h, h, hid_bank(s, c, 1), ALU.mult).then_inc(H["hid"], 1)

        Y = {n: sem("dn_" + n) for n in "mm added passed".split()}
        dw_in, dx_in, d_out = ([sem(f"dn_{n}{s}") for s in range(2)] for n in ("w_in", "x_in", "out"))
        with nc.Block() as block:
            @block.sync
            def _(sp):
                with sp.Fori(0, KD // 2) as i:
                    for s in range(2):
                        sp.wait_ge(Y["mm"], i * 2 + s)
                        sp.sem_inc(Y["passed"], 1)
                        sp.dma_start(w[:, s], w_down[i * 2 + s]).then_inc(dw_in[s], 16)
                        sp.wait_ge(d_out[s], i * 16)
                        sp.sem_inc(Y["passed"], 1)
                        sp.dma_start(side[:, s, 0], x1_t[bass.ds(i * 256 + s * P, P), :]).then_inc(dx_in[s], 16)

            @block.tensor
            def _(pe):
                pe.sem_inc(Y["mm"], 1)
                with pe.Fori(0, KD // 2) as i:
                    for s in range(2):
                        pe.wait_ge(dw_in[s], i * 16 + 16)
                        pe.wait_ge(Y["added"], i * 2 + s)
                        for c, (a, z) in enumerate(COLS):
                            for k in range(KF):
                                last = pe.matmul(bank(s, c), w[:, s, k], big[:, k, a:z], start=(k == 0), stop=(k == KF - 1))
                        last.then_inc(Y["mm"], 1)

            @block.vector
            def _(dve):
                dve.sem_inc(Y["added"], 1)
                with dve.Fori(0, KD // 2) as i:
                    for s in range(2):
                        dve.wait_ge(dx_in[s], i * 16 + 16)
                        dve.wait_ge(Y["mm"], i * 2 + (s + 2))
                        for c, (a, z) in enumerate(COLS):
                            dve.tensor_tensor(side[:, s, 0, a:z], side[:, s, 0, a:z], bank(s, c), ALU.add)
                        dve.drain().then_inc(Y["added"], 1)

            @block.gpsimd
            def _(pool):
                with pool.Fori(0, KD // 2) as i:
                    for s in range(2):
                        pool.wait_ge(Y["added"], i * 2 + (s + 2))
                        pool.dma_start(y_t[bass.ds(i * 256 + s * P, P), :], side[:, s, 0]).then_inc(d_out[s], 16)
                for s in range(2):
                    pool.wait_ge(d_out[s], 16 * (KD // 2))


def build_program(nc, i, o):
    def scratch(name, *shape):
        return nc.dram_tensor(name, shape, F32, kind="Internal").ap()

    feat = scratch("proj_feat", R_GATES + 3 * D, T)
    tok = scratch("proj_tok", T, NTOK)
    qkv = scratch("qkv_rows", T, NQKV)
    heads_t = scratch("heads_t", 6 * P, T)
    strips = scratch("strips", 2, NH, STRIP)
    sample_t = scratch("sample_attn_t", 512, T)
    cmp_kt = scratch("cmp_kt", P, TP // CMP_STRIDE - 1)
    cmp_v = scratch("cmp_v", TP // CMP_STRIDE - 1, P)
    attn_rows = scratch("attn_rows", TP, 512)
    hgrn_t = scratch("hgrn_t", 512, T)
    s5_rows = scratch("s5_rows", T, 512)
    s5_t = scratch("s5_t", 512, T)
    x1_t = scratch("x1_t", D, T)

    norm_project_stage(nc, i["x_t"], i["g_mix"], i["w_feat"], i["w_tok"], feat, tok)
    attention_rows_stage(nc, tok, i["qk_norm"], i["ident"], o["kv_rows"], qkv, heads_t)
    bias_strip_stage(nc, i["rel_ext"], i["onehot"], qkv, i["win_cache"], strips, o["win_p"], o["win_s"])
    sample_attention_stage(nc, i["cache"], i["page_table"], i["win_cache"], heads_t, qkv, tok, strips, i["cmp_w1"], i["cmp_w2"],
                           i["cmp_pe"], i["qk_norm"], i["overlap"], i["rep"], i["ident"], sample_t)
    prompt_compress_stage(nc, tok, i["cmp_w1"], i["cmp_w2"], i["cmp_pe"], i["qk_norm"], i["ident"], cmp_kt, cmp_v)
    prompt_attention_stage(nc, heads_t, qkv, tok, strips, cmp_kt, cmp_v, i["flip"], i["ident"], attn_rows)
    hgrn_stage(nc, feat, tok, i["lb_logits"], i["hg_gain"], i["hg_state"], i["diag"], i["ident"], i["own"], hgrn_t, o["hg_p"], o["hg_s"])
    s5_state_stage(nc, tok, i["s5_a_re"], i["s5_a_im"], i["s5_log_dt"], i["s5_b"], i["s5_c"], i["s5_d"], i["s5_h0"], i["ident"],
                   s5_rows, o["s5_p"], o["s5_s"])
    s5_glu_stage(nc, s5_rows, i["s5_w_glu"], i["ident"], s5_t)
    trunk_stage(nc, i["x_t"], feat, hgrn_t, s5_t, attn_rows, sample_t, i["w_branch"], i["w_out"], i["w_gate_up"], i["w_down"],
                i["g_ffn"], i["ident"], x1_t, o["y_t"])


def rel_buckets(dist):
    n = np.maximum(dist, 0)
    exact = N_BUCKETS // 2
    nf = np.maximum(n, 1).astype(np.float32)
    large = exact + (np.log(nf / np.float32(exact)) / np.float32(np.log(MAX_DIST / exact)) * np.float32(N_BUCKETS - exact)).astype(np.int32)
    return np.where(n < exact, n, np.minimum(large, N_BUCKETS - 1))


def shape_constants():
    f4 = np.float32
    dist = STRIP_AT - np.arange(STRIP)
    onehot = np.zeros((N_BUCKETS + 1, 2, STRIP), f4)
    for w in range(2):
        bad = (dist < 0) | ((dist >= WINDOW) if w else False)
        onehot[rel_buckets(dist), w, np.arange(STRIP)] = 1
        onehot[:, w, bad] = 0
        onehot[N_BUCKETS, w, bad] = NEG
    nb, ns = PAST // CMP_STRIDE - 1, PAST // 64 + 1
    cs, ss = np.arange(nb)[:, None] * CMP_STRIDE, np.arange(ns)[None] * 64
    overlap = np.zeros((2 * P, ns), f4)
    overlap[:nb] = (cs < ss + 64) & (cs + CMP_LEN > ss)
    row = np.arange(NH * ST)
    p = np.arange(P)
    return {
        "onehot": onehot,
        "overlap": np.ascontiguousarray(overlap.reshape(2, P, ns).transpose(1, 0, 2)),
        "rep": ((row[:, None] // (NR * ST) == row // (NR * ST)) & (row[:, None] % ST == row % ST)).astype(f4),
        "ident": np.eye(P, dtype=f4),
        "flip": np.ascontiguousarray(np.eye(P, dtype=f4)[::-1]),
        "diag": (p[:, None] // HC == p // HC).astype(f4),
        "own": (np.arange(SB * ST)[:, None] // ST == np.arange(SB)).astype(f4),
    }


def kernel(**inputs):
    import concourse.bacc as bacc
    from concourse.bass_utils import run_bass_kernel_spmd

    a = {name: np.asarray(v) for name, v in inputs.items()}
    con = np.ascontiguousarray

    def chunks(w, n=P):
        return con(w.reshape(w.shape[0] // P, P, w.shape[1] // n, n).transpose(2, 1, 0, 3))

    def columns(v):
        return con(v.reshape(-1, P).T)

    def pairs(v):
        r = v.reshape(NPR, 2, NST, *v.shape[2:])
        return con(np.moveaxis(r, 0, 2).reshape(P, NPR, *v.shape[2:]))

    x = np.concatenate([a["x_prompt"][0], a["x_sample"].reshape(SB * ST, D)])
    w_in = a["w_in"][0]
    widths = [512] * 6 + [128] * 6 + [24] + [D] * 3
    at = np.cumsum([0] + widths)
    hq, hf, hi, hg, su, nq, kc, vc, ksl, vsl, kwn, vwn, ngate, ga, gb, gc = (w_in[:, at[n]:at[n + 1]] for n in range(16))
    ins = {
        "x_t": con(x.T.reshape(KD, P, T).transpose(1, 0, 2)),
        "g_mix": columns(a["norm_mix"][0]),
        "w_feat": chunks(np.concatenate([hq, hf, hg, ga, gb, gc], axis=1)),
        "w_tok": chunks(np.concatenate([su, hi, nq, kc, vc, ksl, vsl, kwn, vwn, ngate], axis=1), TOK_CHUNK),
        "qk_norm": con(a["nsa_qk_norm"][0]),
        "rel_ext": np.concatenate([a["rel_bias"], np.ones((1, NH), np.float32)]),
        "win_cache": con(a["cache_win_kv"][0].reshape(SB, WINDOW, 2 * P)),
        "cache": con(a["cache_nsa_kv"][0].reshape(-1, P, 4 * P)),
        "page_table": con(a["page_table"].reshape(1, -1)),
        "cmp_w1": con(a["cmp_w1"][0].reshape(2, 16, P, CMP_HID).transpose(2, 0, 1, 3)),
        "cmp_w2": con(a["cmp_w2"][0].transpose(1, 0, 2)),
        "cmp_pe": con(a["cmp_pe"][0].reshape(2, 16, P).transpose(2, 0, 1)),
        "lb_logits": columns(a["hg_lb_logits"][0]),
        "hg_gain": con(a["hg_out_norm"].reshape(P, 1)),
        "hg_state": con(a["state_hgrn"][0]),
        "s5_a_re": pairs(a["s5_a_re"][0]),
        "s5_a_im": pairs(a["s5_a_im"][0]),
        "s5_log_dt": pairs(np.broadcast_to(a["s5_log_dt"][0][:, None], (NGR, NST))),
        "s5_b": np.stack([pairs(a["s5_b_re"][0]), pairs(a["s5_b_im"][0])], axis=1),
        "s5_c": np.stack([pairs(a["s5_c_re"][0].transpose(0, 2, 1)), pairs(a["s5_c_im"][0].transpose(0, 2, 1))], axis=1),
        "s5_d": con(np.broadcast_to(a["s5_d"][0].reshape(NGR, GW).T[None], (SC, GW, NGR)).reshape(P, NGR)),
        "s5_h0": np.stack([pairs(a["state_s5_re"][0].transpose(1, 2, 0)), pairs(a["state_s5_im"][0].transpose(1, 2, 0))], axis=1),
        "s5_w_glu": con(a["s5_w_glu"][0]),
        "w_branch": con(a["w_branch"][0].reshape(3, 4, P, KD, P).transpose(3, 2, 0, 1, 4).reshape(KD, P, 12, P)),
        "w_out": chunks(a["w_out"][0]),
        "w_gate_up": con(a["w_gate_up"][0].reshape(KD, P, 2, KF, P).transpose(3, 1, 2, 0, 4).reshape(KF, P, 2 * KD, P)),
        "w_down": chunks(a["w_down"][0]),
        "g_ffn": columns(a["norm_ffn"][0]),
    }
    ins.update(shape_constants())
    outs = {
        "y_t": (D, T), "kv_rows": (T, 512), "win_p": (WINDOW, 2 * P), "win_s": (SB, WINDOW, 2 * P),
        "hg_p": (4, P, P), "hg_s": (SB, 4, P, P), "s5_p": (P, 2, NPR, 1), "s5_s": (P, 2, NPR, SB),
    }
    nc = bacc.Bacc("TRN2", target_bir_lowering=False, num_devices=1)
    i = {n: nc.dram_tensor(n + "_in", v.shape, mybir.dt.from_np(v.dtype), kind="ExternalInput").ap() for n, v in ins.items()}
    o = {n: nc.dram_tensor(n + "_out", s, F32, kind="ExternalOutput").ap() for n, s in outs.items()}
    build_program(nc, i, o)
    got = run_bass_kernel_spmd(nc, [{n + "_in": v for n, v in ins.items()}], core_ids=[0]).results[0]
    r = {n: got[n + "_out"] for n in outs}

    def unpair(v):
        return con(v.reshape(2, NST, NPR, -1).transpose(3, 2, 0, 1).reshape(1, -1, NGR, NST))

    y = r["y_t"].T
    return (
        con(y[:TP]).reshape(1, TP, D), con(y[TP:]).reshape(SB, ST, D),
        con(r["kv_rows"][:TP]).reshape(1, 1, TP, 4, NG, HD), con(r["kv_rows"][TP:]).reshape(1, SB, ST, 4, NG, HD),
        r["win_p"].reshape(1, 1, WINDOW, 2, NG, HD), r["win_s"].reshape(1, SB, WINDOW, 2, NG, HD),
        r["hg_p"].reshape(1, 1, 4, P, P), r["hg_s"].reshape(1, SB, 4, P, P),
        unpair(r["s5_p"][:, 0]), unpair(r["s5_p"][:, 1]), unpair(r["s5_s"][:, 0]), unpair(r["s5_s"][:, 1]),
    )
```

```python
import concourse.bass as bass
from concourse import mybir
from contextlib import ExitStack, contextmanager
import numpy as np

F32 = mybir.dt.float32
I32 = mybir.dt.int32
ACT = mybir.ActivationFunctionType
ALU = mybir.AluOpType
AX = mybir.AxisListType

P = 128
BANK = 512
D = 1024
KD = D // P
TP = 1024
SB, ST = 8, 8
T = TP + SB * ST
PAST = 4096
EPS = 1e-6
NEG = -1e30
FORCE = 1e9
HD = 64
NH, NG, NR = 8, 2, 4
COLS = [(0, 512), (512, 1024), (1024, T)]
THIRDS = [(0, 364), (364, 728), (728, T)]
TILES = [(i * P, P) for i in range(TP // P)] + [(TP, T - TP)]
NTOK = 2328
TOK_CHUNK = NTOK // 6
C_SU, C_HI, C_NQ, C_KV, C_NGATE = 0, 512, 1024, 1536, 2304
R_HQ, R_HF, R_HG, R_GATES = 0, 512, 1024, 1536
NQKV = 512 + 768

STRIP = 2048
STRIP_AT = 1023
N_BUCKETS, MAX_DIST, WINDOW = 32, 128, 512
CMP_HID, CMP_STRIDE, CMP_LEN = 128, 16, 32
TINY = 1.17549435e-38

R32 = mybir.dt.float32r


def overlaid(nc, ctx, name, shape):
    plain = ctx.enter_context(nc.sbuf_tensor(name, shape, F32))
    return plain, nc.alloc_sbuf_tensor_at(name + "_r", shape, R32, offset=nc.sbuf_base - 4 * int(np.prod(shape[1:])))


def split_product(pe, out, w_hi, w_lo, x_hi, x_lo, first, last):
    pe.matmul(out, w_lo, x_hi, start=first, stop=False)
    pe.matmul(out, w_hi, x_lo, start=False, stop=False)
    return pe.matmul(out, w_hi, x_hi, start=False, stop=last)


@contextmanager
def stage_semaphores(nc):
    held = []

    def new(name, ahead=0):
        held.append(nc.alloc_semaphore(name))
        if ahead:
            nc.gpsimd.sem_inc(held[-1], ahead)
        return held[-1]

    yield new
    nc.clear_and_free_semaphores(held)
    nc.all_engine_barrier()


def norm_project_stage(nc, x_t, g_mix, w_feat, w_tok, feat_out, tok_out):
    with ExitStack() as ctx:
        new_sem = ctx.enter_context(stage_semaphores(nc))
        sb = lambda name, shape: ctx.enter_context(nc.sbuf_tensor("np_" + name, shape, F32))
        sb_r = lambda name, shape: ctx.enter_context(nc.sbuf_tensor("np_" + name, shape, R32))
        sem = lambda name, ahead=0: new_sem("np_" + name, ahead)
        x, x_lo = overlaid(nc, ctx, "np_x", [P, KD, T])
        x_hi = sb_r("x_hi", [P, KD, T])
        rstd = sb("rstd", [P, T])
        sq = sb("sq", [P, 2, T])
        gain = sb("gain", [P, KD])
        ones = sb("ones", [P, P])
        wf, wf_lo = overlaid(nc, ctx, "np_wf", [P, 2, KD, P])
        wf_hi = sb_r("wf_hi", [P, 2, KD, P])
        wt, wt_lo = overlaid(nc, ctx, "np_wt", [P, 2, KD, TOK_CHUNK])
        wt_hi = sb_r("wt_hi", [P, 2, KD, TOK_CHUNK])
        stage = sb("stage", [P, 2, T])
        stage_t = sb("stage_t", [P, 4, TOK_CHUNK])
        ps = ctx.enter_context(nc.psum_tensor("np_ps", [P, 8, BANK], F32))
        x_in, ones_set, squared, sq_used = sem("x_in"), sem("ones_set"), sem("squared"), sem("sq_used")
        var_eps, root, rstd_set, normed = sem("var_eps"), sem("root"), sem("rstd_set"), sem("normed")
        wf_in = [sem("wf_in0"), sem("wf_in1")]
        x_hi_set, x_split = sem("x_hi_set"), sem("x_split")
        wf_hi_set, wf_split, wt_hi_set, wt_split = sem("wf_hi_set"), sem("wf_split"), sem("wt_hi_set"), sem("wt_split")
        wt_in = [sem("wt_in0"), sem("wt_in1")]
        f_mm, f_copied_a, f_copied_v, f_out = sem("f_mm"), sem("f_copied_a", 2), sem("f_copied_v", 2), [sem("f_out0"), sem("f_out1")]
        stage_free = sem("stage_free", 3)
        t_mm, t_copied = sem("t_mm"), sem("t_copied")
        t_out = [sem(f"t_out{i}") for i in range(4)]
        NF = w_feat.shape[0]
        NT = w_tok.shape[0]
        tiles = TILES
        TH = THIRDS[0][1]

        block = ctx.enter_context(nc.Block())

        @block.sync
        def _(sp):
            for k in range(KD):
                sp.dma_start(x[:, k], x_t[:, k]).then_inc(x_in, 16)
            sp.dma_start(gain[:], g_mix).then_inc(x_in, 16)
            for s in range(2):
                sp.dma_start(wf[:, s], w_feat[s]).then_inc(wf_in[s], 16)
            for s in range(2):
                sp.dma_start(wt[:, s], w_tok[s]).then_inc(wt_in[s], 16)
            with sp.Fori(0, NF // 2 - 1) as i:
                for s in range(2):
                    sp.wait_ge(f_mm, i * 6 + 3 * s + 3)
                    sp.dma_start(wf[:, s], w_feat[i * 2 + (s + 2)]).then_inc(wf_in[s], 16)
            for c in range(2, NT):
                sp.wait_ge(t_mm, len(tiles) * (c - 1))
                sp.dma_start(wt[:, c % 2], w_tok[c]).then_inc(wt_in[c % 2], 16)

        @block.gpsimd
        def _(pool):
            pool.memset(ones[:], 1.0).then_inc(ones_set, 1)
            with pool.Fori(0, NF // 2) as i:
                for s in range(2):
                    pool.wait_ge(f_copied_a, i * 2 + (s + 3))
                    pool.wait_ge(f_copied_v, i * 2 + (s + 3))
                    pool.dma_start(feat_out[bass.ds(i * 256 + s * 128, P), :], stage[:, s]).then_inc(f_out[s], 16)
                for s in range(2):
                    pool.wait_ge(f_out[s], i * 16 + 16)
                    pool.sem_inc(stage_free, 1)
            for n in range(NT * len(tiles)):
                c, t = divmod(n, len(tiles))
                t0, tn = tiles[t]
                pool.wait_ge(t_copied, n + 1)
                pool.dma_start(tok_out[t0:t0 + tn, c * TOK_CHUNK:(c + 1) * TOK_CHUNK], stage_t[0:tn, n % 4]).then_inc(t_out[n % 4], 16)
            for s in range(4):
                pool.wait_ge(t_out[s], 16 * len(range(s, NT * len(tiles), 4)))

        @block.tensor
        def _(pe):
            pe.wait_ge(ones_set, 1)
            for k in range(KD):
                pe.wait_ge(squared, k + 1)
                for n, (a, b) in enumerate(THIRDS):
                    last = pe.matmul(ps[:, n, 0:b - a], ones[:], sq[:, k % 2, a:b], start=(k == 0), stop=(k == KD - 1))
                last.then_inc(sq_used, 1)
            pe.wait_ge(x_split, KD)
            pe.wait_ge(var_eps, 3)
            with pe.Fori(0, NF // 2) as i:
                for s in range(2):
                    pe.wait_ge(wf_split, i * 2 + (s + 1))
                    pe.wait_ge(f_copied_a, i * 2 + (s + 1))
                    pe.wait_ge(f_copied_v, i * 2 + (s + 1))
                    for n, (a, b) in enumerate(THIRDS):
                        for k in range(KD):
                            last = split_product(pe, ps[:, 4 * s + n, 0:b - a], wf_hi[:, s, k], wf_lo[:, s, k], x_hi[:, k, a:b], x_lo[:, k, a:b], k == 0, k == KD - 1)
                        last.then_inc(f_mm, 1)
            pe.wait_ge(f_copied_a, NF + 2)
            pe.wait_ge(f_copied_v, NF + 2)
            for c in range(NT):
                pe.wait_ge(wt_split, c + 1)
                for t, (t0, tn) in enumerate(tiles):
                    n = c * len(tiles) + t
                    if n >= 8:
                        pe.wait_ge(t_copied, n - 7)
                    for k in range(KD):
                        last = split_product(pe, ps[0:tn, n % 8, 0:TOK_CHUNK], x_hi[:, k, t0:t0 + tn], x_lo[:, k, t0:t0 + tn], wt_hi[:, c % 2, k], wt_lo[:, c % 2, k], k == 0, k == KD - 1)
                    last.then_inc(t_mm, 1)

        @block.scalar
        def _(act):
            for k in range(KD):
                act.wait_ge(x_in, 16 * (KD + 1))
                if k >= 2:
                    act.wait_ge(sq_used, k - 1)
                act.activation(sq[:, k % 2], x[:, k], ACT.Square).then_inc(squared, 1)
            act.wait_ge(var_eps, 3)
            act.activation(rstd[:], rstd[:], ACT.Sqrt).then_inc(root, 1)
            for k in range(KD):
                act.wait_ge(normed, k + 1)
                act.activation(x_hi[:, k], x[:, k], ACT.Copy).then_inc(x_hi_set, 1)
            for s in range(2):
                act.wait_ge(wf_in[s], 16)
                act.activation(wf_hi[:, s], wf[:, s], ACT.Copy).then_inc(wf_hi_set, 1)
            for s in range(2):
                act.wait_ge(wt_in[s], 16)
                act.activation(wt_hi[:, s], wt[:, s], ACT.Copy).then_inc(wt_hi_set, 1)

            def copy_out(i, s):
                act.wait_ge(stage_free, i * 2 + (s + 2))
                act.wait_ge(f_mm, i * 6 + (3 * s + 1))
                act.activation(stage[:, s, 0:TH], ps[:, 4 * s, 0:TH], ACT.Copy).then_inc(f_copied_a, 1)

            with act.Fori(0, NF // 2 - 1) as i:
                for s in range(2):
                    copy_out(i, s)
                    act.wait_ge(wf_in[s], i * 16 + 32)
                    act.activation(wf_hi[:, s], wf[:, s], ACT.Copy).then_inc(wf_hi_set, 1)
            for s in range(2):
                copy_out(NF // 2 - 1, s)
            for c in range(2, NT):
                act.wait_ge(wt_in[c % 2], 16 * (c // 2 + 1))
                act.activation(wt_hi[:, c % 2], wt[:, c % 2], ACT.Copy).then_inc(wt_hi_set, 1)

        @block.vector
        def _(dve):
            dve.wait_ge(sq_used, KD)
            for n, (a, b) in enumerate(THIRDS):
                dve.tensor_scalar(rstd[:, a:b], ps[:, n, 0:b - a], 1.0 / D, EPS, ALU.mult, ALU.add).then_inc(var_eps, 1)
            dve.wait_ge(root, 1)
            dve.reciprocal(rstd[:], rstd[:]).then_inc(rstd_set, 1)
            dve.wait_ge(rstd_set, 1)
            for k in range(KD):
                dve.scalar_tensor_tensor(out=x[:, k], in0=x[:, k], scalar=gain[:, k:k + 1], in1=rstd[:], op0=ALU.mult, op1=ALU.mult).then_inc(normed, 1)
            for k in range(KD):
                dve.wait_ge(x_hi_set, k + 1)
                dve.tensor_tensor(x_lo[:, k], x[:, k], x_hi[:, k], ALU.subtract).then_inc(x_split, 1)
            for s in range(2):
                dve.wait_ge(wf_hi_set, s + 1)
                dve.tensor_tensor(wf_lo[:, s], wf[:, s], wf_hi[:, s], ALU.subtract).then_inc(wf_split, 1)
            for s in range(2):
                dve.wait_ge(wt_hi_set, s + 1)
                dve.tensor_tensor(wt_lo[:, s], wt[:, s], wt_hi[:, s], ALU.subtract).then_inc(wt_split, 1)

            def copy_out(i, s):
                dve.wait_ge(stage_free, i * 2 + (s + 2))
                dve.wait_ge(f_mm, i * 6 + (3 * s + 3))
                dve.tensor_copy(stage[:, s, TH:2 * TH], ps[:, 4 * s + 1, 0:TH])
                dve.tensor_copy(stage[:, s, 2 * TH:T], ps[:, 4 * s + 2, 0:T - 2 * TH]).then_inc(f_copied_v, 1)

            with dve.Fori(0, NF // 2 - 1) as i:
                for s in range(2):
                    copy_out(i, s)
                    dve.wait_ge(wf_hi_set, i * 2 + (s + 3))
                    dve.tensor_tensor(wf_lo[:, s], wf[:, s], wf_hi[:, s], ALU.subtract).then_inc(wf_split, 1)
            for s in range(2):
                copy_out(NF // 2 - 1, s)
            for n in range(NT * len(tiles)):
                c, t = divmod(n, len(tiles))
                tn = tiles[t][1]
                dve.wait_ge(t_mm, n + 1)
                if n >= 4:
                    dve.wait_ge(t_out[n % 4], 16 * (n // 4))
                dve.tensor_copy(stage_t[0:tn, n % 4], ps[0:tn, n % 8, 0:TOK_CHUNK]).then_inc(t_copied, 1)
                if t == 2 and 2 <= c + 1 < NT:
                    dve.wait_ge(wt_hi_set, c + 2)
                    s = (c + 1) % 2
                    dve.tensor_tensor(wt_lo[:, s], wt[:, s], wt_hi[:, s], ALU.subtract).then_inc(wt_split, 1)


def attention_rows_stage(nc, tok, qk_norm, ident_in, rows_out, qkv, heads_t):
    NHD = NQKV // HD
    K_SEL, K_WIN = (512 + 256) // HD, 1024 // HD
    with ExitStack() as ctx:
        new_sem = ctx.enter_context(stage_semaphores(nc))
        sb = lambda name, shape: ctx.enter_context(nc.sbuf_tensor("ar_" + name, shape, F32))
        sem = lambda name: new_sem("ar_" + name)
        rows = sb("rows", [P, 2, NHD, HD])
        sq = sb("sq", [P, 12, HD])
        ssq = sb("ssq", [P, 12])
        rstd = sb("rstd", [P, 12])
        gain = sb("gain", [P, 4, HD])
        ident = sb("ident", [P, P])
        turned = sb("turned", [P, 2, 6, P])
        ps = ctx.enter_context(nc.psum_tensor("ar_ps", [P, 4, BANK], F32))
        rows_in = [sem("rows_in0"), sem("rows_in1")]
        rows_stored = [sem("rows_stored0"), sem("rows_stored1")]
        turned_stored = [sem("turned_stored0"), sem("turned_stored1")]
        const_in, q_gain, var_set, root, normed, tr_done, copied = (
            sem("const_in"), sem("q_gain"), sem("var_set"), sem("root"), sem("normed"), sem("tr_done"), sem("copied"))
        NTL = len(TILES)
        parts = [(0, 8, 0, 0), (K_SEL, 2, 8, 2), (K_WIN, 2, 10, 3)]
        block = ctx.enter_context(nc.Block())

        @block.sync
        def _(sp):
            sp.dma_start(gain[:], qk_norm.unsqueeze(0).to_broadcast([P, 4, HD])).then_inc(const_in, 16)
            sp.dma_start(ident[:], ident_in).then_inc(const_in, 16)
            for t, (t0, tn) in enumerate(TILES):
                if t >= 2:
                    sp.wait_ge(rows_stored[t % 2], 32 * (t // 2))
                    sp.wait_ge(tr_done, 6 * (t - 1))
                sp.dma_start(rows[0:tn, t % 2].rearrange("p h d -> p (h d)"), tok[t0:t0 + tn, C_NQ:C_NQ + NQKV]).then_inc(rows_in[t % 2], 16)

        @block.gpsimd
        def _(pool):
            for t, (t0, tn) in enumerate(TILES):
                r = rows[0:tn, t % 2].rearrange("p h d -> p (h d)")
                pool.wait_ge(normed, 3 * (t + 1))
                pool.dma_start(rows_out[t0:t0 + tn, :], r[:, 512:1024]).then_inc(rows_stored[t % 2], 16)
                pool.dma_start(qkv[t0:t0 + tn, :], r).then_inc(rows_stored[t % 2], 16)
                pool.wait_ge(copied, 2 * (t + 1))
                pool.dma_start(heads_t[:, t0:t0 + tn].rearrange("(a p) t -> p a t", p=P), turned[:, t % 2, :, 0:tn]).then_inc(turned_stored[t % 2], 16)
            for s in range(2):
                n = len(range(s, NTL, 2))
                pool.wait_ge(rows_stored[s], 32 * n)
                pool.wait_ge(turned_stored[s], 16 * n)

        @block.scalar
        def _(act):
            for t, (t0, tn) in enumerate(TILES):
                act.wait_ge(var_set, t + 1)
                act.activation(rstd[0:tn], ssq[0:tn], ACT.Sqrt).then_inc(root, 1)

        @block.tensor
        def _(pe):
            pe.wait_ge(const_in, 32)
            for t, (t0, tn) in enumerate(TILES):
                pe.wait_ge(normed, 3 * (t + 1))
                if t >= 2:
                    pe.wait_ge(copied, 2 * (t - 1))
                for n, slot in enumerate((0, 2, 4, 6, K_SEL, K_WIN)):
                    pe.transpose(ps[:, 2 * (t % 2) + n // 4, (n % 4) * P:(n % 4) * P + tn],
                                 rows[0:tn, t % 2, slot:slot + 2].rearrange("p h d -> p (h d)"), ident[0:tn, 0:tn]).then_inc(tr_done, 1)

        @block.vector
        def _(dve):
            dve.wait_ge(const_in, 32)
            dve.tensor_scalar(gain[:, 0], gain[:, 0], HD ** -0.5, None, ALU.mult).then_inc(q_gain, 1)
            dve.wait_ge(q_gain, 1)
            for t, (t0, tn) in enumerate(TILES):
                dve.wait_ge(rows_in[t % 2], 16 * (t // 2 + 1))
                for slot, n, at, _g in parts:
                    r = rows[0:tn, t % 2, slot:slot + n]
                    dve.tensor_tensor(sq[0:tn, at:at + n], r, r, ALU.mult)
                dve.drain()
                dve.tensor_reduce(ssq[0:tn], sq[0:tn], AX.X, ALU.add)
                dve.drain()
                dve.tensor_scalar(ssq[0:tn], ssq[0:tn], 1.0 / HD, EPS, ALU.mult, ALU.add).then_inc(var_set, 1)
                dve.wait_ge(root, t + 1)
                dve.reciprocal(rstd[0:tn], rstd[0:tn])
                dve.drain()
                for slot, n, at, _g in parts:
                    r = rows[0:tn, t % 2, slot:slot + n]
                    dve.tensor_tensor(r, r, rstd[0:tn, at:at + n].unsqueeze(2).to_broadcast([tn, n, HD]), ALU.mult)
                dve.drain()
                for slot, n, at, g in parts:
                    r = rows[0:tn, t % 2, slot:slot + n]
                    dve.tensor_tensor(r, r, gain[0:tn, g:g + 1].to_broadcast([tn, n, HD]), ALU.mult).then_inc(normed, 1)
                if t >= 2:
                    dve.wait_ge(turned_stored[t % 2], 16 * (t // 2))
                for b, (h0, hn) in enumerate(((0, 4), (4, 2))):
                    dve.wait_ge(tr_done, 6 * t + h0 + hn)
                    dve.tensor_copy(turned[:, t % 2, h0:h0 + hn, 0:tn],
                                    ps[:, 2 * (t % 2) + b, 0:hn * P].rearrange("p (h t) -> p h t", t=P)[:, :, 0:tn]).then_inc(copied, 1)


def bias_strip_stage(nc, rel_ext, onehot, qkv, win_cache, strips, win_p, win_s):
    with ExitStack() as ctx:
        new_sem = ctx.enter_context(stage_semaphores(nc))
        lhs = ctx.enter_context(nc.sbuf_tensor("bs_lhs", [N_BUCKETS + 1, NH], F32))
        rhs = ctx.enter_context(nc.sbuf_tensor("bs_rhs", [N_BUCKETS + 1, 2 * STRIP], F32))
        out = ctx.enter_context(nc.sbuf_tensor("bs_out", [NH, 2 * STRIP], F32))
        ps = ctx.enter_context(nc.psum_tensor("bs_ps", [P, 8, BANK], F32))
        loaded, summed, copied, stored = (new_sem("bs_" + n) for n in ("loaded", "summed", "copied", "stored"))
        windows_stored = new_sem("bs_windows_stored")
        block = ctx.enter_context(nc.Block())

        @block.scalar
        def _(act):
            act.dma_start(win_p, qkv[TP - WINDOW:TP, 1024:NQKV]).then_inc(windows_stored, 16)
            act.dma_start(win_s[:, 0:WINDOW - ST], win_cache[:, ST:WINDOW]).then_inc(windows_stored, 16)
            act.dma_start(win_s[:, WINDOW - ST:WINDOW], qkv[TP:T, 1024:NQKV].rearrange("(b t) c -> b t c", b=SB)).then_inc(windows_stored, 16)
            act.wait_ge(windows_stored, 48)

        @block.sync
        def _(sp):
            sp.dma_start(lhs[:], rel_ext).then_inc(loaded, 16)
            sp.dma_start(rhs[:], onehot.rearrange("b w m -> b (w m)")).then_inc(loaded, 16)
            sp.wait_ge(copied, 8)
            sp.dma_start(strips.rearrange("w h m -> h w m"), out[:].rearrange("h (w m) -> h w m", w=2)).then_inc(stored, 16)
            sp.wait_ge(stored, 16)

        @block.tensor
        def _(pe):
            pe.wait_ge(loaded, 32)
            for n in range(8):
                pe.matmul(ps[0:NH, n, :], lhs[:], rhs[:, n * BANK:(n + 1) * BANK], start=True, stop=True).then_inc(summed, 1)

        @block.vector
        def _(dve):
            for n in range(8):
                dve.wait_ge(summed, n + 1)
                dve.tensor_copy(out[:, n * BANK:(n + 1) * BANK], ps[0:NH, n, :]).then_inc(copied, 1)


def sample_attention_stage(nc, cache, page_table, win_cache, heads_t, qkv, tok, strips, w1_in, w2_in, pe_in,
                           qk_norm, overlap_in, rep_in, ident_in, out_t):
    NB = (PAST // CMP_STRIDE) - 1
    NU = PAST // 256
    NPG = PAST // 128
    NS = PAST // 64 + 1
    R = NH * ST
    KEYS = PAST + ST
    with ExitStack() as ctx:
        new_sem = ctx.enter_context(stage_semaphores(nc))
        sb = lambda name, shape, dt=F32: ctx.enter_context(nc.sbuf_tensor("sa_" + name, shape, dt))
        sem = lambda name: new_sem("sa_" + name)
        pages = sb("pages", [P, NU, 2, 512])
        paired = sb("paired", [P, 2, 4, 2, HD])
        vals = sb("vals", [P, NU, 2, P])
        raw_t = sb("raw_t", [P, 4, NU * P])
        keys_t = sb("keys_t", [P, KEYS])
        scores = sb("scores", [R, KEYS])
        near_bias = sb("near_bias", [R, 256 + ST])
        probs_t = sb("probs_t", [P, 2 * NU + 1, R])
        w1 = sb("w1", [P, 2, 16, CMP_HID])
        w2 = sb("w2", [P, 2, HD])
        pe_cols = sb("pe_cols", [P, 2, 16])
        hid_bias = sb("hid_bias", [P, 2])
        hid = sb("hid", [P, 2, 2, NB])
        k_norm = sb("k_norm", [P, HD])
        cmp_kv = sb("cmp_kv", [P, 2, 2, P])
        cmp_sq = sb("cmp_sq", [P, 2, P])
        cmp_ssq = sb("cmp_ssq", [P, 4])
        cmp_kt = sb("cmp_kt", [P, NB])
        cmp_s = sb("cmp_s", [R, NB])
        cmp_bias = sb("cmp_bias", [R, NB])
        cmp_pt = sb("cmp_pt", [P, 2, R])
        overlap = sb("overlap", [P, 2, NS])
        rep = sb("rep", [R, R])
        ident = sb("ident", [P, P])
        blk = sb("blk", [R, NS])
        blk_rep = sb("blk_rep", [R, NS])
        top = sb("top", [R, 16])
        mask = sb("mask", [R, NS])
        win = sb("win", [P, 4, 256])
        win_kt = sb("win_kt", [P, WINDOW + ST])
        win_s = sb("win_s", [R, WINDOW + ST])
        win_bias = sb("win_bias", [R, WINDOW + ST])
        win_pt = sb("win_pt", [P, 5, R])
        new_v = sb("new_v", [ST, 2, P])
        q_diag = sb("q_diag", [P, R])
        near = sb("near", [R, 264])
        gates = sb("gates", [R, 3])
        cols = sb("cols", [R, 16])
        out_rows = sb("out_rows", [R, HD])
        out_cols = sb("out_cols", [HD, R])
        table = sb("table", [1, SB * NPG], I32)
        ps = ctx.enter_context(nc.psum_tensor("sa_ps", [P, 8, BANK], F32))
        names = ("const_in table_in bias_in zeroed bias_set pe_done hid_bias_set small_in win_in unit_in tr cmp_copied key_copied val_copied "
                 "hid_mm gelu_done sel_mm sel_biased out2_mm var_set root kv_set kt_tr kt_copied cs_mm cs_neg cs_exp cs_norm cpt_tr cpt_copied "
                 "oc_mm blk_copied rep_mm sel_neg sel_exp spt_tr spt_copied os_mm wk_tr wk_copied ws_mm ws_neg ws_exp wpt_tr wpt_copied ow_mm "
                 "gate_exp out_set ot_tr ot_copied out_stored out_free passed oc_copied new_pt_copied pairs_set").split()
        ahead = "tr pairs_set val_copied cs_mm ws_mm ow_mm os_mm out_set out_free spt_copied wpt_copied".split()
        S = {n: new_sem("sa_" + n, 1 if n in ahead else 0) for n in names}
        unit_in = [sem(f"unit_in{u}") for u in range(NU)]
        block = ctx.enter_context(nc.Block())
        NPT = 5
        strip_q = lambda w, q, lo, n: strips[w, :, lo - q:lo - q + n]
        cmp_far = 192
        mn = ctx.enter_context(nc.allow_non_contiguous_dma(reason="small strided tables, once"))

        @block.sync
        def _(sp):
            sp.dma_start(table[:], page_table).then_inc(S["table_in"], 16)
            sp.wait_ge(S["table_in"], 16)
            with sp.Fori(0, SB) as b:
                for u in range(NU):
                    for j in range(2):
                        page = sp.value_load(table[0:1, bass.ds(b * NPG + (2 * u + j), 1)], min_val=0, max_val=cache.shape[0] - 1)
                        if j == 0:
                            sp.wait_ge(S["tr"], b * (2 * NU) + 1)
                            sp.sem_inc(S["passed"], 1)
                            sp.wait_ge(S["pairs_set"], b * NU + 1)
                            sp.sem_inc(S["passed"], 1)
                            sp.wait_ge(S["val_copied"], b * NU + 1)
                            sp.sem_inc(S["passed"], 1)
                        sp.dma_start(pages[64 * j:64 * j + 64, u].rearrange("p t c -> p (t c)"),
                                     cache[page].rearrange("(p t) c -> p (t c)", t=2)).then_inc(unit_in[u], 16)

        @block.gpsimd
        def _(pool):
            pool.memset(q_diag[:], 0.0).then_inc(S["zeroed"], 1)
            pool.wait_ge(S["zeroed"], 1)
            with pool.Fori(0, SB) as b:
                pool.wait_ge(S["cs_mm"], b + 1)
                pool.wait_ge(S["ws_mm"], b + 1)
                pool.wait_ge(S["ow_mm"], b + 1)
                pool.wait_ge(S["os_mm"], b + 1)
                pool.wait_ge(S["out_set"], b + 1)
                pool.sem_inc(S["passed"], 1)
                at = b * ST + TP
                for g in range(NG):
                    for r in range(NR):
                        h = g * NR + r
                        pool.dma_start(q_diag[HD * g:HD * (g + 1), h * ST:(h + 1) * ST], heads_t[h * HD:(h + 1) * HD, bass.ds(at, ST)]).then_inc(S["small_in"], 16)
                pool.dma_start(keys_t[:, PAST:KEYS], heads_t[4 * P:5 * P, bass.ds(at, ST)]).then_inc(S["small_in"], 16)
                pool.dma_start(win_kt[:, WINDOW:], heads_t[5 * P:6 * P, bass.ds(at, ST)]).then_inc(S["small_in"], 16)
                pool.dma_start(new_v[:, 0], qkv[bass.ds(at, ST), 512 + 384:512 + 512]).then_inc(S["small_in"], 16)
                pool.dma_start(new_v[:, 1], qkv[bass.ds(at, ST), 1024 + 128:1024 + 256]).then_inc(S["small_in"], 16)
                for h in range(NH):
                    pool.dma_start(gates[h * ST:(h + 1) * ST, :], tok[bass.ds(at, ST), C_NGATE:C_NGATE + 24].rearrange("q (n h) -> q n h", n=3)[:, :, h]).then_inc(S["small_in"], 16)
                pool.dma_start(win[:], win_cache[b].rearrange("(a p) c -> p a c", p=P)).then_inc(S["win_in"], 16)
                for u in range(NU):
                    pool.wait_ge(unit_in[u], b * 32 + 32)
                    if u == 0:
                        pool.wait_ge(S["os_mm"], b + 1)
                    pool.sem_inc(S["passed"], 1)
                    pool.tensor_copy(vals[:, u], pages[:, u, :, 384:512]).then_inc(S["val_copied"], 1)
                pool.wait_ge(S["ot_copied"], b + 1)
                pool.sem_inc(S["passed"], 1)
                pool.dma_start(out_t[:, bass.ds(at, ST)].rearrange("(h d) q -> d h q", d=HD), out_cols[:].rearrange("d (h q) -> d h q", q=ST)).then_inc(S["out_stored"], 16)
                pool.wait_ge(S["out_stored"], b * 16 + 16)
                pool.sem_inc(S["out_free"], 1)

        @block.scalar
        def _(act):
            n_const = 0
            for dst, src in ((w1[:], w1_in), (w2[:], w2_in), (pe_cols[:], pe_in), (k_norm[:], qk_norm[1:2, :].to_broadcast([P, HD])),
                             (overlap[:], overlap_in), (rep[:], rep_in), (ident[:], ident_in)):
                act.dma_start(dst, src).then_inc(S["const_in"], 16)
            for q in range(ST):
                act.dma_start(near[q:R:ST], strip_q(0, q, STRIP_AT - 256, 264)).then_inc(S["bias_in"], 16)
                act.dma_start(win_bias[q:R:ST], strip_q(1, q, STRIP_AT - WINDOW, WINDOW + ST)).then_inc(S["bias_in"], 16)
                lo = STRIP_AT - (PAST - (CMP_LEN - 1)) + CMP_STRIDE * cmp_far - q
                act.dma_start(cmp_bias[q:R:ST, cmp_far:].unsqueeze(2), strips[0, :, lo:lo + CMP_STRIDE * (NB - cmp_far)].rearrange("h (i s) -> h i s", s=CMP_STRIDE)[:, :, 0:1]).then_inc(S["bias_in"], 16)
            act.wait_ge(S["pe_done"], 1)
            act.activation(hid_bias[:], ps[:, 6, 0:2], ACT.Copy).then_inc(S["hid_bias_set"], 1)
            with act.Fori(0, SB) as b:
                act.wait_ge(S["wk_tr"], b + 1)
                act.activation(win_kt[:, 0:WINDOW], ps[:, 7, :], ACT.Copy).then_inc(S["wk_copied"], 1)
                for u in range(NU):
                    act.wait_ge(S["tr"], b * (2 * NU) + (2 * u + 1) + 1)
                    act.activation(raw_t[:, :, u * P:(u + 1) * P], ps[:, 2 * (u % 2), :].rearrange("p (s t) -> p s t", t=P), ACT.Copy).then_inc(S["cmp_copied"], 1)
                for s in range(2):
                    act.wait_ge(S["hid_mm"], b * 2 + (s + 1))
                    act.activation(hid[:, s].rearrange("p g i -> p (g i)"), ps[:, 4 + s, 0:2 * NB], ACT.Gelu_apprx_tanh, bias=hid_bias[:, s:s + 1]).then_inc(S["gelu_done"], 1)
                act.wait_ge(S["var_set"], b + 1)
                act.activation(cmp_ssq[:], cmp_ssq[:], ACT.Sqrt).then_inc(S["root"], 1)
                act.wait_ge(S["ws_neg"], b + 1)
                act.activation(win_s[:], win_s[:], ACT.Exp, bias=cols[:, 0:1], accum_out=cols[:, 1:2]).then_inc(S["ws_exp"], 1)
                act.wait_ge(S["small_in"], (b + 1) * 320)
                act.activation(gates[:], gates[:], ACT.Exp, scale=-1.0).then_inc(S["gate_exp"], 1)
                act.wait_ge(S["cs_neg"], b + 1)
                act.activation(cmp_s[:], cmp_s[:], ACT.Exp, bias=cols[:, 2:3], accum_out=cols[:, 3:4]).then_inc(S["cs_exp"], 1)
                act.wait_ge(S["sel_neg"], b + 1)
                act.activation(scores[:], scores[:], ACT.Exp, bias=cols[:, 4:5], accum_out=cols[:, 5:6]).then_inc(S["sel_exp"], 1)
                for n in range(4):
                    act.wait_ge(S["spt_tr"], b * NPT + (n + 1))
                    act.activation(probs_t[:, 8 * n:8 * n + 8].rearrange("p a r -> p (a r)"), ps[:, n, :], ACT.Copy).then_inc(S["spt_copied"], 1)

        @block.tensor
        def _(pe):
            pe.wait_ge(S["const_in"], 16 * 7)
            for s in range(2):
                for j in range(16):
                    last = pe.matmul(ps[:, 6, s:s + 1], w1[:, s, j], pe_cols[:, s, j:j + 1], start=(j == 0), stop=(j == 15))
            last.then_inc(S["pe_done"], 1)
            pe.wait_ge(S["hid_bias_set"], 1)
            with pe.Fori(0, SB) as b:
                pe.wait_ge(S["win_in"], b * 16 + 16)
                pe.wait_ge(S["wpt_copied"], b + 1)
                for a in range(4):
                    last = pe.transpose(ps[:, 7, a * P:(a + 1) * P], win[:, a, 0:P], ident[:])
                last.then_inc(S["wk_tr"], 1)
                for u in range(NU):
                    pe.wait_ge(unit_in[u], b * 32 + 32)
                    pe.wait_ge(S["pairs_set"], b * NU + (u + 2))
                    A = 2 * (u % 2)
                    if u < 2:
                        pe.wait_ge(S["spt_copied"], b * 4 + 1)
                    else:
                        pe.wait_ge(S["cmp_copied"], b * NU + (u - 1))
                        pe.wait_ge(S["key_copied"], b * NU + (u - 1))
                    for sg in range(4):
                        last = pe.transpose(ps[:, A, sg * P:(sg + 1) * P], paired[:, u % 2, sg].rearrange("p t d -> p (t d)"), ident[:])
                    last.then_inc(S["tr"], 1)
                    for t in range(2):
                        last = pe.transpose(ps[:, A + 1, t * P:(t + 1) * P], pages[:, u, t, 256:384], ident[:])
                    last.then_inc(S["tr"], 1)
                pe.wait_ge(S["cmp_copied"], b * NU + NU)
                pe.wait_ge(S["out_set"], b + 1)
                for s in range(2):
                    for j in range(16):
                        last = pe.matmul(ps[:, 4 + s, 0:2 * NB], w1[:, s, j], raw_t[:, 2 * s:2 * s + 2, j:j + 8 * (NB - 1) + 1:8], start=(j == 0), stop=(j == 15))
                    last.then_inc(S["hid_mm"], 1)
                pe.wait_ge(S["small_in"], (b + 1) * 320)
                pe.wait_ge(S["wk_copied"], b + 1)
                pe.matmul(ps[0:R, 7, :], q_diag[:], win_kt[:, 0:WINDOW], start=True, stop=True)
                pe.matmul(ps[0:R, 6, 8:16], q_diag[:], win_kt[:, WINDOW:], start=True, stop=True).then_inc(S["ws_mm"], 1)
                pe.wait_ge(S["key_copied"], b * NU + NU)
                for n in range(8):
                    if n >= 4:
                        pe.wait_ge(S["sel_biased"], b * 9 + (n - 3))
                    pe.matmul(ps[0:R, n % 4, :], q_diag[:], keys_t[:, n * 512:(n + 1) * 512], start=True, stop=True).then_inc(S["sel_mm"], 1)
                pe.matmul(ps[0:R, 6, 0:8], q_diag[:], keys_t[:, PAST:KEYS], start=True, stop=True).then_inc(S["sel_mm"], 1)
                pe.wait_ge(S["gelu_done"], b * 2 + 2)
                for s in range(2):
                    for g in range(2):
                        for c in range(2):
                            m = P if c == 0 else NB - P
                            last = pe.matmul(ps[0:m, 4, ((s * 2 + c) * 2 + g) * HD:((s * 2 + c) * 2 + g + 1) * HD], hid[:, s, g, c * P:c * P + m], w2[:, s], start=True, stop=True)
                last.then_inc(S["out2_mm"], 1)
                pe.wait_ge(S["kv_set"], b + 1)
                pe.transpose(ps[:, 5, 0:P], cmp_kv[:, 0, 0], ident[:])
                pe.transpose(ps[:, 5, P:NB], cmp_kv[0:NB - P, 0, 1], ident[0:NB - P, 0:NB - P]).then_inc(S["kt_tr"], 1)
                pe.wait_ge(S["kt_copied"], b + 1)
                pe.matmul(ps[0:R, 5, 256:256 + NB], q_diag[:], cmp_kt[:], start=True, stop=True).then_inc(S["cs_mm"], 1)
                pe.wait_ge(S["ws_exp"], b + 1)
                pe.sem_inc(S["passed"], 1)
                for a in range(4):
                    pe.transpose(ps[:, 7, a * R:(a + 1) * R], win_s[:, a * P:(a + 1) * P], ident[0:R, 0:R])
                pe.transpose(ps[0:ST, 7, 4 * R:5 * R], win_s[:, WINDOW:], ident[0:R, 0:R]).then_inc(S["wpt_tr"], 1)
                pe.wait_ge(S["wpt_copied"], b + 2)
                for a in range(4):
                    pe.matmul(ps[0:R, 6, 128:256], win_pt[:, a], win[:, a, P:2 * P], start=(a == 0), stop=False)
                pe.matmul(ps[0:R, 6, 128:256], win_pt[0:ST, 4], new_v[:, 1], start=False, stop=True).then_inc(S["ow_mm"], 1)
                pe.wait_ge(S["cs_norm"], b + 1)
                pe.sem_inc(S["passed"], 1)
                pe.transpose(ps[:, 4, 0:R], cmp_s[:, 0:P], ident[0:R, 0:R])
                pe.transpose(ps[0:NB - P, 4, R:2 * R], cmp_s[:, P:NB], ident[0:R, 0:R]).then_inc(S["cpt_tr"], 1)
                pe.wait_ge(S["cpt_copied"], b + 1)
                for c, m in ((0, P), (1, NB - P)):
                    pe.matmul(ps[0:R, 4, 256:256 + NS], cmp_pt[0:m, c], overlap[0:m, c], start=(c == 0), stop=(c == 1))
                for c, m in ((0, P), (1, NB - P)):
                    last = pe.matmul(ps[0:R, 4, 128:256], cmp_pt[0:m, c], cmp_kv[0:m, 1, c], start=(c == 0), stop=(c == 1))
                last.then_inc(S["oc_mm"], 1)
                pe.wait_ge(S["blk_copied"], b + 1)
                pe.sem_inc(S["passed"], 1)
                pe.matmul(ps[0:R, 4, 384:384 + NS], rep[:], blk[:], start=True, stop=True).then_inc(S["rep_mm"], 1)
                pe.wait_ge(S["sel_exp"], b + 1)
                pe.sem_inc(S["passed"], 1)
                for n in range(32):
                    last = pe.transpose(ps[:, n // 8, (n % 8) * R:(n % 8 + 1) * R], scores[:, n * P:(n + 1) * P], ident[0:R, 0:R])
                    if n % 8 == 7:
                        last.then_inc(S["spt_tr"], 1)
                pe.transpose(ps[0:ST, 6, 64:128], scores[:, PAST:KEYS], ident[0:R, 0:R]).then_inc(S["spt_tr"], 1)
                pe.wait_ge(S["val_copied"], b * NU + (NU + 1))
                for n in range(32):
                    if n % 8 == 0:
                        pe.wait_ge(S["spt_copied"], b * 4 + (n // 8 + 2))
                    pe.matmul(ps[0:R, 5, 0:P], probs_t[:, n], vals[:, n // 2, n % 2], start=(n == 0), stop=False)
                pe.wait_ge(S["new_pt_copied"], b + 1)
                pe.sem_inc(S["passed"], 1)
                pe.matmul(ps[0:R, 5, 0:P], probs_t[0:ST, 32], new_v[:, 0], start=False, stop=True).then_inc(S["os_mm"], 1)
                pe.wait_ge(S["out_set"], b + 2)
                pe.sem_inc(S["passed"], 1)
                pe.transpose(ps[0:HD, 6, 256:256 + R], out_rows[:], ident[0:R, 0:R]).then_inc(S["ot_tr"], 1)

        @block.vector
        def _(dve):
            dve.wait_ge(S["bias_in"], 16 * 3 * ST)
            dve.memset(cmp_bias[:, 0:cmp_far], 0.0)
            dve.drain()
            dve.tensor_scalar(cmp_bias[:, 0:cmp_far], cmp_bias[:, 0:cmp_far], near[:, 0:1], None, ALU.add)
            for t in range(2):
                dve.tensor_copy(near_bias[:, t * P:(t + 1) * P], near[:, 0:256].rearrange("r (p t) -> r t p", t=2)[:, t])
            dve.tensor_copy(near_bias[:, 256:], near[:, 256:264])
            dve.drain()
            dve.wait_ge(S["const_in"], 16 * 7)
            with dve.Fori(0, SB) as b:
                def pair(u):
                    dve.wait_ge(unit_in[u], b * 32 + 32)
                    dve.wait_ge(S["tr"], (b * (2 * NU) + (2 * (u - 2) + 1) if u >= 2 else b * (2 * NU)) + 1)
                    dve.tensor_copy(paired[:, u % 2], pages[:, u, :, 0:256].rearrange("p t (s d) -> p s t d", d=HD)).then_inc(S["pairs_set"], 1)

                pair(0)
                for u in range(NU):
                    if u + 1 < NU:
                        pair(u + 1)
                    dve.wait_ge(S["tr"], b * (2 * NU) + (2 * u + 2) + 1)
                    dve.tensor_copy(keys_t[:, u * 256:(u + 1) * 256], ps[:, 2 * (u % 2) + 1, 0:256]).then_inc(S["key_copied"], 1)
                dve.wait_ge(S["ws_mm"], b + 2)
                dve.tensor_tensor(win_s[:, 0:WINDOW], ps[0:R, 7, :], win_bias[:, 0:WINDOW], ALU.add)
                dve.tensor_tensor(win_s[:, WINDOW:], ps[0:R, 6, 8:16], win_bias[:, WINDOW:], ALU.add)
                dve.drain()
                dve.tensor_reduce(cols[:, 6:7], win_s[:], AX.X, ALU.max)
                dve.drain()
                dve.tensor_scalar(cols[:, 0:1], cols[:, 6:7], -1.0, None, ALU.mult).then_inc(S["ws_neg"], 1)
                for n in range(9):
                    dve.wait_ge(S["sel_mm"], b * 9 + (n + 1))
                    if n < 7:
                        last = dve.tensor_scalar(scores[:, n * 512:(n + 1) * 512], ps[0:R, n % 4, :], near[:, 0:1], None, ALU.add)
                    elif n == 7:
                        dve.tensor_scalar(scores[:, PAST - 512:PAST - 256], ps[0:R, 3, 0:256], near[:, 0:1], None, ALU.add)
                        last = dve.tensor_tensor(scores[:, PAST - 256:PAST], ps[0:R, 3, 256:512], near_bias[:, 0:256], ALU.add)
                    else:
                        last = dve.tensor_tensor(scores[:, PAST:KEYS], ps[0:R, 6, 0:ST], near_bias[:, 256:], ALU.add)
                    last.then_inc(S["sel_biased"], 1)
                dve.wait_ge(S["out2_mm"], b + 1)
                for c, m in ((0, P), (1, NB - P)):
                    for s in range(2):
                        dve.tensor_copy(cmp_kv[0:m, s, c], ps[0:m, 4, (s * 2 + c) * P:(s * 2 + c + 1) * P])
                dve.drain()
                for c, m in ((0, P), (1, NB - P)):
                    dve.tensor_tensor(cmp_sq[0:m, c], cmp_kv[0:m, 0, c], cmp_kv[0:m, 0, c], ALU.mult)
                dve.drain()
                dve.memset(cmp_ssq[:], 1.0)
                dve.drain()
                for c, m in ((0, P), (1, NB - P)):
                    dve.tensor_reduce(cmp_ssq[0:m, 2 * c:2 * c + 2], cmp_sq[0:m, c].rearrange("p (g d) -> p g d", g=2), AX.X, ALU.add)
                dve.drain()
                dve.tensor_scalar(cmp_ssq[:], cmp_ssq[:], 1.0 / HD, EPS, ALU.mult, ALU.add).then_inc(S["var_set"], 1)
                dve.wait_ge(S["root"], b + 1)
                dve.reciprocal(cmp_ssq[:], cmp_ssq[:])
                dve.drain()
                for c, m in ((0, P), (1, NB - P)):
                    for g in range(2):
                        k = cmp_kv[0:m, 0, c, g * HD:(g + 1) * HD]
                        last = dve.scalar_tensor_tensor(out=k, in0=k, scalar=cmp_ssq[0:m, 2 * c + g:2 * c + g + 1], in1=k_norm[0:m], op0=ALU.mult, op1=ALU.mult)
                last.then_inc(S["kv_set"], 1)
                dve.wait_ge(S["kt_tr"], b + 1)
                dve.tensor_copy(cmp_kt[:], ps[:, 5, 0:NB]).then_inc(S["kt_copied"], 1)
                dve.wait_ge(S["cs_mm"], b + 2)
                dve.tensor_tensor(cmp_s[:], ps[0:R, 5, 256:256 + NB], cmp_bias[:], ALU.add)
                dve.drain()
                dve.tensor_reduce(cols[:, 6:7], cmp_s[:], AX.X, ALU.max)
                dve.drain()
                dve.tensor_scalar(cols[:, 2:3], cols[:, 6:7], -1.0, None, ALU.mult).then_inc(S["cs_neg"], 1)
                dve.wait_ge(S["wpt_tr"], b + 1)
                dve.tensor_copy(win_pt[:, 0:4].rearrange("p a r -> p (a r)"), ps[:, 7, 0:4 * R])
                dve.tensor_copy(win_pt[0:ST, 4], ps[0:ST, 7, 4 * R:5 * R]).then_inc(S["wpt_copied"], 1)
                dve.wait_ge(S["cs_exp"], b + 1)
                dve.reciprocal(cols[:, 7:8], cols[:, 3:4])
                dve.drain()
                dve.tensor_scalar(cmp_s[:], cmp_s[:], cols[:, 7:8], None, ALU.mult)
                dve.drain()
                dve.scalar_tensor_tensor(out=cmp_s[:], in0=cmp_s[:], scalar=TINY, in1=cmp_s[:], op0=ALU.is_ge, op1=ALU.mult).then_inc(S["cs_norm"], 1)
                dve.wait_ge(S["cpt_tr"], b + 1)
                dve.tensor_copy(cmp_pt[:, 0], ps[:, 4, 0:R])
                dve.tensor_copy(cmp_pt[0:NB - P, 1], ps[0:NB - P, 4, R:2 * R]).then_inc(S["cpt_copied"], 1)
                dve.wait_ge(S["oc_mm"], b + 1)
                dve.tensor_copy(blk[:], ps[0:R, 4, 256:256 + NS]).then_inc(S["blk_copied"], 1)
                dve.wait_ge(S["gate_exp"], b + 1)
                dve.tensor_scalar(gates[:], gates[:], 1.0, None, ALU.add)
                dve.drain()
                dve.reciprocal(gates[:], gates[:])
                dve.wait_ge(S["rep_mm"], b + 1)
                dve.tensor_copy(blk_rep[:], ps[0:R, 4, 384:384 + NS])
                dve.drain()
                dve.memset(blk_rep[:, 0:1], FORCE)
                dve.memset(blk_rep[:, NS - 2:NS], FORCE)
                dve.drain()
                for k in range(2):
                    dve.max(top[:, 8 * k:8 * k + 8], blk_rep[:])
                    dve.drain()
                    dve.match_replace(blk_rep[:], top[:, 8 * k:8 * k + 8], blk_rep[:], -FORCE)
                    dve.drain()
                dve.tensor_scalar(mask[:], blk_rep[:], -1.0, NEG, ALU.is_gt, ALU.mult)
                dve.drain()
                for t in range(2):
                    v = scores[:, 0:PAST].rearrange("r (u t k p) -> r t u k p", u=NU, t=2, k=4)[:, t]
                    dve.tensor_tensor(v, v, mask[:, 0:NS - 1].rearrange("r (u k) -> r u k", k=4).unsqueeze(3).to_broadcast([R, NU, 4, 32]), ALU.add)
                dve.drain()
                dve.tensor_reduce(cols[:, 6:7], scores[:], AX.X, ALU.max)
                dve.drain()
                dve.tensor_scalar(cols[:, 4:5], cols[:, 6:7], -1.0, None, ALU.mult).then_inc(S["sel_neg"], 1)
                for g in range(2):
                    last = dve.tensor_scalar(out_rows[32 * g:32 * g + 32], ps[32 * g:32 * g + 32, 4, 128 + HD * g:128 + HD * (g + 1)], gates[32 * g:32 * g + 32, 0:1], None, ALU.mult)
                last.then_inc(S["oc_copied"], 1)
                dve.wait_ge(S["ws_exp"], b + 1)
                dve.reciprocal(cols[:, 8:9], cols[:, 1:2])
                dve.wait_ge(S["spt_tr"], b * NPT + NPT)
                dve.tensor_copy(probs_t[0:ST, 32], ps[0:ST, 6, 64:128]).then_inc(S["new_pt_copied"], 1)
                dve.reciprocal(cols[:, 9:10], cols[:, 5:6])
                dve.drain()
                dve.tensor_tensor(cols[:, 8:9], cols[:, 8:9], gates[:, 2:3], ALU.mult)
                dve.tensor_tensor(cols[:, 9:10], cols[:, 9:10], gates[:, 1:2], ALU.mult)
                dve.drain()
                dve.wait_ge(S["ow_mm"], b + 2)
                for g in range(2):
                    o = out_rows[32 * g:32 * g + 32]
                    dve.scalar_tensor_tensor(out=o, in0=ps[32 * g:32 * g + 32, 6, 128 + HD * g:128 + HD * (g + 1)], scalar=cols[32 * g:32 * g + 32, 8:9], in1=o, op0=ALU.mult, op1=ALU.add)
                dve.drain()
                dve.wait_ge(S["os_mm"], b + 2)
                for g in range(2):
                    o = out_rows[32 * g:32 * g + 32]
                    last = dve.scalar_tensor_tensor(out=o, in0=ps[32 * g:32 * g + 32, 5, HD * g:HD * (g + 1)], scalar=cols[32 * g:32 * g + 32, 9:10], in1=o, op0=ALU.mult, op1=ALU.add)
                last.then_inc(S["out_set"], 1)
                dve.wait_ge(S["ot_tr"], b + 1)
                dve.wait_ge(S["out_free"], b + 1)
                dve.tensor_copy(out_cols[:], ps[0:HD, 6, 256:256 + R]).then_inc(S["ot_copied"], 1)


def prompt_compress_stage(nc, tok, w1_in, w2_in, pe_in, qk_norm, ident_in, kt_out, v_out):
    NB = TP // CMP_STRIDE - 1
    NU = TP // 256
    with ExitStack() as ctx:
        new_sem = ctx.enter_context(stage_semaphores(nc))
        sb = lambda name, shape: ctx.enter_context(nc.sbuf_tensor("pc_" + name, shape, F32))
        raw = sb("raw", [P, NU, 2, 256])
        paired = sb("paired", [P, NU, 4, 2, HD])
        raw_t = sb("raw_t", [P, 4, NU * P])
        w1 = sb("w1", [P, 2, 16, CMP_HID])
        w2 = sb("w2", [P, 2, HD])
        pe_cols = sb("pe_cols", [P, 2, 16])
        k_norm = sb("k_norm", [P, HD])
        ident = sb("ident", [P, P])
        hid_bias = sb("hid_bias", [P, 2])
        hid = sb("hid", [P, 2, 2, NB])
        kv = sb("kv", [NB, 2, P])
        sq = sb("sq", [NB, P])
        ssq = sb("ssq", [NB, 2])
        kt = sb("kt", [P, NB])
        ps = ctx.enter_context(nc.psum_tensor("pc_ps", [P, 8, BANK], F32))
        S = {n: new_sem("pc_" + n) for n in
             "loaded paired_set tr copied hid_mm bias_set gelu_done out_mm var_set root kv_set kt_tr kt_copied stored".split()}
        block = ctx.enter_context(nc.Block())

        @block.sync
        def _(sp):
            for u in range(NU):
                sp.dma_start(raw[:, u], tok[u * 256:(u + 1) * 256, C_KV:C_KV + 256].rearrange("(p t) c -> p t c", t=2)).then_inc(S["loaded"], 16)
            for dst, src in ((w1[:], w1_in), (w2[:], w2_in), (pe_cols[:], pe_in), (k_norm[:], qk_norm[1:2, :].to_broadcast([P, HD])), (ident[:], ident_in)):
                sp.dma_start(dst, src).then_inc(S["loaded"], 16)
            sp.wait_ge(S["kv_set"], 2)
            sp.dma_start(v_out, kv[:, 1]).then_inc(S["stored"], 16)
            sp.wait_ge(S["kt_copied"], 1)
            sp.dma_start(kt_out, kt[:]).then_inc(S["stored"], 16)
            sp.wait_ge(S["stored"], 32)

        @block.tensor
        def _(pe):
            pe.wait_ge(S["loaded"], 16 * (NU + 5))
            for s in range(2):
                for j in range(16):
                    last = pe.matmul(ps[:, 7, s:s + 1], w1[:, s, j], pe_cols[:, s, j:j + 1], start=(j == 0), stop=(j == 15))
            last.then_inc(S["hid_mm"], 1)
            for u in range(NU):
                pe.wait_ge(S["paired_set"], u + 1)
                for sg in range(4):
                    last = pe.transpose(ps[:, u, sg * P:(sg + 1) * P], paired[:, u, sg].rearrange("p t d -> p (t d)"), ident[:])
                last.then_inc(S["tr"], 1)
            pe.wait_ge(S["copied"], NU)
            for s in range(2):
                for j in range(16):
                    last = pe.matmul(ps[:, 4 + s, 0:2 * NB], w1[:, s, j], raw_t[:, 2 * s:2 * s + 2, j:j + 8 * (NB - 1) + 1:8], start=(j == 0), stop=(j == 15))
                last.then_inc(S["hid_mm"], 1)
            pe.wait_ge(S["gelu_done"], 2)
            for s in range(2):
                for g in range(2):
                    last = pe.matmul(ps[0:NB, 6, (2 * s + g) * HD:(2 * s + g + 1) * HD], hid[:, s, g], w2[:, s], start=True, stop=True)
            last.then_inc(S["out_mm"], 1)
            pe.wait_ge(S["kv_set"], 2)
            pe.transpose(ps[:, 0, 0:NB], kv[:, 0], ident[0:NB, 0:NB]).then_inc(S["kt_tr"], 1)

        @block.scalar
        def _(act):
            act.wait_ge(S["hid_mm"], 1)
            act.activation(hid_bias[:], ps[:, 7, 0:2], ACT.Copy).then_inc(S["bias_set"], 1)
            act.wait_ge(S["bias_set"], 1)
            for s in range(2):
                act.wait_ge(S["hid_mm"], s + 2)
                act.activation(hid[:, s].rearrange("p g i -> p (g i)"), ps[:, 4 + s, 0:2 * NB], ACT.Gelu_apprx_tanh, bias=hid_bias[:, s:s + 1]).then_inc(S["gelu_done"], 1)
            act.wait_ge(S["var_set"], 1)
            act.activation(ssq[:], ssq[:], ACT.Sqrt).then_inc(S["root"], 1)

        @block.vector
        def _(dve):
            dve.wait_ge(S["loaded"], 16 * (NU + 5))
            for u in range(NU):
                dve.tensor_copy(paired[:, u], raw[:, u].rearrange("p t (s d) -> p s t d", d=HD)).then_inc(S["paired_set"], 1)
            for u in range(NU):
                dve.wait_ge(S["tr"], u + 1)
                dve.tensor_copy(raw_t[:, :, u * P:(u + 1) * P], ps[:, u, :].rearrange("p (s t) -> p s t", t=P)).then_inc(S["copied"], 1)
            dve.wait_ge(S["out_mm"], 1)
            dve.tensor_copy(kv[:].rearrange("p s c -> p (s c)"), ps[0:NB, 6, 0:256]).then_inc(S["kv_set"], 1)
            dve.drain()
            dve.tensor_tensor(sq[:], kv[:, 0], kv[:, 0], ALU.mult)
            dve.drain()
            dve.tensor_reduce(ssq[:], sq[:].rearrange("p (g d) -> p g d", g=2), AX.X, ALU.add)
            dve.drain()
            dve.tensor_scalar(ssq[:], ssq[:], 1.0 / HD, EPS, ALU.mult, ALU.add).then_inc(S["var_set"], 1)
            dve.wait_ge(S["root"], 1)
            dve.reciprocal(ssq[:], ssq[:])
            dve.drain()
            for g in range(2):
                k = kv[:, 0, g * HD:(g + 1) * HD]
                last = dve.scalar_tensor_tensor(out=k, in0=k, scalar=ssq[:, g:g + 1], in1=k_norm[0:NB], op0=ALU.mult, op1=ALU.mult)
            last.then_inc(S["kv_set"], 1)
            dve.wait_ge(S["kt_tr"], 1)
            dve.tensor_copy(kt[:], ps[:, 0, 0:NB]).then_inc(S["kt_copied"], 1)


def prompt_attention_stage(nc, heads_t, qkv, tok, strips, kt_cmp, v_cmp, flip_in, ident_in, out_rows):
    NT = TP // P
    NB = TP // CMP_STRIDE - 1
    TW = 1920
    with ExitStack() as ctx:
        new_sem = ctx.enter_context(stage_semaphores(nc))
        sb = lambda name, shape: ctx.enter_context(nc.sbuf_tensor("pa_" + name, shape, F32))
        q_t = sb("q_t", [HD, 2, TP])
        ks_t = sb("ks_t", [HD, 2, TP])
        kw_t = sb("kw_t", [HD, 2, TP])
        kc_t = sb("kc_t", [HD, 2, NB])
        v_all = sb("v_all", [P, 3, NT, P])
        vc = sb("vc", [NB, P])
        flip = sb("flip", [P, P])
        ident = sb("ident", [P, P])
        strip = sb("strip", [P, 2, TW])
        strip_w = sb("strip_w", [P, 2, P])
        table = sb("table", [P, TW])
        far_w = sb("far_w", [P, P])
        s_sel = sb("s_sel", [P, 2, TP])
        s_win = sb("s_win", [P, 2, 5 * P + NB])
        p_sel = sb("p_sel", [P, NT, P])
        p_win = sb("p_win", [P, 6, P])
        gates = sb("gates", [P, NT, 3, NH])
        any_cmp = sb("any_cmp", [P, 1])
        cols = sb("cols", [P, 2, 16])
        out = sb("out", [P, 2, NT, HD])
        ps = ctx.enter_context(nc.psum_tensor("pa_ps", [P, 8, BANK], F32))
        S = {n: new_sem("pa_" + n) for n in
             ("const_in gate_exp gates_set strip_used flip_mm table_set sel_mm win_mm sel_neg win_neg exp_done pt_tr pt_copied_a pt_copied_v o_mm o_read tile_set passed anyc").split()}
        out_stored = [new_sem(f"pa_out_stored{n}") for n in range(2)]
        head_in = [new_sem(f"pa_head_in{n}") for n in range(2)]
        block = ctx.enter_context(nc.Block())
        NTB = 4

        def win_first(i):
            return max(0, i - 4)

        def p_all(n, k, rows):
            return p_sel[0:rows, k] if k < NT else p_win[0:rows, k - NT]

        base_chunk = [0]
        n_tiles = []
        for h in range(NH):
            for i in range(NT):
                n_tiles.append(i + 1 + (i - win_first(i) + 1) + 1)
                base_chunk.append(base_chunk[-1] + (n_tiles[-1] + 3) // 4)

        @block.sync
        def _(sp):
            consts = [(flip[:], flip_in), (ident[:], ident_in), (vc[:], v_cmp)]
            for g in range(NG):
                consts += [(ks_t[:, g], heads_t[4 * P + g * HD:4 * P + (g + 1) * HD, 0:TP]), (kw_t[:, g], heads_t[5 * P + g * HD:5 * P + (g + 1) * HD, 0:TP]),
                           (kc_t[:, g], kt_cmp[g * HD:(g + 1) * HD, :])]
            consts += [(v_all[:, 0], qkv[0:TP, 512 + 384:512 + 512].rearrange("(n p) c -> p n c", p=P)),
                       (v_all[:, 1], qkv[0:TP, 1024 + 128:1024 + 256].rearrange("(n p) c -> p n c", p=P)),
                       (gates[:].rearrange("p n a h -> p n (a h)"), tok[0:TP, C_NGATE:C_NGATE + 24].rearrange("(n p) c -> p n c", p=P))]
            for dst, src in consts:
                sp.dma_start(dst, src).then_inc(S["const_in"], 16)
            for h in range(NH):
                if h >= 2:
                    sp.wait_ge(S["tile_set"], NT * (h - 1))
                sp.dma_start(q_t[:, h % 2], heads_t[h * HD:(h + 1) * HD, 0:TP]).then_inc(head_in[h % 2], 16)
                sp.dma_start(strip[:, h % 2], bass.AP(tensor=strips.tensor, offset=strips[0, h, 0:1].offset, ap=[[1, P], [1, TW]])).then_inc(head_in[h % 2], 16)
                sp.dma_start(strip_w[:, h % 2], bass.AP(tensor=strips.tensor, offset=strips[1, h, 384:385].offset, ap=[[1, P], [1, P]])).then_inc(head_in[h % 2], 16)

        @block.gpsimd
        def _(pool):
            pool.memset(any_cmp[:], 1.0).then_inc(S["anyc"], 1)
            pool.wait_ge(S["anyc"], 1)
            pool.affine_select(out=any_cmp[:], in_=any_cmp[:], compare_op=ALU.is_ge, fill=0.0, base=-(CMP_LEN - 1), pattern=[[0, 1]], channel_multiplier=1).then_inc(S["anyc"], 1)
            for h in range(NH):
                pool.wait_ge(S["tile_set"], NT * (h + 1))
                pool.dma_start(out_rows[:, h * HD:(h + 1) * HD].rearrange("(n p) d -> p n d", p=P), out[:, h % 2]).then_inc(out_stored[h % 2], 16)
            for x in range(2):
                pool.wait_ge(out_stored[x], 16 * (NH // 2))

        @block.tensor
        def _(pe):
            pe.wait_ge(S["const_in"], 16 * 12)

            def scores(h, i):
                g, q = h // NR, q_t[:, h % 2, i * P:(i + 1) * P]
                n = h * NT + i
                if n >= 1:
                    pe.wait_ge(S["sel_neg"], n)
                    pe.wait_ge(S["win_neg"], n)
                hi = (i + 1) * P
                for a in range(0, hi, BANK):
                    z = min(a + BANK, hi)
                    last = pe.matmul(ps[:, a // BANK, 0:z - a], q, ks_t[:, g, a:z], start=True, stop=True)
                last.then_inc(S["sel_mm"], 1)
                w0 = win_first(i) * P
                nw = hi - w0
                m = min(nw, BANK)
                pe.matmul(ps[:, 2, 0:m], q, kw_t[:, g, w0:w0 + m], start=True, stop=True)
                if nw > BANK:
                    pe.matmul(ps[:, 3, 0:nw - BANK], q, kw_t[:, g, w0 + BANK:hi], start=True, stop=True)
                pe.matmul(ps[:, 3, P:P + NB], q, kc_t[:, g], start=True, stop=True).then_inc(S["win_mm"], 1)

            def values(h, i):
                g = h // NR
                n = h * NT + i
                pe.wait_ge(S["exp_done"], 3 * (n + 1))
                tiles = [("s", k) for k in range(i + 1)] + [("w", k) for k in range(i - win_first(i) + 1)] + [("c", 0)]
                for c in range(0, len(tiles), 4):
                    m = base_chunk[n] + c // 4
                    if m >= 3:
                        pe.wait_ge(S["pt_copied_v"], m - 2)
                    for x, (kind, k) in enumerate(tiles[c:c + 4]):
                        if kind == "s":
                            src, w = s_sel[:, n % 2, k * P:(k + 1) * P], P
                        elif kind == "w":
                            src, w = s_win[:, n % 2, k * P:(k + 1) * P], P
                        else:
                            src, w = s_win[:, n % 2, 5 * P:5 * P + NB], NB
                        last = pe.transpose(ps[0:w, 4 + m % 3, x * P:(x + 1) * P], src, ident[:])
                    last.then_inc(S["pt_tr"], 1)
                if n >= 1:
                    pe.wait_ge(S["tile_set"], n)
                pe.wait_ge(S["pt_copied_v"], base_chunk[n] + (len(tiles) + 3) // 4)
                for k in range(i + 1):
                    pe.matmul(ps[:, 7, 0:HD], p_all(n, k, P), v_all[:, 0, k, g * HD:(g + 1) * HD], start=(k == 0), stop=(k == i))
                w0 = win_first(i)
                for k in range(w0, i + 1):
                    pe.matmul(ps[:, 7, HD:2 * HD], p_all(n, i + 1 + k - w0, P), v_all[:, 1, k, g * HD:(g + 1) * HD], start=(k == w0), stop=(k == i))
                pe.matmul(ps[:, 7, 2 * HD:3 * HD], p_all(n, len(tiles) - 1, NB), vc[:, g * HD:(g + 1) * HD], start=True, stop=True).then_inc(S["o_mm"], 1)

            for h in range(NH):
                pe.wait_ge(head_in[h % 2], 48 * (h // 2 + 1))
                for n in range(NTB):
                    a, z = n * BANK, min((n + 1) * BANK, TW)
                    if h >= 1:
                        pe.wait_ge(S["sel_neg"], NT * h)
                        pe.wait_ge(S["win_neg"], NT * h)
                    pe.matmul(ps[:, n, 0:z - a], flip[:], strip[:, h % 2, a:z], start=True, stop=True)
                if h >= 1:
                    values(h - 1, NT - 1)
                    pe.wait_ge(S["pt_copied_v"], base_chunk[NT * h])
                pe.matmul(ps[:, 4, 0:P], flip[:], strip_w[:, h % 2], start=True, stop=True).then_inc(S["flip_mm"], 1)
                pe.wait_ge(S["table_set"], h + 1)
                for i in range(NT):
                    scores(h, i)
                    if i >= 1:
                        values(h, i - 1)
            values(NH - 1, NT - 1)

        @block.scalar
        def _(act):
            act.wait_ge(S["const_in"], 16 * 12)
            act.activation(gates[:], gates[:], ACT.Exp, scale=-1.0).then_inc(S["gate_exp"], 1)
            for h in range(NH):
                for i in range(NT):
                    n = h * NT + i
                    hi = (i + 1) * P
                    nw = hi - win_first(i) * P
                    c = cols[:, n % 2]
                    act.wait_ge(S["sel_neg"], n + 1)
                    act.activation(s_sel[:, n % 2, 0:hi], s_sel[:, n % 2, 0:hi], ACT.Exp, bias=c[:, 0:1], accum_out=c[:, 4:5]).then_inc(S["exp_done"], 1)
                    act.wait_ge(S["win_neg"], n + 1)
                    act.activation(s_win[:, n % 2, 0:nw], s_win[:, n % 2, 0:nw], ACT.Exp, bias=c[:, 1:2], accum_out=c[:, 5:6]).then_inc(S["exp_done"], 1)
                    act.activation(s_win[:, n % 2, 5 * P:5 * P + NB], s_win[:, n % 2, 5 * P:5 * P + NB], ACT.Exp, bias=c[:, 2:3], accum_out=c[:, 6:7]).then_inc(S["exp_done"], 1)

        @block.vector
        def _(dve):
            dve.wait_ge(S["gate_exp"], 1)
            dve.tensor_scalar(gates[:], gates[:], 1.0, None, ALU.add)
            dve.drain()
            dve.reciprocal(gates[:], gates[:])
            dve.wait_ge(S["anyc"], 2)
            dve.drain()
            dve.tensor_scalar(gates[:, 0, 0], gates[:, 0, 0], any_cmp[:], None, ALU.mult)

            def bias_and_max(h, i):
                n = h * NT + i
                hi = (i + 1) * P
                c = cols[:, n % 2]
                s, w = s_sel[:, n % 2], s_win[:, n % 2]
                off = (NT - 1) * P - i * P
                dve.wait_ge(S["sel_mm"], n + 1)
                if n >= 2:
                    dve.wait_ge(S["pt_tr"], base_chunk[n - 1])
                for a in range(0, hi, BANK):
                    z = min(a + BANK, hi)
                    dve.tensor_tensor(s[:, a:z], ps[:, a // BANK, 0:z - a], table[:, off + a:off + z], ALU.add)
                dve.drain()
                dve.tensor_reduce(c[:, 8:9], s[:, 0:hi], AX.X, ALU.max)
                dve.drain()
                dve.tensor_scalar(c[:, 0:1], c[:, 8:9], -1.0, None, ALU.mult).then_inc(S["sel_neg"], 1)
                dve.wait_ge(S["win_mm"], n + 1)
                w0 = win_first(i) * P
                nw = hi - w0
                m = min(nw, BANK)
                if nw > BANK:
                    dve.tensor_tensor(w[:, 0:P], ps[:, 2, 0:P], far_w[:], ALU.add)
                    dve.tensor_tensor(w[:, P:m], ps[:, 2, P:m], table[:, off + w0 + P:off + w0 + m], ALU.add)
                    dve.tensor_tensor(w[:, m:nw], ps[:, 3, 0:nw - BANK], table[:, off + w0 + m:off + hi], ALU.add)
                else:
                    dve.tensor_tensor(w[:, 0:m], ps[:, 2, 0:m], table[:, off + w0:off + hi], ALU.add)
                c0 = off + CMP_LEN - 1
                dve.tensor_tensor(w[:, 5 * P:5 * P + NB], ps[:, 3, P:P + NB], table[:, c0:c0 + CMP_STRIDE * (NB - 1) + 1:CMP_STRIDE], ALU.add)
                dve.drain()
                dve.tensor_reduce(c[:, 9:10], w[:, 0:nw], AX.X, ALU.max)
                dve.tensor_reduce(c[:, 10:11], w[:, 5 * P:5 * P + NB], AX.X, ALU.max)
                dve.drain()
                dve.tensor_scalar(c[:, 1:3], c[:, 9:11], -1.0, None, ALU.mult).then_inc(S["win_neg"], 1)

            def finish(h, i):
                n = h * NT + i
                c = cols[:, n % 2]
                nt = n_tiles[n]
                for k0 in range(0, nt, 4):
                    m = base_chunk[n] + k0 // 4
                    dve.wait_ge(S["pt_tr"], m + 1)
                    if k0 == 0 and n >= 1:
                        dve.wait_ge(S["o_mm"], n)
                    k1 = min(k0 + 4, nt)
                    for a, z, dst in ((k0, min(k1, NT), p_sel), (max(k0, NT), k1, p_win)):
                        for a_, z_, rows in ((a, min(z, nt - 1), P), (max(a, nt - 1), z, NB)):
                            if z_ > a_:
                                base = 0 if dst is p_sel else NT
                                dve.tensor_copy(dst[0:rows, a_ - base:z_ - base], ps[0:rows, 4 + m % 3, (a_ - k0) * P:(z_ - k0) * P].rearrange("p (a b) -> p a b", b=P))
                    dve.drain().then_inc(S["pt_copied_v"], 1)
                dve.wait_ge(S["exp_done"], 3 * (n + 1))
                dve.reciprocal(c[:, 12:15], c[:, 4:7])
                dve.drain()
                for k, br in ((0, 1), (1, 2), (2, 0)):
                    dve.tensor_tensor(c[:, 12 + k:13 + k], c[:, 12 + k:13 + k], gates[:, i, br, h:h + 1], ALU.mult)
                dve.drain()
                dve.wait_ge(S["o_mm"], n + 1)
                if i == 0 and h >= 2:
                    dve.wait_ge(out_stored[h % 2], 16 * (h // 2))
                o = out[:, h % 2, i]
                dve.tensor_scalar(o, ps[:, 7, 0:HD], c[:, 12:13], None, ALU.mult)
                dve.drain()
                dve.scalar_tensor_tensor(out=o, in0=ps[:, 7, HD:2 * HD], scalar=c[:, 13:14], in1=o, op0=ALU.mult, op1=ALU.add)
                dve.drain()
                dve.scalar_tensor_tensor(out=o, in0=ps[:, 7, 2 * HD:3 * HD], scalar=c[:, 14:15], in1=o, op0=ALU.mult, op1=ALU.add).then_inc(S["tile_set"], 1)

            for h in range(NH):
                if h >= 1:
                    finish(h - 1, NT - 1)
                dve.wait_ge(S["flip_mm"], h + 1)
                for n in range(NTB):
                    a, z = n * BANK, min((n + 1) * BANK, TW)
                    dve.tensor_copy(table[:, a:z], ps[:, n, 0:z - a])
                dve.tensor_copy(far_w[:], ps[:, 4, 0:P])
                dve.drain().then_inc(S["table_set"], 1)
                for i in range(NT):
                    bias_and_max(h, i)
                    if i >= 1:
                        finish(h, i - 1)
            finish(NH - 1, NT - 1)


HC = 8
LB_FLOOR = 1e-30


def hgrn_stage(nc, feat, tok, lb_logits, out_gain, state_in, diag_in, ident_in, own_in, out_t, state_p, state_s):
    NHG = 4
    NTL = TP // P
    NBK = P // HC
    NBT = T // HC
    with ExitStack() as ctx:
        new_sem = ctx.enter_context(stage_semaphores(nc))
        sb = lambda name, shape: ctx.enter_context(nc.sbuf_tensor("hg_" + name, shape, F32))
        raw = sb("raw", [P, 3, T])
        v = sb("v", [P, NTL + 1, P])
        state0 = sb("state0", [P, SB, P])
        f = sb("f", [P, T])
        k = sb("k", [P, T])
        q = sb("q", [P, T])
        gate = sb("gate", [P, T])
        sig = sb("sig", [P, 2, T])
        decay = sb("decay", [P, T])
        q_dec = sb("q_dec", [P, T])
        q_tile = sb("q_tile", [P, TP])
        before = sb("before", [P, NTL, NBK + 1])
        kb = sb("kb", [P, 2, T])
        kt = sb("kt", [P, 2, TP])
        attn = sb("attn", [P, NTL + 1, P])
        k_rows = sb("k_rows", [P, NTL + 1, P])
        v_own = sb("v_own", [SB * ST, SB, P])
        states = sb("states", [P, NTL + 1, P])
        s_new = sb("s_new", [P, SB, P])
        o = sb("o", [P, T])
        rstd = sb("rstd", [P, T])
        lb = sb("lb", [P, 6, NHG])
        gain = sb("gain", [P, 1])
        diag = sb("diag", [P, P])
        ident = sb("ident", [P, P])
        own = sb("own", [SB * ST, SB])
        ones = sb("ones", [P, P])
        ps = ctx.enter_context(nc.psum_tensor("hg_ps", [P, 8, BANK], F32))
        ahead = "sig_used states_free out_free o_copied o_mm raw_used s_new_set v_own_set".split()
        S = {n: new_sem("hg_" + n, 1 if n in ahead else 0) for n in
             ("const_in ones_set lb_sub lb_exp lb_set raw_in v_in state_in sig_done1 sig_done2 sig_used raw_used kb_set diag_mm kt_set off_mm attn_set "
              "tr rows_copied u_mm states_set o_mm o_copied sq_done ssq_mm var_set root out_set stored out_free state_stored states_free passed k_end v_own_set s_new_set").split()}
        block = ctx.enter_context(nc.Block())
        blocks = lambda t: t.rearrange("p (b j) -> p b j", j=HC)
        STEPS = NBK + 1

        @block.sync
        def _(sp):
            for dst, src in ((lb[:, 0], lb_logits), (gain[:], out_gain), (diag[:], diag_in), (ident[:], ident_in), (own[:], own_in)):
                sp.dma_start(dst, src).then_inc(S["const_in"], 16)
            with sp.Fori(0, NHG) as h:
                sp.wait_ge(S["raw_used"], h * 3 + 1)
                sp.sem_inc(S["passed"], 1)
                for n, row in enumerate((R_HQ, R_HF, R_HG)):
                    sp.dma_start(raw[:, n], feat[bass.ds(h * P + row, P), :]).then_inc(S["raw_in"], 16)
                sp.wait_ge(S["o_mm"], h + 1)
                sp.sem_inc(S["passed"], 1)
                sp.wait_ge(S["v_own_set"], h + 1)
                sp.sem_inc(S["passed"], 1)
                sp.dma_start(v[:, 0:NTL], tok[0:TP, bass.ds(h * P + C_HI, P)].rearrange("(n p) c -> p n c", p=P)).then_inc(S["v_in"], 16)
                sp.dma_start(v[0:SB * ST, NTL], tok[TP:T, bass.ds(h * P + C_HI, P)]).then_inc(S["v_in"], 16)
                sp.wait_ge(S["s_new_set"], h + 1)
                sp.sem_inc(S["passed"], 1)
                sp.dma_start(state0[:], state_in[:, bass.ds(h, 1)].rearrange("b o d v -> (o d) b v")).then_inc(S["state_in"], 16)

        @block.gpsimd
        def _(pool):
            pool.memset(ones[:], 1.0).then_inc(S["ones_set"], 1)
            with pool.Fori(0, NHG) as h:
                pool.wait_ge(S["s_new_set"], h + 2)
                pool.sem_inc(S["passed"], 1)
                pool.dma_start(state_p[bass.ds(h, 1)].rearrange("o d v -> (o d) v"), states[:, NTL]).then_inc(S["state_stored"], 16)
                pool.dma_start(state_s[:, bass.ds(h, 1)].rearrange("b o d v -> (o d) b v"), s_new[:]).then_inc(S["state_stored"], 16)
                pool.wait_ge(S["out_set"], h + 1)
                pool.sem_inc(S["passed"], 1)
                pool.dma_start(out_t[bass.ds(h * P, P), :], o[:]).then_inc(S["stored"], 16)
                pool.wait_ge(S["state_stored"], h * 32 + 32)
                pool.sem_inc(S["states_free"], 1)
                pool.wait_ge(S["stored"], h * 16 + 16)
                pool.sem_inc(S["out_free"], 1)

        @block.scalar
        def _(act):
            act.wait_ge(S["lb_sub"], 1)
            act.activation(lb[:, 1], lb[:, 1], ACT.Exp).then_inc(S["lb_exp"], 1)
            with act.Fori(0, NHG) as h:
                act.wait_ge(S["raw_in"], (h + 1) * 48)
                act.wait_ge(S["sig_used"], h * 4 + 1)
                act.activation(sig[:, 0], raw[:, 1], ACT.Sigmoid).then_inc(S["sig_done1"], 1)
                act.activation(sig[:, 1], raw[:, 1], ACT.Sigmoid, scale=-1.0).then_inc(S["sig_done1"], 1)
                act.wait_ge(S["sig_used"], h * 4 + 2)
                act.activation(sig[:, 0], raw[:, 0], ACT.Sigmoid).then_inc(S["sig_done2"], 1)
                act.wait_ge(S["sig_used"], h * 4 + 3)
                act.activation(sig[:, 1], raw[:, 2], ACT.Sigmoid).then_inc(S["sig_done2"], 1)
                for n in range(3):
                    act.wait_ge(S["tr"], h * 3 + (n + 1))
                    if n < 2:
                        act.activation(k_rows[:, 4 * n:4 * n + 4].rearrange("p a d -> p (a d)"), ps[:, 5 + n, :], ACT.Copy).then_inc(S["rows_copied"], 1)
                    else:
                        act.activation(k_rows[0:SB * ST, NTL], ps[0:SB * ST, 7, 0:P], ACT.Copy).then_inc(S["rows_copied"], 1)
                act.wait_ge(S["o_mm"], h + 2)
                for n, (a, z) in enumerate(COLS):
                    act.activation(rstd[:, a:z], ps[:, n, 0:z - a], ACT.Square).then_inc(S["sq_done"], 1)
                act.wait_ge(S["var_set"], h + 1)
                act.activation(rstd[:], rstd[:], ACT.Sqrt).then_inc(S["root"], 1)

        @block.tensor
        def _(pe):
            pe.wait_ge(S["const_in"], 80)
            pe.wait_ge(S["ones_set"], 1)
            with pe.Fori(0, NHG) as h:
                pe.wait_ge(S["o_copied"], h + 1)
                for j in range(HC):
                    pe.wait_ge(S["kb_set"], h * HC + (j + 1))
                    for t, (t0, tn) in enumerate(TILES):
                        last = pe.matmul(ps[0:tn, t // 4, (t % 4) * P + j:(t % 4) * P + tn - HC + j + 1:HC], kb[:, j % 2, t0:t0 + tn],
                                         q[:, t0 + j:t0 + tn - HC + j + 1:HC], start=True, stop=True)
                    last.then_inc(S["diag_mm"], 1)
                for i in range(1, NBK):
                    pe.wait_ge(S["kt_set"], h * NBK + i)
                    for t in range(NTL):
                        last = pe.matmul(ps[:, 3 + t // 4, (t % 4) * P + i * HC:(t % 4) * P + (i + 1) * HC], kt[:, i % 2, t * P:(t + 1) * P],
                                         q_dec[:, t * P + i * HC:t * P + (i + 1) * HC], start=True, stop=True)
                    last.then_inc(S["off_mm"], 1)
                pe.wait_ge(S["kt_set"], h * NBK + NBK)
                for t in range(NTL):
                    last = pe.transpose(ps[:, 5 + t // 4, (t % 4) * P:(t % 4 + 1) * P], kt[:, NBK % 2, t * P:(t + 1) * P], ident[:])
                    if t % 4 == 3:
                        last.then_inc(S["tr"], 1)
                pe.transpose(ps[0:SB * ST, 7, 0:P], kb[:, (HC - 1) % 2, TP:T], ident[:]).then_inc(S["tr"], 1)
                pe.wait_ge(S["attn_set"], h + 1)
                pe.wait_ge(S["rows_copied"], h * 3 + 3)
                pe.wait_ge(S["v_in"], h * 32 + 32)
                for t in range(NTL):
                    pe.matmul(ps[:, 3 + t // 4, (t % 4) * P:(t % 4 + 1) * P], k_rows[:, t], v[:, t], start=True, stop=True)
                pe.wait_ge(S["v_own_set"], h + 2)
                for n in range(2):
                    last = pe.matmul(ps[:, 5 + n, :], k_rows[0:SB * ST, NTL], v_own[:, 4 * n:4 * n + 4].rearrange("p b v -> p (b v)"), start=True, stop=True)
                last.then_inc(S["u_mm"], 1)
                pe.wait_ge(S["states_set"], h + 1)
                pe.wait_ge(S["state_in"], h * 16 + 16)
                for t in range(NTL):
                    dst = ps[:, t // 4, (t % 4) * P:(t % 4 + 1) * P]
                    pe.matmul(dst, v[:, t], attn[:, t], start=True, stop=(t == 0))
                    if t:
                        pe.matmul(dst, states[:, t], q_tile[:, t * P:(t + 1) * P], start=False, stop=True)
                for b in range(SB):
                    dst = ps[:, 2, b * ST:(b + 1) * ST]
                    pe.matmul(dst, v[0:SB * ST, NTL], attn[0:SB * ST, NTL, b * ST:(b + 1) * ST], start=True, stop=False)
                    last = pe.matmul(dst, state0[:, b], q_dec[:, TP + b * ST:TP + (b + 1) * ST], start=False, stop=True)
                last.then_inc(S["o_mm"], 1)
                pe.wait_ge(S["sq_done"], h * 3 + 3)
                for n, (a, z) in enumerate(COLS):
                    last = pe.matmul(ps[:, (3, 4, 7)[n], 0:z - a], ones[:], rstd[:, a:z], start=True, stop=True)
                last.then_inc(S["ssq_mm"], 1)

        @block.vector
        def _(dve):
            dve.wait_ge(S["const_in"], 80)
            dve.tensor_tensor(lb[:, 1], lb[:, 0], lb[:, 0], ALU.subtract).then_inc(S["lb_sub"], 1)
            dve.wait_ge(S["lb_exp"], 1)
            dve.reciprocal(lb[:, 2], lb[:, 1])
            dve.drain()
            dve.tensor_tensor(lb[:, 2], lb[:, 1], lb[:, 2], ALU.mult)
            dve.drain()
            dve.tensor_tensor(lb[:, 3], lb[:, 2], lb[:, 2], ALU.subtract)
            dve.drain()
            dve.tensor_scalar(lb[:, 4], lb[:, 3], LB_FLOOR, None, ALU.max)
            dve.tensor_scalar(lb[:, 5], lb[:, 3], -1.0, 1.0, ALU.mult, ALU.add)
            dve.drain()
            f8, k8, q8, d8, qd8 = blocks(f[:]), blocks(k[:]), blocks(q[:]), blocks(decay[:]), blocks(q_dec[:])
            with dve.Fori(0, NHG) as h:
                floor, rest = lb[:, 4, bass.ds(h, 1)], lb[:, 5, bass.ds(h, 1)]
                dve.wait_ge(S["sig_done1"], h * 2 + 2)
                dve.tensor_scalar(f[:], sig[:, 0], rest, floor, ALU.mult, ALU.add).then_inc(S["sig_used"], 1)
                dve.tensor_scalar(k[:], sig[:, 1], rest, None, ALU.mult).then_inc(S["sig_used"], 1)
                dve.wait_ge(S["sig_done2"], h * 2 + 2)
                dve.tensor_tensor(q[:], sig[:, 0], raw[:, 0], ALU.mult).then_inc(S["sig_used"], 1)
                dve.tensor_tensor(gate[:], sig[:, 1], raw[:, 2], ALU.mult).then_inc(S["sig_used"], 1)
                dve.drain().then_inc(S["raw_used"], 3)
                dve.memset(kb[:], 0.0)
                dve.memset(kt[:], 0.0)
                dve.tensor_copy(d8[:, :, 0], f8[:, :, 0])
                dve.drain()
                for j in range(HC):
                    new, old = blocks(kb[:, j % 2]), blocks(kb[:, 1 - j % 2])
                    if j >= 2:
                        dve.wait_ge(S["diag_mm"], h * HC + (j - 1))
                    if j:
                        dve.tensor_tensor(new[:, :, 0:j], old[:, :, 0:j], f8[:, :, j:j + 1].to_broadcast([P, NBT, j]), ALU.mult)
                        dve.tensor_tensor(d8[:, :, j], d8[:, :, j - 1], f8[:, :, j], ALU.mult)
                    dve.tensor_copy(new[:, :, j], k8[:, :, j])
                    dve.drain().then_inc(S["kb_set"], 1)
                dve.tensor_tensor(q_dec[:], q[:], decay[:], ALU.mult)
                dve.memset(before[:, :, 0:1], 1.0)
                dve.drain()
                ends = d8[:, 0:TP // HC, HC - 1].rearrange("p (t b) -> p t b", b=NBK)
                kb_end = kb[:, (HC - 1) % 2, 0:TP].rearrange("p (t s) -> p t s", s=P)
                for i in range(1, NBK + 1):
                    new, old = (kt[:, x].rearrange("p (t s) -> p t s", s=P) for x in (i % 2, 1 - i % 2))
                    if i >= 3:
                        dve.wait_ge(S["off_mm"], h * (NBK - 1) + (i - 2))
                    n = (i - 1) * HC
                    if n:
                        dve.tensor_tensor(new[:, :, 0:n], old[:, :, 0:n], ends[:, :, i - 1:i].to_broadcast([P, NTL, n]), ALU.mult)
                    dve.tensor_tensor(before[:, :, i], before[:, :, i - 1], ends[:, :, i - 1], ALU.mult)
                    dve.tensor_copy(new[:, :, n:n + HC], kb_end[:, :, n:n + HC])
                    dve.drain().then_inc(S["kt_set"], 1)
                dve.tensor_tensor(q_tile[:].rearrange("p (t b j) -> p t b j", b=NBK, j=HC), q_dec[:, 0:TP].rearrange("p (t b j) -> p t b j", b=NBK, j=HC),
                                  before[:, :, 0:NBK].unsqueeze(3).to_broadcast([P, NTL, NBK, HC]), ALU.mult)
                dve.wait_ge(S["v_in"], h * 32 + 32)
                dve.tensor_tensor(v_own[:], v[0:SB * ST, NTL:NTL + 1].to_broadcast([SB * ST, SB, P]), own[:].unsqueeze(2).to_broadcast([SB * ST, SB, P]), ALU.mult).then_inc(S["v_own_set"], 1)
                dve.wait_ge(S["diag_mm"], h * HC + HC)
                dve.wait_ge(S["off_mm"], h * (NBK - 1) + (NBK - 1))
                for n in range(2):
                    dve.tensor_tensor(attn[:, 4 * n:4 * n + 4], ps[:, n, :].rearrange("p (t s) -> p t s", s=P), diag[:].unsqueeze(1).to_broadcast([P, 4, P]), ALU.mult)
                dve.tensor_tensor(attn[0:SB * ST, NTL, 0:SB * ST], ps[0:SB * ST, 2, 0:SB * ST], diag[0:SB * ST, 0:SB * ST], ALU.mult)
                dve.drain()
                for n in range(2):
                    a = attn[:, 4 * n:4 * n + 4, HC:P]
                    dve.tensor_tensor(a, a, ps[:, 3 + n, :].rearrange("p (t s) -> p t s", s=P)[:, :, HC:P], ALU.add)
                dve.memset(states[:, 0], 0.0)
                dve.drain().then_inc(S["attn_set"], 1)
                dve.wait_ge(S["u_mm"], h + 1)
                dve.wait_ge(S["state_in"], h * 16 + 16)
                dve.wait_ge(S["states_free"], h + 1)
                for t in range(NTL):
                    dve.scalar_tensor_tensor(out=states[:, t + 1], in0=states[:, t], scalar=before[:, t, NBK:NBK + 1], in1=ps[:, 3 + t // 4, (t % 4) * P:(t % 4 + 1) * P],
                                             op0=ALU.mult, op1=ALU.add)
                    dve.drain()
                dve.sem_inc(S["states_set"], 1)
                dve.tensor_tensor(s_new[:], state0[:], d8[:, TP // HC:NBT, HC - 1:HC].to_broadcast([P, SB, P]), ALU.mult)
                dve.drain()
                for n in range(2):
                    last = dve.tensor_tensor(s_new[:, 4 * n:4 * n + 4], s_new[:, 4 * n:4 * n + 4], ps[:, 5 + n, :].rearrange("p (b v) -> p b v", v=P), ALU.add)
                last.then_inc(S["s_new_set"], 1)
                dve.wait_ge(S["o_mm"], h + 2)
                dve.wait_ge(S["sq_done"], h * 3 + 3)
                dve.wait_ge(S["out_free"], h + 1)
                for n, (a, z) in enumerate(COLS):
                    dve.scalar_tensor_tensor(out=o[:, a:z], in0=ps[:, n, 0:z - a], scalar=gain[:], in1=gate[:, a:z], op0=ALU.mult, op1=ALU.mult)
                dve.drain().then_inc(S["o_copied"], 1)
                dve.wait_ge(S["ssq_mm"], h + 1)
                for n, (a, z) in enumerate(COLS):
                    last = dve.tensor_scalar(rstd[:, a:z], ps[:, (3, 4, 7)[n], 0:z - a], 1.0 / P, EPS, ALU.mult, ALU.add)
                last.then_inc(S["var_set"], 1)
                dve.wait_ge(S["root"], h + 1)
                dve.reciprocal(rstd[:], rstd[:])
                dve.drain()
                dve.tensor_tensor(o[:], o[:], rstd[:], ALU.mult).then_inc(S["out_set"], 1)


SC = 8
NCH = TP // SC
NCA = T // SC
NGR, GW, NST = 32, 16, 64
NPR = NGR // 2
TWO_PI = 6.283185307179586
TWO_PI_HI = 6.28125
ROUND = 12582912.0


def s5_state_stage(nc, tok, a_re, a_im, log_dt, b_in, c_in, d_in, h0_in, ident_in, rows_out, h_prompt, h_sample):
    with ExitStack() as ctx:
        new_sem = ctx.enter_context(stage_semaphores(nc))
        sb = lambda name, shape: ctx.enter_context(nc.sbuf_tensor("ss_" + name, shape, F32))
        u = sb("u", [P, NGR, NCA])
        rows = sb("rows", [P, SC, 512])
        by_group = sb("by_group", [P, NGR, P])
        small = sb("small", [P, NGR * P])
        toep = sb("toep", [P, NGR, P])
        w_t = sb("w_t", [P, NPR, 2, P])
        w_h = sb("w_h", [P, 2, NPR, NCA])
        ca = sb("ca", [P, 2, NPR, (SC + 1) * GW])
        x = sb("x", [P, 2, NPR, NCA])
        turn = sb("turn", [P, 2, NPR, NCH])
        m0 = sb("m0", [P, NPR, NCH])
        tmp = sb("tmp", [P, 2, NPR, NCH])
        par = sb("par", [P, 24, NPR])
        pw = sb("pw", [P, 2, SC + 1, NPR])
        bb = sb("bb", [P, 2, NPR, GW])
        b_raw = sb("b_raw", [P, 2, NPR, GW])
        c_raw = sb("c_raw", [P, 2, NPR, GW])
        dcol = sb("dcol", [P, NGR])
        ident = sb("ident", [P, P])
        h_end_p = sb("h_end_p", [P, 2, NPR, 1])
        h_end_s = sb("h_end_s", [P, 2, NPR, SB])
        ps = ctx.enter_context(nc.psum_tensor("ss_ps", [P, 8, BANK], F32))
        S = {n: new_sem("ss_" + n) for n in
             ("par_in rows_in grouped grouped_s u_tr u_copied step_set exp_in exp_done sin_in sin_done w_set wt_tr wt_copied ca_set k_mm k_copied k_read toep_zero toep_in "
              "x_mm x_copied h_set y_mm y_sum gelu y_tr y_copied rows_used stored h_stored").split()}
        block = ctx.enter_context(nc.Block())
        ARE, AIM, LDT, STEP, MAG, COS, SIN, MAG8, TH, R_, N_, A_, B_, C_, D_, E_, ZR, ZI, DEN, CS8, SN8 = range(21)
        p = lambda i: par[:, i]
        batches = [(a, min(a + 3, NGR)) for a in range(0, NGR, 3)]
        pair_batches = [(a, min(a + 3, NPR)) for a in range(0, NPR, 3)]
        small_rows = small[32:32 + SB].rearrange("p (s c) -> p s c", s=SC)
        small_group = small[64:64 + SB].rearrange("p (g c) -> p g c", g=NGR)
        taps = small[0:GW].rearrange("p (g c) -> p g c", g=NGR)

        y_batches = [list(range(6 * n + q, min(6 * n + 6, NGR), 2)) for n in range(6) for q in range(2)]
        y_batch_of = {g: n for n, gs in enumerate(y_batches) for g in gs}

        @block.sync
        def _(sp):
            sp.dma_start(rows[:], tok[0:TP, 0:512].rearrange("(c s) n -> c s n", s=SC)).then_inc(S["rows_in"], 16)
            sp.dma_start(small_rows, tok[TP:T, 0:512].rearrange("(c s) n -> c s n", s=SC)).then_inc(S["rows_in"], 16)
            for dst, src in ((par[:, ARE], a_re), (par[:, AIM], a_im), (par[:, LDT], log_dt), (b_raw[:], b_in), (c_raw[:], c_in), (dcol[:], d_in), (ident[:], ident_in),
                             (w_h[:, :, :, NCH:NCA], h0_in)):
                sp.dma_start(dst, src).then_inc(S["par_in"], 16)
            sp.wait_ge(S["k_copied"], 8)
            sp.wait_ge(S["toep_zero"], 1)
            for s in range(SC):
                sp.dma_start(toep[s * GW:(s + 1) * GW, :, s * GW:P], taps[:, :, 0:P - s * GW]).then_inc(S["toep_in"], 16)
            sp.wait_ge(S["h_set"], 1)
            sp.dma_start(h_prompt, h_end_p[:]).then_inc(S["h_stored"], 16)
            sp.dma_start(h_sample, h_end_s[:]).then_inc(S["h_stored"], 16)
            sp.wait_ge(S["y_copied"], 16)
            sp.dma_start(rows_out[0:TP].rearrange("(c s) n -> c s n", s=SC), rows[:]).then_inc(S["stored"], 16)
            sp.dma_start(rows_out[TP:T].rearrange("(c s) n -> c s n", s=SC), small_rows).then_inc(S["stored"], 16)
            sp.wait_ge(S["stored"], 32)
            sp.wait_ge(S["h_stored"], 32)

        @block.gpsimd
        def _(pool):
            pool.memset(toep[:], 0.0).then_inc(S["toep_zero"], 1)
            pool.wait_ge(S["toep_zero"], 1)
            pool.wait_ge(S["rows_in"], 32)
            pool.tensor_copy(small_group.rearrange("p g (s n) -> p g s n", n=GW), small_rows.rearrange("p s (g n) -> p g s n", n=GW)).then_inc(S["grouped_s"], 1)

        @block.scalar
        def _(act):
            act.wait_ge(S["par_in"], 128)
            act.activation(p(STEP), p(LDT), ACT.Exp).then_inc(S["step_set"], 1)
            act.wait_ge(S["exp_in"], 1)
            act.activation(p(MAG), p(A_), ACT.Exp).then_inc(S["exp_done"], 1)
            act.activation(p(MAG8), p(A_), ACT.Exp, scale=float(SC)).then_inc(S["exp_done"], 1)
            act.wait_ge(S["sin_in"], 1)
            act.activation(p(SIN), p(R_), ACT.Sin)
            act.activation(p(COS), p(N_), ACT.Sin).then_inc(S["sin_done"], 1)
            for n, (a, z) in enumerate(batches):
                act.wait_ge(S["u_tr"], n + 1)
                act.activation(u[:, a:z].rearrange("p g c -> p (g c)"), ps[:, n % 2, 0:(z - a) * NCA], ACT.Copy).then_inc(S["u_copied"], 1)
            for n in range(8):
                act.wait_ge(S["wt_tr"], n + 1)
                act.activation(w_t[:, 2 * n:2 * n + 2].rearrange("p a r s -> p (a r s)"), ps[:, 2 + n % 2, :], ACT.Copy).then_inc(S["wt_copied"], 1)
            for n in range(8):
                act.wait_ge(S["k_mm"], n + 1)
                if n == 0:
                    act.wait_ge(S["u_copied"], len(batches))
                g0 = 8 * (n // 2) + n % 2
                act.activation(taps[:, g0:g0 + 7:2], ps[0:GW, 4 + n % 2, :].rearrange("p (g c) -> p g c", c=P), ACT.Copy).then_inc(S["k_copied"], 1)
            for n, gs in enumerate(y_batches):
                act.wait_ge(S["y_sum"], n + 1)
                y = u[:, gs[0]:gs[-1] + 1:2]
                act.activation(y, y, ACT.Gelu_apprx_tanh).then_inc(S["gelu"], 1)

        @block.tensor
        def _(pe):
            pe.wait_ge(S["par_in"], 128)
            pe.wait_ge(S["grouped_s"], 1)
            for n, (a, z) in enumerate(batches):
                pe.wait_ge(S["grouped"], min((z - 1) // 8 + 1, 4))
                if n >= 2:
                    pe.wait_ge(S["u_copied"], n - 1)
                for g in range(a, z):
                    o = (g - a) * NCA
                    pe.transpose(ps[:, n % 2, o:o + NCH], by_group[:, g], ident[:])
                    last = pe.transpose(ps[:, n % 2, o + NCH:o + NCA], small_group[:, g], ident[64:64 + SB, 64:64 + SB])
                last.then_inc(S["u_tr"], 1)
            pe.wait_ge(S["w_set"], 1)
            for n in range(8):
                if n >= 2:
                    pe.wait_ge(S["wt_copied"], n - 1)
                for k in range(4):
                    last = pe.transpose(ps[:, 2 + n % 2, k * P:(k + 1) * P], w_h[:, k % 2, 2 * n + k // 2, 0:P], ident[:])
                last.then_inc(S["wt_tr"], 1)
            pe.wait_ge(S["ca_set"], 1)
            for n in range(8):
                if n >= 2:
                    pe.wait_ge(S["k_copied"], n - 1)
                for k in range(4):
                    g = 8 * (n // 2) + 2 * k + n % 2
                    r = slice(NST * (g % 2), NST * (g % 2) + NST)
                    for c in range(2):
                        last = pe.matmul(ps[0:GW, 4 + n % 2, k * P:(k + 1) * P], bb[r, c, g // 2], ca[r, c, g // 2, 0:P], start=(c == 0), stop=(c == 1))
                last.then_inc(S["k_mm"], 1)
            pe.wait_ge(S["wt_copied"], 8)
            pe.wait_ge(S["u_copied"], len(batches))
            for n, (a, z) in enumerate(pair_batches):
                for c in range(2):
                    m = 2 * n + c
                    if m >= 2:
                        pe.wait_ge(S["x_copied"], m - 1)
                    for pr in range(a, z):
                        for g2 in range(2):
                            last = pe.matmul(ps[NST * g2:NST * (g2 + 1), 6 + c, (pr - a) * NCA:(pr - a + 1) * NCA], w_t[:, pr, c, NST * g2:NST * (g2 + 1)], u[:, 2 * pr + g2], start=True, stop=True)
                    last.then_inc(S["x_mm"], 1)
            pe.wait_ge(S["toep_in"], 16 * SC)
            pe.wait_ge(S["h_set"], 1)
            for n, gs in enumerate(y_batches):
                if n >= 2:
                    pe.wait_ge(S["y_sum"], n - 1)
                for k, g in enumerate(gs):
                    r = slice(NST * (g % 2), NST * (g % 2) + NST)
                    dst = ps[:, n % 2, k * NCA:(k + 1) * NCA]
                    pe.matmul(dst, toep[:, g], u[:, g], start=True, stop=False)
                    pe.matmul(dst, ca[r, 0, g // 2, GW:], w_h[r, 0, g // 2], start=False, stop=False)
                    last = pe.matmul(dst, ca[r, 1, g // 2, GW:], w_h[r, 1, g // 2], start=False, stop=True)
                last.then_inc(S["y_mm"], 1)
            for n in range(8):
                pe.wait_ge(S["gelu"], max(y_batch_of[g] for g in range(4 * n, 4 * n + 4)) + 1)
                if n >= 2:
                    pe.wait_ge(S["y_copied"], 2 * (n - 1))
                for k in range(4):
                    pe.transpose(ps[:, 2 + n % 2, k * P:(k + 1) * P], u[:, 4 * n + k, 0:NCH], ident[:])
                    last = pe.transpose(ps[0:SB, 4 + n % 2, k * P:(k + 1) * P], u[:, 4 * n + k, NCH:NCA], ident[:])
                last.then_inc(S["y_tr"], 1)

        @block.vector
        def _(dve):
            tt, ts = dve.tensor_tensor, dve.tensor_scalar
            MUL, ADD, SUB = ALU.mult, ALU.add, ALU.subtract

            def cmul(out_r, out_i, xr, xi, yr, yi, t1, t2, conj=False):
                tt(t1, xi, yi, MUL)
                tt(t2, xr, yi, MUL)
                dve.drain()
                tt(out_r, xr, yr, MUL)
                tt(out_i, xi, yr, MUL)
                dve.drain()
                tt(out_r, out_r, t1, ADD if conj else SUB)
                tt(out_i, out_i, t2, SUB if conj else ADD)
                dve.drain()

            dve.wait_ge(S["rows_in"], 32)
            for n in range(4):
                dve.tensor_copy(by_group[:, 8 * n:8 * n + 8].rearrange("p g (s n) -> p g s n", n=GW),
                                rows[:, :, n * P:(n + 1) * P].rearrange("p s (g n) -> p g s n", n=GW)).then_inc(S["grouped"], 1)
            dve.wait_ge(S["par_in"], 128)
            dve.wait_ge(S["step_set"], 1)
            tt(p(A_), p(ARE), p(STEP), MUL)
            tt(p(TH), p(AIM), p(STEP), MUL)
            dve.drain().then_inc(S["exp_in"], 1)
            ts(p(B_), p(TH), 1.0 / TWO_PI, None, MUL)
            ts(p(C_), p(TH), 1.0 / TWO_PI, 0.25, MUL, ADD)
            dve.drain()
            for src, dst, quarter in ((B_, R_, 0.0), (C_, N_, TWO_PI / 4)):
                ts(p(D_), p(src), ROUND, None, ADD)
                dve.drain()
                ts(p(D_), p(D_), ROUND, None, SUB)
                dve.drain()
                dve.scalar_tensor_tensor(out=p(E_), in0=p(D_), scalar=-TWO_PI_HI, in1=p(TH), op0=MUL, op1=ADD)
                dve.drain()
                dve.scalar_tensor_tensor(out=p(E_), in0=p(D_), scalar=-(TWO_PI - TWO_PI_HI), in1=p(E_), op0=MUL, op1=ADD)
                dve.drain()
                ts(p(E_), p(E_), quarter, 3.1415925, ADD, ALU.min)
                dve.drain()
                ts(p(dst), p(E_), -3.1415925, None, ALU.max)
                dve.drain()
            dve.sem_inc(S["sin_in"], 1)
            dve.wait_ge(S["exp_done"], 2)
            dve.wait_ge(S["sin_done"], 1)
            dve.memset(pw[:, 0, 0], 1.0)
            dve.memset(pw[:, 1, 0], 0.0)
            tt(pw[:, 0, 1], p(MAG), p(COS), MUL)
            tt(pw[:, 1, 1], p(MAG), p(SIN), MUL)
            dve.drain()
            for k in range(2, SC + 1):
                cmul(pw[:, 0, k], pw[:, 1, k], pw[:, 0, k - 1], pw[:, 1, k - 1], pw[:, 0, 1], pw[:, 1, 1], p(A_), p(B_))
            ts(p(A_), pw[:, 0, 1], -1.0, None, ADD)
            tt(p(DEN), p(ARE), p(ARE), MUL)
            tt(p(B_), p(AIM), p(AIM), MUL)
            dve.drain()
            tt(p(DEN), p(DEN), p(B_), ADD)
            dve.drain()
            dve.reciprocal(p(DEN), p(DEN))
            cmul(p(ZR), p(ZI), p(A_), pw[:, 1, 1], p(ARE), p(AIM), p(C_), p(D_), conj=True)
            tt(p(ZR), p(ZR), p(DEN), MUL)
            tt(p(ZI), p(ZI), p(DEN), MUL)
            dve.drain()
            wide = lambda t, n=GW: t.unsqueeze(2).to_broadcast([P, NPR, n])
            t1, t2 = tmp[:, 0, :, 0:GW], tmp[:, 1, :, 0:GW]
            cmul(bb[:, 0], bb[:, 1], b_raw[:, 0], b_raw[:, 1], wide(p(ZR)), wide(p(ZI)), t1, t2)
            for s in range(SC):
                k = SC - 1 - s
                cmul(w_h[:, 0, :, s * GW:(s + 1) * GW], w_h[:, 1, :, s * GW:(s + 1) * GW], bb[:, 0], bb[:, 1], wide(pw[:, 0, k]), wide(pw[:, 1, k]), t1, t2)
            dve.sem_inc(S["w_set"], 1)
            for k in range(SC + 1):
                cmul(ca[:, 0, :, k * GW:(k + 1) * GW], ca[:, 1, :, k * GW:(k + 1) * GW], c_raw[:, 0], c_raw[:, 1], wide(pw[:, 0, k]), wide(pw[:, 1, k]), t1, t2)
            ts(ca[:, 1], ca[:, 1], -1.0, None, MUL)
            dve.drain()
            dve.sem_inc(S["ca_set"], 1)
            tt(p(CS8), p(COS), p(COS), MUL)
            for n in range(3):
                c, s = (p(COS), p(SIN)) if n == 0 else (p(CS8), p(SN8))
                tt(p(A_), c, c, MUL)
                tt(p(B_), s, s, MUL)
                tt(p(C_), c, s, MUL)
                dve.drain()
                tt(p(CS8), p(A_), p(B_), SUB)
                ts(p(SN8), p(C_), 2.0, None, MUL)
                dve.drain()
            dve.tensor_copy(turn[:, 0, :, 0], p(CS8))
            dve.tensor_copy(turn[:, 1, :, 0], p(SN8))
            dve.memset(m0[:], 0.0)
            dve.drain()
            n = 1
            while n < NCH:
                cmul(turn[:, 0, :, n:2 * n], turn[:, 1, :, n:2 * n], turn[:, 0, :, 0:n], turn[:, 1, :, 0:n],
                     turn[:, 0, :, n - 1:n].to_broadcast([P, NPR, n]), turn[:, 1, :, n - 1:n].to_broadcast([P, NPR, n]), tmp[:, 0, :, 0:n], tmp[:, 1, :, 0:n])
                n *= 2
            tt(tmp[:, 0], turn[:, 0], turn[:, 0], MUL)
            tt(tmp[:, 1], turn[:, 1], turn[:, 1], MUL)
            dve.drain()
            tt(tmp[:, 0], tmp[:, 0], tmp[:, 1], ADD)
            dve.drain()
            ts(tmp[:, 0], tmp[:, 0], -0.5, 1.5, MUL, ADD)
            dve.drain()
            tt(turn[:, 0], turn[:, 0], tmp[:, 0], MUL)
            tt(turn[:, 1], turn[:, 1], tmp[:, 0], MUL)
            tt(m0[:, :, 1:], m0[:, :, 1:], p(MAG8).unsqueeze(2).to_broadcast([P, NPR, NCH - 1]), ADD)
            dve.drain()
            for n, (a, z) in enumerate(pair_batches):
                for c in range(2):
                    dve.wait_ge(S["x_mm"], 2 * n + c + 1)
                    dve.tensor_copy(x[:, c, a:z].rearrange("p g c -> p (g c)"), ps[:, 6 + c, 0:(z - a) * NCA]).then_inc(S["x_copied"], 1)
            dve.drain()
            xr, xi = x[:, 0, :, 0:NCH], x[:, 1, :, 0:NCH]
            dve.wait_ge(S["wt_tr"], 8)
            hr, hi = w_h[:, 0, :, 0:NCH], w_h[:, 1, :, 0:NCH]
            cmul(tmp[:, 0], tmp[:, 1], xr, xi, turn[:, 0], turn[:, 1], hr, hi, conj=True)
            for c in range(2):
                flat = tmp[:, c].rearrange("p g c -> p (g c)")
                dve.tensor_tensor_scan(flat, m0[:].rearrange("p g c -> p (g c)"), flat, 0.0, MUL, ADD)
            dve.drain()
            cmul(xr, xi, tmp[:, 0], tmp[:, 1], turn[:, 0], turn[:, 1], hr, hi)
            for c in range(2):
                dve.tensor_copy(w_h[:, c, :, 1:NCH], x[:, c, :, 0:NCH - 1])
                dve.memset(w_h[:, c, :, 0:1], 0.0)
                dve.tensor_copy(h_end_p[:, c], x[:, c, :, NCH - 1:NCH])
            s0r, s0i = w_h[:, 0, :, NCH:NCA], w_h[:, 1, :, NCH:NCA]
            cmul(h_end_s[:, 0], h_end_s[:, 1], s0r, s0i, wide(pw[:, 0, SC], SB), wide(pw[:, 1, SC], SB), tmp[:, 0, :, 0:SB], tmp[:, 1, :, 0:SB])
            for c in range(2):
                tt(h_end_s[:, c], h_end_s[:, c], x[:, c, :, NCH:NCA], ADD)
            dve.drain().then_inc(S["h_set"], 1)
            for n, gs in enumerate(y_batches):
                dve.wait_ge(S["y_mm"], n + 1)
                for k, g in enumerate(gs):
                    last = dve.scalar_tensor_tensor(out=u[:, g], in0=u[:, g], scalar=dcol[:, g:g + 1], in1=ps[:, n % 2, k * NCA:(k + 1) * NCA], op0=MUL, op1=ADD)
                last.then_inc(S["y_sum"], 1)
            for n in range(8):
                dve.wait_ge(S["y_tr"], n + 1)
                dve.tensor_copy(rows[:, :, n * HD:(n + 1) * HD].rearrange("p s (g n) -> p g s n", n=GW), ps[:, 2 + n % 2, :].rearrange("p (g s n) -> p g s n", s=SC, n=GW)).then_inc(S["y_copied"], 1)
                dve.tensor_copy(small_rows[:, :, n * HD:(n + 1) * HD].rearrange("p s (g n) -> p g s n", n=GW), ps[0:SB, 4 + n % 2, :].rearrange("p (g s n) -> p g s n", s=SC, n=GW)).then_inc(S["y_copied"], 1)


def s5_glu_stage(nc, rows_in, w_in, ident_in, out_t):
    NK = 4
    with ExitStack() as ctx:
        new_sem = ctx.enter_context(stage_semaphores(nc))
        sb = lambda name, shape: ctx.enter_context(nc.sbuf_tensor("gl_" + name, shape, F32))
        rows = sb("rows", [P, len(TILES), 512])
        y = sb("y", [P, NK, T])
        w = sb("w", [P, NK, 512])
        ident = sb("ident", [P, P])
        gate = sb("gate", [P, NK, T])
        ps = ctx.enter_context(nc.psum_tensor("gl_ps", [P, 8, BANK], F32))
        S = {n: new_sem("gl_" + n) for n in "w_in rows_in tr copied mm sig out_set stored".split()}
        block = ctx.enter_context(nc.Block())
        NTL = len(TILES)

        @block.sync
        def _(sp):
            sp.dma_start(rows[:, 0:TP // P], rows_in[0:TP].rearrange("(n p) c -> p n c", p=P)).then_inc(S["rows_in"], 16)
            sp.dma_start(rows[0:T - TP, TP // P], rows_in[TP:T]).then_inc(S["rows_in"], 16)
            sp.dma_start(ident[:], ident_in).then_inc(S["rows_in"], 16)
            sp.dma_start(w[:], w_in.rearrange("(k p) n -> p k n", p=P)).then_inc(S["w_in"], 16)
            for n in range(NK):
                sp.wait_ge(S["out_set"], n + 1)
                sp.dma_start(out_t[n * P:(n + 1) * P], gate[:, n]).then_inc(S["stored"], 16)
            sp.wait_ge(S["stored"], 16 * NK)

        @block.tensor
        def _(pe):
            pe.wait_ge(S["rows_in"], 48)
            for t, (t0, tn) in enumerate(TILES):
                if t >= 2:
                    pe.wait_ge(S["copied"], t - 1)
                for k in range(NK):
                    last = pe.transpose(ps[:, t % 2, k * P:k * P + tn], rows[0:tn, t, k * P:(k + 1) * P], ident[0:tn, 0:tn])
                last.then_inc(S["tr"], 1)
            pe.wait_ge(S["copied"], NTL)
            pe.wait_ge(S["w_in"], 16)
            for n in range(NK):
                if n >= 2:
                    pe.wait_ge(S["sig"], 3 * (n - 1))
                for c, (a, z) in enumerate(COLS):
                    for k in range(NK):
                        last = pe.matmul(ps[:, 2 + 3 * (n % 2) + c, 0:z - a], w[:, k, n * P:(n + 1) * P], y[:, k, a:z], start=(k == 0), stop=(k == NK - 1))
                    last.then_inc(S["mm"], 1)

        @block.scalar
        def _(act):
            for n in range(NK):
                for c, (a, z) in enumerate(COLS):
                    act.wait_ge(S["mm"], 3 * n + c + 1)
                    act.activation(gate[:, n, a:z], ps[:, 2 + 3 * (n % 2) + c, 0:z - a], ACT.Sigmoid).then_inc(S["sig"], 1)

        @block.vector
        def _(dve):
            for t, (t0, tn) in enumerate(TILES):
                dve.wait_ge(S["tr"], t + 1)
                dve.tensor_copy(y[:, :, t0:t0 + tn], ps[:, t % 2, :].rearrange("p (k t) -> p k t", t=P)[:, :, 0:tn]).then_inc(S["copied"], 1)
            for n in range(NK):
                dve.wait_ge(S["sig"], 3 * n + 3)
                if n == 0:
                    dve.wait_ge(S["copied"], NTL)
                dve.tensor_tensor(gate[:, n], gate[:, n], y[:, n], ALU.mult).then_inc(S["out_set"], 1)


D_FF = 2816
KF = D_FF // P
KH = KF // 2


def trunk_stage(nc, x_t, feat, a_t, b_t, c_rows, c_t, w_branch, w_out, w_gu, w_down, g_ffn, ident_in, x1_t, y_t):
    with ExitStack() as ctx:
        new_sem = ctx.enter_context(stage_semaphores(nc))
        sb = lambda name, shape, dt=F32: ctx.enter_context(nc.sbuf_tensor("tr_" + name, shape, dt))
        sem = lambda name, ahead=0: new_sem("tr_" + name, ahead)
        act_in, act_in_r = overlaid(nc, ctx, "tr_act_in", [P, 2, KD, T])
        wide, wide_r = overlaid(nc, ctx, "tr_wide", [P, 24, T])
        w, w_lo = overlaid(nc, ctx, "tr_w", [P, 2, 12, P])
        w_hi = sb("w_hi", [P, 2, 12, P], R32)
        gain = sb("gain", [P, KD])
        ident = sb("ident", [P, P])
        ones = sb("ones", [P, P])
        ps = ctx.enter_context(nc.psum_tensor("tr_ps", [P, 8, BANK], F32))
        NTL = TP // P
        flat = lambda part: part.rearrange("p o t -> p (o t)")
        rows = flat(act_in[:, 0, 0:4])[:, 0:NTL * 512].rearrange("p (n c) -> p n c", c=512)
        merged = act_in[:, 0]
        side = lambda s: act_in[:, 1, 3 * s:3 * s + 3]
        normed, in_lo, in_hi = act_in[:, 0], act_in_r[:, 0], act_in_r[:, 1]
        branch, br_lo, br_hi = wide[:, 0:12], wide_r[:, 0:12], wide_r[:, 12:24]
        rstd, ssq, sq = wide[:, 20], wide[:, 21], wide[:, 22:24]
        hid_lo, hid_hi = wide_r[:, 0:KH], wide_r[:, KH:2 * KH]
        tmp, resid = wide[:, 22], wide[:, 22:24]

        MERGE, OUT = (0, KD // 2, 12), (KD, KD // 2, KD)
        UP = [(2 * KD + h * (KF + KD), KH, KD) for h in range(2)]
        DOWN = [(2 * KD + h * (KF + KD) + KF, KD // 2, KH) for h in range(2)]
        next_tiles = {MERGE: KD, OUT: KD, UP[0]: KH, DOWN[0]: KD, UP[1]: KH, DOWN[1]: 0}
        SETS_OUT, SETS_UP, SETS_HALF = 3 * KD // 2, 3 * KD // 2 + KD // 2, KH + KD // 2
        set_use = lambda s, h: SETS_UP + (1 if s == 0 else 0) + h * SETS_HALF

        def bank_parts(s, row):
            n = THIRDS[0][1]
            return ((ps[:, 3 * s:3 * s + 2, 0:n], row[:, 0:2 * n].rearrange("p (c t) -> p c t", t=n)),
                    (ps[:, 3 * s + 2, 0:T - 2 * n], row[:, 2 * n:T]))

        const_in, rows_in, c_in, br_in = sem("const_in"), sem("rows_in"), sem("c_in"), [sem("a_in"), sem("b_in")]
        ones_set, tr, tr_hi, tr_split, br_hi_set, br_split = (sem(n) for n in "ones_set tr tr_hi tr_split br_hi_set br_split".split())
        w_in, g_in = [sem("w_in0"), sem("w_in1")], [sem("g_in0"), sem("g_in1")]
        w_hi_set, w_split, mm, passed = sem("w_hi_set"), sem("w_split"), sem("mm", KD + 2), sem("passed")
        set_free = [sem("set_free0", 1), sem("set_free1", 1)]
        br_mm, sig, merged_set = sem("br_mm", 6), sem("sig"), sem("merged_set", 2)
        x_in, x1_out, squared, summed = sem("x_in"), sem("x1_out"), sem("squared"), sem("summed", 2)
        in_hi_set, in_split, in_set = sem("in_hi_set"), sem("in_split"), sem("in_set")
        var_mm, var_set, root = sem("var_mm"), sem("var_set"), sem("root")
        hid_set, hid_hi_set, hid_split = sem("hid_set"), sem("hid_hi_set"), sem("hid_split", 1)
        r_in, added, y_out = [sem("r_in0"), sem("r_in1")], sem("added"), [sem("y_out0"), sem("y_out1")]

        block = ctx.enter_context(nc.Block())

        @block.sync
        def _(sp):
            def load_weights(i, u0, s, src, merging=False):
                if merging:
                    sp.wait_ge(br_mm, i * 6 + 3 * (u0 + s + 1))
                else:
                    sp.wait_ge(mm, i * 2 + (u0 + s + 1))
                sp.sem_inc(passed, 1)
                sp.dma_start(w[:, s, 0:src.shape[-2]], src).then_inc(w_in[s], 16)

            for dst, src in ((rows, c_rows.rearrange("(n p) c -> p n c", p=P)), (ident[:], ident_in)):
                sp.dma_start(dst, src).then_inc(rows_in, 16)
            sp.dma_start(branch[:, 0:4], a_t.rearrange("(k p) t -> p k t", p=P)).then_inc(br_in[0], 16)
            u0, pairs, _ = MERGE
            for s in range(2):
                load_weights(0, u0, s, w_branch[s], True)
            sp.dma_start(branch[:, 4:8], b_t.rearrange("(k p) t -> p k t", p=P)).then_inc(br_in[1], 16)
            sp.dma_start(branch[:, 8:12, TP:T], c_t.rearrange("(k p) t -> p k t", p=P)[:, :, TP:T]).then_inc(c_in, 16)
            sp.dma_start(gain[:], g_ffn).then_inc(const_in, 16)
            for s in range(2):
                for b in range(3):
                    sp.dma_start(side(s)[:, b], feat[R_GATES + b * D + s * P:R_GATES + b * D + (s + 1) * P, :]).then_inc(g_in[s], 16)
            with sp.Fori(0, pairs - 1) as i:
                for s in range(2):
                    load_weights(i, u0 + 2, s, w_branch[i * 2 + (s + 2)], True)
                    sp.wait_ge(merged_set, i * 2 + (s + 3))
                    sp.sem_inc(passed, 1)
                    for b in range(3):
                        sp.dma_start(side(s)[:, b], feat[bass.ds(i * 256 + (R_GATES + b * D + (s + 2) * P), P), :]).then_inc(g_in[s], 16)
            u0, pairs, _ = OUT
            for s in range(2):
                load_weights(0, u0, s, w_out[s], True)
            sp.dma_start(wide[:, 0:KD], x_t).then_inc(x_in, 16)
            with sp.Fori(0, pairs - 1) as i:
                for s in range(2):
                    load_weights(i, u0 + 2, s, w_out[i * 2 + (s + 2)])
            for h in range(2):
                u0, pairs, _ = UP[h]
                with sp.Fori(0, pairs) as i:
                    for s in range(2):
                        load_weights(i, u0, s, w_gu[i + h * KH, :, s * KD:(s + 1) * KD])
                u0, pairs, _ = DOWN[h]
                for s in range(2):
                    load_weights(0, u0, s, w_down[s][:, h * KH:(h + 1) * KH])
                sp.wait_ge(hid_split, KH * (h + 1) + 1)
                sp.wait_ge(x1_out, 16 * KD)
                for s in range(2):
                    if h == 1:
                        sp.wait_ge(y_out[s], 16 * KD // 2)
                for s in range(2):
                    sp.dma_start(resid[:, s], x1_t[s * P:(s + 1) * P]).then_inc(r_in[s], 16)
                with sp.Fori(0, pairs - 1) as i:
                    for s in range(2):
                        load_weights(i, u0 + 2, s, w_down[i * 2 + (s + 2)][:, h * KH:(h + 1) * KH])
                        sp.wait_ge(y_out[s], i * 16 + (16 * (1 + h * KD // 2)))
                        sp.sem_inc(passed, 1)
                        sp.dma_start(resid[:, s], x1_t[bass.ds(i * 256 + (s + 2) * P, P), :]).then_inc(r_in[s], 16)

        @block.gpsimd
        def _(pool):
            pool.memset(ones[:], 1.0).then_inc(ones_set, 1)
            with pool.Fori(0, KD // 2) as i:
                for s in range(2):
                    pool.wait_ge(added, i * 2 + (s + 1))
                    pool.sem_inc(passed, 1)
                    pool.dma_start(x1_t[bass.ds(i * 256 + s * P, P), :], flat(wide[:, bass.ds(i * 2 + s, 1)])).then_inc(x1_out, 16)
            for k in range(KD):
                pool.wait_ge(in_hi_set, KD + k + 1)
                pool.tensor_tensor(in_lo[:, k], normed[:, k], in_hi[:, k], ALU.subtract).then_inc(in_split, 1)
            for h, dst in ((0, x1_t), (1, y_t)):
                with pool.Fori(0, KD // 2) as i:
                    for s in range(2):
                        pool.wait_ge(added, i * 2 + (KD * (h + 1) + s + 1))
                        pool.dma_start(dst[bass.ds(i * 256 + s * P, P), :], resid[:, s]).then_inc(y_out[s], 16)
            for s in range(2):
                pool.wait_ge(y_out[s], 16 * KD)

        @block.tensor
        def _(pe):
            def products(bs, ws, tiles, hi, lo, at_tile=None):
                for k, wk in enumerate(tiles):
                    if at_tile:
                        at_tile(k)
                    wh, wl = w_hi[:, ws, wk], w_lo[:, ws, wk]
                    for n, (wp, xp) in enumerate(((wl, hi), (wh, lo), (wh, hi))):
                        for c, (a, z) in enumerate(THIRDS):
                            last = pe.matmul(ps[:, 3 * bs + c, 0:z - a], wp, xp[:, k, a:z], start=(k == 0 and n == 0), stop=(k == len(tiles) - 1 and n == 2))
                return last

            pe.wait_ge(rows_in, 32)
            for t in range(NTL):
                if t >= 2:
                    pe.wait_ge(tr_split, t - 1)
                for k in range(4):
                    last = pe.transpose(ps[:, 6 + t % 2, k * P:(k + 1) * P], rows[:, t, k * P:(k + 1) * P], ident[:])
                last.then_inc(tr, 1)
            u0, pairs, _ = MERGE
            with pe.Fori(0, pairs) as i:
                for s in range(2):
                    pe.wait_ge(w_split, i * 2 + (u0 + s + 1))
                    for b in range(3):
                        pe.wait_ge(br_split, b + 1)
                        bs = (3 * s + b) % 2
                        pe.wait_ge(set_free[bs], i * 3 + ((3 * s + b) // 2 + 1))
                        products(bs, s, range(4 * b, 4 * b + 4), br_hi[:, 4 * b:4 * b + 4], br_lo[:, 4 * b:4 * b + 4]).then_inc(br_mm, 1)
            u0, pairs, n = OUT

            def out_unit(i, s, at_tile=None):
                pe.wait_ge(w_split, i * 2 + (u0 + s + 1))
                pe.wait_ge(set_free[s], i + (SETS_OUT + 1))
                products(s, s, range(n), in_hi, in_lo, at_tile).then_inc(mm, 1)

            out_unit(0, 0, lambda k: pe.wait_ge(in_split, k + 1))
            out_unit(0, 1)
            with pe.Fori(1, pairs) as i:
                for s in range(2):
                    out_unit(i, s)
            pe.wait_ge(ones_set, 1)
            pe.wait_ge(summed, KD + 2)
            pe.wait_ge(set_free[0], SETS_UP + 1)
            for c, (a, z) in enumerate(THIRDS):
                last = pe.matmul(ps[:, c, 0:z - a], ones[:], ssq[:, a:z], start=True, stop=True)
            last.then_inc(var_mm, 1)
            for h in range(2):
                u0, pairs, n = UP[h]

                def up_unit(i, s, at_tile=None):
                    pe.wait_ge(w_split, i * 2 + (u0 + s + 1))
                    pe.wait_ge(set_free[s], i + (set_use(s, h) + 1))
                    products(s, s, range(n), in_hi, in_lo, at_tile).then_inc(mm, 1)

                first = 0
                if h == 0:
                    up_unit(0, 0, lambda k: pe.wait_ge(in_split, KD + k + 1))
                    up_unit(0, 1)
                    first = 1
                with pe.Fori(first, pairs) as i:
                    for s in range(2):
                        up_unit(i, s)
                u0, pairs, n = DOWN[h]

                def down_unit(i, s, at_tile=None):
                    pe.wait_ge(w_split, i * 2 + (u0 + s + 1))
                    pe.wait_ge(set_free[s], i + (set_use(s, h) + KH + 1))
                    products(s, s, range(n), hid_hi, hid_lo, at_tile).then_inc(mm, 1)

                down_unit(0, 0, lambda k: pe.wait_ge(hid_split, h * KH + k + 2))
                down_unit(0, 1)
                with pe.Fori(1, pairs) as i:
                    for s in range(2):
                        down_unit(i, s)

        @block.scalar
        def _(act):
            def weights_hi(i, u0, s, n):
                act.wait_ge(w_in[s], i * 16 + (16 * (u0 // 2 + 1)))
                act.activation(w_hi[:, s, 0:n], w[:, s, 0:n], ACT.Copy).then_inc(w_hi_set, 1)

            for t in range(NTL):
                act.wait_ge(tr, t + 1)
                act.activation(br_hi[:, 8:12, t * P:(t + 1) * P], ps[:, 6 + t % 2, :].rearrange("p (k t) -> p k t", t=P), ACT.Copy).then_inc(tr_hi, 1)
            for b in range(2):
                act.wait_ge(br_in[b], 16)
                act.activation(br_hi[:, 4 * b:4 * b + 4], branch[:, 4 * b:4 * b + 4], ACT.Copy).then_inc(br_hi_set, 1)
                if b == 0:
                    for s in range(2):
                        weights_hi(0, 0, s, 12)
            act.wait_ge(c_in, 16)
            act.activation(br_hi[:, 8:12, TP:T], branch[:, 8:12, TP:T], ACT.Copy).then_inc(br_hi_set, 1)
            u0, pairs, n = MERGE
            for s in range(2):
                act.wait_ge(g_in[s], 48)
                act.activation(side(s), side(s), ACT.Sigmoid).then_inc(sig, 1)
            with act.Fori(0, pairs - 1) as i:
                for s in range(2):
                    weights_hi(i, u0 + 2, s, n)
                    act.wait_ge(g_in[s], i * 48 + 96)
                    act.activation(side(s), side(s), ACT.Sigmoid).then_inc(sig, 1)
            for s in range(2):
                weights_hi(0, OUT[0], s, KD)
            act.wait_ge(merged_set, KD + 2)
            for k in range(KD):
                act.activation(in_hi[:, k], merged[:, k], ACT.Copy).then_inc(in_hi_set, 1)
            u0, pairs, n = OUT

            def out_unit(i, s, n_next):
                act.wait_ge(summed, i * 2 + (s + 1))
                act.wait_ge(added, i * 2 + (s + 1))
                act.sem_inc(passed, 1)
                act.activation(sq[:, s], flat(wide[:, bass.ds(i * 2 + s, 1)]), ACT.Square).then_inc(squared, 1)
                weights_hi(i, u0 + 2, s, n_next)

            with act.Fori(0, pairs) as i:
                for s in range(2):
                    out_unit(i, s, n)
            act.wait_ge(var_set, 1)
            act.activation(rstd, rstd, ACT.Sqrt).then_inc(root, 1)
            for k in range(KD):
                act.wait_ge(in_set, k + 1)
                act.activation(in_hi[:, k], normed[:, k], ACT.Copy).then_inc(in_hi_set, 1)
            for h in range(2):
                u0, pairs, n = UP[h]
                if h == 1:
                    act.wait_ge(y_out[0], 16 * KD // 2)

                def up_chunk(i, n_next):
                    act.wait_ge(hid_split, i + (h * KH + 1))
                    act.wait_ge(mm, i * 2 + (u0 + 3))
                    act.sem_inc(passed, 1)
                    for banks, row in bank_parts(0, tmp):
                        last = act.activation(row, banks, ACT.Silu)
                    last.then_inc(set_free[0], 1)
                    weights_hi(i, u0 + 2, 0, n_next)
                    act.wait_ge(hid_set, i + (h * KH + 1))
                    act.sem_inc(passed, 1)
                    act.activation(flat(hid_hi[:, bass.ds(i, 1)]), tmp, ACT.Copy).then_inc(hid_hi_set, 1)
                    weights_hi(i, u0 + 2, 1, n_next)

                with act.Fori(0, pairs - 1) as i:
                    up_chunk(i, n)
                up_chunk(pairs - 1, next_tiles[UP[h]])
                u0, pairs, n = DOWN[h]
                with act.Fori(0, pairs - 1) as i:
                    for s in range(2):
                        weights_hi(i, u0 + 2, s, n)
                if h == 0:
                    for s in range(2):
                        weights_hi(0, UP[1][0], s, KD)

        @block.vector
        def _(dve):
            def weights_lo(i, u0, s, n):
                dve.wait_ge(w_hi_set, i * 2 + (u0 + s + 1))
                dve.tensor_tensor(w_lo[:, s, 0:n], w[:, s, 0:n], w_hi[:, s, 0:n], ALU.subtract).then_inc(w_split, 1)

            for t in range(NTL):
                dve.wait_ge(tr_hi, t + 1)
                dve.tensor_tensor(br_lo[:, 8:12, t * P:(t + 1) * P], ps[:, 6 + t % 2, :].rearrange("p (k t) -> p k t", t=P),
                                  br_hi[:, 8:12, t * P:(t + 1) * P], ALU.subtract).then_inc(tr_split, 1)
            for b in range(2):
                dve.wait_ge(br_hi_set, b + 1)
                dve.tensor_tensor(br_lo[:, 4 * b:4 * b + 4], branch[:, 4 * b:4 * b + 4], br_hi[:, 4 * b:4 * b + 4], ALU.subtract).then_inc(br_split, 1)
                if b == 0:
                    for s in range(2):
                        weights_lo(0, 0, s, 12)
            dve.wait_ge(br_hi_set, 3)
            dve.tensor_tensor(br_lo[:, 8:12, TP:T], branch[:, 8:12, TP:T], br_hi[:, 8:12, TP:T], ALU.subtract)
            dve.drain().then_inc(br_split, 1)

            u0, pairs, n = MERGE

            def merge_chunk(i, s, n_next):
                dve.wait_ge(sig, i * 2 + (s + 1))
                for b in range(3):
                    bs = (3 * s + b) % 2
                    dve.wait_ge(br_mm, i * 6 + (3 * s + b + 7))
                    for banks, row in bank_parts(bs, side(s)[:, b]):
                        last = dve.tensor_tensor(row, row, banks, ALU.mult)
                    last.then_inc(set_free[bs], 1)
                dve.drain()
                dve.tensor_tensor(side(s)[:, 0], side(s)[:, 0], side(s)[:, 1], ALU.add)
                dve.drain()
                dve.tensor_tensor(flat(merged[:, bass.ds(i * 2 + s, 1)]), side(s)[:, 0], side(s)[:, 2], ALU.add).then_inc(merged_set, 1)
                weights_lo(i, u0 + 2, s, n_next)

            with dve.Fori(0, pairs - 1) as i:
                for s in range(2):
                    merge_chunk(i, s, n)
            for s in range(2):
                merge_chunk(pairs - 1, s, next_tiles[MERGE])
            for k in range(KD):
                dve.wait_ge(in_hi_set, k + 1)
                dve.tensor_tensor(in_lo[:, k], merged[:, k], in_hi[:, k], ALU.subtract).then_inc(in_split, 1)

            u0, pairs, n = OUT
            dve.wait_ge(x_in, 16)
            dve.memset(ssq, 0.0)
            with dve.Fori(0, pairs) as i:
                for s in range(2):
                    dve.wait_ge(mm, i * 2 + (u0 + s + 3))
                    for banks, row in bank_parts(s, flat(wide[:, bass.ds(i * 2 + s, 1)])):
                        dve.tensor_tensor(row, row, banks, ALU.add)
                    dve.drain().then_inc(added, 1)
                    dve.sem_inc(set_free[s], 1)
                    dve.wait_ge(squared, i * 2 + (s + 1))
                    dve.tensor_tensor(ssq, ssq, sq[:, s], ALU.add)
                    dve.drain().then_inc(summed, 1)
                    weights_lo(i, u0 + 2, s, n)

            dve.wait_ge(var_mm, 1)
            for banks, row in bank_parts(0, rstd):
                dve.tensor_scalar(row, banks, 1.0 / D, EPS, ALU.mult, ALU.add)
            dve.drain().then_inc(var_set, 1)
            dve.sem_inc(set_free[0], 1)
            dve.wait_ge(root, 1)
            dve.reciprocal(rstd, rstd)
            dve.wait_ge(const_in, 16)
            dve.drain()
            for k in range(KD):
                dve.scalar_tensor_tensor(out=normed[:, k], in0=wide[:, k], scalar=gain[:, k:k + 1], in1=rstd, op0=ALU.mult, op1=ALU.mult).then_inc(in_set, 1)
            dve.wait_ge(x1_out, 16 * KD)
            for h in range(2):
                u0, pairs, n = UP[h]

                def up_chunk(i, n_next):
                    weights_lo(i, u0 + 2, 0, n_next)
                    dve.wait_ge(set_free[0], i + (set_use(0, h) + 2))
                    dve.wait_ge(mm, i * 2 + (u0 + 4))
                    for banks, row in bank_parts(1, tmp):
                        last = dve.tensor_tensor(row, row, banks, ALU.mult)
                    last.then_inc(set_free[1], 1)
                    dve.drain().then_inc(hid_set, 1)
                    dve.wait_ge(hid_hi_set, i + (h * KH + 1))
                    dve.tensor_tensor(flat(hid_lo[:, bass.ds(i, 1)]), tmp, flat(hid_hi[:, bass.ds(i, 1)]), ALU.subtract).then_inc(hid_split, 1)
                    weights_lo(i, u0 + 2, 1, n_next)

                with dve.Fori(0, pairs - 1) as i:
                    up_chunk(i, n)
                up_chunk(pairs - 1, next_tiles[UP[h]])

                u0, pairs, n = DOWN[h]

                def down_unit(i, s, n_next):
                    dve.wait_ge(r_in[s], i * 16 + (16 * (1 + h * KD // 2)))
                    dve.wait_ge(mm, i * 2 + (u0 + s + 3))
                    for banks, row in bank_parts(s, resid[:, s]):
                        last = dve.tensor_tensor(row, row, banks, ALU.add)
                    last.then_inc(set_free[s], 1)
                    dve.drain().then_inc(added, 1)
                    if n_next:
                        weights_lo(i, u0 + 2, s, n_next)

                with dve.Fori(0, pairs - 1) as i:
                    for s in range(2):
                        down_unit(i, s, n)
                for s in range(2):
                    down_unit(pairs - 1, s, next_tiles[DOWN[h]])


def build_program(nc, i, o):
    def scratch(name, *shape):
        return nc.dram_tensor(name, shape, F32, kind="Internal").ap()

    feat = scratch("proj_feat", R_GATES + 3 * D, T)
    tok = scratch("proj_tok", T, NTOK)
    qkv = scratch("qkv_rows", T, NQKV)
    heads_t = scratch("heads_t", 6 * P, T)
    strips = scratch("strips", 2, NH, STRIP)
    sample_t = scratch("sample_attn_t", 512, T)
    cmp_kt = scratch("cmp_kt", P, TP // CMP_STRIDE - 1)
    cmp_v = scratch("cmp_v", TP // CMP_STRIDE - 1, P)
    attn_rows = scratch("attn_rows", TP, 512)
    hgrn_t = scratch("hgrn_t", 512, T)
    s5_rows = scratch("s5_rows", T, 512)
    s5_t = scratch("s5_t", 512, T)
    x1_t = scratch("x1_t", D, T)

    norm_project_stage(nc, i["x_t"], i["g_mix"], i["w_feat"], i["w_tok"], feat, tok)
    attention_rows_stage(nc, tok, i["qk_norm"], i["ident"], o["kv_rows"], qkv, heads_t)
    bias_strip_stage(nc, i["rel_ext"], i["onehot"], qkv, i["win_cache"], strips, o["win_p"], o["win_s"])
    sample_attention_stage(nc, i["cache"], i["page_table"], i["win_cache"], heads_t, qkv, tok, strips, i["cmp_w1"], i["cmp_w2"],
                           i["cmp_pe"], i["qk_norm"], i["overlap"], i["rep"], i["ident"], sample_t)
    prompt_compress_stage(nc, tok, i["cmp_w1"], i["cmp_w2"], i["cmp_pe"], i["qk_norm"], i["ident"], cmp_kt, cmp_v)
    prompt_attention_stage(nc, heads_t, qkv, tok, strips, cmp_kt, cmp_v, i["flip"], i["ident"], attn_rows)
    hgrn_stage(nc, feat, tok, i["lb_logits"], i["hg_gain"], i["hg_state"], i["diag"], i["ident"], i["own"], hgrn_t, o["hg_p"], o["hg_s"])
    s5_state_stage(nc, tok, i["s5_a_re"], i["s5_a_im"], i["s5_log_dt"], i["s5_b"], i["s5_c"], i["s5_d"], i["s5_h0"], i["ident"],
                   s5_rows, o["s5_p"], o["s5_s"])
    s5_glu_stage(nc, s5_rows, i["s5_w_glu"], i["ident"], s5_t)
    trunk_stage(nc, i["x_t"], feat, hgrn_t, s5_t, attn_rows, sample_t, i["w_branch"], i["w_out"], i["w_gate_up"], i["w_down"],
                i["g_ffn"], i["ident"], x1_t, o["y_t"])


def rel_buckets(dist):
    n = np.maximum(dist, 0)
    exact = N_BUCKETS // 2
    nf = np.maximum(n, 1).astype(np.float32)
    large = exact + (np.log(nf / np.float32(exact)) / np.float32(np.log(MAX_DIST / exact)) * np.float32(N_BUCKETS - exact)).astype(np.int32)
    return np.where(n < exact, n, np.minimum(large, N_BUCKETS - 1))


def shape_constants():
    f4 = np.float32
    dist = STRIP_AT - np.arange(STRIP)
    onehot = np.zeros((N_BUCKETS + 1, 2, STRIP), f4)
    for w in range(2):
        bad = (dist < 0) | ((dist >= WINDOW) if w else False)
        onehot[rel_buckets(dist), w, np.arange(STRIP)] = 1
        onehot[:, w, bad] = 0
        onehot[N_BUCKETS, w, bad] = NEG
    nb, ns = PAST // CMP_STRIDE - 1, PAST // 64 + 1
    cs, ss = np.arange(nb)[:, None] * CMP_STRIDE, np.arange(ns)[None] * 64
    overlap = np.zeros((2 * P, ns), f4)
    overlap[:nb] = (cs < ss + 64) & (cs + CMP_LEN > ss)
    row = np.arange(NH * ST)
    p = np.arange(P)
    return {
        "onehot": onehot,
        "overlap": np.ascontiguousarray(overlap.reshape(2, P, ns).transpose(1, 0, 2)),
        "rep": ((row[:, None] // (NR * ST) == row // (NR * ST)) & (row[:, None] % ST == row % ST)).astype(f4),
        "ident": np.eye(P, dtype=f4),
        "flip": np.ascontiguousarray(np.eye(P, dtype=f4)[::-1]),
        "diag": (p[:, None] // HC == p // HC).astype(f4),
        "own": (np.arange(SB * ST)[:, None] // ST == np.arange(SB)).astype(f4),
    }


def kernel(**inputs):
    import concourse.bacc as bacc
    from concourse.bass_utils import run_bass_kernel_spmd

    a = {name: np.asarray(v) for name, v in inputs.items()}
    con = np.ascontiguousarray

    def chunks(w, n=P):
        return con(w.reshape(w.shape[0] // P, P, w.shape[1] // n, n).transpose(2, 1, 0, 3))

    def columns(v):
        return con(v.reshape(-1, P).T)

    def pairs(v):
        r = v.reshape(NPR, 2, NST, *v.shape[2:])
        return con(np.moveaxis(r, 0, 2).reshape(P, NPR, *v.shape[2:]))

    x = np.concatenate([a["x_prompt"][0], a["x_sample"].reshape(SB * ST, D)])
    w_in = a["w_in"][0]
    widths = [512] * 6 + [128] * 6 + [24] + [D] * 3
    at = np.cumsum([0] + widths)
    hq, hf, hi, hg, su, nq, kc, vc, ksl, vsl, kwn, vwn, ngate, ga, gb, gc = (w_in[:, at[n]:at[n + 1]] for n in range(16))
    ins = {
        "x_t": con(x.T.reshape(KD, P, T).transpose(1, 0, 2)),
        "g_mix": columns(a["norm_mix"][0]),
        "w_feat": chunks(np.concatenate([hq, hf, hg, ga, gb, gc], axis=1)),
        "w_tok": chunks(np.concatenate([su, hi, nq, kc, vc, ksl, vsl, kwn, vwn, ngate], axis=1), TOK_CHUNK),
        "qk_norm": con(a["nsa_qk_norm"][0]),
        "rel_ext": np.concatenate([a["rel_bias"], np.ones((1, NH), np.float32)]),
        "win_cache": con(a["cache_win_kv"][0].reshape(SB, WINDOW, 2 * P)),
        "cache": con(a["cache_nsa_kv"][0].reshape(-1, P, 4 * P)),
        "page_table": con(a["page_table"].reshape(1, -1)),
        "cmp_w1": con(a["cmp_w1"][0].reshape(2, 16, P, CMP_HID).transpose(2, 0, 1, 3)),
        "cmp_w2": con(a["cmp_w2"][0].transpose(1, 0, 2)),
        "cmp_pe": con(a["cmp_pe"][0].reshape(2, 16, P).transpose(2, 0, 1)),
        "lb_logits": columns(a["hg_lb_logits"][0]),
        "hg_gain": con(a["hg_out_norm"].reshape(P, 1)),
        "hg_state": con(a["state_hgrn"][0]),
        "s5_a_re": pairs(a["s5_a_re"][0]),
        "s5_a_im": pairs(a["s5_a_im"][0]),
        "s5_log_dt": pairs(np.broadcast_to(a["s5_log_dt"][0][:, None], (NGR, NST))),
        "s5_b": np.stack([pairs(a["s5_b_re"][0]), pairs(a["s5_b_im"][0])], axis=1),
        "s5_c": np.stack([pairs(a["s5_c_re"][0].transpose(0, 2, 1)), pairs(a["s5_c_im"][0].transpose(0, 2, 1))], axis=1),
        "s5_d": con(np.broadcast_to(a["s5_d"][0].reshape(NGR, GW).T[None], (SC, GW, NGR)).reshape(P, NGR)),
        "s5_h0": np.stack([pairs(a["state_s5_re"][0].transpose(1, 2, 0)), pairs(a["state_s5_im"][0].transpose(1, 2, 0))], axis=1),
        "s5_w_glu": con(a["s5_w_glu"][0]),
        "w_branch": con(a["w_branch"][0].reshape(3, 4, P, KD, P).transpose(3, 2, 0, 1, 4).reshape(KD, P, 12, P)),
        "w_out": chunks(a["w_out"][0]),
        "w_gate_up": con(a["w_gate_up"][0].reshape(KD, P, 2, KF, P).transpose(3, 1, 2, 0, 4).reshape(KF, P, 2 * KD, P)),
        "w_down": chunks(a["w_down"][0]),
        "g_ffn": columns(a["norm_ffn"][0]),
    }
    ins.update(shape_constants())
    outs = {
        "y_t": (D, T), "kv_rows": (T, 512), "win_p": (WINDOW, 2 * P), "win_s": (SB, WINDOW, 2 * P),
        "hg_p": (4, P, P), "hg_s": (SB, 4, P, P), "s5_p": (P, 2, NPR, 1), "s5_s": (P, 2, NPR, SB),
    }
    nc = bacc.Bacc("TRN2", target_bir_lowering=False, num_devices=1)
    i = {n: nc.dram_tensor(n + "_in", v.shape, mybir.dt.from_np(v.dtype), kind="ExternalInput").ap() for n, v in ins.items()}
    o = {n: nc.dram_tensor(n + "_out", s, F32, kind="ExternalOutput").ap() for n, s in outs.items()}
    build_program(nc, i, o)
    got = run_bass_kernel_spmd(nc, [{n + "_in": v for n, v in ins.items()}], core_ids=[0]).results[0]
    r = {n: got[n + "_out"] for n in outs}

    def unpair(v):
        return con(v.reshape(2, NST, NPR, -1).transpose(3, 2, 0, 1).reshape(1, -1, NGR, NST))

    y = r["y_t"].T
    return (
        con(y[:TP]).reshape(1, TP, D), con(y[TP:]).reshape(SB, ST, D),
        con(r["kv_rows"][:TP]).reshape(1, 1, TP, 4, NG, HD), con(r["kv_rows"][TP:]).reshape(1, SB, ST, 4, NG, HD),
        r["win_p"].reshape(1, 1, WINDOW, 2, NG, HD), r["win_s"].reshape(1, SB, WINDOW, 2, NG, HD),
        r["hg_p"].reshape(1, 1, 4, P, P), r["hg_s"].reshape(1, SB, 4, P, P),
        unpair(r["s5_p"][:, 0]), unpair(r["s5_p"][:, 1]), unpair(r["s5_s"][:, 0]), unpair(r["s5_s"][:, 1]),
    )
```

```python
import concourse.bass as bass
from concourse import mybir
from contextlib import ExitStack, contextmanager
import numpy as np

F32 = mybir.dt.float32
I32 = mybir.dt.int32
ACT = mybir.ActivationFunctionType
ALU = mybir.AluOpType
AX = mybir.AxisListType

P = 128
BANK = 512
D = 1024
KD = D // P
TP = 1024
SB, ST = 8, 8
T = TP + SB * ST
PAST = 4096
EPS = 1e-6
NEG = -1e30
FORCE = 1e9
HD = 64
NH, NG, NR = 8, 2, 4
COLS = [(0, 512), (512, 1024), (1024, T)]
THIRDS = [(0, 364), (364, 728), (728, T)]
TILES = [(i * P, P) for i in range(TP // P)] + [(TP, T - TP)]
NTOK = 2328
TOK_CHUNK = NTOK // 6
C_SU, C_HI, C_NQ, C_KV, C_NGATE = 0, 512, 1024, 1536, 2304
R_HQ, R_HF, R_HG, R_GATES = 0, 512, 1024, 1536
NQKV = 512 + 768

STRIP = 2048
STRIP_AT = 1023
N_BUCKETS, MAX_DIST, WINDOW = 32, 128, 512
CMP_HID, CMP_STRIDE, CMP_LEN = 128, 16, 32
TINY = 1.17549435e-38

R32 = mybir.dt.float32r


def overlaid(nc, ctx, name, shape):
    plain = ctx.enter_context(nc.sbuf_tensor(name, shape, F32))
    return plain, nc.alloc_sbuf_tensor_at(name + "_r", shape, R32, offset=nc.sbuf_base - 4 * int(np.prod(shape[1:])))


def split_product(pe, out, w_hi, w_lo, x_hi, x_lo, first, last):
    pe.matmul(out, w_lo, x_hi, start=first, stop=False)
    pe.matmul(out, w_hi, x_lo, start=False, stop=False)
    return pe.matmul(out, w_hi, x_hi, start=False, stop=last)


@contextmanager
def stage_semaphores(nc):
    held = []

    def new(name, ahead=0):
        held.append(nc.alloc_semaphore(name))
        if ahead:
            nc.gpsimd.sem_inc(held[-1], ahead)
        return held[-1]

    yield new
    nc.clear_and_free_semaphores(held)
    nc.all_engine_barrier()


def norm_project_stage(nc, x_t, g_mix, x, x_lo, x_hi, w_feat, w_tok, feat_out, tok_out):
    with ExitStack() as ctx:
        new_sem = ctx.enter_context(stage_semaphores(nc))
        sb = lambda name, shape: ctx.enter_context(nc.sbuf_tensor("np_" + name, shape, F32))
        sb_r = lambda name, shape: ctx.enter_context(nc.sbuf_tensor("np_" + name, shape, R32))
        sem = lambda name, ahead=0: new_sem("np_" + name, ahead)
        rstd = sb("rstd", [P, T])
        sq = sb("sq", [P, 2, T])
        gain = sb("gain", [P, KD])
        ones = sb("ones", [P, P])
        wf, wf_lo = overlaid(nc, ctx, "np_wf", [P, 2, KD, P])
        wf_hi = sb_r("wf_hi", [P, 2, KD, P])
        wt, wt_lo = overlaid(nc, ctx, "np_wt", [P, 2, KD, TOK_CHUNK])
        wt_hi = sb_r("wt_hi", [P, 2, KD, TOK_CHUNK])
        stage = sb("stage", [P, 2, T])
        stage_t = sb("stage_t", [P, 4, TOK_CHUNK])
        ps = ctx.enter_context(nc.psum_tensor("np_ps", [P, 8, BANK], F32))
        x_in, gain_in, ones_set, squared, sq_used = [sem(f"x_in{k}") for k in range(KD)], sem("gain_in"), sem("ones_set"), sem("squared"), sem("sq_used")
        var_eps, root, rstd_set, normed = sem("var_eps"), sem("root"), sem("rstd_set"), sem("normed")
        wf_in = [sem("wf_in0"), sem("wf_in1")]
        x_hi_set, x_split = sem("x_hi_set"), sem("x_split")
        wf_hi_set, wf_split, wt_hi_set, wt_split = sem("wf_hi_set"), sem("wf_split"), sem("wt_hi_set"), sem("wt_split")
        wt_in = [sem("wt_in0"), sem("wt_in1")]
        f_mm, f_copied_a, f_copied_v, f_out = sem("f_mm"), sem("f_copied_a", 2), sem("f_copied_v", 2), [sem("f_out0"), sem("f_out1")]
        stage_free = sem("stage_free", 3)
        t_mm, t_copied = sem("t_mm"), sem("t_copied")
        t_out = [sem(f"t_out{i}") for i in range(4)]
        NF = w_feat.shape[0]
        NT = w_tok.shape[0]
        tiles = TILES
        TH = THIRDS[0][1]

        block = ctx.enter_context(nc.Block())

        @block.sync
        def _(sp):
            for k in range(KD):
                sp.dma_start(x[:, k], x_t[:, k]).then_inc(x_in[k], 16)
            sp.dma_start(gain[:], g_mix).then_inc(gain_in, 16)
            for s in range(2):
                sp.dma_start(wf[:, s], w_feat[s]).then_inc(wf_in[s], 16)
            for s in range(2):
                sp.dma_start(wt[:, s], w_tok[s]).then_inc(wt_in[s], 16)
            with sp.Fori(0, NF // 2 - 1) as i:
                for s in range(2):
                    sp.wait_ge(f_mm, i * 6 + 3 * s + 3)
                    sp.dma_start(wf[:, s], w_feat[i * 2 + (s + 2)]).then_inc(wf_in[s], 16)
            for c in range(2, NT):
                sp.wait_ge(t_mm, len(tiles) * (c - 1))
                sp.dma_start(wt[:, c % 2], w_tok[c]).then_inc(wt_in[c % 2], 16)

        @block.gpsimd
        def _(pool):
            pool.memset(ones[:], 1.0).then_inc(ones_set, 1)
            with pool.Fori(0, NF // 2) as i:
                for s in range(2):
                    pool.wait_ge(f_copied_a, i * 2 + (s + 3))
                    pool.wait_ge(f_copied_v, i * 2 + (s + 3))
                    pool.dma_start(feat_out[bass.ds(i * 256 + s * 128, P), :], stage[:, s]).then_inc(f_out[s], 16)
                for s in range(2):
                    pool.wait_ge(f_out[s], i * 16 + 16)
                    pool.sem_inc(stage_free, 1)
            for n in range(NT * len(tiles)):
                c, t = divmod(n, len(tiles))
                t0, tn = tiles[t]
                pool.wait_ge(t_copied, n + 1)
                pool.dma_start(tok_out[t0:t0 + tn, c * TOK_CHUNK:(c + 1) * TOK_CHUNK], stage_t[0:tn, n % 4]).then_inc(t_out[n % 4], 16)
            for s in range(4):
                pool.wait_ge(t_out[s], 16 * len(range(s, NT * len(tiles), 4)))

        @block.tensor
        def _(pe):
            pe.wait_ge(ones_set, 1)
            for k in range(KD):
                pe.wait_ge(squared, k + 1)
                for n, (a, b) in enumerate(THIRDS):
                    last = pe.matmul(ps[:, n, 0:b - a], ones[:], sq[:, k % 2, a:b], start=(k == 0), stop=(k == KD - 1))
                last.then_inc(sq_used, 1)
            pe.wait_ge(var_eps, 3)

            def chunk(i, s, at_tile=None):
                pe.wait_ge(wf_split, i * 2 + (s + 1))
                pe.wait_ge(f_copied_a, i * 2 + (s + 1))
                pe.wait_ge(f_copied_v, i * 2 + (s + 1))
                for k in range(KD):
                    if at_tile:
                        at_tile(k)
                    for n, (a, b) in enumerate(THIRDS):
                        done = split_product(pe, ps[:, 4 * s + n, 0:b - a], wf_hi[:, s, k], wf_lo[:, s, k], x_hi[:, k, a:b], x_lo[:, k, a:b], k == 0, k == KD - 1)
                        if k == KD - 1:
                            done.then_inc(f_mm, 1)

            chunk(0, 0, lambda k: pe.wait_ge(x_split, k + 1))
            chunk(0, 1)
            with pe.Fori(1, NF // 2) as i:
                for s in range(2):
                    chunk(i, s)
            pe.wait_ge(f_copied_a, NF + 2)
            pe.wait_ge(f_copied_v, NF + 2)
            for c in range(NT):
                pe.wait_ge(wt_split, c + 1)
                for t, (t0, tn) in enumerate(tiles):
                    n = c * len(tiles) + t
                    if n >= 8:
                        pe.wait_ge(t_copied, n - 7)
                    for k in range(KD):
                        last = split_product(pe, ps[0:tn, n % 8, 0:TOK_CHUNK], x_hi[:, k, t0:t0 + tn], x_lo[:, k, t0:t0 + tn], wt_hi[:, c % 2, k], wt_lo[:, c % 2, k], k == 0, k == KD - 1)
                    last.then_inc(t_mm, 1)

        @block.scalar
        def _(act):
            for k in range(KD):
                act.wait_ge(x_in[k], 16)
                if k >= 2:
                    act.wait_ge(sq_used, k - 1)
                act.activation(sq[:, k % 2], x[:, k], ACT.Square).then_inc(squared, 1)
            act.wait_ge(var_eps, 3)
            act.activation(rstd[:], rstd[:], ACT.Sqrt).then_inc(root, 1)
            for s in range(2):
                act.wait_ge(wf_in[s], 16)
                act.activation(wf_hi[:, s], wf[:, s], ACT.Copy).then_inc(wf_hi_set, 1)
            for k in range(KD):
                act.wait_ge(normed, k + 1)
                act.activation(x_hi[:, k], x[:, k], ACT.Copy).then_inc(x_hi_set, 1)
            for s in range(2):
                act.wait_ge(wt_in[s], 16)
                act.activation(wt_hi[:, s], wt[:, s], ACT.Copy).then_inc(wt_hi_set, 1)

            def copy_out(i, s):
                act.wait_ge(stage_free, i * 2 + (s + 2))
                act.wait_ge(f_mm, i * 6 + (3 * s + 1))
                act.activation(stage[:, s, 0:TH], ps[:, 4 * s, 0:TH], ACT.Copy).then_inc(f_copied_a, 1)

            with act.Fori(0, NF // 2 - 1) as i:
                for s in range(2):
                    copy_out(i, s)
                    act.wait_ge(wf_in[s], i * 16 + 32)
                    act.activation(wf_hi[:, s], wf[:, s], ACT.Copy).then_inc(wf_hi_set, 1)
            for s in range(2):
                copy_out(NF // 2 - 1, s)
            for c in range(2, NT):
                act.wait_ge(wt_in[c % 2], 16 * (c // 2 + 1))
                act.activation(wt_hi[:, c % 2], wt[:, c % 2], ACT.Copy).then_inc(wt_hi_set, 1)

        @block.vector
        def _(dve):
            dve.wait_ge(sq_used, KD)
            for n, (a, b) in enumerate(THIRDS):
                dve.tensor_scalar(rstd[:, a:b], ps[:, n, 0:b - a], 1.0 / D, EPS, ALU.mult, ALU.add).then_inc(var_eps, 1)
            dve.wait_ge(root, 1)
            dve.reciprocal(rstd[:], rstd[:]).then_inc(rstd_set, 1)
            dve.wait_ge(rstd_set, 1)
            for s in range(2):
                dve.wait_ge(wf_hi_set, s + 1)
                dve.tensor_tensor(wf_lo[:, s], wf[:, s], wf_hi[:, s], ALU.subtract).then_inc(wf_split, 1)
            dve.wait_ge(gain_in, 16)
            for k in range(KD + 1):
                if k < KD:
                    dve.scalar_tensor_tensor(out=x[:, k], in0=x[:, k], scalar=gain[:, k:k + 1], in1=rstd[:], op0=ALU.mult, op1=ALU.mult).then_inc(normed, 1)
                if k:
                    dve.wait_ge(x_hi_set, k)
                    dve.tensor_tensor(x_lo[:, k - 1], x[:, k - 1], x_hi[:, k - 1], ALU.subtract).then_inc(x_split, 1)
            for s in range(2):
                dve.wait_ge(wt_hi_set, s + 1)
                dve.tensor_tensor(wt_lo[:, s], wt[:, s], wt_hi[:, s], ALU.subtract).then_inc(wt_split, 1)

            def copy_out(i, s):
                dve.wait_ge(stage_free, i * 2 + (s + 2))
                dve.wait_ge(f_mm, i * 6 + (3 * s + 3))
                dve.tensor_copy(stage[:, s, TH:2 * TH], ps[:, 4 * s + 1, 0:TH])
                dve.tensor_copy(stage[:, s, 2 * TH:T], ps[:, 4 * s + 2, 0:T - 2 * TH]).then_inc(f_copied_v, 1)

            with dve.Fori(0, NF // 2 - 1) as i:
                for s in range(2):
                    copy_out(i, s)
                    dve.wait_ge(wf_hi_set, i * 2 + (s + 3))
                    dve.tensor_tensor(wf_lo[:, s], wf[:, s], wf_hi[:, s], ALU.subtract).then_inc(wf_split, 1)
            for s in range(2):
                copy_out(NF // 2 - 1, s)
            for n in range(NT * len(tiles)):
                c, t = divmod(n, len(tiles))
                tn = tiles[t][1]
                dve.wait_ge(t_mm, n + 1)
                if n >= 4:
                    dve.wait_ge(t_out[n % 4], 16 * (n // 4))
                dve.tensor_copy(stage_t[0:tn, n % 4], ps[0:tn, n % 8, 0:TOK_CHUNK]).then_inc(t_copied, 1)
                if t == 2 and 2 <= c + 1 < NT:
                    dve.wait_ge(wt_hi_set, c + 2)
                    s = (c + 1) % 2
                    dve.tensor_tensor(wt_lo[:, s], wt[:, s], wt_hi[:, s], ALU.subtract).then_inc(wt_split, 1)


def attention_rows_stage(nc, tok, qk_norm, ident_in, rows_out, qkv, heads_t):
    NHD = NQKV // HD
    K_SEL, K_WIN = (512 + 256) // HD, 1024 // HD
    with ExitStack() as ctx:
        new_sem = ctx.enter_context(stage_semaphores(nc))
        sb = lambda name, shape: ctx.enter_context(nc.sbuf_tensor("ar_" + name, shape, F32))
        sem = lambda name: new_sem("ar_" + name)
        rows = sb("rows", [P, 2, NHD, HD])
        sq = sb("sq", [P, 12, HD])
        ssq = sb("ssq", [P, 12])
        rstd = sb("rstd", [P, 12])
        gain = sb("gain", [P, 4, HD])
        ident = sb("ident", [P, P])
        turned = sb("turned", [P, 2, 6, P])
        ps = ctx.enter_context(nc.psum_tensor("ar_ps", [P, 4, BANK], F32))
        rows_in = [sem("rows_in0"), sem("rows_in1")]
        rows_stored = [sem("rows_stored0"), sem("rows_stored1")]
        turned_stored = [sem("turned_stored0"), sem("turned_stored1")]
        const_in, q_gain, var_set, root, normed, tr_done, copied = (
            sem("const_in"), sem("q_gain"), sem("var_set"), sem("root"), sem("normed"), sem("tr_done"), sem("copied"))
        NTL = len(TILES)
        parts = [(0, 8, 0, 0), (K_SEL, 2, 8, 2), (K_WIN, 2, 10, 3)]
        block = ctx.enter_context(nc.Block())

        @block.sync
        def _(sp):
            sp.dma_start(gain[:], qk_norm.unsqueeze(0).to_broadcast([P, 4, HD])).then_inc(const_in, 16)
            sp.dma_start(ident[:], ident_in).then_inc(const_in, 16)
            for t, (t0, tn) in enumerate(TILES):
                if t >= 2:
                    sp.wait_ge(rows_stored[t % 2], 32 * (t // 2))
                    sp.wait_ge(tr_done, 6 * (t - 1))
                sp.dma_start(rows[0:tn, t % 2].rearrange("p h d -> p (h d)"), tok[t0:t0 + tn, C_NQ:C_NQ + NQKV]).then_inc(rows_in[t % 2], 16)

        @block.gpsimd
        def _(pool):
            for t, (t0, tn) in enumerate(TILES):
                r = rows[0:tn, t % 2].rearrange("p h d -> p (h d)")
                pool.wait_ge(normed, 3 * (t + 1))
                pool.dma_start(rows_out[t0:t0 + tn, :], r[:, 512:1024]).then_inc(rows_stored[t % 2], 16)
                pool.dma_start(qkv[t0:t0 + tn, :], r).then_inc(rows_stored[t % 2], 16)
                pool.wait_ge(copied, 2 * (t + 1))
                pool.dma_start(heads_t[:, t0:t0 + tn].rearrange("(a p) t -> p a t", p=P), turned[:, t % 2, :, 0:tn]).then_inc(turned_stored[t % 2], 16)
            for s in range(2):
                n = len(range(s, NTL, 2))
                pool.wait_ge(rows_stored[s], 32 * n)
                pool.wait_ge(turned_stored[s], 16 * n)

        @block.scalar
        def _(act):
            for t, (t0, tn) in enumerate(TILES):
                act.wait_ge(var_set, t + 1)
                act.activation(rstd[0:tn], ssq[0:tn], ACT.Sqrt).then_inc(root, 1)

        @block.tensor
        def _(pe):
            pe.wait_ge(const_in, 32)
            for t, (t0, tn) in enumerate(TILES):
                pe.wait_ge(normed, 3 * (t + 1))
                if t >= 2:
                    pe.wait_ge(copied, 2 * (t - 1))
                for n, slot in enumerate((0, 2, 4, 6, K_SEL, K_WIN)):
                    pe.transpose(ps[:, 2 * (t % 2) + n // 4, (n % 4) * P:(n % 4) * P + tn],
                                 rows[0:tn, t % 2, slot:slot + 2].rearrange("p h d -> p (h d)"), ident[0:tn, 0:tn]).then_inc(tr_done, 1)

        @block.vector
        def _(dve):
            dve.wait_ge(const_in, 32)
            dve.tensor_scalar(gain[:, 0], gain[:, 0], HD ** -0.5, None, ALU.mult).then_inc(q_gain, 1)
            dve.wait_ge(q_gain, 1)
            for t, (t0, tn) in enumerate(TILES):
                dve.wait_ge(rows_in[t % 2], 16 * (t // 2 + 1))
                for slot, n, at, _g in parts:
                    r = rows[0:tn, t % 2, slot:slot + n]
                    dve.tensor_tensor(sq[0:tn, at:at + n], r, r, ALU.mult)
                dve.drain()
                dve.tensor_reduce(ssq[0:tn], sq[0:tn], AX.X, ALU.add)
                dve.drain()
                dve.tensor_scalar(ssq[0:tn], ssq[0:tn], 1.0 / HD, EPS, ALU.mult, ALU.add).then_inc(var_set, 1)
                dve.wait_ge(root, t + 1)
                dve.reciprocal(rstd[0:tn], rstd[0:tn])
                dve.drain()
                for slot, n, at, _g in parts:
                    r = rows[0:tn, t % 2, slot:slot + n]
                    dve.tensor_tensor(r, r, rstd[0:tn, at:at + n].unsqueeze(2).to_broadcast([tn, n, HD]), ALU.mult)
                dve.drain()
                for slot, n, at, g in parts:
                    r = rows[0:tn, t % 2, slot:slot + n]
                    dve.tensor_tensor(r, r, gain[0:tn, g:g + 1].to_broadcast([tn, n, HD]), ALU.mult).then_inc(normed, 1)
                if t >= 2:
                    dve.wait_ge(turned_stored[t % 2], 16 * (t // 2))
                for b, (h0, hn) in enumerate(((0, 4), (4, 2))):
                    dve.wait_ge(tr_done, 6 * t + h0 + hn)
                    dve.tensor_copy(turned[:, t % 2, h0:h0 + hn, 0:tn],
                                    ps[:, 2 * (t % 2) + b, 0:hn * P].rearrange("p (h t) -> p h t", t=P)[:, :, 0:tn]).then_inc(copied, 1)


def bias_strip_stage(nc, rel_ext, onehot, qkv, win_cache, strips, win_p, win_s):
    with ExitStack() as ctx:
        new_sem = ctx.enter_context(stage_semaphores(nc))
        lhs = ctx.enter_context(nc.sbuf_tensor("bs_lhs", [N_BUCKETS + 1, NH], F32))
        rhs = ctx.enter_context(nc.sbuf_tensor("bs_rhs", [N_BUCKETS + 1, 2 * STRIP], F32))
        out = ctx.enter_context(nc.sbuf_tensor("bs_out", [NH, 2 * STRIP], F32))
        ps = ctx.enter_context(nc.psum_tensor("bs_ps", [P, 8, BANK], F32))
        loaded, summed, copied, stored = (new_sem("bs_" + n) for n in ("loaded", "summed", "copied", "stored"))
        windows_stored = new_sem("bs_windows_stored")
        block = ctx.enter_context(nc.Block())

        @block.scalar
        def _(act):
            act.dma_start(win_p, qkv[TP - WINDOW:TP, 1024:NQKV]).then_inc(windows_stored, 16)
            act.dma_start(win_s[:, 0:WINDOW - ST], win_cache[:, ST:WINDOW]).then_inc(windows_stored, 16)
            act.dma_start(win_s[:, WINDOW - ST:WINDOW], qkv[TP:T, 1024:NQKV].rearrange("(b t) c -> b t c", b=SB)).then_inc(windows_stored, 16)
            act.wait_ge(windows_stored, 48)

        @block.sync
        def _(sp):
            sp.dma_start(lhs[:], rel_ext).then_inc(loaded, 16)
            sp.dma_start(rhs[:], onehot.rearrange("b w m -> b (w m)")).then_inc(loaded, 16)
            sp.wait_ge(copied, 8)
            sp.dma_start(strips.rearrange("w h m -> h w m"), out[:].rearrange("h (w m) -> h w m", w=2)).then_inc(stored, 16)
            sp.wait_ge(stored, 16)

        @block.tensor
        def _(pe):
            pe.wait_ge(loaded, 32)
            for n in range(8):
                pe.matmul(ps[0:NH, n, :], lhs[:], rhs[:, n * BANK:(n + 1) * BANK], start=True, stop=True).then_inc(summed, 1)

        @block.vector
        def _(dve):
            for n in range(8):
                dve.wait_ge(summed, n + 1)
                dve.tensor_copy(out[:, n * BANK:(n + 1) * BANK], ps[0:NH, n, :]).then_inc(copied, 1)


def sample_attention_stage(nc, cache, page_table, win_cache, heads_t, qkv, tok, strips, w1_in, w2_in, pe_in,
                           qk_norm, overlap_in, rep_in, ident_in, out_t):
    NB = (PAST // CMP_STRIDE) - 1
    NU = PAST // 256
    NPG = PAST // 128
    NS = PAST // 64 + 1
    R = NH * ST
    KEYS = PAST + ST
    with ExitStack() as ctx:
        new_sem = ctx.enter_context(stage_semaphores(nc))
        sb = lambda name, shape, dt=F32: ctx.enter_context(nc.sbuf_tensor("sa_" + name, shape, dt))
        sem = lambda name: new_sem("sa_" + name)
        pages = sb("pages", [P, NU, 2, 512])
        paired = sb("paired", [P, 4, 4, 2, HD])
        vals = sb("vals", [P, NU, 2, P])
        raw_t = sb("raw_t", [P, 4, NU * P])
        keys_t = sb("keys_t", [P, KEYS])
        scores = sb("scores", [R, KEYS])
        near_bias = sb("near_bias", [R, 256 + ST])
        probs_t = sb("probs_t", [P, 2 * NU + 1, R])
        w1 = sb("w1", [P, 2, 16, CMP_HID])
        w2 = sb("w2", [P, 2, HD])
        pe_cols = sb("pe_cols", [P, 2, 16])
        hid_bias = sb("hid_bias", [P, 2])
        hid = sb("hid", [P, 2, 2, NB])
        k_norm = sb("k_norm", [P, HD])
        cmp_kv = sb("cmp_kv", [P, 2, 2, P])
        cmp_sq = sb("cmp_sq", [P, 2, P])
        cmp_ssq = sb("cmp_ssq", [P, 4])
        cmp_kt = sb("cmp_kt", [P, NB])
        cmp_s = sb("cmp_s", [R, NB])
        cmp_bias = sb("cmp_bias", [R, NB])
        cmp_pt = sb("cmp_pt", [P, 2, R])
        overlap = sb("overlap", [P, 2, NS])
        rep = sb("rep", [R, R])
        ident = sb("ident", [P, P])
        blk = sb("blk", [R, NS])
        blk_rep = sb("blk_rep", [R, NS])
        top = sb("top", [R, 16])
        mask = sb("mask", [R, NS])
        win = sb("win", [P, 4, 256])
        win_kt = sb("win_kt", [P, WINDOW + ST])
        win_s = sb("win_s", [R, WINDOW + ST])
        win_bias = sb("win_bias", [R, WINDOW + ST])
        win_pt = sb("win_pt", [P, 5, R])
        new_v = sb("new_v", [ST, 2, P])
        q_diag = sb("q_diag", [P, R])
        near = sb("near", [R, 264])
        gates = sb("gates", [R, 3])
        cols = sb("cols", [R, 16])
        out_rows = sb("out_rows", [R, HD])
        out_cols = sb("out_cols", [HD, R])
        table = sb("table", [1, SB * NPG], I32)
        ps = ctx.enter_context(nc.psum_tensor("sa_ps", [P, 8, BANK], F32))
        names = ("const_in table_in bias_in zeroed bias_set pe_done hid_bias_set small_in win_in unit_in tr unit_copied val_copied "
                 "hid_mm gelu_done sel_mm sel_biased out2_mm var_set root kv_set kt_tr kt_copied cs_mm cs_neg cs_exp cs_norm cpt_tr cpt_copied "
                 "oc_mm blk_copied rep_mm sel_neg sel_exp spt_tr spt_copied os_mm wk_tr wk_copied ws_mm ws_neg ws_exp wpt_tr wpt_copied ow_mm "
                 "gate_exp out_set ot_tr ot_copied out_stored out_free passed oc_copied new_pt_copied pairs_set").split()
        ahead = "ot_copied cs_mm ws_mm ow_mm os_mm out_set out_free spt_copied wpt_copied".split()
        ahead_by = {"tr": 2 * NU, "pairs_set": NU, "val_copied": NU}
        S = {n: new_sem("sa_" + n, ahead_by.get(n, 1 if n in ahead else 0)) for n in names}
        unit_in = [sem(f"unit_in{u}") for u in range(NU)]
        block = ctx.enter_context(nc.Block())
        U_KEYS, U_NORM = 2, 4
        NPT = 5
        strip_q = lambda w, q, lo, n: strips[w, :, lo - q:lo - q + n]
        cmp_far = 192
        mn = ctx.enter_context(nc.allow_non_contiguous_dma(reason="small strided tables, once"))

        @block.sync
        def _(sp):
            sp.dma_start(table[:], page_table).then_inc(S["table_in"], 16)
            sp.wait_ge(S["table_in"], 16)
            with sp.Fori(0, SB) as b:
                for u in range(NU):
                    for j in range(2):
                        page = sp.value_load(table[0:1, bass.ds(b * NPG + (2 * u + j), 1)], min_val=0, max_val=cache.shape[0] - 1)
                        if j == 0:
                            sp.wait_ge(S["tr"], b * (2 * NU) + (2 * u + 2))
                            sp.sem_inc(S["passed"], 1)
                            sp.wait_ge(S["pairs_set"], b * NU + (u + 1))
                            sp.sem_inc(S["passed"], 1)
                            sp.wait_ge(S["val_copied"], b * NU + (u + 1))
                            sp.sem_inc(S["passed"], 1)
                        sp.dma_start(pages[64 * j:64 * j + 64, u].rearrange("p t c -> p (t c)"),
                                     cache[page].rearrange("(p t) c -> p (t c)", t=2)).then_inc(unit_in[u], 16)

        @block.gpsimd
        def _(pool):
            pool.memset(q_diag[:], 0.0).then_inc(S["zeroed"], 1)
            pool.wait_ge(S["zeroed"], 1)

            def pair(b, d, u):
                pool.wait_ge(unit_in[u], b * 32 + (32 * d + 32))
                pool.wait_ge(S["tr"], b * (2 * NU) + (2 * NU * (d + 1) + 2 * u - 7))
                pool.sem_inc(S["passed"], 1)
                pool.tensor_copy(paired[:, u % 4], pages[:, u, :, 0:256].rearrange("p t (s d) -> p s t d", d=HD)).then_inc(S["pairs_set"], 1)

            def sequence(b, more):
                pool.wait_ge(S["os_mm"], b + 1)
                pool.sem_inc(S["passed"], 1)
                for u in range(NU):
                    pool.wait_ge(unit_in[u], b * 32 + 32)
                    pool.sem_inc(S["passed"], 1)
                    pool.tensor_copy(vals[:, u], pages[:, u, :, 384:512]).then_inc(S["val_copied"], 1)
                if more:
                    for u in range(NU):
                        pair(b, 1, u)
                pool.wait_ge(S["ot_copied"], b + 2)
                pool.sem_inc(S["passed"], 1)
                pool.dma_start(out_t[:, bass.ds(b * ST + TP, ST)].rearrange("(h d) q -> d h q", d=HD), out_cols[:].rearrange("d (h q) -> d h q", q=ST)).then_inc(S["out_stored"], 16)
                pool.wait_ge(S["out_stored"], b * 16 + 16)
                pool.sem_inc(S["out_free"], 1)

            for u in range(NU):
                pair(0, 0, u)
            with pool.Fori(0, SB - 1) as b:
                sequence(b, True)
            sequence(SB - 1, False)

        @block.scalar
        def _(act):
            n_const = 0
            for dst, src in ((w1[:], w1_in), (w2[:], w2_in), (pe_cols[:], pe_in), (k_norm[:], qk_norm[1:2, :].to_broadcast([P, HD])),
                             (overlap[:], overlap_in), (rep[:], rep_in), (ident[:], ident_in)):
                act.dma_start(dst, src).then_inc(S["const_in"], 16)
            for q in range(ST):
                act.dma_start(near[q:R:ST], strip_q(0, q, STRIP_AT - 256, 264)).then_inc(S["bias_in"], 16)
                act.dma_start(win_bias[q:R:ST], strip_q(1, q, STRIP_AT - WINDOW, WINDOW + ST)).then_inc(S["bias_in"], 16)
                lo = STRIP_AT - (PAST - (CMP_LEN - 1)) + CMP_STRIDE * cmp_far - q
                act.dma_start(cmp_bias[q:R:ST, cmp_far:].unsqueeze(2), strips[0, :, lo:lo + CMP_STRIDE * (NB - cmp_far)].rearrange("h (i s) -> h i s", s=CMP_STRIDE)[:, :, 0:1]).then_inc(S["bias_in"], 16)
            act.wait_ge(S["pe_done"], 1)
            act.activation(hid_bias[:], ps[:, 6, 0:2], ACT.Copy).then_inc(S["hid_bias_set"], 1)

            def copy_units(b, d, first, last):
                for u in range(first, last):
                    A = 2 * (u % 2)
                    act.wait_ge(S["tr"], b * (2 * NU) + (2 * NU * (d + 1) + 2 * u + 1))
                    act.activation(raw_t[:, :, u * P:(u + 1) * P], ps[:, A, :].rearrange("p (s t) -> p s t", t=P), ACT.Copy)
                    act.wait_ge(S["tr"], b * (2 * NU) + (2 * NU * (d + 1) + 2 * u + 2))
                    act.activation(keys_t[:, u * 256:(u + 1) * 256], ps[:, A + 1, 0:256], ACT.Copy).then_inc(S["unit_copied"], 1)

            def sequence(b, more):
                act.wait_ge(S["cs_mm"], b + 1)
                act.wait_ge(S["ws_mm"], b + 1)
                act.wait_ge(S["ow_mm"], b + 1)
                act.wait_ge(S["os_mm"], b + 1)
                act.wait_ge(S["out_set"], b + 1)
                act.sem_inc(S["passed"], 1)
                at = b * ST + TP
                for g in range(NG):
                    for r in range(NR):
                        h = g * NR + r
                        act.dma_start(q_diag[HD * g:HD * (g + 1), h * ST:(h + 1) * ST], heads_t[h * HD:(h + 1) * HD, bass.ds(at, ST)]).then_inc(S["small_in"], 16)
                act.dma_start(keys_t[:, PAST:KEYS], heads_t[4 * P:5 * P, bass.ds(at, ST)]).then_inc(S["small_in"], 16)
                act.dma_start(win_kt[:, WINDOW:], heads_t[5 * P:6 * P, bass.ds(at, ST)]).then_inc(S["small_in"], 16)
                act.dma_start(new_v[:, 0], qkv[bass.ds(at, ST), 512 + 384:512 + 512]).then_inc(S["small_in"], 16)
                act.dma_start(new_v[:, 1], qkv[bass.ds(at, ST), 1024 + 128:1024 + 256]).then_inc(S["small_in"], 16)
                for h in range(NH):
                    act.dma_start(gates[h * ST:(h + 1) * ST, :], tok[bass.ds(at, ST), C_NGATE:C_NGATE + 24].rearrange("q (n h) -> q n h", n=3)[:, :, h]).then_inc(S["small_in"], 16)
                act.dma_start(win[:], win_cache[b].rearrange("(a p) c -> p a c", p=P)).then_inc(S["win_in"], 16)
                for s in range(2):
                    act.wait_ge(S["hid_mm"], b * 2 + (s + 1))
                    act.activation(hid[:, s].rearrange("p g i -> p (g i)"), ps[:, 4 + s, 0:2 * NB], ACT.Gelu_apprx_tanh, bias=hid_bias[:, s:s + 1]).then_inc(S["gelu_done"], 1)
                act.wait_ge(S["wk_tr"], b + 1)
                act.activation(win_kt[:, 0:WINDOW], ps[:, 7, :], ACT.Copy).then_inc(S["wk_copied"], 1)
                act.wait_ge(S["var_set"], b + 1)
                act.activation(cmp_ssq[:], cmp_ssq[:], ACT.Sqrt).then_inc(S["root"], 1)
                act.wait_ge(S["ws_neg"], b + 1)
                act.activation(win_s[:], win_s[:], ACT.Exp, bias=cols[:, 0:1], accum_out=cols[:, 1:2]).then_inc(S["ws_exp"], 1)
                act.wait_ge(S["small_in"], (b + 1) * 320)
                act.activation(gates[:], gates[:], ACT.Exp, scale=-1.0).then_inc(S["gate_exp"], 1)
                if more:
                    act.wait_ge(S["sel_mm"], b * 9 + 9)
                    copy_units(b, 1, 0, U_NORM)
                act.wait_ge(S["cs_neg"], b + 1)
                act.activation(cmp_s[:], cmp_s[:], ACT.Exp, bias=cols[:, 2:3], accum_out=cols[:, 3:4]).then_inc(S["cs_exp"], 1)
                if more:
                    copy_units(b, 1, U_NORM, NU)
                act.wait_ge(S["sel_neg"], b + 1)
                act.activation(scores[:], scores[:], ACT.Exp, bias=cols[:, 4:5], accum_out=cols[:, 5:6]).then_inc(S["sel_exp"], 1)
                for n in range(4):
                    act.wait_ge(S["spt_tr"], b * NPT + (n + 1))
                    act.activation(probs_t[:, 8 * n:8 * n + 8].rearrange("p a r -> p (a r)"), ps[:, n, :], ACT.Copy).then_inc(S["spt_copied"], 1)

            copy_units(0, 0, 0, NU)
            act.wait_ge(S["zeroed"], 1)
            with act.Fori(0, SB - 1) as b:
                sequence(b, True)
            sequence(SB - 1, False)

        @block.tensor
        def _(pe):
            pe.wait_ge(S["const_in"], 16 * 7)
            for s in range(2):
                for j in range(16):
                    last = pe.matmul(ps[:, 6, s:s + 1], w1[:, s, j], pe_cols[:, s, j:j + 1], start=(j == 0), stop=(j == 15))
            last.then_inc(S["pe_done"], 1)
            pe.wait_ge(S["hid_bias_set"], 1)

            def transpose_units(b, d, first, last):
                for u in range(first, last):
                    pe.wait_ge(unit_in[u], b * 32 + (32 * d + 32))
                    pe.wait_ge(S["pairs_set"], b * NU + (NU * (d + 1) + u + 1))
                    A = 2 * (u % 2)
                    if u >= 2:
                        pe.wait_ge(S["unit_copied"], b * NU + (NU * d + u - 1))
                    elif d:
                        pe.wait_ge(S["sel_biased"], b * 9 + 8)
                    for sg in range(4):
                        done = pe.transpose(ps[:, A, sg * P:(sg + 1) * P], paired[:, u % 4, sg].rearrange("p t d -> p (t d)"), ident[:])
                    done.then_inc(S["tr"], 1)
                    for t in range(2):
                        done = pe.transpose(ps[:, A + 1, t * P:(t + 1) * P], pages[:, u, t, 256:384], ident[:])
                    done.then_inc(S["tr"], 1)

            def key_scores(b, n):
                if n >= 4:
                    pe.wait_ge(S["sel_biased"], b * 9 + (n - 3))
                pe.matmul(ps[0:R, n % 4, :], q_diag[:], keys_t[:, n * 512:(n + 1) * 512], start=True, stop=True).then_inc(S["sel_mm"], 1)

            def sequence(b, more):
                pe.wait_ge(S["unit_copied"], b * NU + NU)
                pe.wait_ge(S["out_set"], b + 1)
                for s in range(2):
                    for j in range(16):
                        last = pe.matmul(ps[:, 4 + s, 0:2 * NB], w1[:, s, j], raw_t[:, 2 * s:2 * s + 2, j:j + 8 * (NB - 1) + 1:8], start=(j == 0), stop=(j == 15))
                    last.then_inc(S["hid_mm"], 1)
                pe.wait_ge(S["win_in"], b * 16 + 16)
                pe.wait_ge(S["wpt_copied"], b + 1)
                for a in range(4):
                    last = pe.transpose(ps[:, 7, a * P:(a + 1) * P], win[:, a, 0:P], ident[:])
                last.then_inc(S["wk_tr"], 1)
                pe.wait_ge(S["small_in"], (b + 1) * 320)
                pe.wait_ge(S["spt_copied"], b * 4 + 1)
                key_scores(b, 0)
                pe.wait_ge(S["wk_copied"], b + 1)
                pe.wait_ge(S["ot_copied"], b + 1)
                pe.matmul(ps[0:R, 7, :], q_diag[:], win_kt[:, 0:WINDOW], start=True, stop=True)
                pe.matmul(ps[0:R, 6, 8:16], q_diag[:], win_kt[:, WINDOW:], start=True, stop=True).then_inc(S["ws_mm"], 1)
                for n in range(1, 8):
                    key_scores(b, n)
                pe.matmul(ps[0:R, 6, 0:8], q_diag[:], keys_t[:, PAST:KEYS], start=True, stop=True).then_inc(S["sel_mm"], 1)
                pe.wait_ge(S["gelu_done"], b * 2 + 2)
                for s in range(2):
                    for g in range(2):
                        for c in range(2):
                            m = P if c == 0 else NB - P
                            last = pe.matmul(ps[0:m, 4, ((s * 2 + c) * 2 + g) * HD:((s * 2 + c) * 2 + g + 1) * HD], hid[:, s, g, c * P:c * P + m], w2[:, s], start=True, stop=True)
                last.then_inc(S["out2_mm"], 1)
                if more:
                    transpose_units(b, 1, 0, U_KEYS)
                pe.wait_ge(S["kv_set"], b + 1)
                pe.transpose(ps[:, 5, 0:P], cmp_kv[:, 0, 0], ident[:])
                pe.transpose(ps[:, 5, P:NB], cmp_kv[0:NB - P, 0, 1], ident[0:NB - P, 0:NB - P]).then_inc(S["kt_tr"], 1)
                pe.wait_ge(S["kt_copied"], b + 1)
                pe.matmul(ps[0:R, 5, 256:256 + NB], q_diag[:], cmp_kt[:], start=True, stop=True).then_inc(S["cs_mm"], 1)
                pe.wait_ge(S["ws_exp"], b + 1)
                pe.sem_inc(S["passed"], 1)
                for a in range(4):
                    pe.transpose(ps[:, 7, a * R:(a + 1) * R], win_s[:, a * P:(a + 1) * P], ident[0:R, 0:R])
                pe.transpose(ps[0:ST, 7, 4 * R:5 * R], win_s[:, WINDOW:], ident[0:R, 0:R]).then_inc(S["wpt_tr"], 1)
                pe.wait_ge(S["wpt_copied"], b + 2)
                for a in range(4):
                    pe.matmul(ps[0:R, 6, 128:256], win_pt[:, a], win[:, a, P:2 * P], start=(a == 0), stop=False)
                pe.matmul(ps[0:R, 6, 128:256], win_pt[0:ST, 4], new_v[:, 1], start=False, stop=True).then_inc(S["ow_mm"], 1)
                if more:
                    transpose_units(b, 1, U_KEYS, U_NORM)
                pe.wait_ge(S["cs_norm"], b + 1)
                pe.sem_inc(S["passed"], 1)
                pe.transpose(ps[:, 4, 0:R], cmp_s[:, 0:P], ident[0:R, 0:R])
                pe.transpose(ps[0:NB - P, 4, R:2 * R], cmp_s[:, P:NB], ident[0:R, 0:R]).then_inc(S["cpt_tr"], 1)
                pe.wait_ge(S["cpt_copied"], b + 1)
                for c, m in ((0, P), (1, NB - P)):
                    pe.matmul(ps[0:R, 4, 256:256 + NS], cmp_pt[0:m, c], overlap[0:m, c], start=(c == 0), stop=(c == 1))
                for c, m in ((0, P), (1, NB - P)):
                    last = pe.matmul(ps[0:R, 4, 128:256], cmp_pt[0:m, c], cmp_kv[0:m, 1, c], start=(c == 0), stop=(c == 1))
                last.then_inc(S["oc_mm"], 1)
                if more:
                    transpose_units(b, 1, U_NORM, U_NORM + 1)
                pe.wait_ge(S["blk_copied"], b + 1)
                pe.sem_inc(S["passed"], 1)
                pe.matmul(ps[0:R, 4, 384:384 + NS], rep[:], blk[:], start=True, stop=True).then_inc(S["rep_mm"], 1)
                if more:
                    transpose_units(b, 1, U_NORM + 1, NU)
                    pe.wait_ge(S["unit_copied"], b * NU + 2 * NU)
                pe.wait_ge(S["sel_exp"], b + 1)
                pe.sem_inc(S["passed"], 1)
                for n in range(32):
                    last = pe.transpose(ps[:, n // 8, (n % 8) * R:(n % 8 + 1) * R], scores[:, n * P:(n + 1) * P], ident[0:R, 0:R])
                    if n % 8 == 7:
                        last.then_inc(S["spt_tr"], 1)
                pe.transpose(ps[0:ST, 6, 64:128], scores[:, PAST:KEYS], ident[0:R, 0:R]).then_inc(S["spt_tr"], 1)
                pe.wait_ge(S["val_copied"], b * NU + 2 * NU)
                for n in range(32):
                    if n % 8 == 0:
                        pe.wait_ge(S["spt_copied"], b * 4 + (n // 8 + 2))
                    pe.matmul(ps[0:R, 5, 0:P], probs_t[:, n], vals[:, n // 2, n % 2], start=(n == 0), stop=False)
                pe.wait_ge(S["new_pt_copied"], b + 1)
                pe.sem_inc(S["passed"], 1)
                pe.matmul(ps[0:R, 5, 0:P], probs_t[0:ST, 32], new_v[:, 0], start=False, stop=True).then_inc(S["os_mm"], 1)
                pe.wait_ge(S["out_set"], b + 2)
                pe.sem_inc(S["passed"], 1)
                pe.transpose(ps[0:HD, 6, 256:256 + R], out_rows[:], ident[0:R, 0:R]).then_inc(S["ot_tr"], 1)

            transpose_units(0, 0, 0, NU)
            with pe.Fori(0, SB - 1) as b:
                sequence(b, True)
            sequence(SB - 1, False)

        @block.vector
        def _(dve):
            dve.wait_ge(S["bias_in"], 16 * 3 * ST)
            dve.memset(cmp_bias[:, 0:cmp_far], 0.0)
            dve.drain()
            dve.tensor_scalar(cmp_bias[:, 0:cmp_far], cmp_bias[:, 0:cmp_far], near[:, 0:1], None, ALU.add)
            for t in range(2):
                dve.tensor_copy(near_bias[:, t * P:(t + 1) * P], near[:, 0:256].rearrange("r (p t) -> r t p", t=2)[:, t])
            dve.tensor_copy(near_bias[:, 256:], near[:, 256:264])
            dve.drain()
            dve.wait_ge(S["const_in"], 16 * 7)
            with dve.Fori(0, SB) as b:
                dve.wait_ge(S["ws_mm"], b + 2)
                dve.tensor_tensor(win_s[:, 0:WINDOW], ps[0:R, 7, :], win_bias[:, 0:WINDOW], ALU.add)
                dve.tensor_tensor(win_s[:, WINDOW:], ps[0:R, 6, 8:16], win_bias[:, WINDOW:], ALU.add)
                dve.drain()
                dve.tensor_reduce(cols[:, 6:7], win_s[:], AX.X, ALU.max)
                dve.drain()
                dve.tensor_scalar(cols[:, 0:1], cols[:, 6:7], -1.0, None, ALU.mult).then_inc(S["ws_neg"], 1)
                for n in range(9):
                    dve.wait_ge(S["sel_mm"], b * 9 + (n + 1))
                    if n < 7:
                        last = dve.tensor_scalar(scores[:, n * 512:(n + 1) * 512], ps[0:R, n % 4, :], near[:, 0:1], None, ALU.add)
                    elif n == 7:
                        dve.tensor_scalar(scores[:, PAST - 512:PAST - 256], ps[0:R, 3, 0:256], near[:, 0:1], None, ALU.add)
                        last = dve.tensor_tensor(scores[:, PAST - 256:PAST], ps[0:R, 3, 256:512], near_bias[:, 0:256], ALU.add)
                    else:
                        last = dve.tensor_tensor(scores[:, PAST:KEYS], ps[0:R, 6, 0:ST], near_bias[:, 256:], ALU.add)
                    last.then_inc(S["sel_biased"], 1)
                dve.wait_ge(S["out2_mm"], b + 1)
                for c, m in ((0, P), (1, NB - P)):
                    for s in range(2):
                        dve.tensor_copy(cmp_kv[0:m, s, c], ps[0:m, 4, (s * 2 + c) * P:(s * 2 + c + 1) * P])
                dve.drain()
                for c, m in ((0, P), (1, NB - P)):
                    dve.tensor_tensor(cmp_sq[0:m, c], cmp_kv[0:m, 0, c], cmp_kv[0:m, 0, c], ALU.mult)
                dve.drain()
                dve.memset(cmp_ssq[:], 1.0)
                dve.drain()
                for c, m in ((0, P), (1, NB - P)):
                    dve.tensor_reduce(cmp_ssq[0:m, 2 * c:2 * c + 2], cmp_sq[0:m, c].rearrange("p (g d) -> p g d", g=2), AX.X, ALU.add)
                dve.drain()
                dve.tensor_scalar(cmp_ssq[:], cmp_ssq[:], 1.0 / HD, EPS, ALU.mult, ALU.add).then_inc(S["var_set"], 1)
                dve.wait_ge(S["root"], b + 1)
                dve.reciprocal(cmp_ssq[:], cmp_ssq[:])
                dve.drain()
                for c, m in ((0, P), (1, NB - P)):
                    for g in range(2):
                        k = cmp_kv[0:m, 0, c, g * HD:(g + 1) * HD]
                        last = dve.scalar_tensor_tensor(out=k, in0=k, scalar=cmp_ssq[0:m, 2 * c + g:2 * c + g + 1], in1=k_norm[0:m], op0=ALU.mult, op1=ALU.mult)
                last.then_inc(S["kv_set"], 1)
                dve.wait_ge(S["kt_tr"], b + 1)
                dve.tensor_copy(cmp_kt[:], ps[:, 5, 0:NB]).then_inc(S["kt_copied"], 1)
                dve.wait_ge(S["cs_mm"], b + 2)
                dve.tensor_tensor(cmp_s[:], ps[0:R, 5, 256:256 + NB], cmp_bias[:], ALU.add)
                dve.drain()
                dve.tensor_reduce(cols[:, 6:7], cmp_s[:], AX.X, ALU.max)
                dve.drain()
                dve.tensor_scalar(cols[:, 2:3], cols[:, 6:7], -1.0, None, ALU.mult).then_inc(S["cs_neg"], 1)
                dve.wait_ge(S["wpt_tr"], b + 1)
                dve.tensor_copy(win_pt[:, 0:4].rearrange("p a r -> p (a r)"), ps[:, 7, 0:4 * R])
                dve.tensor_copy(win_pt[0:ST, 4], ps[0:ST, 7, 4 * R:5 * R]).then_inc(S["wpt_copied"], 1)
                dve.wait_ge(S["cs_exp"], b + 1)
                dve.reciprocal(cols[:, 7:8], cols[:, 3:4])
                dve.drain()
                dve.tensor_scalar(cmp_s[:], cmp_s[:], cols[:, 7:8], None, ALU.mult)
                dve.drain()
                dve.scalar_tensor_tensor(out=cmp_s[:], in0=cmp_s[:], scalar=TINY, in1=cmp_s[:], op0=ALU.is_ge, op1=ALU.mult).then_inc(S["cs_norm"], 1)
                dve.wait_ge(S["cpt_tr"], b + 1)
                dve.tensor_copy(cmp_pt[:, 0], ps[:, 4, 0:R])
                dve.tensor_copy(cmp_pt[0:NB - P, 1], ps[0:NB - P, 4, R:2 * R]).then_inc(S["cpt_copied"], 1)
                dve.wait_ge(S["oc_mm"], b + 1)
                dve.tensor_copy(blk[:], ps[0:R, 4, 256:256 + NS]).then_inc(S["blk_copied"], 1)
                dve.wait_ge(S["gate_exp"], b + 1)
                dve.tensor_scalar(gates[:], gates[:], 1.0, None, ALU.add)
                dve.drain()
                dve.reciprocal(gates[:], gates[:])
                dve.wait_ge(S["rep_mm"], b + 1)
                dve.tensor_copy(blk_rep[:], ps[0:R, 4, 384:384 + NS])
                dve.drain()
                dve.memset(blk_rep[:, 0:1], FORCE)
                dve.memset(blk_rep[:, NS - 2:NS], FORCE)
                dve.drain()
                for k in range(2):
                    dve.max(top[:, 8 * k:8 * k + 8], blk_rep[:])
                    dve.drain()
                    dve.match_replace(blk_rep[:], top[:, 8 * k:8 * k + 8], blk_rep[:], -FORCE)
                    dve.drain()
                dve.tensor_scalar(mask[:], blk_rep[:], -1.0, NEG, ALU.is_gt, ALU.mult)
                dve.drain()
                for t in range(2):
                    v = scores[:, 0:PAST].rearrange("r (u t k p) -> r t u k p", u=NU, t=2, k=4)[:, t]
                    dve.tensor_tensor(v, v, mask[:, 0:NS - 1].rearrange("r (u k) -> r u k", k=4).unsqueeze(3).to_broadcast([R, NU, 4, 32]), ALU.add)
                dve.drain()
                dve.tensor_reduce(cols[:, 6:7], scores[:], AX.X, ALU.max)
                dve.drain()
                dve.tensor_scalar(cols[:, 4:5], cols[:, 6:7], -1.0, None, ALU.mult).then_inc(S["sel_neg"], 1)
                for g in range(2):
                    last = dve.tensor_scalar(out_rows[32 * g:32 * g + 32], ps[32 * g:32 * g + 32, 4, 128 + HD * g:128 + HD * (g + 1)], gates[32 * g:32 * g + 32, 0:1], None, ALU.mult)
                last.then_inc(S["oc_copied"], 1)
                dve.wait_ge(S["ws_exp"], b + 1)
                dve.reciprocal(cols[:, 8:9], cols[:, 1:2])
                dve.wait_ge(S["spt_tr"], b * NPT + NPT)
                dve.tensor_copy(probs_t[0:ST, 32], ps[0:ST, 6, 64:128]).then_inc(S["new_pt_copied"], 1)
                dve.reciprocal(cols[:, 9:10], cols[:, 5:6])
                dve.drain()
                dve.tensor_tensor(cols[:, 8:9], cols[:, 8:9], gates[:, 2:3], ALU.mult)
                dve.tensor_tensor(cols[:, 9:10], cols[:, 9:10], gates[:, 1:2], ALU.mult)
                dve.drain()
                dve.wait_ge(S["ow_mm"], b + 2)
                for g in range(2):
                    o = out_rows[32 * g:32 * g + 32]
                    dve.scalar_tensor_tensor(out=o, in0=ps[32 * g:32 * g + 32, 6, 128 + HD * g:128 + HD * (g + 1)], scalar=cols[32 * g:32 * g + 32, 8:9], in1=o, op0=ALU.mult, op1=ALU.add)
                dve.drain()
                dve.wait_ge(S["os_mm"], b + 2)
                for g in range(2):
                    o = out_rows[32 * g:32 * g + 32]
                    last = dve.scalar_tensor_tensor(out=o, in0=ps[32 * g:32 * g + 32, 5, HD * g:HD * (g + 1)], scalar=cols[32 * g:32 * g + 32, 9:10], in1=o, op0=ALU.mult, op1=ALU.add)
                last.then_inc(S["out_set"], 1)
                dve.wait_ge(S["ot_tr"], b + 1)
                dve.wait_ge(S["out_free"], b + 1)
                dve.tensor_copy(out_cols[:], ps[0:HD, 6, 256:256 + R]).then_inc(S["ot_copied"], 1)


def prompt_compress_stage(nc, tok, w1_in, w2_in, pe_in, qk_norm, ident_in, kt_out, v_out):
    NB = TP // CMP_STRIDE - 1
    NU = TP // 256
    with ExitStack() as ctx:
        new_sem = ctx.enter_context(stage_semaphores(nc))
        sb = lambda name, shape: ctx.enter_context(nc.sbuf_tensor("pc_" + name, shape, F32))
        raw = sb("raw", [P, NU, 2, 256])
        paired = sb("paired", [P, NU, 4, 2, HD])
        raw_t = sb("raw_t", [P, 4, NU * P])
        w1 = sb("w1", [P, 2, 16, CMP_HID])
        w2 = sb("w2", [P, 2, HD])
        pe_cols = sb("pe_cols", [P, 2, 16])
        k_norm = sb("k_norm", [P, HD])
        ident = sb("ident", [P, P])
        hid_bias = sb("hid_bias", [P, 2])
        hid = sb("hid", [P, 2, 2, NB])
        kv = sb("kv", [NB, 2, P])
        sq = sb("sq", [NB, P])
        ssq = sb("ssq", [NB, 2])
        kt = sb("kt", [P, NB])
        ps = ctx.enter_context(nc.psum_tensor("pc_ps", [P, 8, BANK], F32))
        S = {n: new_sem("pc_" + n) for n in
             "loaded paired_set tr copied hid_mm bias_set gelu_done out_mm var_set root kv_set kt_tr kt_copied stored".split()}
        block = ctx.enter_context(nc.Block())

        @block.sync
        def _(sp):
            for u in range(NU):
                sp.dma_start(raw[:, u], tok[u * 256:(u + 1) * 256, C_KV:C_KV + 256].rearrange("(p t) c -> p t c", t=2)).then_inc(S["loaded"], 16)
            for dst, src in ((w1[:], w1_in), (w2[:], w2_in), (pe_cols[:], pe_in), (k_norm[:], qk_norm[1:2, :].to_broadcast([P, HD])), (ident[:], ident_in)):
                sp.dma_start(dst, src).then_inc(S["loaded"], 16)
            sp.wait_ge(S["kv_set"], 2)
            sp.dma_start(v_out, kv[:, 1]).then_inc(S["stored"], 16)
            sp.wait_ge(S["kt_copied"], 1)
            sp.dma_start(kt_out, kt[:]).then_inc(S["stored"], 16)
            sp.wait_ge(S["stored"], 32)

        @block.tensor
        def _(pe):
            pe.wait_ge(S["loaded"], 16 * (NU + 5))
            for s in range(2):
                for j in range(16):
                    last = pe.matmul(ps[:, 7, s:s + 1], w1[:, s, j], pe_cols[:, s, j:j + 1], start=(j == 0), stop=(j == 15))
            last.then_inc(S["hid_mm"], 1)
            for u in range(NU):
                pe.wait_ge(S["paired_set"], u + 1)
                for sg in range(4):
                    last = pe.transpose(ps[:, u, sg * P:(sg + 1) * P], paired[:, u, sg].rearrange("p t d -> p (t d)"), ident[:])
                last.then_inc(S["tr"], 1)
            pe.wait_ge(S["copied"], NU)
            for s in range(2):
                for j in range(16):
                    last = pe.matmul(ps[:, 4 + s, 0:2 * NB], w1[:, s, j], raw_t[:, 2 * s:2 * s + 2, j:j + 8 * (NB - 1) + 1:8], start=(j == 0), stop=(j == 15))
                last.then_inc(S["hid_mm"], 1)
            pe.wait_ge(S["gelu_done"], 2)
            for s in range(2):
                for g in range(2):
                    last = pe.matmul(ps[0:NB, 6, (2 * s + g) * HD:(2 * s + g + 1) * HD], hid[:, s, g], w2[:, s], start=True, stop=True)
            last.then_inc(S["out_mm"], 1)
            pe.wait_ge(S["kv_set"], 2)
            pe.transpose(ps[:, 0, 0:NB], kv[:, 0], ident[0:NB, 0:NB]).then_inc(S["kt_tr"], 1)

        @block.scalar
        def _(act):
            act.wait_ge(S["hid_mm"], 1)
            act.activation(hid_bias[:], ps[:, 7, 0:2], ACT.Copy).then_inc(S["bias_set"], 1)
            act.wait_ge(S["bias_set"], 1)
            for s in range(2):
                act.wait_ge(S["hid_mm"], s + 2)
                act.activation(hid[:, s].rearrange("p g i -> p (g i)"), ps[:, 4 + s, 0:2 * NB], ACT.Gelu_apprx_tanh, bias=hid_bias[:, s:s + 1]).then_inc(S["gelu_done"], 1)
            act.wait_ge(S["var_set"], 1)
            act.activation(ssq[:], ssq[:], ACT.Sqrt).then_inc(S["root"], 1)

        @block.vector
        def _(dve):
            dve.wait_ge(S["loaded"], 16 * (NU + 5))
            for u in range(NU):
                dve.tensor_copy(paired[:, u], raw[:, u].rearrange("p t (s d) -> p s t d", d=HD)).then_inc(S["paired_set"], 1)
            for u in range(NU):
                dve.wait_ge(S["tr"], u + 1)
                dve.tensor_copy(raw_t[:, :, u * P:(u + 1) * P], ps[:, u, :].rearrange("p (s t) -> p s t", t=P)).then_inc(S["copied"], 1)
            dve.wait_ge(S["out_mm"], 1)
            dve.tensor_copy(kv[:].rearrange("p s c -> p (s c)"), ps[0:NB, 6, 0:256]).then_inc(S["kv_set"], 1)
            dve.drain()
            dve.tensor_tensor(sq[:], kv[:, 0], kv[:, 0], ALU.mult)
            dve.drain()
            dve.tensor_reduce(ssq[:], sq[:].rearrange("p (g d) -> p g d", g=2), AX.X, ALU.add)
            dve.drain()
            dve.tensor_scalar(ssq[:], ssq[:], 1.0 / HD, EPS, ALU.mult, ALU.add).then_inc(S["var_set"], 1)
            dve.wait_ge(S["root"], 1)
            dve.reciprocal(ssq[:], ssq[:])
            dve.drain()
            for g in range(2):
                k = kv[:, 0, g * HD:(g + 1) * HD]
                last = dve.scalar_tensor_tensor(out=k, in0=k, scalar=ssq[:, g:g + 1], in1=k_norm[0:NB], op0=ALU.mult, op1=ALU.mult)
            last.then_inc(S["kv_set"], 1)
            dve.wait_ge(S["kt_tr"], 1)
            dve.tensor_copy(kt[:], ps[:, 0, 0:NB]).then_inc(S["kt_copied"], 1)


def prompt_attention_stage(nc, heads_t, qkv, tok, strips, kt_cmp, v_cmp, flip_in, ident_in, out_rows):
    NT = TP // P
    NB = TP // CMP_STRIDE - 1
    LEAST = -3.4e38
    TW = 1920
    with ExitStack() as ctx:
        new_sem = ctx.enter_context(stage_semaphores(nc))
        sb = lambda name, shape: ctx.enter_context(nc.sbuf_tensor("pa_" + name, shape, F32))
        sb_r = lambda name, shape: ctx.enter_context(nc.sbuf_tensor("pa_" + name, shape, R32))
        q_t, q_s = sb("q_t", [P, 2, TP]), sb_r("q_s", [P, 2, TP])
        (ks_t, ks_lo), ks_hi = overlaid(nc, ctx, "pa_ks_t", [P, 2, TP]), sb_r("ks_hi", [P, 2, TP])
        (kw_t, kw_lo), kw_hi = overlaid(nc, ctx, "pa_kw_t", [P, 2, TP]), sb_r("kw_hi", [P, 2, TP])
        (kc_t, kc_lo), kc_hi = overlaid(nc, ctx, "pa_kc_t", [P, 2, NB + 1]), sb_r("kc_hi", [P, 2, NB + 1])
        v_all = sb("v_all", [P, 3, NT, P])
        vc = sb("vc", [NB, P])
        flip = sb("flip", [P, P])
        ident = sb("ident", [P, P])
        strip = sb("strip", [P, 2, TW])
        strip_w = sb("strip_w", [P, 2, P])
        table = sb("table", [P, TW])
        far_w = sb("far_w", [P, P])
        s_sel = sb("s_sel", [P, 2, TP])
        s_win = sb("s_win", [P, 2, 5 * P + NB])
        p_sel = sb("p_sel", [P, NT, P])
        p_win = sb("p_win", [P, 6, P])
        gates = sb("gates", [P, NT, 3, NH])
        any_cmp = sb("any_cmp", [P, 1])
        cols = sb("cols", [P, 2, 24])
        out = sb("out", [P, 2, NT, HD])
        ps = ctx.enter_context(nc.psum_tensor("pa_ps", [P, 8, BANK], F32))
        S = {n: new_sem("pa_" + n) for n in
             ("const_in gate_exp gates_set strip_used flip_mm table_set sel_mm win_mm sel_neg win_neg exp_done pt_tr pt_copied o_mm o_read tile_set passed anyc k_zero k_hi k_split q_hi q_split").split()}
        out_stored = [new_sem(f"pa_out_stored{n}") for n in range(2)]
        head_in = [new_sem(f"pa_head_in{n}") for n in range(2)]
        block = ctx.enter_context(nc.Block())
        FAR = TW % BANK
        N_CONST = 16 * (3 + 6 * NG + 3)
        NTB = 4

        def win_first(i):
            return max(0, i - 4)

        def p_all(n, k, rows):
            return p_sel[0:rows, k] if k < NT else p_win[0:rows, k - NT]

        base_chunk = [0]
        n_tiles = []
        for h in range(NH):
            for i in range(NT):
                n_tiles.append(i + 1 + (i - win_first(i) + 1) + 1)
                base_chunk.append(base_chunk[-1] + (n_tiles[-1] + 3) // 4)

        @block.sync
        def _(sp):
            consts = [(flip[:], flip_in), (ident[:], ident_in), (vc[:], v_cmp)]
            halves = (slice(0, HD), slice(HD, P))
            for g in range(NG):
                for half in halves:
                    consts += [(ks_t[half, g], heads_t[4 * P + g * HD:4 * P + (g + 1) * HD, 0:TP]), (kw_t[half, g], heads_t[5 * P + g * HD:5 * P + (g + 1) * HD, 0:TP]),
                               (kc_t[half, g, 0:NB], kt_cmp[g * HD:(g + 1) * HD, :])]
            consts += [(v_all[:, 0], qkv[0:TP, 512 + 384:512 + 512].rearrange("(n p) c -> p n c", p=P)),
                       (v_all[:, 1], qkv[0:TP, 1024 + 128:1024 + 256].rearrange("(n p) c -> p n c", p=P)),
                       (gates[:].rearrange("p n a h -> p n (a h)"), tok[0:TP, C_NGATE:C_NGATE + 24].rearrange("(n p) c -> p n c", p=P))]
            for dst, src in consts:
                sp.dma_start(dst, src).then_inc(S["const_in"], 16)
            for h in range(NH):
                if h >= 2:
                    sp.wait_ge(S["tile_set"], NT * (h - 1))
                for half in halves:
                    sp.dma_start(q_t[half, h % 2], heads_t[h * HD:(h + 1) * HD, 0:TP]).then_inc(head_in[h % 2], 16)
                sp.dma_start(strip[:, h % 2], bass.AP(tensor=strips.tensor, offset=strips[0, h, 0:1].offset, ap=[[1, P], [1, TW]])).then_inc(head_in[h % 2], 16)
                sp.dma_start(strip_w[:, h % 2], bass.AP(tensor=strips.tensor, offset=strips[1, h, 384:385].offset, ap=[[1, P], [1, P]])).then_inc(head_in[h % 2], 16)

        @block.gpsimd
        def _(pool):
            pool.memset(kc_t[:, :, NB:NB + 1], 0.0).then_inc(S["k_zero"], 1)
            pool.memset(any_cmp[:], 1.0).then_inc(S["anyc"], 1)
            pool.wait_ge(S["anyc"], 1)
            pool.affine_select(out=any_cmp[:], in_=any_cmp[:], compare_op=ALU.is_ge, fill=0.0, base=-(CMP_LEN - 1), pattern=[[0, 1]], channel_multiplier=1).then_inc(S["anyc"], 1)
            for h in range(NH):
                pool.wait_ge(S["tile_set"], NT * (h + 1))
                pool.dma_start(out_rows[:, h * HD:(h + 1) * HD].rearrange("(n p) d -> p n d", p=P), out[:, h % 2]).then_inc(out_stored[h % 2], 16)
            for x in range(2):
                pool.wait_ge(out_stored[x], 16 * (NH // 2))

        @block.tensor
        def _(pe):
            pe.wait_ge(S["const_in"], N_CONST)

            def scores(h, i):
                g, q = h // NR, q_s[:, h % 2, i * P:(i + 1) * P]
                n = h * NT + i
                if n >= 1:
                    pe.wait_ge(S["sel_neg"], n)
                    pe.wait_ge(S["win_neg"], n)
                hi = (i + 1) * P
                for a in range(0, hi, BANK):
                    z = min(a + BANK, hi)
                    pe.matmul(ps[:, a // BANK, 0:z - a], q, ks_lo[:, g, a:z], start=True, stop=False)
                    last = pe.matmul(ps[:, a // BANK, 0:z - a], q, ks_hi[:, g, a:z], start=False, stop=True)
                last.then_inc(S["sel_mm"], 1)
                w0 = win_first(i) * P
                nw = hi - w0
                m = min(nw, BANK)
                pe.matmul(ps[:, 2, 0:m], q, kw_lo[:, g, w0:w0 + m], start=True, stop=False)
                pe.matmul(ps[:, 2, 0:m], q, kw_hi[:, g, w0:w0 + m], start=False, stop=True)
                if nw > BANK:
                    pe.matmul(ps[:, 3, 0:nw - BANK], q, kw_lo[:, g, w0 + BANK:hi], start=True, stop=False)
                    pe.matmul(ps[:, 3, 0:nw - BANK], q, kw_hi[:, g, w0 + BANK:hi], start=False, stop=True)
                pe.matmul(ps[:, 3, P:P + NB + 1], q, kc_lo[:, g], start=True, stop=False)
                pe.matmul(ps[:, 3, P:P + NB + 1], q, kc_hi[:, g], start=False, stop=True).then_inc(S["win_mm"], 1)

            def values(h, i):
                g = h // NR
                n = h * NT + i
                pe.wait_ge(S["exp_done"], 3 * (n + 1))
                tiles = [("s", k) for k in range(i + 1)] + [("w", k) for k in range(i - win_first(i) + 1)] + [("c", 0)]
                for c in range(0, len(tiles), 4):
                    m = base_chunk[n] + c // 4
                    if m >= 3:
                        pe.wait_ge(S["pt_copied"], m - 2)
                    for x, (kind, k) in enumerate(tiles[c:c + 4]):
                        if kind == "s":
                            src, w = s_sel[:, n % 2, k * P:(k + 1) * P], P
                        elif kind == "w":
                            src, w = s_win[:, n % 2, k * P:(k + 1) * P], P
                        else:
                            src, w = s_win[:, n % 2, 5 * P:5 * P + NB], NB
                        last = pe.transpose(ps[0:w, 4 + m % 3, x * P:(x + 1) * P], src, ident[:])
                    last.then_inc(S["pt_tr"], 1)
                if n >= 1:
                    pe.wait_ge(S["tile_set"], n)

                def copied(x):
                    if x % 4 == 0:
                        pe.wait_ge(S["pt_copied"], base_chunk[n] + x // 4 + 1)

                for k in range(i + 1):
                    copied(k)
                    pe.matmul(ps[:, 7, 0:HD], p_all(n, k, P), v_all[:, 0, k, g * HD:(g + 1) * HD], start=(k == 0), stop=(k == i))
                w0 = win_first(i)
                for k in range(w0, i + 1):
                    copied(i + 1 + k - w0)
                    pe.matmul(ps[:, 7, HD:2 * HD], p_all(n, i + 1 + k - w0, P), v_all[:, 1, k, g * HD:(g + 1) * HD], start=(k == w0), stop=(k == i))
                copied(len(tiles) - 1)
                pe.matmul(ps[:, 7, 2 * HD:3 * HD], p_all(n, len(tiles) - 1, NB), vc[:, g * HD:(g + 1) * HD], start=True, stop=True).then_inc(S["o_mm"], 1)

            for h in range(NH):
                pe.wait_ge(head_in[h % 2], 64 * (h // 2 + 1))
                for n in range(NTB):
                    a, z = n * BANK, min((n + 1) * BANK, TW)
                    if h >= 1:
                        pe.wait_ge(S["sel_neg"], NT * h)
                        pe.wait_ge(S["win_neg"], NT * h)
                    pe.matmul(ps[:, n, 0:z - a], flip[:], strip[:, h % 2, a:z], start=True, stop=True)
                pe.matmul(ps[:, NTB - 1, FAR:FAR + P], flip[:], strip_w[:, h % 2], start=True, stop=True).then_inc(S["flip_mm"], 1)
                pe.wait_ge(S["table_set"], h + 1)
                pe.wait_ge(S["k_split"], 3)
                pe.wait_ge(S["q_split"], h + 1)
                for i in range(NT):
                    scores(h, i)
                    if h or i:
                        values(*divmod(h * NT + i - 1, NT))
            values(NH - 1, NT - 1)

        @block.scalar
        def _(act):
            act.wait_ge(S["const_in"], N_CONST)
            act.activation(gates[:], gates[:], ACT.Exp, scale=-1.0).then_inc(S["gate_exp"], 1)
            act.wait_ge(S["k_zero"], 1)
            for k_hi, k_t in ((ks_hi, ks_t), (kw_hi, kw_t), (kc_hi, kc_t)):
                act.activation(k_hi[:], k_t[:], ACT.Copy).then_inc(S["k_hi"], 1)

            def queries_hi(h):
                act.wait_ge(head_in[h % 2], 64 * (h // 2 + 1))
                act.activation(q_s[:, h % 2], q_t[:, h % 2], ACT.Copy).then_inc(S["q_hi"], 1)

            queries_hi(0)

            def copy_probs(n):
                nt = n_tiles[n]
                for k0 in range(0, nt, 4):
                    m = base_chunk[n] + k0 // 4
                    act.wait_ge(S["pt_tr"], m + 1)
                    if k0 == 0 and n >= 1:
                        act.wait_ge(S["o_mm"], n)
                    k1 = min(k0 + 4, nt)
                    for a, z, dst in ((k0, min(k1, NT), p_sel), (max(k0, NT), k1, p_win)):
                        for a_, z_, rows in ((a, min(z, nt - 1), P), (max(a, nt - 1), z, NB)):
                            if z_ > a_:
                                base = 0 if dst is p_sel else NT
                                last = act.activation(dst[0:rows, a_ - base:z_ - base], ps[0:rows, 4 + m % 3, (a_ - k0) * P:(z_ - k0) * P].rearrange("p (a b) -> p a b", b=P), ACT.Copy)
                    last.then_inc(S["pt_copied"], 1)

            for h in range(NH):
                for i in range(NT):
                    n = h * NT + i
                    hi = (i + 1) * P
                    nw = hi - win_first(i) * P
                    c = cols[:, n % 2]
                    if n >= 1:
                        copy_probs(n - 1)
                    if i == NT // 2 and h + 1 < NH:
                        queries_hi(h + 1)
                    act.wait_ge(S["sel_neg"], n + 1)
                    act.activation(s_sel[:, n % 2, 0:hi], s_sel[:, n % 2, 0:hi], ACT.Exp, bias=c[:, 0:1], accum_out=c[:, 5:6]).then_inc(S["exp_done"], 1)
                    act.wait_ge(S["win_neg"], n + 1)
                    act.activation(s_win[:, n % 2, 0:nw], s_win[:, n % 2, 0:nw], ACT.Exp, bias=c[:, 1:2], accum_out=c[:, 6:7]).then_inc(S["exp_done"], 1)
                    act.activation(s_win[:, n % 2, 5 * P:5 * P + NB], s_win[:, n % 2, 5 * P:5 * P + NB], ACT.Exp, bias=c[:, 2:3], accum_out=c[:, 4:5]).then_inc(S["exp_done"], 1)
            copy_probs(NH * NT - 1)

        @block.vector
        def _(dve):
            dve.wait_ge(S["gate_exp"], 1)
            dve.tensor_scalar(gates[:], gates[:], 1.0, None, ALU.add)
            dve.drain()
            dve.reciprocal(gates[:], gates[:])
            dve.wait_ge(S["anyc"], 2)
            dve.drain()
            dve.tensor_scalar(gates[:, 0, 0], gates[:, 0, 0], any_cmp[:], None, ALU.mult)
            for n, (k_lo, k_t, k_hi) in enumerate(((ks_lo, ks_t, ks_hi), (kw_lo, kw_t, kw_hi), (kc_lo, kc_t, kc_hi))):
                dve.wait_ge(S["k_hi"], n + 1)
                dve.tensor_tensor(k_lo[:], k_t[:], k_hi[:], ALU.subtract).then_inc(S["k_split"], 1)

            def queries_lo(h):
                dve.wait_ge(S["q_hi"], h + 1)
                q = q_s[HD:P, h % 2]
                dve.tensor_tensor(q, q_t[HD:P, h % 2], q, ALU.subtract).then_inc(S["q_split"], 1)

            queries_lo(0)

            def add_and_max(out, scores, bias, greatest):
                dve.tensor_tensor_reduce(out, scores, bias, 1.0, LEAST, ALU.add, ALU.max, greatest)

            def bias_and_max(h, i):
                n = h * NT + i
                hi = (i + 1) * P
                c = cols[:, n % 2]
                s, w = s_sel[:, n % 2], s_win[:, n % 2]
                off = (NT - 1) * P - i * P
                dve.wait_ge(S["sel_mm"], n + 1)
                if n >= 2:
                    dve.wait_ge(S["pt_tr"], base_chunk[n - 1])
                for a in range(0, hi, BANK):
                    z = min(a + BANK, hi)
                    add_and_max(s[:, a:z], ps[:, a // BANK, 0:z - a], table[:, off + a:off + z], c[:, 16 + a // BANK:17 + a // BANK])
                dve.drain()
                dve.tensor_scalar(c[:, 0:1], c[:, 16:17], c[:, 17:18] if hi > BANK else c[:, 16:17], -1.0, ALU.max, ALU.mult).then_inc(S["sel_neg"], 1)
                dve.wait_ge(S["win_mm"], n + 1)
                w0 = win_first(i) * P
                nw = hi - w0
                m = min(nw, BANK)
                if nw > BANK:
                    add_and_max(w[:, 0:P], ps[:, 2, 0:P], far_w[:], c[:, 20:21])
                    add_and_max(w[:, P:m], ps[:, 2, P:m], table[:, off + w0 + P:off + w0 + m], c[:, 21:22])
                    add_and_max(w[:, m:nw], ps[:, 3, 0:nw - BANK], table[:, off + w0 + m:off + hi], c[:, 22:23])
                else:
                    add_and_max(w[:, 0:m], ps[:, 2, 0:m], table[:, off + w0:off + hi], c[:, 18:19])
                c0 = off + CMP_LEN - 1
                add_and_max(w[:, 5 * P:5 * P + NB], ps[:, 3, P:P + NB], table[:, c0:c0 + CMP_STRIDE * (NB - 1) + 1:CMP_STRIDE], c[:, 19:20])
                dve.drain()
                if nw > BANK:
                    dve.tensor_reduce(c[:, 18:19], c[:, 20:23], AX.X, ALU.max)
                    dve.drain()
                dve.tensor_scalar(c[:, 1:3], c[:, 18:20], -1.0, None, ALU.mult).then_inc(S["win_neg"], 1)

            def finish(h, i):
                n = h * NT + i
                c = cols[:, n % 2]
                dve.wait_ge(S["exp_done"], 3 * (n + 1))
                dve.reciprocal(c[:, 12:15], c[:, 4:7])
                dve.drain()
                dve.tensor_tensor(c[:, 12:15], c[:, 12:15], gates[:, i, :, h], ALU.mult)
                dve.drain()
                dve.wait_ge(S["o_mm"], n + 1)
                if i == 0 and h >= 2:
                    dve.wait_ge(out_stored[h % 2], 16 * (h // 2))
                o = out[:, h % 2, i]
                dve.tensor_scalar(o, ps[:, 7, 0:HD], c[:, 13:14], None, ALU.mult)
                dve.drain()
                dve.scalar_tensor_tensor(out=o, in0=ps[:, 7, HD:2 * HD], scalar=c[:, 14:15], in1=o, op0=ALU.mult, op1=ALU.add)
                dve.drain()
                dve.scalar_tensor_tensor(out=o, in0=ps[:, 7, 2 * HD:3 * HD], scalar=c[:, 12:13], in1=o, op0=ALU.mult, op1=ALU.add).then_inc(S["tile_set"], 1)

            for h in range(NH):
                dve.wait_ge(S["flip_mm"], h + 1)
                for n in range(NTB):
                    a, z = n * BANK, min((n + 1) * BANK, TW)
                    dve.tensor_copy(table[:, a:z], ps[:, n, 0:z - a])
                dve.tensor_copy(far_w[:], ps[:, NTB - 1, FAR:FAR + P])
                dve.drain().then_inc(S["table_set"], 1)
                for i in range(NT):
                    bias_and_max(h, i)
                    if h or i:
                        finish(*divmod(h * NT + i - 1, NT))
                    if i == NT // 2 + 1 and h + 1 < NH:
                        queries_lo(h + 1)
            finish(NH - 1, NT - 1)


HC = 8
LB_FLOOR = 1e-30


def hgrn_stage(nc, feat, tok, x_lo, x_hi, w_gates, lb_logits, out_gain, state_in, diag_in, ident_in, own_in, out_t, state_p, state_s):
    NHG = 4
    NTL = TP // P
    NBK = P // HC
    NBT = T // HC
    with ExitStack() as ctx:
        new_sem = ctx.enter_context(stage_semaphores(nc))
        sb = lambda name, shape: ctx.enter_context(nc.sbuf_tensor("hg_" + name, shape, F32))
        raw = sb("raw", [P, 3, T])
        v = sb("v", [P, NTL + 1, P])
        state0 = sb("state0", [P, SB, P])
        f = sb("f", [P, T])
        k = sb("k", [P, T])
        q = sb("q", [P, T])
        gate = sb("gate", [P, T])
        sig = sb("sig", [P, 2, T])
        decay = sb("decay", [P, T])
        q_dec = sb("q_dec", [P, T])
        q_tile = sb("q_tile", [P, TP])
        before = sb("before", [P, NTL, NBK + 1])
        kb = sb("kb", [P, 2, T])
        kt = sb("kt", [P, 2, TP])
        attn = sb("attn", [P, NTL + 1, P])
        k_rows = sb("k_rows", [P, NTL + 1, P])
        v_own = sb("v_own", [SB * ST, SB, P])
        states = sb("states", [P, NTL + 1, P])
        s_new = sb("s_new", [P, SB, P])
        o = sb("o", [P, T])
        rstd = sb("rstd", [P, T])
        lb = sb("lb", [P, 6, NHG])
        gain = sb("gain", [P, 1])
        diag = sb("diag", [P, P])
        ident = sb("ident", [P, P])
        own = sb("own", [SB * ST, SB])
        ones = sb("ones", [P, P])
        ps = ctx.enter_context(nc.psum_tensor("hg_ps", [P, 8, BANK], F32))
        ahead = "sig_used o_copied o_mm raw_used s_new_set v_own_set".split()
        gw, gw_lo = overlaid(nc, ctx, "hg_gw", [P, 2, KD, P])
        gw_hi = ctx.enter_context(nc.sbuf_tensor("hg_gw_hi", [P, 2, KD, P], R32))
        g_stage = sb("g_stage", [P, 2, T])
        CHUNKS = 3 * KD // NHG
        gw_in, g_out = [new_sem("hg_gw_in0"), new_sem("hg_gw_in1")], [new_sem("hg_g_out0"), new_sem("hg_g_out1")]
        gw_split, g_mm, g_copied = new_sem("hg_gw_split"), new_sem("hg_g_mm", 6), new_sem("hg_g_copied", 3)
        g_free = new_sem("hg_g_free", 2)
        S = {n: new_sem("hg_" + n, 1 if n in ahead else 0) for n in
             ("const_in ones_set lb_sub lb_exp lb_set raw_in v_in state_in sig_done1 sig_done2 sig_used raw_used kb_set diag_mm kt_set off_mm attn_set "
              "tr rows_copied u_mm states_set o_mm o_copied sq_done ssq_mm var_set root out_set stored state_stored passed k_end v_own_set s_new_set").split()}
        block = ctx.enter_context(nc.Block())
        blocks = lambda t: t.rearrange("p (b j) -> p b j", j=HC)
        AT_START = 5

        @block.sync
        def _(sp):
            for dst, src in ((lb[:, 0], lb_logits), (gain[:], out_gain), (ident[:], ident_in)):
                sp.dma_start(dst, src).then_inc(S["const_in"], 16)
            sp.dma_start(diag[:], diag_in).then_inc(S["stored"], 16)
            sp.dma_start(own[:], own_in).then_inc(S["state_stored"], 16)

            def load_gate_weights(h, m):
                sp.wait_ge(g_mm, h * (3 * CHUNKS) + (3 * (m + 1)))
                sp.sem_inc(S["passed"], 1)
                sp.dma_start(gw[:, m % 2], w_gates[h * CHUNKS + m]).then_inc(gw_in[m % 2], 16)

            def head(h, more):
                sp.wait_ge(S["raw_used"], h * 3 + 1)
                sp.sem_inc(S["passed"], 1)
                for n, row in enumerate((R_HQ, R_HF, R_HG)):
                    sp.dma_start(raw[:, n], feat[bass.ds(h * P + row, P), :]).then_inc(S["raw_in"], 16)
                sp.wait_ge(S["o_mm"], h + 1)
                sp.sem_inc(S["passed"], 1)
                sp.wait_ge(S["v_own_set"], h + 1)
                sp.sem_inc(S["passed"], 1)
                sp.dma_start(v[:, 0:NTL], tok[0:TP, bass.ds(h * P + C_HI, P)].rearrange("(n p) c -> p n c", p=P)).then_inc(S["v_in"], 16)
                sp.dma_start(v[0:SB * ST, NTL], tok[TP:T, bass.ds(h * P + C_HI, P)]).then_inc(S["v_in"], 16)
                sp.wait_ge(S["s_new_set"], h + 1)
                sp.sem_inc(S["passed"], 1)
                sp.dma_start(state0[:], state_in[:, bass.ds(h, 1)].rearrange("b o d v -> (o d) b v")).then_inc(S["state_in"], 16)
                for m in range(1, CHUNKS + more):
                    load_gate_weights(h, m)

            load_gate_weights(0, 0)
            with sp.Fori(0, NHG - 1) as h:
                head(h, 1)
            head(NHG - 1, 0)
            sp.wait_ge(S["stored"], 16 * (NHG + 1))
            sp.wait_ge(S["state_stored"], 16 * (2 * NHG + 1))

        @block.gpsimd
        def _(pool):
            pool.memset(ones[:], 1.0).then_inc(S["ones_set"], 1)

            def split_weights(h, m):
                s = m % 2
                pool.wait_ge(gw_in[s], h * (16 * CHUNKS // 2) + 16 * (m // 2 + 1))
                pool.sem_inc(S["passed"], 1)
                pool.tensor_copy(gw_hi[:, s], gw[:, s])
                pool.drain()
                pool.tensor_tensor(gw_lo[:, s], gw[:, s], gw_hi[:, s], ALU.subtract).then_inc(gw_split, 1)

            def head(h, more):
                for m in range(CHUNKS):
                    s = m % 2
                    if m + 1 < CHUNKS + more:
                        split_weights(h, m + 1)
                    pool.wait_ge(g_copied, h * (3 * CHUNKS) + (3 * m + 6))
                    pool.dma_start(feat[bass.ds(h * (CHUNKS * P) + (R_GATES + m * P), P), :], g_stage[:, s]).then_inc(g_out[s], 16)
                    pool.wait_ge(g_out[s], h * (16 * CHUNKS // 2) + 16 * (m // 2 + 1))
                    pool.sem_inc(g_free, 1)

            split_weights(0, 0)
            with pool.Fori(0, NHG - 1) as h:
                head(h, 1)
            head(NHG - 1, 0)

        @block.scalar
        def _(act):
            act.wait_ge(S["lb_sub"], 1)
            act.activation(lb[:, 1], lb[:, 1], ACT.Exp).then_inc(S["lb_exp"], 1)

            def copy_gates(h, first, last):
                for m, c in (divmod(n, 3) for n in range(first, last)):
                    s, (a, z) = m % 2, THIRDS[c]
                    if c == 0:
                        act.wait_ge(g_free, h * CHUNKS + (m + 1))
                    act.wait_ge(g_mm, h * (3 * CHUNKS) + (3 * m + c + 7))
                    act.activation(g_stage[:, s, a:z], ps[:, 5 + c, 0:z - a], ACT.Copy).then_inc(g_copied, 1)

            with act.Fori(0, NHG) as h:
                act.wait_ge(S["raw_in"], (h + 1) * 48)
                act.wait_ge(S["sig_used"], h * 4 + 1)
                act.activation(sig[:, 0], raw[:, 1], ACT.Sigmoid).then_inc(S["sig_done1"], 1)
                act.activation(sig[:, 1], raw[:, 1], ACT.Sigmoid, scale=-1.0).then_inc(S["sig_done1"], 1)
                act.wait_ge(S["sig_used"], h * 4 + 2)
                act.activation(sig[:, 0], raw[:, 0], ACT.Sigmoid).then_inc(S["sig_done2"], 1)
                act.wait_ge(S["sig_used"], h * 4 + 3)
                act.activation(sig[:, 1], raw[:, 2], ACT.Sigmoid).then_inc(S["sig_done2"], 1)
                copy_gates(h, 0, AT_START + 9)
                for n in range(3):
                    act.wait_ge(S["tr"], h * 3 + (n + 1))
                    if n < 2:
                        act.activation(k_rows[:, 4 * n:4 * n + 4].rearrange("p a d -> p (a d)"), ps[:, n, :], ACT.Copy).then_inc(S["rows_copied"], 1)
                    else:
                        act.activation(k_rows[0:SB * ST, NTL], ps[0:SB * ST, 2, 0:P], ACT.Copy).then_inc(S["rows_copied"], 1)
                copy_gates(h, AT_START + 9, 3 * CHUNKS - 1)
                act.wait_ge(S["o_mm"], h + 2)
                for n, (a, z) in enumerate(COLS):
                    act.activation(rstd[:, a:z], ps[:, n, 0:z - a], ACT.Square).then_inc(S["sq_done"], 1)
                act.wait_ge(S["var_set"], h + 1)
                act.activation(rstd[:], rstd[:], ACT.Sqrt).then_inc(S["root"], 1)
                copy_gates(h, 3 * CHUNKS - 1, 3 * CHUNKS)
                act.wait_ge(S["s_new_set"], h + 2)
                act.dma_start(state_p[bass.ds(h, 1)].rearrange("o d v -> (o d) v"), states[:, NTL]).then_inc(S["state_stored"], 16)
                act.dma_start(state_s[:, bass.ds(h, 1)].rearrange("b o d v -> (o d) b v"), s_new[:]).then_inc(S["state_stored"], 16)
                act.wait_ge(S["out_set"], h + 1)
                act.dma_start(out_t[bass.ds(h * P, P), :], o[:]).then_inc(S["stored"], 16)

        @block.tensor
        def _(pe):
            pe.wait_ge(S["const_in"], 48)
            pe.wait_ge(S["ones_set"], 1)


            def gate_pieces(h, first, last):
                for m, c in (divmod(n, 3) for n in range(first, last)):
                    s, (a, z) = m % 2, THIRDS[c]
                    if c == 0:
                        pe.wait_ge(gw_split, h * CHUNKS + (m + 1))
                    pe.wait_ge(g_copied, h * (3 * CHUNKS) + (3 * m + c + 1))
                    for k in range(KD):
                        done = split_product(pe, ps[:, 5 + c, 0:z - a], gw_hi[:, s, k], gw_lo[:, s, k], x_hi[:, k, a:z], x_lo[:, k, a:z], k == 0, k == KD - 1)
                    done.then_inc(g_mm, 1)

            with pe.Fori(0, NHG) as h:
                gate_pieces(h, 0, AT_START)
                pe.wait_ge(S["o_copied"], h + 1)
                for j in range(HC):
                    pe.wait_ge(S["kb_set"], h * HC + (j + 1))
                    for t, (t0, tn) in enumerate(TILES):
                        last = pe.matmul(ps[0:tn, t // 4, (t % 4) * P + j:(t % 4) * P + tn - HC + j + 1:HC], kb[:, j % 2, t0:t0 + tn],
                                         q[:, t0 + j:t0 + tn - HC + j + 1:HC], start=True, stop=True)
                    last.then_inc(S["diag_mm"], 1)
                    if j % 2:
                        gate_pieces(h, AT_START + j // 2, AT_START + j // 2 + 1)
                for i in range(1, NBK):
                    pe.wait_ge(S["kt_set"], h * NBK + i)
                    for t in range(NTL):
                        last = pe.matmul(ps[:, 3 + t // 4, (t % 4) * P + i * HC:(t % 4) * P + (i + 1) * HC], kt[:, i % 2, t * P:(t + 1) * P],
                                         q_dec[:, t * P + i * HC:t * P + (i + 1) * HC], start=True, stop=True)
                    last.then_inc(S["off_mm"], 1)
                    if i % 3 == 0:
                        gate_pieces(h, AT_START + 3 + i // 3, AT_START + 4 + i // 3)
                pe.wait_ge(S["kt_set"], h * NBK + NBK)
                pe.wait_ge(S["attn_set"], h + 1)
                for t in range(NTL):
                    last = pe.transpose(ps[:, t // 4, (t % 4) * P:(t % 4 + 1) * P], kt[:, NBK % 2, t * P:(t + 1) * P], ident[:])
                    if t % 4 == 3:
                        last.then_inc(S["tr"], 1)
                pe.transpose(ps[0:SB * ST, 2, 0:P], kb[:, (HC - 1) % 2, TP:T], ident[:]).then_inc(S["tr"], 1)
                gate_pieces(h, AT_START + 9, AT_START + 10)
                pe.wait_ge(S["rows_copied"], h * 3 + 3)
                pe.wait_ge(S["v_in"], h * 32 + 32)
                for t in range(NTL):
                    pe.matmul(ps[:, 3 + t // 4, (t % 4) * P:(t % 4 + 1) * P], k_rows[:, t], v[:, t], start=True, stop=True)
                pe.wait_ge(S["v_own_set"], h + 2)
                for n in range(2):
                    last = pe.matmul(ps[:, n, :], k_rows[0:SB * ST, NTL], v_own[:, 4 * n:4 * n + 4].rearrange("p b v -> p (b v)"), start=True, stop=True)
                last.then_inc(S["u_mm"], 1)
                gate_pieces(h, AT_START + 10, 3 * CHUNKS - 1)
                pe.wait_ge(S["s_new_set"], h + 2)
                pe.wait_ge(S["states_set"], h + 1)
                pe.wait_ge(S["state_in"], h * 16 + 16)
                for t in range(NTL):
                    dst = ps[:, t // 4, (t % 4) * P:(t % 4 + 1) * P]
                    pe.matmul(dst, v[:, t], attn[:, t], start=True, stop=(t == 0))
                    if t:
                        pe.matmul(dst, states[:, t], q_tile[:, t * P:(t + 1) * P], start=False, stop=True)
                for b in range(SB):
                    dst = ps[:, 2, b * ST:(b + 1) * ST]
                    pe.matmul(dst, v[0:SB * ST, NTL], attn[0:SB * ST, NTL, b * ST:(b + 1) * ST], start=True, stop=False)
                    last = pe.matmul(dst, state0[:, b], q_dec[:, TP + b * ST:TP + (b + 1) * ST], start=False, stop=True)
                last.then_inc(S["o_mm"], 1)
                pe.wait_ge(S["sq_done"], h * 3 + 3)
                pe.wait_ge(S["o_copied"], h + 2)
                for n, (a, z) in enumerate(COLS):
                    last = pe.matmul(ps[:, (3, 4, 2)[n], 0:z - a], ones[:], rstd[:, a:z], start=True, stop=True)
                last.then_inc(S["ssq_mm"], 1)
                gate_pieces(h, 3 * CHUNKS - 1, 3 * CHUNKS)

        @block.vector
        def _(dve):
            dve.wait_ge(S["const_in"], 48)
            dve.wait_ge(S["stored"], 16)
            dve.wait_ge(S["state_stored"], 16)
            dve.tensor_tensor(lb[:, 1], lb[:, 0], lb[:, 0], ALU.subtract).then_inc(S["lb_sub"], 1)
            dve.wait_ge(S["lb_exp"], 1)
            dve.reciprocal(lb[:, 2], lb[:, 1])
            dve.drain()
            dve.tensor_tensor(lb[:, 2], lb[:, 1], lb[:, 2], ALU.mult)
            dve.drain()
            dve.tensor_tensor(lb[:, 3], lb[:, 2], lb[:, 2], ALU.subtract)
            dve.drain()
            dve.tensor_scalar(lb[:, 4], lb[:, 3], LB_FLOOR, None, ALU.max)
            dve.tensor_scalar(lb[:, 5], lb[:, 3], -1.0, 1.0, ALU.mult, ALU.add)
            dve.drain()
            f8, k8, q8, d8, qd8 = blocks(f[:]), blocks(k[:]), blocks(q[:]), blocks(decay[:]), blocks(q_dec[:])
            with dve.Fori(0, NHG) as h:
                floor, rest = lb[:, 4, bass.ds(h, 1)], lb[:, 5, bass.ds(h, 1)]
                dve.wait_ge(S["sig_done1"], h * 2 + 2)
                dve.tensor_scalar(f[:], sig[:, 0], rest, floor, ALU.mult, ALU.add).then_inc(S["sig_used"], 1)
                dve.tensor_scalar(k[:], sig[:, 1], rest, None, ALU.mult).then_inc(S["sig_used"], 1)
                dve.wait_ge(S["sig_done2"], h * 2 + 2)
                dve.tensor_tensor(q[:], sig[:, 0], raw[:, 0], ALU.mult).then_inc(S["sig_used"], 1)
                dve.tensor_tensor(gate[:], sig[:, 1], raw[:, 2], ALU.mult).then_inc(S["sig_used"], 1)
                dve.drain().then_inc(S["raw_used"], 3)
                dve.memset(kb[:], 0.0)
                dve.memset(kt[:], 0.0)
                dve.tensor_copy(d8[:, :, 0], f8[:, :, 0])
                dve.drain()
                for j in range(HC):
                    new, old = blocks(kb[:, j % 2]), blocks(kb[:, 1 - j % 2])
                    if j >= 2:
                        dve.wait_ge(S["diag_mm"], h * HC + (j - 1))
                    if j:
                        dve.tensor_tensor(new[:, :, 0:j], old[:, :, 0:j], f8[:, :, j:j + 1].to_broadcast([P, NBT, j]), ALU.mult)
                        dve.tensor_tensor(d8[:, :, j], d8[:, :, j - 1], f8[:, :, j], ALU.mult)
                    dve.tensor_copy(new[:, :, j], k8[:, :, j])
                    dve.drain().then_inc(S["kb_set"], 1)
                dve.tensor_tensor(q_dec[:], q[:], decay[:], ALU.mult)
                dve.memset(before[:, :, 0:1], 1.0)
                dve.drain()
                ends = d8[:, 0:TP // HC, HC - 1].rearrange("p (t b) -> p t b", b=NBK)
                kb_end = kb[:, (HC - 1) % 2, 0:TP].rearrange("p (t s) -> p t s", s=P)
                for i in range(1, NBK + 1):
                    new, old = (kt[:, x].rearrange("p (t s) -> p t s", s=P) for x in (i % 2, 1 - i % 2))
                    if i >= 3:
                        dve.wait_ge(S["off_mm"], h * (NBK - 1) + (i - 2))
                    n = (i - 1) * HC
                    if n:
                        dve.tensor_tensor(new[:, :, 0:n], old[:, :, 0:n], ends[:, :, i - 1:i].to_broadcast([P, NTL, n]), ALU.mult)
                    dve.tensor_tensor(before[:, :, i], before[:, :, i - 1], ends[:, :, i - 1], ALU.mult)
                    dve.tensor_copy(new[:, :, n:n + HC], kb_end[:, :, n:n + HC])
                    dve.drain().then_inc(S["kt_set"], 1)
                dve.tensor_tensor(q_tile[:].rearrange("p (t b j) -> p t b j", b=NBK, j=HC), q_dec[:, 0:TP].rearrange("p (t b j) -> p t b j", b=NBK, j=HC),
                                  before[:, :, 0:NBK].unsqueeze(3).to_broadcast([P, NTL, NBK, HC]), ALU.mult)
                dve.wait_ge(S["v_in"], h * 32 + 32)
                dve.tensor_tensor(v_own[:], v[0:SB * ST, NTL:NTL + 1].to_broadcast([SB * ST, SB, P]), own[:].unsqueeze(2).to_broadcast([SB * ST, SB, P]), ALU.mult).then_inc(S["v_own_set"], 1)
                dve.wait_ge(S["diag_mm"], h * HC + HC)
                dve.wait_ge(S["off_mm"], h * (NBK - 1) + (NBK - 1))
                for n in range(2):
                    dve.tensor_tensor(attn[:, 4 * n:4 * n + 4], ps[:, n, :].rearrange("p (t s) -> p t s", s=P), diag[:].unsqueeze(1).to_broadcast([P, 4, P]), ALU.mult)
                dve.tensor_tensor(attn[0:SB * ST, NTL, 0:SB * ST], ps[0:SB * ST, 2, 0:SB * ST], diag[0:SB * ST, 0:SB * ST], ALU.mult)
                dve.drain()
                for n in range(2):
                    a = attn[:, 4 * n:4 * n + 4, HC:P]
                    dve.tensor_tensor(a, a, ps[:, 3 + n, :].rearrange("p (t s) -> p t s", s=P)[:, :, HC:P], ALU.add)
                dve.memset(states[:, 0], 0.0)
                dve.drain().then_inc(S["attn_set"], 1)
                dve.wait_ge(S["u_mm"], h + 1)
                dve.wait_ge(S["state_in"], h * 16 + 16)
                dve.wait_ge(S["state_stored"], h * 32 + 16)
                for t in range(NTL):
                    dve.scalar_tensor_tensor(out=states[:, t + 1], in0=states[:, t], scalar=before[:, t, NBK:NBK + 1], in1=ps[:, 3 + t // 4, (t % 4) * P:(t % 4 + 1) * P],
                                             op0=ALU.mult, op1=ALU.add)
                    dve.drain()
                dve.sem_inc(S["states_set"], 1)
                dve.tensor_tensor(s_new[:], state0[:], d8[:, TP // HC:NBT, HC - 1:HC].to_broadcast([P, SB, P]), ALU.mult)
                dve.drain()
                for n in range(2):
                    last = dve.tensor_tensor(s_new[:, 4 * n:4 * n + 4], s_new[:, 4 * n:4 * n + 4], ps[:, n, :].rearrange("p (b v) -> p b v", v=P), ALU.add)
                last.then_inc(S["s_new_set"], 1)
                dve.wait_ge(S["o_mm"], h + 2)
                dve.wait_ge(S["sq_done"], h * 3 + 3)
                dve.wait_ge(S["stored"], h * 16 + 16)
                for n, (a, z) in enumerate(COLS):
                    dve.scalar_tensor_tensor(out=o[:, a:z], in0=ps[:, n, 0:z - a], scalar=gain[:], in1=gate[:, a:z], op0=ALU.mult, op1=ALU.mult)
                dve.drain().then_inc(S["o_copied"], 1)
                dve.wait_ge(S["ssq_mm"], h + 1)
                for n, (a, z) in enumerate(COLS):
                    last = dve.tensor_scalar(rstd[:, a:z], ps[:, (3, 4, 2)[n], 0:z - a], 1.0 / P, EPS, ALU.mult, ALU.add)
                last.then_inc(S["var_set"], 1)
                dve.wait_ge(S["root"], h + 1)
                dve.reciprocal(rstd[:], rstd[:])
                dve.drain()
                dve.tensor_tensor(o[:], o[:], rstd[:], ALU.mult).then_inc(S["out_set"], 1)


SC = 8
NCH = TP // SC
NCA = T // SC
NGR, GW, NST = 32, 16, 64
NPR = NGR // 2
TWO_PI = 6.283185307179586
TWO_PI_HI = 6.28125
ROUND = 12582912.0


def s5_state_stage(nc, tok, a_re, a_im, log_dt, b_in, c_in, d_in, h0_in, ident_in, rows_out, h_prompt, h_sample):
    with ExitStack() as ctx:
        new_sem = ctx.enter_context(stage_semaphores(nc))
        sb = lambda name, shape: ctx.enter_context(nc.sbuf_tensor("ss_" + name, shape, F32))
        u = sb("u", [P, NGR, NCA])
        rows = sb("rows", [P, SC, 512])
        by_group = sb("by_group", [P, NGR, P])
        small = sb("small", [P, NGR * P])
        toep = sb("toep", [P, NGR, P])
        w_t = sb("w_t", [P, NPR, 2, P])
        w_h = sb("w_h", [P, 2, NPR, NCA])
        ca = sb("ca", [P, 2, NPR, (SC + 1) * GW])
        x = sb("x", [P, 2, NPR, NCA])
        turn = sb("turn", [P, 2, NPR, NCH])
        m0 = sb("m0", [P, NPR, NCH])
        tmp = sb("tmp", [P, 2, NPR, NCH])
        par = sb("par", [P, 24, NPR])
        pw = sb("pw", [P, 2, SC + 1, NPR])
        bb = sb("bb", [P, 2, NPR, GW])
        b_raw = sb("b_raw", [P, 2, NPR, GW])
        c_raw = sb("c_raw", [P, 2, NPR, GW])
        dcol = sb("dcol", [P, NGR])
        ident = sb("ident", [P, P])
        h_end_p = sb("h_end_p", [P, 2, NPR, 1])
        h_end_s = sb("h_end_s", [P, 2, NPR, SB])
        ps = ctx.enter_context(nc.psum_tensor("ss_ps", [P, 8, BANK], F32))
        S = {n: new_sem("ss_" + n) for n in
             ("par_in rows_in grouped grouped_s u_tr u_copied step_set exp_in exp_done sin_in sin_done w_set wt_tr wt_copied ca_set k_mm k_copied k_read toep_zero toep_in "
              "x_mm x_copied h_set y_mm y_sum gelu y_tr y_copied rows_used stored h_stored").split()}
        block = ctx.enter_context(nc.Block())
        ARE, AIM, LDT, STEP, MAG, COS, SIN, MAG8, TH, R_, N_, A_, B_, C_, D_, E_, ZR, ZI, DEN, CS8, SN8 = range(21)
        p = lambda i: par[:, i]
        batches = [(a, min(a + 3, NGR)) for a in range(0, NGR, 3)]
        pair_batches = [(a, min(a + 3, NPR)) for a in range(0, NPR, 3)]
        small_rows = small[32:32 + SB].rearrange("p (s c) -> p s c", s=SC)
        small_group = small[64:64 + SB].rearrange("p (g c) -> p g c", g=NGR)
        taps = small[0:GW].rearrange("p (g c) -> p g c", g=NGR)

        y_batches = [list(range(6 * n + q, min(6 * n + 6, NGR), 2)) for n in range(6) for q in range(2)]
        y_batch_of = {g: n for n, gs in enumerate(y_batches) for g in gs}

        @block.sync
        def _(sp):
            sp.dma_start(rows[:], tok[0:TP, 0:512].rearrange("(c s) n -> c s n", s=SC)).then_inc(S["rows_in"], 16)
            sp.dma_start(small_rows, tok[TP:T, 0:512].rearrange("(c s) n -> c s n", s=SC)).then_inc(S["rows_in"], 16)
            for dst, src in ((par[:, ARE], a_re), (par[:, AIM], a_im), (par[:, LDT], log_dt), (b_raw[:], b_in), (c_raw[:], c_in), (dcol[:], d_in), (ident[:], ident_in),
                             (w_h[:, :, :, NCH:NCA], h0_in)):
                sp.dma_start(dst, src).then_inc(S["par_in"], 16)
            sp.wait_ge(S["k_copied"], 8)
            sp.wait_ge(S["toep_zero"], 1)
            for s in range(SC):
                sp.dma_start(toep[s * GW:(s + 1) * GW, :, s * GW:P], taps[:, :, 0:P - s * GW]).then_inc(S["toep_in"], 16)
            sp.wait_ge(S["h_set"], 1)
            sp.dma_start(h_prompt, h_end_p[:]).then_inc(S["h_stored"], 16)
            sp.dma_start(h_sample, h_end_s[:]).then_inc(S["h_stored"], 16)
            sp.wait_ge(S["y_copied"], 16)
            sp.dma_start(rows_out[0:TP].rearrange("(c s) n -> c s n", s=SC), rows[:]).then_inc(S["stored"], 16)
            sp.dma_start(rows_out[TP:T].rearrange("(c s) n -> c s n", s=SC), small_rows).then_inc(S["stored"], 16)
            sp.wait_ge(S["stored"], 32)
            sp.wait_ge(S["h_stored"], 32)

        @block.gpsimd
        def _(pool):
            pool.memset(toep[:], 0.0).then_inc(S["toep_zero"], 1)
            pool.wait_ge(S["toep_zero"], 1)
            pool.wait_ge(S["rows_in"], 32)
            pool.tensor_copy(small_group.rearrange("p g (s n) -> p g s n", n=GW), small_rows.rearrange("p s (g n) -> p g s n", n=GW)).then_inc(S["grouped_s"], 1)

        @block.scalar
        def _(act):
            act.wait_ge(S["par_in"], 128)
            act.activation(p(STEP), p(LDT), ACT.Exp).then_inc(S["step_set"], 1)
            act.wait_ge(S["exp_in"], 1)
            act.activation(p(MAG), p(A_), ACT.Exp).then_inc(S["exp_done"], 1)
            act.activation(p(MAG8), p(A_), ACT.Exp, scale=float(SC)).then_inc(S["exp_done"], 1)
            act.wait_ge(S["sin_in"], 1)
            act.activation(p(SIN), p(R_), ACT.Sin)
            act.activation(p(COS), p(N_), ACT.Sin).then_inc(S["sin_done"], 1)
            for n, (a, z) in enumerate(batches):
                act.wait_ge(S["u_tr"], n + 1)
                act.activation(u[:, a:z].rearrange("p g c -> p (g c)"), ps[:, n % 2, 0:(z - a) * NCA], ACT.Copy).then_inc(S["u_copied"], 1)
            for n in range(8):
                act.wait_ge(S["wt_tr"], n + 1)
                act.activation(w_t[:, 2 * n:2 * n + 2].rearrange("p a r s -> p (a r s)"), ps[:, 2 + n % 2, :], ACT.Copy).then_inc(S["wt_copied"], 1)
            for n in range(8):
                act.wait_ge(S["k_mm"], n + 1)
                if n == 0:
                    act.wait_ge(S["u_copied"], len(batches))
                g0 = 8 * (n // 2) + n % 2
                act.activation(taps[:, g0:g0 + 7:2], ps[0:GW, 4 + n % 2, :].rearrange("p (g c) -> p g c", c=P), ACT.Copy).then_inc(S["k_copied"], 1)
            for n, gs in enumerate(y_batches):
                act.wait_ge(S["y_sum"], n + 1)
                y = u[:, gs[0]:gs[-1] + 1:2]
                act.activation(y, y, ACT.Gelu_apprx_tanh).then_inc(S["gelu"], 1)

        @block.tensor
        def _(pe):
            pe.wait_ge(S["par_in"], 128)
            pe.wait_ge(S["grouped_s"], 1)
            for n, (a, z) in enumerate(batches):
                pe.wait_ge(S["grouped"], min((z - 1) // 8 + 1, 4))
                if n >= 2:
                    pe.wait_ge(S["u_copied"], n - 1)
                for g in range(a, z):
                    o = (g - a) * NCA
                    pe.transpose(ps[:, n % 2, o:o + NCH], by_group[:, g], ident[:])
                    last = pe.transpose(ps[:, n % 2, o + NCH:o + NCA], small_group[:, g], ident[64:64 + SB, 64:64 + SB])
                last.then_inc(S["u_tr"], 1)
            pe.wait_ge(S["w_set"], 1)
            for n in range(8):
                if n >= 2:
                    pe.wait_ge(S["wt_copied"], n - 1)
                for k in range(4):
                    last = pe.transpose(ps[:, 2 + n % 2, k * P:(k + 1) * P], w_h[:, k % 2, 2 * n + k // 2, 0:P], ident[:])
                last.then_inc(S["wt_tr"], 1)
            pe.wait_ge(S["ca_set"], 1)
            for n in range(8):
                if n >= 2:
                    pe.wait_ge(S["k_copied"], n - 1)
                for k in range(4):
                    g = 8 * (n // 2) + 2 * k + n % 2
                    r = slice(NST * (g % 2), NST * (g % 2) + NST)
                    for c in range(2):
                        last = pe.matmul(ps[0:GW, 4 + n % 2, k * P:(k + 1) * P], bb[r, c, g // 2], ca[r, c, g // 2, 0:P], start=(c == 0), stop=(c == 1))
                last.then_inc(S["k_mm"], 1)
            pe.wait_ge(S["wt_copied"], 8)
            pe.wait_ge(S["u_copied"], len(batches))
            for n, (a, z) in enumerate(pair_batches):
                for c in range(2):
                    m = 2 * n + c
                    if m >= 2:
                        pe.wait_ge(S["x_copied"], m - 1)
                    for pr in range(a, z):
                        for g2 in range(2):
                            last = pe.matmul(ps[NST * g2:NST * (g2 + 1), 6 + c, (pr - a) * NCA:(pr - a + 1) * NCA], w_t[:, pr, c, NST * g2:NST * (g2 + 1)], u[:, 2 * pr + g2], start=True, stop=True)
                    last.then_inc(S["x_mm"], 1)
            pe.wait_ge(S["toep_in"], 16 * SC)
            pe.wait_ge(S["h_set"], 1)
            for n, gs in enumerate(y_batches):
                if n >= 2:
                    pe.wait_ge(S["y_sum"], n - 1)
                for k, g in enumerate(gs):
                    r = slice(NST * (g % 2), NST * (g % 2) + NST)
                    dst = ps[:, n % 2, k * NCA:(k + 1) * NCA]
                    pe.matmul(dst, toep[:, g], u[:, g], start=True, stop=False)
                    pe.matmul(dst, ca[r, 0, g // 2, GW:], w_h[r, 0, g // 2], start=False, stop=False)
                    last = pe.matmul(dst, ca[r, 1, g // 2, GW:], w_h[r, 1, g // 2], start=False, stop=True)
                last.then_inc(S["y_mm"], 1)
            for n in range(8):
                pe.wait_ge(S["gelu"], max(y_batch_of[g] for g in range(4 * n, 4 * n + 4)) + 1)
                if n >= 2:
                    pe.wait_ge(S["y_copied"], 2 * (n - 1))
                for k in range(4):
                    pe.transpose(ps[:, 2 + n % 2, k * P:(k + 1) * P], u[:, 4 * n + k, 0:NCH], ident[:])
                    last = pe.transpose(ps[0:SB, 4 + n % 2, k * P:(k + 1) * P], u[:, 4 * n + k, NCH:NCA], ident[:])
                last.then_inc(S["y_tr"], 1)

        @block.vector
        def _(dve):
            tt, ts = dve.tensor_tensor, dve.tensor_scalar
            MUL, ADD, SUB = ALU.mult, ALU.add, ALU.subtract

            def cmul(out_r, out_i, xr, xi, yr, yi, t1, t2, conj=False):
                tt(t1, xi, yi, MUL)
                tt(t2, xr, yi, MUL)
                dve.drain()
                tt(out_r, xr, yr, MUL)
                tt(out_i, xi, yr, MUL)
                dve.drain()
                tt(out_r, out_r, t1, ADD if conj else SUB)
                tt(out_i, out_i, t2, SUB if conj else ADD)
                dve.drain()

            dve.wait_ge(S["rows_in"], 32)
            for n in range(4):
                dve.tensor_copy(by_group[:, 8 * n:8 * n + 8].rearrange("p g (s n) -> p g s n", n=GW),
                                rows[:, :, n * P:(n + 1) * P].rearrange("p s (g n) -> p g s n", n=GW)).then_inc(S["grouped"], 1)
            dve.wait_ge(S["par_in"], 128)
            dve.wait_ge(S["step_set"], 1)
            tt(p(A_), p(ARE), p(STEP), MUL)
            tt(p(TH), p(AIM), p(STEP), MUL)
            dve.drain().then_inc(S["exp_in"], 1)
            ts(p(B_), p(TH), 1.0 / TWO_PI, None, MUL)
            ts(p(C_), p(TH), 1.0 / TWO_PI, 0.25, MUL, ADD)
            dve.drain()
            for src, dst, quarter in ((B_, R_, 0.0), (C_, N_, TWO_PI / 4)):
                ts(p(D_), p(src), ROUND, None, ADD)
                dve.drain()
                ts(p(D_), p(D_), ROUND, None, SUB)
                dve.drain()
                dve.scalar_tensor_tensor(out=p(E_), in0=p(D_), scalar=-TWO_PI_HI, in1=p(TH), op0=MUL, op1=ADD)
                dve.drain()
                dve.scalar_tensor_tensor(out=p(E_), in0=p(D_), scalar=-(TWO_PI - TWO_PI_HI), in1=p(E_), op0=MUL, op1=ADD)
                dve.drain()
                ts(p(E_), p(E_), quarter, 3.1415925, ADD, ALU.min)
                dve.drain()
                ts(p(dst), p(E_), -3.1415925, None, ALU.max)
                dve.drain()
            dve.sem_inc(S["sin_in"], 1)
            dve.wait_ge(S["exp_done"], 2)
            dve.wait_ge(S["sin_done"], 1)
            dve.memset(pw[:, 0, 0], 1.0)
            dve.memset(pw[:, 1, 0], 0.0)
            tt(pw[:, 0, 1], p(MAG), p(COS), MUL)
            tt(pw[:, 1, 1], p(MAG), p(SIN), MUL)
            dve.drain()
            for k in range(2, SC + 1):
                cmul(pw[:, 0, k], pw[:, 1, k], pw[:, 0, k - 1], pw[:, 1, k - 1], pw[:, 0, 1], pw[:, 1, 1], p(A_), p(B_))
            ts(p(A_), pw[:, 0, 1], -1.0, None, ADD)
            tt(p(DEN), p(ARE), p(ARE), MUL)
            tt(p(B_), p(AIM), p(AIM), MUL)
            dve.drain()
            tt(p(DEN), p(DEN), p(B_), ADD)
            dve.drain()
            dve.reciprocal(p(DEN), p(DEN))
            cmul(p(ZR), p(ZI), p(A_), pw[:, 1, 1], p(ARE), p(AIM), p(C_), p(D_), conj=True)
            tt(p(ZR), p(ZR), p(DEN), MUL)
            tt(p(ZI), p(ZI), p(DEN), MUL)
            dve.drain()
            wide = lambda t, n=GW: t.unsqueeze(2).to_broadcast([P, NPR, n])
            t1, t2 = tmp[:, 0, :, 0:GW], tmp[:, 1, :, 0:GW]
            cmul(bb[:, 0], bb[:, 1], b_raw[:, 0], b_raw[:, 1], wide(p(ZR)), wide(p(ZI)), t1, t2)
            for s in range(SC):
                k = SC - 1 - s
                cmul(w_h[:, 0, :, s * GW:(s + 1) * GW], w_h[:, 1, :, s * GW:(s + 1) * GW], bb[:, 0], bb[:, 1], wide(pw[:, 0, k]), wide(pw[:, 1, k]), t1, t2)
            dve.sem_inc(S["w_set"], 1)
            for k in range(SC + 1):
                cmul(ca[:, 0, :, k * GW:(k + 1) * GW], ca[:, 1, :, k * GW:(k + 1) * GW], c_raw[:, 0], c_raw[:, 1], wide(pw[:, 0, k]), wide(pw[:, 1, k]), t1, t2)
            ts(ca[:, 1], ca[:, 1], -1.0, None, MUL)
            dve.drain()
            dve.sem_inc(S["ca_set"], 1)
            tt(p(CS8), p(COS), p(COS), MUL)
            for n in range(3):
                c, s = (p(COS), p(SIN)) if n == 0 else (p(CS8), p(SN8))
                tt(p(A_), c, c, MUL)
                tt(p(B_), s, s, MUL)
                tt(p(C_), c, s, MUL)
                dve.drain()
                tt(p(CS8), p(A_), p(B_), SUB)
                ts(p(SN8), p(C_), 2.0, None, MUL)
                dve.drain()
            dve.tensor_copy(turn[:, 0, :, 0], p(CS8))
            dve.tensor_copy(turn[:, 1, :, 0], p(SN8))
            dve.memset(m0[:], 0.0)
            dve.drain()
            n = 1
            while n < NCH:
                cmul(turn[:, 0, :, n:2 * n], turn[:, 1, :, n:2 * n], turn[:, 0, :, 0:n], turn[:, 1, :, 0:n],
                     turn[:, 0, :, n - 1:n].to_broadcast([P, NPR, n]), turn[:, 1, :, n - 1:n].to_broadcast([P, NPR, n]), tmp[:, 0, :, 0:n], tmp[:, 1, :, 0:n])
                n *= 2
            tt(tmp[:, 0], turn[:, 0], turn[:, 0], MUL)
            tt(tmp[:, 1], turn[:, 1], turn[:, 1], MUL)
            dve.drain()
            tt(tmp[:, 0], tmp[:, 0], tmp[:, 1], ADD)
            dve.drain()
            ts(tmp[:, 0], tmp[:, 0], -0.5, 1.5, MUL, ADD)
            dve.drain()
            tt(turn[:, 0], turn[:, 0], tmp[:, 0], MUL)
            tt(turn[:, 1], turn[:, 1], tmp[:, 0], MUL)
            tt(m0[:, :, 1:], m0[:, :, 1:], p(MAG8).unsqueeze(2).to_broadcast([P, NPR, NCH - 1]), ADD)
            dve.drain()
            for n, (a, z) in enumerate(pair_batches):
                for c in range(2):
                    dve.wait_ge(S["x_mm"], 2 * n + c + 1)
                    dve.tensor_copy(x[:, c, a:z].rearrange("p g c -> p (g c)"), ps[:, 6 + c, 0:(z - a) * NCA]).then_inc(S["x_copied"], 1)
            dve.drain()
            xr, xi = x[:, 0, :, 0:NCH], x[:, 1, :, 0:NCH]
            dve.wait_ge(S["wt_tr"], 8)
            hr, hi = w_h[:, 0, :, 0:NCH], w_h[:, 1, :, 0:NCH]
            cmul(tmp[:, 0], tmp[:, 1], xr, xi, turn[:, 0], turn[:, 1], hr, hi, conj=True)
            for c in range(2):
                flat = tmp[:, c].rearrange("p g c -> p (g c)")
                dve.tensor_tensor_scan(flat, m0[:].rearrange("p g c -> p (g c)"), flat, 0.0, MUL, ADD)
            dve.drain()
            cmul(xr, xi, tmp[:, 0], tmp[:, 1], turn[:, 0], turn[:, 1], hr, hi)
            for c in range(2):
                dve.tensor_copy(w_h[:, c, :, 1:NCH], x[:, c, :, 0:NCH - 1])
                dve.memset(w_h[:, c, :, 0:1], 0.0)
                dve.tensor_copy(h_end_p[:, c], x[:, c, :, NCH - 1:NCH])
            s0r, s0i = w_h[:, 0, :, NCH:NCA], w_h[:, 1, :, NCH:NCA]
            cmul(h_end_s[:, 0], h_end_s[:, 1], s0r, s0i, wide(pw[:, 0, SC], SB), wide(pw[:, 1, SC], SB), tmp[:, 0, :, 0:SB], tmp[:, 1, :, 0:SB])
            for c in range(2):
                tt(h_end_s[:, c], h_end_s[:, c], x[:, c, :, NCH:NCA], ADD)
            dve.drain().then_inc(S["h_set"], 1)
            for n, gs in enumerate(y_batches):
                dve.wait_ge(S["y_mm"], n + 1)
                for k, g in enumerate(gs):
                    last = dve.scalar_tensor_tensor(out=u[:, g], in0=u[:, g], scalar=dcol[:, g:g + 1], in1=ps[:, n % 2, k * NCA:(k + 1) * NCA], op0=MUL, op1=ADD)
                last.then_inc(S["y_sum"], 1)
            for n in range(8):
                dve.wait_ge(S["y_tr"], n + 1)
                dve.tensor_copy(rows[:, :, n * HD:(n + 1) * HD].rearrange("p s (g n) -> p g s n", n=GW), ps[:, 2 + n % 2, :].rearrange("p (g s n) -> p g s n", s=SC, n=GW)).then_inc(S["y_copied"], 1)
                dve.tensor_copy(small_rows[:, :, n * HD:(n + 1) * HD].rearrange("p s (g n) -> p g s n", n=GW), ps[0:SB, 4 + n % 2, :].rearrange("p (g s n) -> p g s n", s=SC, n=GW)).then_inc(S["y_copied"], 1)


def s5_glu_stage(nc, rows_in, w_in, ident_in, out_t):
    NK = 4
    with ExitStack() as ctx:
        new_sem = ctx.enter_context(stage_semaphores(nc))
        sb = lambda name, shape: ctx.enter_context(nc.sbuf_tensor("gl_" + name, shape, F32))
        rows = sb("rows", [P, len(TILES), 512])
        y = sb("y", [P, NK, T])
        w = sb("w", [P, NK, 512])
        ident = sb("ident", [P, P])
        gate = sb("gate", [P, NK, T])
        ps = ctx.enter_context(nc.psum_tensor("gl_ps", [P, 8, BANK], F32))
        S = {n: new_sem("gl_" + n) for n in "w_in rows_in tr copied mm sig out_set stored".split()}
        block = ctx.enter_context(nc.Block())
        NTL = len(TILES)

        @block.sync
        def _(sp):
            sp.dma_start(rows[:, 0:TP // P], rows_in[0:TP].rearrange("(n p) c -> p n c", p=P)).then_inc(S["rows_in"], 16)
            sp.dma_start(rows[0:T - TP, TP // P], rows_in[TP:T]).then_inc(S["rows_in"], 16)
            sp.dma_start(ident[:], ident_in).then_inc(S["rows_in"], 16)
            sp.dma_start(w[:], w_in.rearrange("(k p) n -> p k n", p=P)).then_inc(S["w_in"], 16)
            for n in range(NK):
                sp.wait_ge(S["out_set"], n + 1)
                sp.dma_start(out_t[n * P:(n + 1) * P], gate[:, n]).then_inc(S["stored"], 16)
            sp.wait_ge(S["stored"], 16 * NK)

        @block.tensor
        def _(pe):
            pe.wait_ge(S["rows_in"], 48)
            for t, (t0, tn) in enumerate(TILES):
                if t >= 2:
                    pe.wait_ge(S["copied"], t - 1)
                for k in range(NK):
                    last = pe.transpose(ps[:, t % 2, k * P:k * P + tn], rows[0:tn, t, k * P:(k + 1) * P], ident[0:tn, 0:tn])
                last.then_inc(S["tr"], 1)
            pe.wait_ge(S["copied"], NTL)
            pe.wait_ge(S["w_in"], 16)
            for n in range(NK):
                if n >= 2:
                    pe.wait_ge(S["sig"], 3 * (n - 1))
                for c, (a, z) in enumerate(COLS):
                    for k in range(NK):
                        last = pe.matmul(ps[:, 2 + 3 * (n % 2) + c, 0:z - a], w[:, k, n * P:(n + 1) * P], y[:, k, a:z], start=(k == 0), stop=(k == NK - 1))
                    last.then_inc(S["mm"], 1)

        @block.scalar
        def _(act):
            for n in range(NK):
                for c, (a, z) in enumerate(COLS):
                    act.wait_ge(S["mm"], 3 * n + c + 1)
                    act.activation(gate[:, n, a:z], ps[:, 2 + 3 * (n % 2) + c, 0:z - a], ACT.Sigmoid).then_inc(S["sig"], 1)

        @block.vector
        def _(dve):
            for t, (t0, tn) in enumerate(TILES):
                dve.wait_ge(S["tr"], t + 1)
                dve.tensor_copy(y[:, :, t0:t0 + tn], ps[:, t % 2, :].rearrange("p (k t) -> p k t", t=P)[:, :, 0:tn]).then_inc(S["copied"], 1)
            for n in range(NK):
                dve.wait_ge(S["sig"], 3 * n + 3)
                if n == 0:
                    dve.wait_ge(S["copied"], NTL)
                dve.tensor_tensor(gate[:, n], gate[:, n], y[:, n], ALU.mult).then_inc(S["out_set"], 1)


D_FF = 2816
KF = D_FF // P
KH = KF // 2


def trunk_stage(nc, x_t, feat, a_t, b_t, c_rows, c_t, w_branch, w_out, w_gu, w_down, g_ffn, ident_in, x1_t, y_t):
    with ExitStack() as ctx:
        new_sem = ctx.enter_context(stage_semaphores(nc))
        sb = lambda name, shape, dt=F32: ctx.enter_context(nc.sbuf_tensor("tr_" + name, shape, dt))
        sem = lambda name, ahead=0: new_sem("tr_" + name, ahead)
        act_in, act_in_r = overlaid(nc, ctx, "tr_act_in", [P, 2, KD, T])
        wide, wide_r = overlaid(nc, ctx, "tr_wide", [P, 24, T])
        w, w_lo = overlaid(nc, ctx, "tr_w", [P, 2, 12, P])
        w_hi = sb("w_hi", [P, 2, 12, P], R32)
        gain = sb("gain", [P, KD])
        ident = sb("ident", [P, P])
        ones = sb("ones", [P, P])
        ps = ctx.enter_context(nc.psum_tensor("tr_ps", [P, 8, BANK], F32))
        NTL = TP // P
        flat = lambda part: part.rearrange("p o t -> p (o t)")
        rows = flat(act_in[:, 0, 0:4])[:, 0:NTL * 512].rearrange("p (n c) -> p n c", c=512)
        merged = act_in[:, 0]
        side = lambda s: act_in[:, 1, 3 * s:3 * s + 3]
        normed, in_lo, in_hi = act_in[:, 0], act_in_r[:, 0], act_in_r[:, 1]
        branch, br_lo, br_hi = wide[:, 0:12], wide_r[:, 0:12], wide_r[:, 12:24]
        rstd, ssq, sq = wide[:, 20], wide[:, 21], wide[:, 22:24]
        hid_lo, hid_hi = wide_r[:, 0:KH], wide_r[:, KH:2 * KH]
        tmp, resid = wide[:, 22], wide[:, 22:24]

        MERGE, OUT = (0, KD // 2, 12), (KD, KD // 2, KD)
        UP = [(2 * KD + h * (KF + KD), KH, KD) for h in range(2)]
        DOWN = [(2 * KD + h * (KF + KD) + KF, KD // 2, KH) for h in range(2)]
        next_tiles = {MERGE: KD, OUT: KD, UP[0]: KH, DOWN[0]: KD, UP[1]: KH, DOWN[1]: 0}
        SETS_OUT, SETS_UP, SETS_HALF = 3 * KD // 2, 3 * KD // 2 + KD // 2, KH + KD // 2
        set_use = lambda s, h: SETS_UP + (1 if s == 0 else 0) + h * SETS_HALF

        def bank_parts(s, row):
            n = THIRDS[0][1]
            return ((ps[:, 3 * s:3 * s + 2, 0:n], row[:, 0:2 * n].rearrange("p (c t) -> p c t", t=n)),
                    (ps[:, 3 * s + 2, 0:T - 2 * n], row[:, 2 * n:T]))

        const_in, rows_in, c_in, br_in = sem("const_in"), sem("rows_in"), sem("c_in"), [sem("a_in"), sem("b_in")]
        ones_set, tr, tr_hi, tr_split, br_hi_set, br_split = (sem(n) for n in "ones_set tr tr_hi tr_split br_hi_set br_split".split())
        w_in, g_in = [sem("w_in0"), sem("w_in1")], [sem("g_in0"), sem("g_in1")]
        w_hi_set, w_split, mm, passed = sem("w_hi_set"), sem("w_split"), sem("mm", KD + 2), sem("passed")
        set_free = [sem("set_free0", 1), sem("set_free1", 1)]
        br_mm, sig, merged_set = sem("br_mm", 6), sem("sig"), sem("merged_set", 2)
        x_in, x1_out, squared, summed = sem("x_in"), sem("x1_out"), sem("squared"), sem("summed", 2)
        in_hi_set, in_split, in_set = sem("in_hi_set"), sem("in_split"), sem("in_set")
        var_mm, var_set, root = sem("var_mm"), sem("var_set"), sem("root")
        hid_set, hid_hi_set, hid_split = sem("hid_set"), sem("hid_hi_set"), sem("hid_split", 1)
        r_in, added, y_out = [sem("r_in0"), sem("r_in1")], sem("added"), [sem("y_out0"), sem("y_out1")]

        block = ctx.enter_context(nc.Block())

        @block.sync
        def _(sp):
            def load_weights(i, u0, s, src, merging=False):
                if merging:
                    sp.wait_ge(br_mm, i * 6 + 3 * (u0 + s + 1))
                else:
                    sp.wait_ge(mm, i * 2 + (u0 + s + 1))
                sp.sem_inc(passed, 1)
                sp.dma_start(w[:, s, 0:src.shape[-2]], src).then_inc(w_in[s], 16)

            for dst, src in ((rows, c_rows.rearrange("(n p) c -> p n c", p=P)), (ident[:], ident_in)):
                sp.dma_start(dst, src).then_inc(rows_in, 16)
            sp.dma_start(branch[:, 0:4], a_t.rearrange("(k p) t -> p k t", p=P)).then_inc(br_in[0], 16)
            u0, pairs, _ = MERGE
            for s in range(2):
                load_weights(0, u0, s, w_branch[s], True)
            sp.dma_start(branch[:, 4:8], b_t.rearrange("(k p) t -> p k t", p=P)).then_inc(br_in[1], 16)
            sp.dma_start(branch[:, 8:12, TP:T], c_t.rearrange("(k p) t -> p k t", p=P)[:, :, TP:T]).then_inc(c_in, 16)
            sp.dma_start(gain[:], g_ffn).then_inc(const_in, 16)
            for s in range(2):
                for b in range(3):
                    sp.dma_start(side(s)[:, b], feat[R_GATES + b * D + s * P:R_GATES + b * D + (s + 1) * P, :]).then_inc(g_in[s], 16)
            with sp.Fori(0, pairs - 1) as i:
                for s in range(2):
                    load_weights(i, u0 + 2, s, w_branch[i * 2 + (s + 2)], True)
                    sp.wait_ge(merged_set, i * 2 + (s + 3))
                    sp.sem_inc(passed, 1)
                    for b in range(3):
                        sp.dma_start(side(s)[:, b], feat[bass.ds(i * 256 + (R_GATES + b * D + (s + 2) * P), P), :]).then_inc(g_in[s], 16)
            u0, pairs, _ = OUT
            for s in range(2):
                load_weights(0, u0, s, w_out[s], True)
            sp.dma_start(wide[:, 0:KD], x_t).then_inc(x_in, 16)
            with sp.Fori(0, pairs - 1) as i:
                for s in range(2):
                    load_weights(i, u0 + 2, s, w_out[i * 2 + (s + 2)])
            for h in range(2):
                u0, pairs, _ = UP[h]
                with sp.Fori(0, pairs) as i:
                    for s in range(2):
                        load_weights(i, u0, s, w_gu[i + h * KH, :, s * KD:(s + 1) * KD])
                u0, pairs, _ = DOWN[h]
                for s in range(2):
                    load_weights(0, u0, s, w_down[s][:, h * KH:(h + 1) * KH])
                sp.wait_ge(hid_split, KH * (h + 1) + 1)
                sp.wait_ge(x1_out, 16 * KD)
                for s in range(2):
                    if h == 1:
                        sp.wait_ge(y_out[s], 16 * KD // 2)
                for s in range(2):
                    sp.dma_start(resid[:, s], x1_t[s * P:(s + 1) * P]).then_inc(r_in[s], 16)
                with sp.Fori(0, pairs - 1) as i:
                    for s in range(2):
                        load_weights(i, u0 + 2, s, w_down[i * 2 + (s + 2)][:, h * KH:(h + 1) * KH])
                        sp.wait_ge(y_out[s], i * 16 + (16 * (1 + h * KD // 2)))
                        sp.sem_inc(passed, 1)
                        sp.dma_start(resid[:, s], x1_t[bass.ds(i * 256 + (s + 2) * P, P), :]).then_inc(r_in[s], 16)

        @block.gpsimd
        def _(pool):
            pool.memset(ones[:], 1.0).then_inc(ones_set, 1)
            with pool.Fori(0, KD // 2) as i:
                for s in range(2):
                    pool.wait_ge(added, i * 2 + (s + 1))
                    pool.sem_inc(passed, 1)
                    pool.dma_start(x1_t[bass.ds(i * 256 + s * P, P), :], flat(wide[:, bass.ds(i * 2 + s, 1)])).then_inc(x1_out, 16)
            for k in range(KD):
                pool.wait_ge(in_hi_set, KD + k + 1)
                pool.tensor_tensor(in_lo[:, k], normed[:, k], in_hi[:, k], ALU.subtract).then_inc(in_split, 1)
            for h, dst in ((0, x1_t), (1, y_t)):
                with pool.Fori(0, KD // 2) as i:
                    for s in range(2):
                        pool.wait_ge(added, i * 2 + (KD * (h + 1) + s + 1))
                        pool.dma_start(dst[bass.ds(i * 256 + s * P, P), :], resid[:, s]).then_inc(y_out[s], 16)
            for s in range(2):
                pool.wait_ge(y_out[s], 16 * KD)

        @block.tensor
        def _(pe):
            def products(bs, ws, tiles, hi, lo, at_tile=None):
                for k, wk in enumerate(tiles):
                    if at_tile:
                        at_tile(k)
                    wh, wl = w_hi[:, ws, wk], w_lo[:, ws, wk]
                    for n, (wp, xp) in enumerate(((wl, hi), (wh, lo), (wh, hi))):
                        for c, (a, z) in enumerate(THIRDS):
                            last = pe.matmul(ps[:, 3 * bs + c, 0:z - a], wp, xp[:, k, a:z], start=(k == 0 and n == 0), stop=(k == len(tiles) - 1 and n == 2))
                return last

            pe.wait_ge(rows_in, 32)
            for t in range(NTL):
                if t >= 2:
                    pe.wait_ge(tr_split, t - 1)
                for k in range(4):
                    last = pe.transpose(ps[:, 6 + t % 2, k * P:(k + 1) * P], rows[:, t, k * P:(k + 1) * P], ident[:])
                last.then_inc(tr, 1)
            u0, pairs, _ = MERGE
            with pe.Fori(0, pairs) as i:
                for s in range(2):
                    pe.wait_ge(w_split, i * 2 + (u0 + s + 1))
                    for b in range(3):
                        pe.wait_ge(br_split, b + 1)
                        bs = (3 * s + b) % 2
                        pe.wait_ge(set_free[bs], i * 3 + ((3 * s + b) // 2 + 1))
                        products(bs, s, range(4 * b, 4 * b + 4), br_hi[:, 4 * b:4 * b + 4], br_lo[:, 4 * b:4 * b + 4]).then_inc(br_mm, 1)
            u0, pairs, n = OUT

            def out_unit(i, s, at_tile=None):
                pe.wait_ge(w_split, i * 2 + (u0 + s + 1))
                pe.wait_ge(set_free[s], i + (SETS_OUT + 1))
                products(s, s, range(n), in_hi, in_lo, at_tile).then_inc(mm, 1)

            out_unit(0, 0, lambda k: pe.wait_ge(in_split, k + 1))
            out_unit(0, 1)
            with pe.Fori(1, pairs) as i:
                for s in range(2):
                    out_unit(i, s)
            pe.wait_ge(ones_set, 1)
            pe.wait_ge(summed, KD + 2)
            pe.wait_ge(set_free[0], SETS_UP + 1)
            for c, (a, z) in enumerate(THIRDS):
                last = pe.matmul(ps[:, c, 0:z - a], ones[:], ssq[:, a:z], start=True, stop=True)
            last.then_inc(var_mm, 1)
            for h in range(2):
                u0, pairs, n = UP[h]

                def up_unit(i, s, at_tile=None):
                    pe.wait_ge(w_split, i * 2 + (u0 + s + 1))
                    pe.wait_ge(set_free[s], i + (set_use(s, h) + 1))
                    products(s, s, range(n), in_hi, in_lo, at_tile).then_inc(mm, 1)

                first = 0
                if h == 0:
                    up_unit(0, 0, lambda k: pe.wait_ge(in_split, KD + k + 1))
                    up_unit(0, 1)
                    first = 1
                with pe.Fori(first, pairs) as i:
                    for s in range(2):
                        up_unit(i, s)
                u0, pairs, n = DOWN[h]

                def down_unit(i, s, at_tile=None):
                    pe.wait_ge(w_split, i * 2 + (u0 + s + 1))
                    pe.wait_ge(set_free[s], i + (set_use(s, h) + KH + 1))
                    products(s, s, range(n), hid_hi, hid_lo, at_tile).then_inc(mm, 1)

                down_unit(0, 0, lambda k: pe.wait_ge(hid_split, h * KH + k + 2))
                down_unit(0, 1)
                with pe.Fori(1, pairs) as i:
                    for s in range(2):
                        down_unit(i, s)

        @block.scalar
        def _(act):
            def weights_hi(i, u0, s, n):
                act.wait_ge(w_in[s], i * 16 + (16 * (u0 // 2 + 1)))
                act.activation(w_hi[:, s, 0:n], w[:, s, 0:n], ACT.Copy).then_inc(w_hi_set, 1)

            for t in range(NTL):
                act.wait_ge(tr, t + 1)
                act.activation(br_hi[:, 8:12, t * P:(t + 1) * P], ps[:, 6 + t % 2, :].rearrange("p (k t) -> p k t", t=P), ACT.Copy).then_inc(tr_hi, 1)
            for b in range(2):
                act.wait_ge(br_in[b], 16)
                act.activation(br_hi[:, 4 * b:4 * b + 4], branch[:, 4 * b:4 * b + 4], ACT.Copy).then_inc(br_hi_set, 1)
                if b == 0:
                    for s in range(2):
                        weights_hi(0, 0, s, 12)
            act.wait_ge(c_in, 16)
            act.activation(br_hi[:, 8:12, TP:T], branch[:, 8:12, TP:T], ACT.Copy).then_inc(br_hi_set, 1)
            u0, pairs, n = MERGE
            for s in range(2):
                act.wait_ge(g_in[s], 48)
                act.activation(side(s), side(s), ACT.Sigmoid).then_inc(sig, 1)
            with act.Fori(0, pairs - 1) as i:
                for s in range(2):
                    weights_hi(i, u0 + 2, s, n)
                    act.wait_ge(g_in[s], i * 48 + 96)
                    act.activation(side(s), side(s), ACT.Sigmoid).then_inc(sig, 1)
            for s in range(2):
                weights_hi(0, OUT[0], s, KD)
            act.wait_ge(merged_set, KD + 2)
            for k in range(KD):
                act.activation(in_hi[:, k], merged[:, k], ACT.Copy).then_inc(in_hi_set, 1)
            u0, pairs, n = OUT

            def out_unit(i, s, n_next):
                act.wait_ge(summed, i * 2 + (s + 1))
                act.wait_ge(added, i * 2 + (s + 1))
                act.sem_inc(passed, 1)
                act.activation(sq[:, s], flat(wide[:, bass.ds(i * 2 + s, 1)]), ACT.Square).then_inc(squared, 1)
                weights_hi(i, u0 + 2, s, n_next)

            with act.Fori(0, pairs) as i:
                for s in range(2):
                    out_unit(i, s, n)
            act.wait_ge(var_set, 1)
            act.activation(rstd, rstd, ACT.Sqrt).then_inc(root, 1)
            for k in range(KD):
                act.wait_ge(in_set, k + 1)
                act.activation(in_hi[:, k], normed[:, k], ACT.Copy).then_inc(in_hi_set, 1)
            for h in range(2):
                u0, pairs, n = UP[h]
                if h == 1:
                    act.wait_ge(y_out[0], 16 * KD // 2)

                def up_chunk(i, n_next):
                    act.wait_ge(hid_split, i + (h * KH + 1))
                    act.wait_ge(mm, i * 2 + (u0 + 3))
                    act.sem_inc(passed, 1)
                    for banks, row in bank_parts(0, tmp):
                        last = act.activation(row, banks, ACT.Silu)
                    last.then_inc(set_free[0], 1)
                    weights_hi(i, u0 + 2, 0, n_next)
                    act.wait_ge(hid_set, i + (h * KH + 1))
                    act.sem_inc(passed, 1)
                    act.activation(flat(hid_hi[:, bass.ds(i, 1)]), tmp, ACT.Copy).then_inc(hid_hi_set, 1)
                    weights_hi(i, u0 + 2, 1, n_next)

                with act.Fori(0, pairs - 1) as i:
                    up_chunk(i, n)
                up_chunk(pairs - 1, next_tiles[UP[h]])
                u0, pairs, n = DOWN[h]
                with act.Fori(0, pairs - 1) as i:
                    for s in range(2):
                        weights_hi(i, u0 + 2, s, n)
                if h == 0:
                    for s in range(2):
                        weights_hi(0, UP[1][0], s, KD)

        @block.vector
        def _(dve):
            def weights_lo(i, u0, s, n):
                dve.wait_ge(w_hi_set, i * 2 + (u0 + s + 1))
                dve.tensor_tensor(w_lo[:, s, 0:n], w[:, s, 0:n], w_hi[:, s, 0:n], ALU.subtract).then_inc(w_split, 1)

            for t in range(NTL):
                dve.wait_ge(tr_hi, t + 1)
                dve.tensor_tensor(br_lo[:, 8:12, t * P:(t + 1) * P], ps[:, 6 + t % 2, :].rearrange("p (k t) -> p k t", t=P),
                                  br_hi[:, 8:12, t * P:(t + 1) * P], ALU.subtract).then_inc(tr_split, 1)
            for b in range(2):
                dve.wait_ge(br_hi_set, b + 1)
                dve.tensor_tensor(br_lo[:, 4 * b:4 * b + 4], branch[:, 4 * b:4 * b + 4], br_hi[:, 4 * b:4 * b + 4], ALU.subtract).then_inc(br_split, 1)
                if b == 0:
                    for s in range(2):
                        weights_lo(0, 0, s, 12)
            dve.wait_ge(br_hi_set, 3)
            dve.tensor_tensor(br_lo[:, 8:12, TP:T], branch[:, 8:12, TP:T], br_hi[:, 8:12, TP:T], ALU.subtract)
            dve.drain().then_inc(br_split, 1)

            u0, pairs, n = MERGE

            def merge_chunk(i, s, n_next):
                dve.wait_ge(sig, i * 2 + (s + 1))
                for b in range(3):
                    bs = (3 * s + b) % 2
                    dve.wait_ge(br_mm, i * 6 + (3 * s + b + 7))
                    for banks, row in bank_parts(bs, side(s)[:, b]):
                        last = dve.tensor_tensor(row, row, banks, ALU.mult)
                    last.then_inc(set_free[bs], 1)
                dve.drain()
                dve.tensor_tensor(side(s)[:, 0], side(s)[:, 0], side(s)[:, 1], ALU.add)
                dve.drain()
                dve.tensor_tensor(flat(merged[:, bass.ds(i * 2 + s, 1)]), side(s)[:, 0], side(s)[:, 2], ALU.add).then_inc(merged_set, 1)
                weights_lo(i, u0 + 2, s, n_next)

            with dve.Fori(0, pairs - 1) as i:
                for s in range(2):
                    merge_chunk(i, s, n)
            for s in range(2):
                merge_chunk(pairs - 1, s, next_tiles[MERGE])
            for k in range(KD):
                dve.wait_ge(in_hi_set, k + 1)
                dve.tensor_tensor(in_lo[:, k], merged[:, k], in_hi[:, k], ALU.subtract).then_inc(in_split, 1)

            u0, pairs, n = OUT
            dve.wait_ge(x_in, 16)
            dve.memset(ssq, 0.0)
            with dve.Fori(0, pairs) as i:
                for s in range(2):
                    dve.wait_ge(mm, i * 2 + (u0 + s + 3))
                    for banks, row in bank_parts(s, flat(wide[:, bass.ds(i * 2 + s, 1)])):
                        dve.tensor_tensor(row, row, banks, ALU.add)
                    dve.drain().then_inc(added, 1)
                    dve.sem_inc(set_free[s], 1)
                    dve.wait_ge(squared, i * 2 + (s + 1))
                    dve.tensor_tensor(ssq, ssq, sq[:, s], ALU.add)
                    dve.drain().then_inc(summed, 1)
                    weights_lo(i, u0 + 2, s, n)

            dve.wait_ge(var_mm, 1)
            for banks, row in bank_parts(0, rstd):
                dve.tensor_scalar(row, banks, 1.0 / D, EPS, ALU.mult, ALU.add)
            dve.drain().then_inc(var_set, 1)
            dve.sem_inc(set_free[0], 1)
            dve.wait_ge(root, 1)
            dve.reciprocal(rstd, rstd)
            dve.wait_ge(const_in, 16)
            dve.drain()
            for k in range(KD):
                dve.scalar_tensor_tensor(out=normed[:, k], in0=wide[:, k], scalar=gain[:, k:k + 1], in1=rstd, op0=ALU.mult, op1=ALU.mult).then_inc(in_set, 1)
            dve.wait_ge(x1_out, 16 * KD)
            for h in range(2):
                u0, pairs, n = UP[h]

                def up_chunk(i, n_next):
                    weights_lo(i, u0 + 2, 0, n_next)
                    dve.wait_ge(set_free[0], i + (set_use(0, h) + 2))
                    dve.wait_ge(mm, i * 2 + (u0 + 4))
                    for banks, row in bank_parts(1, tmp):
                        last = dve.tensor_tensor(row, row, banks, ALU.mult)
                    last.then_inc(set_free[1], 1)
                    dve.drain().then_inc(hid_set, 1)
                    dve.wait_ge(hid_hi_set, i + (h * KH + 1))
                    dve.tensor_tensor(flat(hid_lo[:, bass.ds(i, 1)]), tmp, flat(hid_hi[:, bass.ds(i, 1)]), ALU.subtract).then_inc(hid_split, 1)
                    weights_lo(i, u0 + 2, 1, n_next)

                with dve.Fori(0, pairs - 1) as i:
                    up_chunk(i, n)
                up_chunk(pairs - 1, next_tiles[UP[h]])

                u0, pairs, n = DOWN[h]

                def down_unit(i, s, n_next):
                    dve.wait_ge(r_in[s], i * 16 + (16 * (1 + h * KD // 2)))
                    dve.wait_ge(mm, i * 2 + (u0 + s + 3))
                    for banks, row in bank_parts(s, resid[:, s]):
                        last = dve.tensor_tensor(row, row, banks, ALU.add)
                    last.then_inc(set_free[s], 1)
                    dve.drain().then_inc(added, 1)
                    if n_next:
                        weights_lo(i, u0 + 2, s, n_next)

                with dve.Fori(0, pairs - 1) as i:
                    for s in range(2):
                        down_unit(i, s, n)
                for s in range(2):
                    down_unit(pairs - 1, s, next_tiles[DOWN[h]])


def build_program(nc, i, o):
    def scratch(name, *shape):
        return nc.dram_tensor(name, shape, F32, kind="Internal").ap()

    feat = scratch("proj_feat", R_GATES + 3 * D, T)
    tok = scratch("proj_tok", T, NTOK)
    qkv = scratch("qkv_rows", T, NQKV)
    heads_t = scratch("heads_t", 6 * P, T)
    strips = scratch("strips", 2, NH, STRIP)
    sample_t = scratch("sample_attn_t", 512, T)
    cmp_kt = scratch("cmp_kt", P, TP // CMP_STRIDE - 1)
    cmp_v = scratch("cmp_v", TP // CMP_STRIDE - 1, P)
    attn_rows = scratch("attn_rows", TP, 512)
    hgrn_t = scratch("hgrn_t", 512, T)
    s5_rows = scratch("s5_rows", T, 512)
    s5_t = scratch("s5_t", 512, T)
    x1_t = scratch("x1_t", D, T)

    with ExitStack() as ctx:
        x, x_lo = overlaid(nc, ctx, "tokens", [P, KD, T])
        x_hi = ctx.enter_context(nc.sbuf_tensor("tokens_hi", [P, KD, T], R32))
        norm_project_stage(nc, i["x_t"], i["g_mix"], x, x_lo, x_hi, i["w_feat"], i["w_tok"], feat, tok)
        hgrn_stage(nc, feat, tok, x_lo, x_hi, i["w_gates"], i["lb_logits"], i["hg_gain"], i["hg_state"], i["diag"], i["ident"], i["own"],
                   hgrn_t, o["hg_p"], o["hg_s"])
    attention_rows_stage(nc, tok, i["qk_norm"], i["ident"], o["kv_rows"], qkv, heads_t)
    bias_strip_stage(nc, i["rel_ext"], i["onehot"], qkv, i["win_cache"], strips, o["win_p"], o["win_s"])
    sample_attention_stage(nc, i["cache"], i["page_table"], i["win_cache"], heads_t, qkv, tok, strips, i["cmp_w1"], i["cmp_w2"],
                           i["cmp_pe"], i["qk_norm"], i["overlap"], i["rep"], i["ident"], sample_t)
    prompt_compress_stage(nc, tok, i["cmp_w1"], i["cmp_w2"], i["cmp_pe"], i["qk_norm"], i["ident"], cmp_kt, cmp_v)
    prompt_attention_stage(nc, heads_t, qkv, tok, strips, cmp_kt, cmp_v, i["flip"], i["ident"], attn_rows)
    s5_state_stage(nc, tok, i["s5_a_re"], i["s5_a_im"], i["s5_log_dt"], i["s5_b"], i["s5_c"], i["s5_d"], i["s5_h0"], i["ident"],
                   s5_rows, o["s5_p"], o["s5_s"])
    s5_glu_stage(nc, s5_rows, i["s5_w_glu"], i["ident"], s5_t)
    trunk_stage(nc, i["x_t"], feat, hgrn_t, s5_t, attn_rows, sample_t, i["w_branch"], i["w_out"], i["w_gate_up"], i["w_down"],
                i["g_ffn"], i["ident"], x1_t, o["y_t"])


def rel_buckets(dist):
    n = np.maximum(dist, 0)
    exact = N_BUCKETS // 2
    nf = np.maximum(n, 1).astype(np.float32)
    large = exact + (np.log(nf / np.float32(exact)) / np.float32(np.log(MAX_DIST / exact)) * np.float32(N_BUCKETS - exact)).astype(np.int32)
    return np.where(n < exact, n, np.minimum(large, N_BUCKETS - 1))


def shape_constants():
    f4 = np.float32
    dist = STRIP_AT - np.arange(STRIP)
    onehot = np.zeros((N_BUCKETS + 1, 2, STRIP), f4)
    for w in range(2):
        bad = (dist < 0) | ((dist >= WINDOW) if w else False)
        onehot[rel_buckets(dist), w, np.arange(STRIP)] = 1
        onehot[:, w, bad] = 0
        onehot[N_BUCKETS, w, bad] = NEG
    nb, ns = PAST // CMP_STRIDE - 1, PAST // 64 + 1
    cs, ss = np.arange(nb)[:, None] * CMP_STRIDE, np.arange(ns)[None] * 64
    overlap = np.zeros((2 * P, ns), f4)
    overlap[:nb] = (cs < ss + 64) & (cs + CMP_LEN > ss)
    row = np.arange(NH * ST)
    p = np.arange(P)
    return {
        "onehot": onehot,
        "overlap": np.ascontiguousarray(overlap.reshape(2, P, ns).transpose(1, 0, 2)),
        "rep": ((row[:, None] // (NR * ST) == row // (NR * ST)) & (row[:, None] % ST == row % ST)).astype(f4),
        "ident": np.eye(P, dtype=f4),
        "flip": np.ascontiguousarray(np.eye(P, dtype=f4)[::-1]),
        "diag": (p[:, None] // HC == p // HC).astype(f4),
        "own": (np.arange(SB * ST)[:, None] // ST == np.arange(SB)).astype(f4),
    }


def kernel(**inputs):
    import concourse.bacc as bacc
    from concourse.bass_utils import run_bass_kernel_spmd

    a = {name: np.asarray(v) for name, v in inputs.items()}
    con = np.ascontiguousarray

    def chunks(w, n=P):
        return con(w.reshape(w.shape[0] // P, P, w.shape[1] // n, n).transpose(2, 1, 0, 3))

    def columns(v):
        return con(v.reshape(-1, P).T)

    def pairs(v):
        r = v.reshape(NPR, 2, NST, *v.shape[2:])
        return con(np.moveaxis(r, 0, 2).reshape(P, NPR, *v.shape[2:]))

    x = np.concatenate([a["x_prompt"][0], a["x_sample"].reshape(SB * ST, D)])
    w_in = a["w_in"][0]
    widths = [512] * 6 + [128] * 6 + [24] + [D] * 3
    at = np.cumsum([0] + widths)
    hq, hf, hi, hg, su, nq, kc, vc, ksl, vsl, kwn, vwn, ngate, ga, gb, gc = (w_in[:, at[n]:at[n + 1]] for n in range(16))
    ins = {
        "x_t": con(x.T.reshape(KD, P, T).transpose(1, 0, 2)),
        "g_mix": columns(a["norm_mix"][0]),
        "w_feat": chunks(np.concatenate([hq, hf, hg], axis=1)),
        "w_gates": chunks(np.concatenate([ga, gb, gc], axis=1)),
        "w_tok": chunks(np.concatenate([su, hi, nq, kc, vc, ksl, vsl, kwn, vwn, ngate], axis=1), TOK_CHUNK),
        "qk_norm": con(a["nsa_qk_norm"][0]),
        "rel_ext": np.concatenate([a["rel_bias"], np.ones((1, NH), np.float32)]),
        "win_cache": con(a["cache_win_kv"][0].reshape(SB, WINDOW, 2 * P)),
        "cache": con(a["cache_nsa_kv"][0].reshape(-1, P, 4 * P)),
        "page_table": con(a["page_table"].reshape(1, -1)),
        "cmp_w1": con(a["cmp_w1"][0].reshape(2, 16, P, CMP_HID).transpose(2, 0, 1, 3)),
        "cmp_w2": con(a["cmp_w2"][0].transpose(1, 0, 2)),
        "cmp_pe": con(a["cmp_pe"][0].reshape(2, 16, P).transpose(2, 0, 1)),
        "lb_logits": columns(a["hg_lb_logits"][0]),
        "hg_gain": con(a["hg_out_norm"].reshape(P, 1)),
        "hg_state": con(a["state_hgrn"][0]),
        "s5_a_re": pairs(a["s5_a_re"][0]),
        "s5_a_im": pairs(a["s5_a_im"][0]),
        "s5_log_dt": pairs(np.broadcast_to(a["s5_log_dt"][0][:, None], (NGR, NST))),
        "s5_b": np.stack([pairs(a["s5_b_re"][0]), pairs(a["s5_b_im"][0])], axis=1),
        "s5_c": np.stack([pairs(a["s5_c_re"][0].transpose(0, 2, 1)), pairs(a["s5_c_im"][0].transpose(0, 2, 1))], axis=1),
        "s5_d": con(np.broadcast_to(a["s5_d"][0].reshape(NGR, GW).T[None], (SC, GW, NGR)).reshape(P, NGR)),
        "s5_h0": np.stack([pairs(a["state_s5_re"][0].transpose(1, 2, 0)), pairs(a["state_s5_im"][0].transpose(1, 2, 0))], axis=1),
        "s5_w_glu": con(a["s5_w_glu"][0]),
        "w_branch": con(a["w_branch"][0].reshape(3, 4, P, KD, P).transpose(3, 2, 0, 1, 4).reshape(KD, P, 12, P)),
        "w_out": chunks(a["w_out"][0]),
        "w_gate_up": con(a["w_gate_up"][0].reshape(KD, P, 2, KF, P).transpose(3, 1, 2, 0, 4).reshape(KF, P, 2 * KD, P)),
        "w_down": chunks(a["w_down"][0]),
        "g_ffn": columns(a["norm_ffn"][0]),
    }
    ins.update(shape_constants())
    outs = {
        "y_t": (D, T), "kv_rows": (T, 512), "win_p": (WINDOW, 2 * P), "win_s": (SB, WINDOW, 2 * P),
        "hg_p": (4, P, P), "hg_s": (SB, 4, P, P), "s5_p": (P, 2, NPR, 1), "s5_s": (P, 2, NPR, SB),
    }
    nc = bacc.Bacc("TRN2", target_bir_lowering=False, num_devices=1)
    i = {n: nc.dram_tensor(n + "_in", v.shape, mybir.dt.from_np(v.dtype), kind="ExternalInput").ap() for n, v in ins.items()}
    o = {n: nc.dram_tensor(n + "_out", s, F32, kind="ExternalOutput").ap() for n, s in outs.items()}
    build_program(nc, i, o)
    got = run_bass_kernel_spmd(nc, [{n + "_in": v for n, v in ins.items()}], core_ids=[0]).results[0]
    r = {n: got[n + "_out"] for n in outs}

    def unpair(v):
        return con(v.reshape(2, NST, NPR, -1).transpose(3, 2, 0, 1).reshape(1, -1, NGR, NST))

    y = r["y_t"].T
    return (
        con(y[:TP]).reshape(1, TP, D), con(y[TP:]).reshape(SB, ST, D),
        con(r["kv_rows"][:TP]).reshape(1, 1, TP, 4, NG, HD), con(r["kv_rows"][TP:]).reshape(1, SB, ST, 4, NG, HD),
        r["win_p"].reshape(1, 1, WINDOW, 2, NG, HD), r["win_s"].reshape(1, SB, WINDOW, 2, NG, HD),
        r["hg_p"].reshape(1, 1, 4, P, P), r["hg_s"].reshape(1, SB, 4, P, P),
        unpair(r["s5_p"][:, 0]), unpair(r["s5_p"][:, 1]), unpair(r["s5_s"][:, 0]), unpair(r["s5_s"][:, 1]),
    )
```
